# Optimizing a Trainium2 kernel written in Bass

```python
import jax, jax.numpy as jnp
from jax import lax
import numpy as np

D_MODEL = 1024
BATCH = 1
SEQ = 128
DEPTH = 1
DEC_BATCH = 1
DEC_SEQ = 2048
PAST_LEN = 128

GRID_W = 64
N_DIR = 2
D_MIX = D_MODEL
NORM_EPS = 1e-6
D_LRU = D_MIX // 4
LRU_BLOCKS = 4
LRU_BW = D_LRU // LRU_BLOCKS
CONV_W = 4
LRU_C = 8.0
D_RW = 3 * D_MIX // 8
RW_HD = 64
RW_HEADS = D_RW // RW_HD
RW_R_W = 64
RW_R_A = 64
RW_R_G = 128
RW_GN_EPS = 64e-5
D_GLA = D_MIX - D_LRU - D_RW
GLA_HEADS = 4
GLA_DV = D_GLA // GLA_HEADS
GLA_DK = GLA_DV // 2
D_GLA_K = GLA_HEADS * GLA_DK
GLA_R = 16
GLA_TAU = 16.0
GLA_CHUNK = 64
RW_COLS = 3 * D_RW + 2 * RW_R_W + 2 * RW_R_A + RW_R_G
GLA_COLS = 2 * D_GLA_K + 2 * D_GLA + N_DIR * GLA_R
N_IN = 2 * D_LRU + RW_COLS + GLA_COLS
N_EXPERTS = 16
D_EXPERT = 1024
EC_FACTOR = 2

kernel_name = 'hybrid_lru_rwkv7_gla_ec_moe_diffusion_step'

def _split(x, sizes):
    return jnp.split(x, np.cumsum(sizes)[:-1].tolist(), axis=-1)

def _rmsnorm(x, g):
    xf = x.astype(jnp.float32)
    y = xf * lax.rsqrt(jnp.mean(xf * xf, axis=-1, keepdims=True) + NORM_EPS)
    return (y * g.astype(jnp.float32)).astype(x.dtype)

def _bidir_shared(z):
    return jnp.stack([z, jnp.flip(z, 1)], 0)

def _bidir_split(z):
    return jnp.stack([z[:, :, 0], jnp.flip(z[:, :, 1], 1)], 0)

def _merge_dirs(o):
    return o[0] + jnp.flip(o[1], 1)

def _to_colmajor(z):
    B, L, C = z.shape
    rows = L // GRID_W
    return z.reshape(B, rows, GRID_W, C).transpose(0, 2, 1, 3).reshape(B, L, C)

def _from_colmajor(z):
    B, L, C = z.shape
    rows = L // GRID_W
    return z.reshape(B, GRID_W, rows, C).transpose(0, 2, 1, 3).reshape(B, L, C)

def _lin_combine(e1, e2):
    a1, b1 = e1
    a2, b2 = e2
    return a1 * a2, a2 * b1 + b2

def _rglru(xl, yl, p, h0):
    B, L, C = xl.shape
    f32 = jnp.float32
    pad = (CONV_W // 2, CONV_W - 1 - CONV_W // 2)
    xc = lax.conv_general_dilated(xl, p['lru_conv_w'][:, None, :], window_strides=(1,), padding=[pad],
                                  dimension_numbers=('NWC', 'WIO', 'NWC'), feature_group_count=C) + p['lru_conv_b']
    xs = _bidir_shared(xc)
    xb = xs.reshape(N_DIR, B, L, LRU_BLOCKS, LRU_BW)
    r = jax.nn.sigmoid(jnp.einsum('dblni,dnij->dblnj', xb, p['lru_wa']).reshape(N_DIR, B, L, C) + p['lru_ba'][:, None, None, :])
    i = jax.nn.sigmoid(jnp.einsum('dblni,dnij->dblnj', xb, p['lru_wx']).reshape(N_DIR, B, L, C) + p['lru_bx'][:, None, None, :])
    log_a = -LRU_C * r.astype(f32) * jax.nn.softplus(-p['lru_lambda'].astype(f32))[:, None, None, :]
    a = jnp.exp(log_a)
    u = jnp.sqrt(-jnp.expm1(2.0 * log_a)) * (i * xs).astype(f32)
    a_cum, u_cum = lax.associative_scan(_lin_combine, (a, u), axis=2)
    h = a_cum * jnp.moveaxis(h0.astype(f32), 1, 0)[:, :, None, :] + u_cum
    out = _merge_dirs(h) * jax.nn.gelu(yl.astype(f32))
    return out.astype(xl.dtype), jnp.moveaxis(h[:, :, -1], 0, 1)

def _rwkv7(cols, p, S0):
    B, L, _ = cols.shape
    f32 = jnp.float32
    prev = jnp.pad(cols, ((0, 0), (1, 0), (0, 0)))[:, :-1]
    nxt = jnp.pad(cols, ((0, 0), (0, 1), (0, 0)))[:, 1:]
    xs = cols + p['rw_mu'][0] * (prev - cols) + p['rw_mu'][1] * (nxt - cols)
    r, k, v, wd, ad, gd = _split(xs, (D_RW, D_RW, D_RW, N_DIR * RW_R_W, N_DIR * RW_R_A, RW_R_G))
    wd = wd.reshape(B, L, N_DIR, RW_R_W)
    ad = ad.reshape(B, L, N_DIR, RW_R_A)
    w_log = -jax.nn.softplus(-(p['rw_w0'] + jnp.einsum('bldr,drc->bldc', jnp.tanh(wd), p['rw_w2'])).astype(f32)) - 0.5
    decay = jnp.exp(-jnp.exp(w_log))
    a = jax.nn.sigmoid((p['rw_a0'] + jnp.einsum('bldr,drc->bldc', ad, p['rw_a2'])).astype(f32))
    g = jax.nn.sigmoid(gd) @ p['rw_g2']
    heads = lambda z: z.reshape(z.shape[:-1] + (RW_HEADS, RW_HD))
    r, k, v = r.astype(f32), k.astype(f32), v.astype(f32)
    kk = heads(k * p['rw_kk'])
    kk = kk * lax.rsqrt(jnp.sum(kk * kk, axis=-1, keepdims=True) + 1e-12)
    kd = k[:, :, None, :] * (1.0 + (a - 1.0) * p['rw_ka'])
    rh, vh, kdh = heads(r), heads(v), heads(kd)
    seq = (_bidir_shared(rh), _bidir_split(heads(decay)), _bidir_shared(kk),
           _bidir_split(heads(a)), _bidir_shared(vh), _bidir_split(kdh))
    seq = tuple(jnp.moveaxis(z, 2, 0) for z in seq)

    def step(S, inp):
        r_t, w_t, kk_t, a_t, v_t, k_t = inp
        sa = jnp.einsum('dbhij,dbhj->dbhi', S, -kk_t)
        S = S * w_t[..., None, :] + sa[..., None] * (kk_t * a_t)[..., None, :] + v_t[..., None] * k_t[..., None, :]
        return S, jnp.einsum('dbhij,dbhj->dbhi', S, r_t)

    S_fin, o = lax.scan(step, jnp.moveaxis(S0.astype(f32), 1, 0), seq)
    o = _merge_dirs(jnp.moveaxis(o, 0, 2))
    mu = jnp.mean(o, axis=-1, keepdims=True)
    var = jnp.mean(jnp.square(o - mu), axis=-1, keepdims=True)
    on = (o - mu) * lax.rsqrt(var + RW_GN_EPS) * heads(p['rw_ln_w']) + heads(p['rw_ln_b'])
    bonus = jnp.einsum('blhn,bldhn,dhn->blh', rh, kdh, p['rw_rk'])[..., None] * vh
    out = (on + bonus).reshape(B, L, D_RW) * g
    return out.astype(cols.dtype), jnp.moveaxis(S_fin, 0, 1)

def _gla(cols, p, S0):
    B, L, _ = cols.shape
    f32 = jnp.float32
    q, k, v, g, gd = _split(cols, (D_GLA_K, D_GLA_K, D_GLA, D_GLA, N_DIR * GLA_R))
    q = q.astype(f32).reshape(B, L, GLA_HEADS, GLA_DK) * (GLA_DK ** -0.5)
    k = k.astype(f32).reshape(B, L, GLA_HEADS, GLA_DK)
    v = v.astype(f32).reshape(B, L, GLA_HEADS, GLA_DV)
    la = jax.nn.log_sigmoid((jnp.einsum('bldr,drc->bldc', gd.reshape(B, L, N_DIR, GLA_R), p['gla_wg2'])
                             + p['gla_bg']).astype(f32)) / GLA_TAU
    la = la.reshape(B, L, N_DIR, GLA_HEADS, GLA_DK)
    n_chunks = L // GLA_CHUNK
    chunked = lambda z: jnp.moveaxis(z.reshape((N_DIR, B, n_chunks, GLA_CHUNK) + z.shape[3:]), 2, 0)
    seq = (chunked(_bidir_shared(q)), chunked(_bidir_shared(k)), chunked(_bidir_shared(v)), chunked(_bidir_split(la)))
    mask = jnp.tril(jnp.ones((GLA_CHUNK, GLA_CHUNK), dtype=bool))[:, :, None, None]

    def step(S, inp):
        qc, kc, vc, lac = inp
        b = jnp.cumsum(lac, axis=2)
        diff = b[:, :, :, None] - b[:, :, None, :]
        dec = jnp.exp(jnp.where(mask, diff, -jnp.inf))
        att = jnp.einsum('dbthk,dbshk,dbtshk->dbhts', qc, kc, dec)
        o = jnp.einsum('dbhts,dbshv->dbthv', att, vc) + jnp.einsum('dbthk,dbhkv->dbthv', qc * jnp.exp(b), S)
        bl = b[:, :, -1]
        S = S * jnp.exp(bl)[..., None] + jnp.einsum('dbshk,dbshv->dbhkv', kc * jnp.exp(bl[:, :, None] - b), vc)
        return S, o

    S_fin, o = lax.scan(step, jnp.moveaxis(S0.astype(f32), 1, 0), seq)
    o = jnp.moveaxis(o, 0, 2).reshape(N_DIR, B, L, GLA_HEADS, GLA_DV)
    o = _merge_dirs(o)
    o = o * lax.rsqrt(jnp.mean(o * o, axis=-1, keepdims=True) + NORM_EPS) * p['gla_norm_w']
    out = o.reshape(B, L, D_GLA) * jax.nn.silu(g.astype(f32))
    return out.astype(cols.dtype), jnp.moveaxis(S_fin, 0, 1)

def _mixers(h, p, states, grid):
    s_lru, s_rw, s_gla = states
    proj = h @ p['w_in']
    xl, yl, rw_cols, gla_cols = _split(proj, (D_LRU, D_LRU, RW_COLS, GLA_COLS))
    o_lru, n_lru = _rglru(xl, yl, p, s_lru)
    o_rw, n_rw = _rwkv7(rw_cols, p, s_rw)
    if grid:
        gla_cols = _to_colmajor(gla_cols)
    o_gla, n_gla = _gla(gla_cols, p, s_gla)
    if grid:
        o_gla = _from_colmajor(o_gla)
    out = jnp.concatenate([o_lru, o_rw, o_gla], axis=-1) @ p['w_out']
    return out, (n_lru, n_rw, n_gla)

def _expert_choice_ffn(h, p):
    B, N, D = h.shape
    cap = EC_FACTOR * N // N_EXPERTS
    probs = jax.nn.softmax((h @ p['w_router']).astype(jnp.float32), axis=-1)
    gates, idx = lax.top_k(jnp.swapaxes(probs, 1, 2), cap)
    xsel = jax.vmap(lambda hb, ib: hb[ib])(h, idx)
    hid = jax.nn.silu(jnp.einsum('becd,edf->becf', xsel, p['w_gate'])) * jnp.einsum('becd,edf->becf', xsel, p['w_up'])
    yo = jnp.einsum('becf,efd->becd', hid, p['w_down']) * gates[..., None].astype(h.dtype)
    return jax.vmap(lambda ib, yb: jnp.zeros((N, D), yb.dtype).at[ib.reshape(-1)].add(yb.reshape(-1, D)))(idx, yo)

def _layer(x, cvec, p, states, grid):
    mods = (jax.nn.silu(cvec) @ p['w_ada'] + p['b_ada'])[..., None, :]
    sh1, sc1, g1, sh2, sc2, g2 = jnp.split(mods, 6, axis=-1)
    h = _rmsnorm(x, p['norm1_g']) * (1 + sc1) + sh1
    o, new_states = _mixers(h, p, states, grid)
    x = x + g1 * o
    h = _rmsnorm(x, p['norm2_g']) * (1 + sc2) + sh2
    x = x + g2 * _expert_choice_ffn(h, p)
    return x, new_states

def setup_inputs(seed: int = 0) -> dict:
    key = jax.random.key(seed)
    ks = iter(jax.random.split(key, 48))
    f32 = jnp.float32
    nrm = lambda shape, scale: jax.random.normal(next(ks), shape, f32) * scale
    unif = lambda shape, lo, hi: jax.random.uniform(next(ks), shape, f32, lo, hi)
    u = unif((DEPTH, N_DIR, D_LRU), 0.9, 0.999)
    sig = u ** (1.0 / LRU_C)
    return {
        'x_prompt': nrm((BATCH, SEQ, D_MODEL), 1.0),
        'x_sample': nrm((DEC_BATCH, DEC_SEQ, D_MODEL), 1.0),
        'c': nrm((DEC_BATCH, D_MODEL), 1.0),
        'state_lru': nrm((DEC_BATCH, DEPTH, N_DIR, D_LRU), 0.5),
        'state_rwkv': nrm((DEC_BATCH, DEPTH, N_DIR, RW_HEADS, RW_HD, RW_HD), 0.1),
        'state_gla': nrm((DEC_BATCH, DEPTH, N_DIR, GLA_HEADS, GLA_DK, GLA_DV), 0.1),
        'c_ctx': nrm((D_MODEL,), 1.0),
        'norm1_g': 1.0 + nrm((DEPTH, D_MODEL), 0.05),
        'norm2_g': 1.0 + nrm((DEPTH, D_MODEL), 0.05),
        'w_ada': nrm((DEPTH, D_MODEL, 6 * D_MODEL), 0.5 * D_MODEL ** -0.5),
        'b_ada': nrm((DEPTH, 6 * D_MODEL), 0.05),
        'w_in': nrm((DEPTH, D_MODEL, N_IN), D_MODEL ** -0.5),
        'lru_conv_w': nrm((DEPTH, CONV_W, D_LRU), CONV_W ** -0.5),
        'lru_conv_b': nrm((DEPTH, D_LRU), 0.01),
        'lru_wa': nrm((DEPTH, N_DIR, LRU_BLOCKS, LRU_BW, LRU_BW), LRU_BW ** -0.5),
        'lru_ba': nrm((DEPTH, N_DIR, D_LRU), 0.01),
        'lru_wx': nrm((DEPTH, N_DIR, LRU_BLOCKS, LRU_BW, LRU_BW), LRU_BW ** -0.5),
        'lru_bx': nrm((DEPTH, N_DIR, D_LRU), 0.01),
        'lru_lambda': jnp.log(sig) - jnp.log1p(-sig),
        'rw_mu': unif((DEPTH, 2, RW_COLS), 0.0, 0.5),
        'rw_w0': unif((DEPTH, N_DIR, D_RW), -6.0, 1.0),
        'rw_w2': nrm((DEPTH, N_DIR, RW_R_W, D_RW), RW_R_W ** -0.5),
        'rw_a0': nrm((DEPTH, N_DIR, D_RW), 0.1),
        'rw_a2': nrm((DEPTH, N_DIR, RW_R_A, D_RW), RW_R_A ** -0.5),
        'rw_g2': nrm((DEPTH, RW_R_G, D_RW), RW_R_G ** -0.5),
        'rw_kk': 0.85 + nrm((DEPTH, D_RW), 0.05),
        'rw_ka': 1.0 + nrm((DEPTH, D_RW), 0.05),
        'rw_rk': nrm((DEPTH, N_DIR, RW_HEADS, RW_HD), 0.1),
        'rw_ln_w': 1.0 + nrm((DEPTH, D_RW), 0.05),
        'rw_ln_b': nrm((DEPTH, D_RW), 0.01),
        'gla_wg2': nrm((DEPTH, N_DIR, GLA_R, D_GLA_K), GLA_R ** -0.5),
        'gla_bg': nrm((DEPTH, N_DIR, D_GLA_K), 0.5),
        'gla_norm_w': 1.0 + nrm((DEPTH, GLA_HEADS, GLA_DV), 0.05),
        'w_out': nrm((DEPTH, D_MIX, D_MODEL), D_MIX ** -0.5),
        'w_router': nrm((DEPTH, D_MODEL, N_EXPERTS), D_MODEL ** -0.5),
        'w_gate': nrm((DEPTH, N_EXPERTS, D_MODEL, D_EXPERT), D_MODEL ** -0.5),
        'w_up': nrm((DEPTH, N_EXPERTS, D_MODEL, D_EXPERT), D_MODEL ** -0.5),
        'w_down': nrm((DEPTH, N_EXPERTS, D_EXPERT, D_MODEL), D_EXPERT ** -0.5),
        'final_norm_g': 1.0 + nrm((D_MODEL,), 0.05),
    }

def reference(x_prompt, x_sample, c, state_lru, state_rwkv, state_gla, c_ctx, norm1_g, norm2_g, w_ada, b_ada,
              w_in, lru_conv_w, lru_conv_b, lru_wa, lru_ba, lru_wx, lru_bx, lru_lambda, rw_mu, rw_w0, rw_w2,
              rw_a0, rw_a2, rw_g2, rw_kk, rw_ka, rw_rk, rw_ln_w, rw_ln_b, gla_wg2, gla_bg, gla_norm_w, w_out,
              w_router, w_gate, w_up, w_down, final_norm_g):
    def layer_params(l):
        return {'norm1_g': norm1_g[l], 'norm2_g': norm2_g[l], 'w_ada': w_ada[l], 'b_ada': b_ada[l],
                'w_in': w_in[l], 'lru_conv_w': lru_conv_w[l], 'lru_conv_b': lru_conv_b[l],
                'lru_wa': lru_wa[l], 'lru_ba': lru_ba[l], 'lru_wx': lru_wx[l], 'lru_bx': lru_bx[l],
                'lru_lambda': lru_lambda[l], 'rw_mu': rw_mu[l], 'rw_w0': rw_w0[l], 'rw_w2': rw_w2[l],
                'rw_a0': rw_a0[l], 'rw_a2': rw_a2[l], 'rw_g2': rw_g2[l], 'rw_kk': rw_kk[l], 'rw_ka': rw_ka[l],
                'rw_rk': rw_rk[l], 'rw_ln_w': rw_ln_w[l], 'rw_ln_b': rw_ln_b[l], 'gla_wg2': gla_wg2[l],
                'gla_bg': gla_bg[l], 'gla_norm_w': gla_norm_w[l], 'w_out': w_out[l], 'w_router': w_router[l],
                'w_gate': w_gate[l], 'w_up': w_up[l], 'w_down': w_down[l]}

    params = [layer_params(l) for l in range(DEPTH)]
    f32 = jnp.float32

    bp = x_prompt.shape[0]
    zero = (jnp.zeros((bp, N_DIR, D_LRU), f32),
            jnp.zeros((bp, N_DIR, RW_HEADS, RW_HD, RW_HD), f32),
            jnp.zeros((bp, N_DIR, GLA_HEADS, GLA_DK, GLA_DV), f32))
    xp = x_prompt
    ctx_states = []
    for l in range(DEPTH):
        xp, st = _layer(xp, c_ctx, params[l], zero, False)
        ctx_states.append(st)
    y_prompt = _rmsnorm(xp, final_norm_g)
    new_state_lru = jnp.stack([s[0] for s in ctx_states], axis=1).astype(x_prompt.dtype)
    new_state_rwkv = jnp.stack([s[1] for s in ctx_states], axis=1).astype(x_prompt.dtype)
    new_state_gla = jnp.stack([s[2] for s in ctx_states], axis=1).astype(x_prompt.dtype)

    xs = x_sample
    for l in range(DEPTH):
        xs, _ = _layer(xs, c, params[l], (state_lru[:, l], state_rwkv[:, l], state_gla[:, l]), True)
    y_sample = _rmsnorm(xs, final_norm_g)
    return (y_prompt, y_sample, new_state_lru, new_state_rwkv, new_state_gla)


_drawn_inputs = setup_inputs


def setup_inputs(seed=0):
    import zlib

    import numpy as np

    out = dict(_drawn_inputs(seed))
    spreads = {}
    factors = {'state_lru': 5.888,
     'state_rwkv': 8.0,
     'state_gla': 8.0,
     'norm2_g': 5.187,
     'lru_ba': 36.369,
     'lru_bx': 8.0,
     'rw_ln_w': 6.862,
     'rw_ln_b': 24.618,
     'gla_norm_w': 8.0}
    for name, (base, spread) in spreads.items():
        noise = np.random.default_rng([zlib.crc32(name.encode()), seed]).standard_normal(out[name].shape)
        drawn = base * np.exp(spread * noise) if base else spread * noise
        out[name] = __import__('jax').numpy.asarray(drawn.astype(out[name].dtype))
    for name, factor in factors.items():
        out[name] = (out[name] * factor).astype(out[name].dtype)
    return out
```

```python
from contextlib import ExitStack

import numpy as np

import concourse.bass as bass
from concourse import mybir

F32 = mybir.dt.float32
U32 = mybir.dt.uint32
ALU = mybir.AluOpType
ACT = mybir.ActivationFunctionType
AX = mybir.AxisListType

P = 128
D = 1024
KD = D // P
T_CTX, T_LAT = 128, 2048
T = T_CTX + T_LAT
GRID_W = 64
GRID_H = T_LAT // GRID_W
SEGS = ((0, T_CTX), (T_CTX, T_LAT))
BANK = 512
D_LRU = 256
RW_HEADS, RW_HD = 6, 64
D_RW = RW_HEADS * RW_HD
GLA_HEADS, GLA_DK, GLA_DV = 4, 48, 96
D_GLA = GLA_HEADS * GLA_DV
D_GLA_K = GLA_HEADS * GLA_DK
GLA_R = 16
RW0 = 2 * D_LRU
RW_LORA = RW0 + 3 * D_RW
GLA0 = RW_LORA + 3 * P
N_IN = GLA0 + 2 * D_GLA_K + 2 * D_GLA + 2 * GLA_R
C = 64
NCH = T // C
NCH_CTX = T_CTX // C
LEVELS = 6
REC = 1 + 5 * C
N_EXP, D_EXP = 16, 1024
CAP_LAT, CAP_CTX = 2 * T_LAT // N_EXP, 2 * T_CTX // N_EXP
EPS = 1e-6
TOK_BLOCKS = [(b, min(BANK, T - b)) for b in range(0, T, BANK)]


class Stage:

    def __init__(self, nc, name):
        self.nc, self.name, self.stack, self.sems = nc, name, ExitStack(), {}

    def __enter__(self):
        return self

    def __exit__(self, *_):
        self.stack.close()
        self.nc.clear_and_free_semaphores(list(self.sems.values()))
        self.nc.all_engine_barrier()

    def sb(self, name, shape, dt=F32):
        return self.stack.enter_context(self.nc.sbuf_tensor(f"{self.name}_{name}", shape, dt))

    def ps(self, name, shape=(P, BANK)):
        return self.stack.enter_context(self.nc.psum_tensor(f"{self.name}_{name}", list(shape), F32))

    def sem(self, name):
        self.sems[name] = self.nc.alloc_semaphore(name=f"{self.name}_{name}")
        return self.sems[name]

    def sem2(self, name):
        return [self.sem(f"{name}_{u}") for u in range(2)]

    def block(self):
        return self.nc.Block()


def stage_modulation(nc, c, c_ctx, w_ada, b_ada, mods):
    NB = 6 * D // BANK
    with Stage(nc, "mod") as st:
        cvec, sil = st.sb("cvec", [P, 2, KD]), st.sb("sil", [P, KD, 2])
        w = [st.sb(f"w{u}", [P, KD, BANK]) for u in range(2)]
        bias, out = st.sb("bias", [2, 6 * D]), st.sb("out", [2, 6 * D])
        acc = [st.ps(f"acc{u}") for u in range(2)]
        cvec_in, bias_in, silu_done = st.sem("cvec_in"), st.sem("bias_in"), st.sem("silu_done")
        w_in, product, biased = st.sem2("w_in"), st.sem2("product"), st.sem2("biased")
        stored = st.sem("stored")
        wv = w_ada[0].rearrange("(p k) n -> p k n", k=KD)
        with st.block() as block:
            @block.sync
            def _(sp):
                sp.dma_start(cvec[:, 0, :], c_ctx.rearrange("(p k) -> p k", k=KD)).then_inc(cvec_in, 16)
                sp.dma_start(cvec[:, 1, :], c[0].rearrange("(p k) -> p k", k=KD)).then_inc(cvec_in, 16)
                for v in range(2):
                    sp.dma_start(bias[v:v + 1, :], b_ada).then_inc(bias_in, 16)
                with sp.Fori(0, NB // 2) as i:
                    for u in range(2):
                        sp.wait_ge(product[u], i)
                        sp.dma_start(w[u][:, :, :], wv[:, :, bass.ds((2 * i + u) * BANK, BANK)]).then_inc(w_in[u], 16)
                for u in range(2):
                    sp.wait_ge(biased[u], NB // 2)
                sp.dma_start(mods, out[:, :]).then_inc(stored, 16)
                sp.wait_ge(stored, 16)

            @block.scalar
            def _(act):
                act.wait_ge(cvec_in, 32)
                act.activation(sil[:, :, :], cvec[:, :, :].rearrange("p v k -> p k v"), ACT.Silu).then_inc(silu_done, 1)

            @block.tensor
            def _(pe):
                pe.wait_ge(silu_done, 1)
                with pe.Fori(0, NB // 2) as i:
                    for u in range(2):
                        pe.wait_ge(w_in[u], 16 * i + 16)
                        pe.wait_ge(biased[u], i)
                        for k in range(KD):
                            mm = pe.matmul(acc[u][0:2, :], sil[:, k, :], w[u][:, k, :], start=k == 0, stop=k == KD - 1)
                        mm.then_inc(product[u], 1)

            @block.vector
            def _(dve):
                dve.wait_ge(bias_in, 32)
                with dve.Fori(0, NB // 2) as i:
                    for u in range(2):
                        cols = bass.ds((2 * i + u) * BANK, BANK)
                        dve.wait_ge(product[u], i + 1)
                        dve.tensor_tensor(out[:, cols], acc[u][0:2, :], bias[:, cols], ALU.add).then_inc(biased[u], 1)


def paired(eng, body, pairs):
    body(0, 1, 0, 0)
    with eng.Fori(0, pairs) as i:
        body(0, i + 2, 2 * i + 1, 1)
        body(1, i + 1, 2 * i + 2, 1)


def load_modulated_norm(sp, st_sem, rows, mods, norm_g, scale_col, shift_col):
    g_row, scale_row, shift_row = rows
    sp.dma_start(g_row[:, :], norm_g.to_broadcast([P, D])).then_inc(st_sem, 16)
    for v in range(2):
        sp.dma_start(scale_row[:, v, :], mods[v:v + 1, scale_col * D:(scale_col + 1) * D].to_broadcast([P, D])).then_inc(st_sem, 16)
        sp.dma_start(shift_row[:, v, :], mods[v:v + 1, shift_col * D:(shift_col + 1) * D].to_broadcast([P, D])).then_inc(st_sem, 16)


def stage_project(nc, x_prompt, x_sample, norm1_g, mods, w_in, ident_d, proj):
    CT = N_IN // P
    REM = N_IN - CT * P
    with Stage(nc, "proj") as st:
        hT = st.sb("hT", [P, KD, T])
        ident = st.sb("ident", [P, P])
        g_row, scale_row, shift_row = st.sb("g", [P, D]), st.sb("scale", [P, 2, D]), st.sb("shift", [P, 2, D])
        x = [st.sb(f"x{u}", [P, D]) for u in range(2)]
        h = [st.sb(f"h{u}", [P, D]) for u in range(2)]
        ss = [st.sb(f"ss{u}", [P, 4]) for u in range(2)]
        w = [st.sb(f"w{u}", [P, KD, P]) for u in range(2)]
        out = [st.sb(f"out{u}", [P, T]) for u in range(2)]
        ps_t = [st.ps(f"t{u}", [P, D // 2]) for u in range(2)]
        ps = [st.ps(f"acc{b}") for b in range(len(TOK_BLOCKS))]
        rows_in, ident_in, rows_ready, scaled1 = st.sem("rows_in"), st.sem("ident_in"), st.sem("rows_ready"), st.sem("scaled1")
        x_in, sumsq, meansq, root, rstd = (st.sem2(n) for n in ("x_in", "sumsq", "meansq", "root", "rstd"))
        normed, h_ready = st.sem2("normed"), st.sem2("h_ready")
        turned, kept = st.sem2("turned"), st.sem2("kept")
        w_ld, block_done = st.sem2("w_ld"), st.sem2("block_done")
        block_out = [st.sem(f"block_out{b}") for b in range(len(TOK_BLOCKS))]
        stored = st.sem2("stored")
        wv = w_in[0].rearrange("(k p) n -> p k n", p=P)
        NBLK = len(TOK_BLOCKS)

        def x_tile(tile, seg):
            return x_prompt[0] if seg == 0 else x_sample[0, bass.ds((tile - 1) * P, P), :]

        PAIRS = CT // 2
        TAIL = [(0, PAIRS + 1, CT - 1, P), (1, PAIRS + 1, CT, REM)]
        assert CT % 2 == 1 and REM

        def column_tiles(eng, body):
            with eng.Fori(0, PAIRS) as i:
                body(0, i + 1, 2 * i, P)
                body(1, i + 1, 2 * i + 1, P)
            for t in TAIL:
                body(*t)

        with st.block() as block:
            @block.sync
            def _(sp):
                sp.dma_start(ident[:, :], ident_d).then_inc(ident_in, 16)
                load_modulated_norm(sp, rows_in, (g_row, scale_row, shift_row), mods, norm1_g, 1, 0)

                def load_x(u, n, tile, seg):
                    sp.wait_ge(normed[u], n - 1)
                    sp.dma_start(x[u][:, :], x_tile(tile, seg)).then_inc(x_in[u], 16)
                paired(sp, load_x, 8)

                def store(u, n, ct, width):
                    for b in range(NBLK):
                        sp.wait_ge(block_out[b], ct + 1)
                    sp.dma_start(proj[bass.ds(ct * P, width), :], out[u][0:width, :]).then_inc(stored[u], 16)
                column_tiles(sp, store)
                for u in range(2):
                    sp.wait_ge(stored[u], 16 * (PAIRS + 1))

            @block.gpsimd
            def _(pool):
                def load_w(u, n, ct, width):
                    pool.wait_ge(ident_in, 16)
                    pool.wait_ge(block_done[u], NBLK * (n - 1))
                    pool.dma_start(w[u][:, :, 0:width], wv[:, :, bass.ds(ct * P, width)]).then_inc(w_ld[u], 16)
                column_tiles(pool, load_w)

            @block.scalar
            def _(act):
                def norm(u, n, tile, seg):
                    act.wait_ge(x_in[u], 16 * n)
                    act.wait_ge(normed[u], n - 1)
                    act.wait_ge(turned[u], 2 * n - 2)
                    act.activation(h[u][:, :], x[u][:, :], ACT.Square, accum_out=ss[u][:, 0:1]).then_inc(sumsq[u], 1)
                    act.wait_ge(meansq[u], n)
                    act.activation(ss[u][:, 2:3], ss[u][:, 1:2], ACT.Sqrt).then_inc(root[u], 1)
                    act.wait_ge(turned[u], 2 * n)
                    act.copy(hT[:, 4:8, bass.ds(tile * P, P)], ps_t[1][:, :].rearrange("p (k t) -> p k t", k=4)).then_inc(kept[1], 1)
                paired(act, norm, 8)

                def evacuate(u, n, ct, width):
                    act.wait_ge(stored[u], 16 * n - 16)
                    for b in range(0, NBLK, 2):
                        t0, tn = TOK_BLOCKS[b]
                        act.wait_ge(block_done[u], NBLK * (n - 1) + b + 1)
                        act.copy(out[u][0:width, t0:t0 + tn], ps[b][0:width, 0:tn]).then_inc(block_out[b], 1)
                column_tiles(act, evacuate)

            @block.vector
            def _(dve):
                dve.wait_ge(rows_in, 5 * 16)
                for v in range(2):
                    dve.scalar_tensor_tensor(scale_row[:, v, :], scale_row[:, v, :], 1.0, g_row[:, :], ALU.add, ALU.mult).then_inc(rows_ready, 1)

                def norm(u, n, tile, seg):
                    dve.wait_ge(sumsq[u], n)
                    dve.tensor_scalar(ss[u][:, 1:2], ss[u][:, 0:1], 1.0 / D, EPS, ALU.mult, ALU.add).then_inc(meansq[u], 1)
                    dve.wait_ge(root[u], n)
                    dve.reciprocal(ss[u][:, 3:4], ss[u][:, 2:3]).then_inc(rstd[u], 1)
                    dve.wait_ge(rstd[u], n)
                    dve.wait_ge(rows_ready, 2)
                    dve.scalar_tensor_tensor(h[u][:, :], x[u][:, :], ss[u][:, 3:4], scale_row[:, seg, :], ALU.mult, ALU.mult).then_inc(normed[u], 1)
                    dve.wait_ge(normed[u], n)
                    dve.tensor_tensor(h[u][:, :], h[u][:, :], shift_row[:, seg, :], ALU.add).then_inc(h_ready[u], 1)
                    dve.wait_ge(turned[u], 2 * n - 1)
                    dve.tensor_copy(hT[:, 0:4, bass.ds(tile * P, P)], ps_t[0][:, :].rearrange("p (k t) -> p k t", k=4)).then_inc(kept[0], 1)
                paired(dve, norm, 8)

                def evacuate(u, n, ct, width):
                    dve.wait_ge(stored[u], 16 * n - 16)
                    for b in range(1, NBLK, 2):
                        t0, tn = TOK_BLOCKS[b]
                        dve.wait_ge(block_done[u], NBLK * (n - 1) + b + 1)
                        dve.tensor_copy(out[u][0:width, t0:t0 + tn], ps[b][0:width, 0:tn]).then_inc(block_out[b], 1)
                column_tiles(dve, evacuate)

            @block.tensor
            def _(pe):
                pe.wait_ge(ident_in, 16)

                def turn(u, n, tile, seg):
                    pe.wait_ge(h_ready[u], n)
                    for half in range(2):
                        pe.wait_ge(kept[half], tile)
                        for k in range(4):
                            mm = pe.transpose(ps_t[half][:, k * P:(k + 1) * P], h[u][:, (4 * half + k) * P:(4 * half + k + 1) * P], ident[:, :])
                        mm.then_inc(turned[u], 1)
                paired(pe, turn, 8)
                for half in range(2):
                    pe.wait_ge(kept[half], T // P)

                def product(u, n, ct, width):
                    pe.wait_ge(w_ld[u], 16 * n)
                    for b, (t0, tn) in enumerate(TOK_BLOCKS):
                        pe.wait_ge(block_out[b], ct)
                        for k in range(KD):
                            mm = pe.matmul(ps[b][0:width, 0:tn], w[u][:, k, 0:width], hT[:, k, t0:t0 + tn], start=k == 0, stop=k == KD - 1)
                        mm.then_inc(block_done[u], 1)
                column_tiles(pe, product)


def stage_lru(nc, proj, conv_w, conv_b, wa, ba, wx, bx, lam, h0, mixT, new_state):
    NT = D_LRU // P
    with Stage(nc, "lru") as st:
        xl, yl, xc = st.sb("xl", [P, T]), st.sb("yl", [P, T]), st.sb("xc", [P, T])
        sig = st.sb("sig", [P, 2, 2, T])
        a = st.sb("a", [P, 2, T])
        tanh = st.sb("tanh", [P, 2, T])
        hid = st.sb("hid", [P, 2, T])
        par = st.sb("par", [P, 4 + 1 + 2 + 2 + 2 + 2])
        cw, cb, bias, lm, st0 = par[:, 0:4], par[:, 4:5], par[:, 5:9], par[:, 9:11], par[:, 11:13]
        sp_t = st.sb("sp_t", [P, 6, 2])
        bd = st.sb("bd", [P, 2, 2, P])
        bank = [st.ps(f"b{b}") for b in range(len(TOK_BLOCKS))]
        zeroed, ld, wts_in = st.sem("zeroed"), st.sem("ld"), st.sem("wts_in")
        conv, soft, gate_mm = st.sem("conv"), st.sem("soft"), st.sem("gate_mm")
        gated = [st.sem(f"gated{b}") for b in range(len(TOK_BLOCKS))]
        lam_abs, lam_exp = st.sem("lam_abs"), st.sem("lam_exp")
        decay_done, tanh_done, square_done, under_root, root_done = (st.sem(n) for n in (
            "decay_done", "tanh_done", "square_done", "under_root", "root_done"))
        drive, scanned, summed, gelu_done, out_done = (st.sem(n) for n in ("drive", "scanned", "summed", "gelu_done", "out_done"))
        stored = st.sem("stored")
        SERIES = 9
        N_CONV = 7
        N_LD = 2 + 1 + 1 + 4 + 2 + 2
        N_SOFT = 4 + SERIES + 3
        N_ST = 1 + 2

        def chan(v, i):
            return v[bass.ds(i * P, P)]

        with st.block() as block:
            @block.sync
            def _(sp):
                with sp.Fori(0, NT) as i:
                    sp.wait_ge(stored, 16 * N_ST * i)
                    sp.dma_start(xl[:, :], proj[bass.ds(i * P, P), :]).then_inc(ld, 16)
                    sp.dma_start(yl[:, :], proj[bass.ds(D_LRU + i * P, P), :]).then_inc(ld, 16)
                    sp.dma_start(cw, conv_w[0, :, bass.ds(i * P, P)].rearrange("w p -> p w"), allow_slow_non_contiguous=True).then_inc(ld, 16)
                    sp.dma_start(cb, chan(conv_b[0], i).unsqueeze(1)).then_inc(ld, 16)
                    for d in range(2):
                        sp.dma_start(bias[:, 2 * d:2 * d + 1], chan(ba[0, d], i).unsqueeze(1)).then_inc(ld, 16)
                        sp.dma_start(bias[:, 2 * d + 1:2 * d + 2], chan(bx[0, d], i).unsqueeze(1)).then_inc(ld, 16)
                        sp.dma_start(lm[:, d:d + 1], chan(lam[0, d], i).unsqueeze(1)).then_inc(ld, 16)
                        sp.dma_start(st0[:, d:d + 1], chan(h0[0, 0, d], i).unsqueeze(1)).then_inc(ld, 16)
                    sp.wait_ge(zeroed, 1)
                    for d in range(2):
                        for g, wt in enumerate((wa, wx)):
                            for n in range(2):
                                sp.dma_start(bd[64 * n:64 * n + 64, d, g, 64 * n:64 * n + 64],
                                             wt[0, d, bass.ds(2 * i + n, 1)].squeeze(0)).then_inc(wts_in, 16)
                    sp.wait_ge(out_done, i + 1)
                    sp.dma_start(mixT[bass.ds(i * P, P), :], xc[:, :]).then_inc(stored, 16)
                    for d, t in ((0, T_CTX - 1), (1, 0)):
                        sp.dma_start(chan(new_state[0, 0, d], i).unsqueeze(1), hid[:, d, t:t + 1]).then_inc(stored, 16)
                sp.wait_ge(stored, 16 * N_ST * NT)

            @block.gpsimd
            def _(pool):
                pool.memset(bd[:, :, :, :], 0.0).then_inc(zeroed, 1)

            @block.scalar
            def _(act):
                with act.Fori(0, NT) as i:
                    act.wait_ge(ld, 16 * N_LD * (i + 1))
                    act.activation(sp_t[:, 0, :], lm, ACT.Abs).then_inc(lam_abs, 1)
                    act.wait_ge(lam_abs, i + 1)
                    act.activation(sp_t[:, 1, :], sp_t[:, 0, :], ACT.Exp, scale=-1.0).then_inc(lam_exp, 1)
                    for d in range(2):
                        for g in range(2):
                            for b, (t0, tn) in enumerate(TOK_BLOCKS):
                                act.wait_ge(gate_mm, (4 * i + 2 * d + g) * len(TOK_BLOCKS) + b + 1)
                                act.activation(sig[:, d, g, t0:t0 + tn], bank[b][:, 0:tn], ACT.Sigmoid,
                                               bias=bias[:, 2 * d + g:2 * d + g + 1]).then_inc(gated[b], 1)
                    act.wait_ge(soft, N_SOFT * (i + 1))
                    for b in range(len(TOK_BLOCKS)):
                        act.wait_ge(gated[b], 4 * i + 4)
                    for d in range(2):
                        act.activation(a[:, d, :], sig[:, d, 0, :], ACT.Exp, scale=sp_t[:, 4, d:d + 1]).then_inc(decay_done, 1)
                    for d in range(2):
                        act.activation(tanh[:, d, :], sig[:, d, 0, :], ACT.Tanh, scale=sp_t[:, 5, d:d + 1]).then_inc(tanh_done, 1)
                    act.wait_ge(decay_done, 2 * i + 2)
                    act.wait_ge(tanh_done, 2 * i + 2)
                    for d in range(2):
                        act.activation(sig[:, d, 0, :], a[:, d, :], ACT.Square).then_inc(square_done, 1)
                    for d in range(2):
                        act.wait_ge(under_root, 2 * i + d + 1)
                        act.activation(tanh[:, d, :], sig[:, d, 0, :], ACT.Sqrt).then_inc(root_done, 1)
                    act.activation(yl[:, :], yl[:, :], ACT.Gelu_apprx_tanh).then_inc(gelu_done, 1)

            @block.tensor
            def _(pe):
                with pe.Fori(0, NT) as i:
                    pe.wait_ge(wts_in, 16 * 8 * (i + 1))
                    pe.wait_ge(conv, N_CONV * (i + 1))
                    for d in range(2):
                        for g in range(2):
                            for b, (t0, tn) in enumerate(TOK_BLOCKS):
                                pe.wait_ge(gated[b], 4 * i + 2 * d + g)
                                pe.matmul(bank[b][:, 0:tn], bd[:, d, g, :], xc[:, t0:t0 + tn], start=True, stop=True).then_inc(gate_mm, 1)

            @block.vector
            def _(dve):
                with dve.Fori(0, NT) as i:
                    dve.wait_ge(ld, 16 * N_LD * (i + 1))
                    dve.tensor_scalar(xc[:, :], xl[:, :], cw[:, 2:3], cb, ALU.mult, ALU.add).then_inc(conv, 1)
                    k = 1
                    for s, n in SEGS:
                        for w in (0, 1, 3):
                            o = w - 2
                            lo, hi = max(s, s - o), min(s + n, s + n - o)
                            dve.wait_ge(conv, N_CONV * i + k)
                            dve.scalar_tensor_tensor(xc[:, lo:hi], xl[:, lo + o:hi + o], cw[:, w:w + 1], xc[:, lo:hi],
                                                     ALU.mult, ALU.add).then_inc(conv, 1)
                            k += 1
                    e, y, y2, acc, neg, pos = sp_t[:, 1, :], sp_t[:, 0, :], sp_t[:, 2, :], sp_t[:, 3, :], sp_t[:, 4, :], sp_t[:, 5, :]
                    k = 0

                    def step(ins):
                        nonlocal k
                        k += 1
                        ins.then_inc(soft, 1)
                        dve.wait_ge(soft, N_SOFT * i + k)
                    dve.wait_ge(lam_exp, i + 1)
                    step(dve.tensor_scalar(y2, e, 2.0, None, ALU.add))
                    step(dve.reciprocal(acc, y2))
                    step(dve.tensor_tensor(y, e, acc, ALU.mult))
                    step(dve.tensor_tensor(y2, y, y, ALU.mult))
                    step(dve.tensor_scalar(acc, y2, 1.0 / (2 * SERIES - 1), None, ALU.mult))
                    for m in range(SERIES - 2, -1, -1):
                        step(dve.scalar_tensor_tensor(acc, acc, 1.0 / (2 * m + 1), y2 if m else y, ALU.add, ALU.mult))
                    step(dve.tensor_scalar(pos, lm, -8.0, 0.0, ALU.mult, ALU.max))
                    step(dve.scalar_tensor_tensor(pos, acc, 16.0, pos, ALU.mult, ALU.add))
                    step(dve.tensor_scalar(neg, pos, -1.0, None, ALU.mult))
                    assert k == N_SOFT, k
                    for d in range(2):
                        dve.wait_ge(square_done, 2 * i + d + 1)
                        dve.scalar_tensor_tensor(sig[:, d, 0, :], sig[:, d, 0, :], 1.0, tanh[:, d, :], ALU.add, ALU.mult).then_inc(under_root, 1)
                        dve.tensor_tensor(hid[:, d, :], sig[:, d, 1, :], xc[:, :], ALU.mult).then_inc(drive, 1)
                    for d in range(2):
                        dve.wait_ge(root_done, 2 * i + d + 1)
                        dve.wait_ge(drive, 4 * i + 2 + d)
                        dve.tensor_tensor(sig[:, d, 1, :], hid[:, d, :], tanh[:, d, :], ALU.mult).then_inc(drive, 1)
                    dve.wait_ge(drive, 4 * i + 4)
                    for d in range(2):
                        for g, (s, n) in enumerate(SEGS):
                            way = slice(s, s + n) if d == 0 else slice(s + n - 1, s - 1 if s else None, -1)
                            dve.tensor_tensor_scan(hid[:, d, way], a[:, d, way], sig[:, d, 1, way],
                                                   st0[:, d:d + 1] if g else 0.0, ALU.mult, ALU.add).then_inc(scanned, 1)
                    dve.wait_ge(scanned, 4 * i + 4)
                    dve.tensor_tensor(sig[:, 0, 0, :], hid[:, 0, :], hid[:, 1, :], ALU.add).then_inc(summed, 1)
                    dve.wait_ge(summed, i + 1)
                    dve.wait_ge(gelu_done, i + 1)
                    dve.tensor_tensor(xc[:, :], sig[:, 0, 0, :], yl[:, :], ALU.mult).then_inc(out_done, 1)


def scan_order(ap, d, s, n):
    return ap[:, s:s + n] if d == 0 else ap[:, slice(s + n - 1, s - 1 if s else None, -1)]


def in_chunks(ap):
    return ap.rearrange("p (c t) -> p c t", t=C)


def stage_rwkv_prep(nc, proj, mu, w0, w2, a0, a2, g2, kkw, kaw, rk, blockones_d, rec, gate, bonus):
    RATE = float(2.718281828459045 ** -0.5)
    HP = D_RW // P
    NBLK = len(TOK_BLOCKS)
    with Stage(nc, "rwp") as st:
        raw = [st.sb(f"raw{j}", [P, T]) for j in range(3)]
        lora = [st.sb(f"lora{j}", [P, T]) for j in range(3)]
        r, k, v = (st.sb(n, [P, T]) for n in ("r", "k", "v"))
        sg, cum, eb, ebm, ebi, bs = (st.sb(n, [P, T]) for n in ("sg", "cum", "eb", "ebm", "ebi", "bs"))
        kk, kd, av = raw
        recs = st.sb("recs", [P, NCH, REC])
        keep = st.sb("keep", [P, T])
        mus = st.sb("mus", [P, 3, 3])
        par = st.sb("par", [P, 10])
        p_kk, p_ka, p_rk, p_w0, p_a0, p_1ka = par[:, 0:1], par[:, 1:2], par[:, 2:4], par[:, 4:6], par[:, 6:8], par[:, 8:9]
        tiny = st.sb("tiny", [P, 1])
        w2s, a2s, g2s, ones = (st.sb(n, [P, P]) for n in ("w2s", "a2s", "g2s", "ones"))
        bank = [st.ps(f"b{b}") for b in range(NBLK)]
        const_in, consts, lora_in, lora_mu, lora_mixed, lora_act = (st.sem(n) for n in (
            "const_in", "consts", "lora_in", "lora_mu", "lora_mixed", "lora_act"))
        ld, coef, mixed, product = st.sem("ld"), st.sem("coef"), st.sem("mixed"), st.sem("product")
        freed = [st.sem(f"freed{b}") for b in range(NBLK)]
        gate_ready, kk_raw, squares, norm_root, kk_ready = (st.sem(n) for n in ("gate_ready", "kk_raw", "squares", "norm_root", "kk_ready"))
        sig_ready, a_ready, cum_ready, arg_ready, exps, kd_step = (st.sem(n) for n in (
            "sig_ready", "a_ready", "cum_ready", "arg_ready", "exps", "kd_step"))
        rec_dve, rec_pool, rec_act, rec_stored, bonus_step, bonus_out = (st.sem(n) for n in (
            "rec_dve", "rec_pool", "rec_act", "rec_stored", "bonus_step", "bonus_out"))
        gate_stored, bonus_stored = st.sem("gate_stored"), st.sem("bonus_stored")
        N_LD = 3 + 6 + 2 + 6 + 5
        N_COEF = 2
        JOBS = 7

        def column(vec, c0):
            return vec[bass.ds(c0, P)].unsqueeze(1)

        def shift_mix(eng, out, x, m, done, base):
            eng.tensor_scalar(out[:, :], x[:, :], m[:, 2:3], None, ALU.mult).then_inc(done, 1)
            q = 1
            for s, n in SEGS:
                eng.wait_ge(done, base + q)
                eng.scalar_tensor_tensor(out[:, s + 1:s + n], x[:, s:s + n - 1], m[:, 0:1], out[:, s + 1:s + n], ALU.mult, ALU.add).then_inc(done, 1)
                eng.wait_ge(done, base + q + 1)
                eng.scalar_tensor_tensor(out[:, s:s + n - 1], x[:, s + 1:s + n], m[:, 1:2], out[:, s:s + n - 1], ALU.mult, ALU.add).then_inc(done, 1)
                q += 2
        MIX = 5

        with st.block() as block:
            @block.sync
            def _(sp):
                sp.dma_start(ones[:, :], blockones_d).then_inc(const_in, 16)
                for j in range(3):
                    c0 = 3 * D_RW + j * P
                    sp.dma_start(raw[j][:, :], proj[RW0 + c0:RW0 + c0 + P, :]).then_inc(lora_in, 16)
                    for m in range(2):
                        sp.dma_start(mus[:, j, m:m + 1], column(mu[0, m], c0)).then_inc(lora_in, 16)
                with sp.Fori(0, HP) as i:
                    c0 = i * P
                    sp.wait_ge(bonus_out, NBLK * i)
                    sp.wait_ge(lora_mixed, 3 * MIX)
                    for j in range(3):
                        sp.dma_start(raw[j][:, :], proj[bass.ds(RW0 + j * D_RW + c0, P), :]).then_inc(ld, 16)
                        for m in range(2):
                            sp.dma_start(mus[:, j, m:m + 1], column(mu[0, m], j * D_RW + c0)).then_inc(ld, 16)
                    sp.dma_start(p_kk, column(kkw[0], c0)).then_inc(ld, 16)
                    sp.dma_start(p_ka, column(kaw[0], c0)).then_inc(ld, 16)
                    for d in range(2):
                        sp.dma_start(p_rk[:, d:d + 1], column(rk[0, d].rearrange("h n -> (h n)"), c0)).then_inc(ld, 16)
                        sp.dma_start(p_w0[:, d:d + 1], column(w0[0, d], c0)).then_inc(ld, 16)
                        sp.dma_start(p_a0[:, d:d + 1], column(a0[0, d], c0)).then_inc(ld, 16)
                    for d in range(2):
                        sp.dma_start(w2s[64 * d:64 * d + 64, :], w2[0, d, :, bass.ds(c0, P)]).then_inc(ld, 16)
                        sp.dma_start(a2s[64 * d:64 * d + 64, :], a2[0, d, :, bass.ds(c0, P)]).then_inc(ld, 16)
                    sp.dma_start(g2s[:, :], g2[0, :, bass.ds(c0, P)]).then_inc(ld, 16)
                    sp.wait_ge(gate_ready, NBLK * (i + 1))
                    sp.dma_start(gate[bass.ds(c0, P), :], ebi[:, :]).then_inc(gate_stored, 16)
                    for d in range(2):
                        for part in (rec_dve, rec_pool, rec_act):
                            sp.wait_ge(part, 2 * i + d + 1)
                        sp.dma_start(rec[bass.ds(d * HP + i, 1)].squeeze(0), recs[:, :, :]).then_inc(rec_stored, 16)
                    sp.wait_ge(bonus_out, NBLK * (i + 1))
                    sp.dma_start(bonus[bass.ds(c0, P), :], bs[:, :]).then_inc(bonus_stored, 16)
                sp.wait_ge(gate_stored, 16 * HP)
                sp.wait_ge(bonus_stored, 16 * HP)
                sp.wait_ge(rec_stored, 16 * 2 * HP)

            @block.gpsimd
            def _(pool):
                pool.memset(keep[:, :], 1.0).then_inc(consts, 1)
                pool.memset(tiny[:, :], 1e-12).then_inc(consts, 1)
                pool.wait_ge(consts, 2)
                pool.memset(in_chunks(keep[:, :])[:, :, 0:1], 0.0).then_inc(consts, 1)
                with pool.Fori(0, HP) as i:
                    for d in range(2):
                        pool.wait_ge(kd_step, 3 * (2 * i + d) + 3)
                        pool.wait_ge(exps, 3 * (2 * i + d) + 3)
                        pool.wait_ge(rec_stored, 16 * (2 * i + d))
                        pool.wait_ge(consts, 3)
                        pool.tensor_tensor(recs[:, :, 1 + 3 * C:1 + 4 * C], in_chunks(kd[:, :]), in_chunks(ebi[:, :]), ALU.mult).then_inc(rec_pool, 1)

            @block.scalar
            def _(act):
                act.wait_ge(lora_mixed, MIX)
                act.activation(lora[0][:, :], lora[0][:, :], ACT.Tanh).then_inc(lora_act, 1)
                act.wait_ge(lora_mixed, 3 * MIX)
                act.activation(lora[2][:, :], lora[2][:, :], ACT.Sigmoid).then_inc(lora_act, 1)
                act.wait_ge(consts, 3)
                with act.Fori(0, HP) as i:
                    def evacuate(job, out, done, func, **kw):
                        for b, (t0, tn) in enumerate(TOK_BLOCKS):
                            act.wait_ge(product, NBLK * (JOBS * i + job) + b + 1)
                            act.activation(out[:, t0:t0 + tn], bank[b][:, 0:tn], func, **kw).then_inc(done, 1)
                    act.wait_ge(rec_dve, 2 * i)
                    act.wait_ge(rec_pool, 2 * i)
                    act.wait_ge(rec_act, 2 * i)
                    evacuate(0, ebi, gate_ready, ACT.Copy)
                    evacuate(1, eb, norm_root, ACT.Sqrt, bias=tiny[:, :])
                    for d in range(2):
                        act.wait_ge(arg_ready, 2 * i + d)
                        act.wait_ge(rec_dve, 2 * i + d)
                        act.wait_ge(mixed, 3 * MIX * (i + 1))
                        evacuate(2 + 2 * d, sg, sig_ready, ACT.Sigmoid, bias=p_w0[:, d:d + 1])
                        evacuate(3 + 2 * d, av, a_ready, ACT.Sigmoid, bias=p_a0[:, d:d + 1])
                        act.wait_ge(kk_ready, 2 * i + 2)
                        act.wait_ge(cum_ready, 2 * i + d + 1)
                        act.wait_ge(arg_ready, 2 * i + d + 1)
                        act.wait_ge(rec_pool, 2 * i + d)
                        act.wait_ge(gate_stored, 16 * (i + 1))
                        act.activation(eb[:, :], cum[:, :], ACT.Exp, scale=-RATE).then_inc(exps, 1)
                        act.activation(ebi[:, :], cum[:, :], ACT.Exp, scale=RATE).then_inc(exps, 1)
                        act.activation(ebm[:, :], ebm[:, :], ACT.Exp, scale=-RATE).then_inc(exps, 1)
                        act.wait_ge(exps, 3 * (2 * i + d) + 3)
                        act.wait_ge(rec_stored, 16 * (2 * i + d))
                        act.copy(recs[:, :, 1 + 4 * C:], in_chunks(v[:, :]))
                        end = 0 if d else C - 1
                        act.copy(recs[:, :, 0:1], in_chunks(eb[:, :])[:, :, end:end + 1]).then_inc(rec_act, 1)

            @block.tensor
            def _(pe):
                pe.wait_ge(const_in, 16)
                with pe.Fori(0, HP) as i:
                    def job(j, lhsT, rhs, also=None, at=0):
                        for b, (t0, tn) in enumerate(TOK_BLOCKS):
                            pe.wait_ge(freed_or(j, b)[0], freed_or(j, b)[1])
                            if also is not None:
                                pe.wait_ge(*also)
                            pe.matmul(bank[b][:, 0:tn], lhsT, rhs[at:at + lhsT.shape[0], t0:t0 + tn], start=True, stop=True).then_inc(product, 1)

                    def freed_or(j, b):
                        return [(bonus_out, NBLK * i), (gate_ready, NBLK * i + b + 1), (norm_root, NBLK * i + b + 1),
                                (sig_ready, NBLK * 2 * i + b + 1), (a_ready, NBLK * 2 * i + b + 1),
                                (sig_ready, NBLK * (2 * i + 1) + b + 1), (a_ready, NBLK * (2 * i + 1) + b + 1)][j]
                    pe.wait_ge(ld, 16 * N_LD * (i + 1))
                    pe.wait_ge(lora_act, 2)
                    job(0, g2s[:, :], lora[2])
                    job(1, ones[:, :], kd, (squares, i + 1))
                    for d in range(2):
                        job(2 + 2 * d, w2s[64 * d:64 * d + 64, :], lora[0], None, 64 * d)
                        job(3 + 2 * d, a2s[64 * d:64 * d + 64, :], lora[1], None, 64 * d)
                    job(6, ones[:, :], bs, (bonus_step, 3 * i + 3))

            @block.vector
            def _(dve):
                dve.wait_ge(lora_in, 9 * 16)
                dve.tensor_tensor(mus[:, :, 2], mus[:, :, 0], mus[:, :, 1], ALU.add).then_inc(lora_mu, 1)
                dve.wait_ge(lora_mu, 1)
                dve.tensor_scalar(mus[:, :, 2], mus[:, :, 2], -1.0, 1.0, ALU.mult, ALU.add).then_inc(lora_mu, 1)
                dve.wait_ge(lora_mu, 2)
                for j in range(3):
                    shift_mix(dve, lora[j], raw[j], mus[:, j, :], lora_mixed, MIX * j)
                dve.wait_ge(consts, 3)
                with dve.Fori(0, HP) as i:
                    dve.wait_ge(ld, 16 * N_LD * (i + 1))
                    dve.tensor_tensor(mus[:, :, 2], mus[:, :, 0], mus[:, :, 1], ALU.add).then_inc(coef, 1)
                    dve.tensor_scalar(p_1ka, p_ka, -1.0, 1.0, ALU.mult, ALU.add).then_inc(coef, 1)
                    dve.wait_ge(coef, 3 * i + 2)
                    dve.tensor_scalar(mus[:, :, 2], mus[:, :, 2], -1.0, 1.0, ALU.mult, ALU.add).then_inc(coef, 1)
                    dve.wait_ge(coef, 3 * i + 3)
                    dve.wait_ge(rec_act, 2 * i)
                    for j, out in enumerate((r, k, v)):
                        shift_mix(dve, out, raw[j], mus[:, j, :], mixed, 3 * MIX * i + MIX * j)
                    dve.wait_ge(mixed, 3 * MIX * (i + 1))
                    dve.tensor_scalar(kk[:, :], k[:, :], p_kk, None, ALU.mult).then_inc(kk_raw, 1)
                    dve.wait_ge(kk_raw, i + 1)
                    dve.tensor_tensor(kd[:, :], kk[:, :], kk[:, :], ALU.mult).then_inc(squares, 1)
                    dve.wait_ge(norm_root, NBLK * (i + 1))
                    dve.reciprocal(eb[:, :], eb[:, :]).then_inc(kk_ready, 1)
                    dve.wait_ge(kk_ready, 2 * i + 1)
                    dve.tensor_tensor(kk[:, :], kk[:, :], eb[:, :], ALU.mult).then_inc(kk_ready, 1)
                    for d in range(2):
                        u = 2 * i + d
                        dve.wait_ge(sig_ready, NBLK * (u + 1))
                        dve.wait_ge(exps, 3 * u)
                        dve.tensor_tensor_scan(scan_order(cum, d, 0, T), keep[:, :], scan_order(sg, d, 0, T), 0.0, ALU.mult, ALU.add).then_inc(cum_ready, 1)
                        dve.wait_ge(cum_ready, u + 1)
                        dve.tensor_tensor(ebm[:, :], cum[:, :], sg[:, :], ALU.subtract).then_inc(arg_ready, 1)
                        dve.wait_ge(a_ready, NBLK * (u + 1))
                        dve.wait_ge(rec_pool, u)
                        dve.tensor_scalar(kd[:, :], av[:, :], p_ka, p_1ka, ALU.mult, ALU.add).then_inc(kd_step, 1)
                        dve.wait_ge(kd_step, 3 * u + 1)
                        dve.tensor_tensor(kd[:, :], kd[:, :], k[:, :], ALU.mult).then_inc(kd_step, 1)
                        dve.wait_ge(kk_ready, 2 * i + 2)
                        dve.tensor_tensor(av[:, :], av[:, :], kk[:, :], ALU.mult).then_inc(kd_step, 1)
                        dve.wait_ge(kd_step, 3 * u + 3)
                        if d == 0:
                            dve.wait_ge(bonus_stored, 16 * i)
                            dve.tensor_scalar(bs[:, :], kd[:, :], p_rk[:, 0:1], None, ALU.mult).then_inc(bonus_step, 1)
                        else:
                            dve.wait_ge(bonus_step, 3 * i + 1)
                            dve.scalar_tensor_tensor(bs[:, :], kd[:, :], p_rk[:, 1:2], bs[:, :], ALU.mult, ALU.add).then_inc(bonus_step, 1)
                        dve.wait_ge(rec_stored, 16 * u)
                        dve.wait_ge(exps, 3 * u + 3)
                        for q, (x, y) in enumerate(((kk, ebm), (r, eb), (av, ebi))):
                            out = recs[:, :, 1 + q * C:1 + (q + 1) * C]
                            if q == 0:
                                dve.scalar_tensor_tensor(out, in_chunks(x[:, :]), -1.0, in_chunks(y[:, :]), ALU.mult, ALU.mult)
                            else:
                                last = dve.tensor_tensor(out, in_chunks(x[:, :]), in_chunks(y[:, :]), ALU.mult)
                        last.then_inc(rec_dve, 1)
                    dve.wait_ge(bonus_step, 3 * i + 2)
                    dve.tensor_tensor(bs[:, :], bs[:, :], r[:, :], ALU.mult).then_inc(bonus_step, 1)
                    for b, (t0, tn) in enumerate(TOK_BLOCKS):
                        dve.wait_ge(product, NBLK * (JOBS * i + 6) + b + 1)
                        dve.tensor_tensor(bs[:, t0:t0 + tn], bank[b][:, 0:tn], v[:, t0:t0 + tn], ALU.mult).then_inc(bonus_out, 1)


def joins(d):
    t = np.arange(C)[::-1] if d else np.arange(C)
    return [(t[:, None] >> (l + 1) == t[None, :] >> (l + 1)) & (t[:, None] >> l & 1 == 1) & (t[None, :] >> l & 1 == 0)
            for l in range(LEVELS)]


def rwkv_constants():
    two = lambda m: np.concatenate([m, m], 0)
    diag = lambda m: np.kron(np.eye(2), m)
    parts = []
    for d in range(2):
        later = sum(joins(d)).T
        parts += [two(later), two(later + np.eye(C)), two(joins(d)[0])] + [diag(j.T) for j in joins(d)]
    return np.concatenate(parts + [two(np.eye(C)), np.kron(np.eye(2), np.ones((C, 1))), np.eye(P)], 1).astype(np.float32)


def stage_rwkv_scan(nc, rec, consts_d, state_in, new_state, o):
    G, UN = 2, 3
    NL = LEVELS - 1
    W = rwkv_constants().shape[1]
    with Stage(nc, "rws") as st:
        con = st.sb("con", [P, W])
        per_d = 3 * C + LEVELS * P
        mask2 = [con[:, g * per_d:g * per_d + 2 * C].rearrange("p (q t) -> p q t", q=2) for g in range(G)]
        m0 = [con[:, g * per_d + 2 * C:g * per_d + 3 * C] for g in range(G)]
        mT = [con[:, g * per_d + 3 * C:(g + 1) * per_d].rearrange("p (l s) -> p l s", l=LEVELS) for g in range(G)]
        eye, eye128 = con[:, G * per_d:G * per_d + C], con[:, W - P:W]
        own = con[:, W - P - 2:W - P]
        plain = [st.sb(f"plain{u}", [P, G * UN, REC]) for u in range(2)]
        bd = [st.sb(f"bd{u}", [P, G * UN, 5, 2, C]) for u in range(2)]
        LR = [st.sb(f"LR{g}", [P, UN, 2, 2, C]) for g in range(G)]
        KR = [st.sb(f"KR{g}", [P, UN, 2, 2, C]) for g in range(G)]
        ET = [st.sb(f"ET{g}", [P, NL, UN, P]) for g in range(G)]
        Ti = [st.sb(f"T{g}", [P, UN, C]) for g in range(G)]
        Ui = [st.sb(f"U{g}", [P, UN, P]) for g in range(G)]
        Ys = [st.sb(f"Ys{g}", [P, UN, C]) for g in range(G)]
        Yd = [st.sb(f"Yd{g}", [P, UN, 2, C]) for g in range(G)]
        Vs, Xs, SAs, S, Sn = ([st.sb(f"{x}{g}", [P, UN, C]) for g in range(G)] for x in ("V", "X", "SA", "S", "Sn"))
        BT, KT = ([st.sb(f"{x}{g}", [P, UN, P]) for g in range(G)] for x in ("BT", "KT"))
        Os = [[st.sb(f"O{g}{u}", [P, UN, C]) for u in range(2)] for g in range(G)]
        SX = st.sb("SX", [P, G * UN, 2, C])
        bank = [st.ps(f"b{b}") for b in range(8)]
        pA, pB, pC, pD, pE, pF, pG, pH = bank
        pV, pYU, pS = [pF, pG], [pF, pG], [pF, pG]
        pY, pX, pO = [pH, pC], [pA, pB], [pD, pE]

        def each(name):
            return [st.sem(f"{name}_{g}") for g in range(G)]
        con_in, cleared, rec_in = st.sem("con_in"), st.sem("cleared"), st.sem2("rec_in")
        mm_v, mm_a, mm_b, mm_c, mm_d, mm_e = (each(n) for n in ("mm_v", "mm_a", "mm_b", "mm_c", "mm_d", "mm_e"))
        lr_done, kr_done, t_mask, t0_done, vs_done, bt_done, kt_done = (each(n) for n in (
            "lr_done", "kr_done", "t_mask", "t0_done", "vs_done", "bt_done", "kt_done"))
        et_done, u_mask, u0_done = each("et_done"), each("u_mask"), each("u0_done")
        y_mm, ys_act, ys_dve, ty_mm, yu_mm, t_step, u_step = (each(n) for n in (
            "y_mm", "ys_act", "ys_dve", "ty_mm", "yu_mm", "t_step", "u_step"))
        x_mm, x_done, sa_mm, sa_done, o_mm, o_done, s_mm, s_sum, s_done = (each(n) for n in (
            "x_mm", "x_done", "sa_mm", "sa_done", "o_mm", "o_done", "s_mm", "s_sum", "s_done"))
        o_out = [st.sem2(f"o_out{g}") for g in range(G)]
        state0 = st.sem("state0")
        sx_ready, sx_mm, sx_out, sx_stored, sx_in, imported = (st.sem(n) for n in (
            "sx_ready", "sx_mm", "sx_out", "sx_stored", "sx_in", "imported"))

        def q_bd(u, j, q):
            return bd[u][:, j, q, :, :].rearrange("p h t -> p (h t)")

        def cols(ps, j, w):
            return ps[:, j * w:(j + 1) * w]

        def v3(ap):
            return ap.rearrange("p (j t) -> p j t", j=UN)

        def both(eng, chunk, between):
            for c in range(NCH_CTX):
                chunk(c % 2, 1, c, (c, NCH_CTX - 1 - c))
            between()
            with eng.Fori(0, (NCH - NCH_CTX) // 2) as i:
                for u in range(2):
                    chunk(u, i + 2, 2 * i + 2 + u, (2 * i + 2 + u, NCH - 1 - u - 2 * i))

        def nothing():
            pass

        with st.block() as block:
            @block.sync
            def _(sp):
                sp.dma_start(con[:, :], consts_d).then_inc(con_in, 16)
                sp.wait_ge(cleared, 3 + 3 * G)

                def load(u, m, c, at):
                    for g in range(G):
                        sp.wait_ge(s_done[g], c - 1 if not isinstance(c, int) else 0)
                    for g in range(G):
                        js = slice(UN * g, UN * (g + 1))
                        sp.dma_start(plain[u][:, js, :], rec[js, :, bass.ds(at[g], 1), :].rearrange("j p c w -> p j (c w)")).then_inc(rec_in[u], 16)
                        for h in range(2):
                            p = slice(64 * h, 64 * h + 64)
                            for j in range(UN * g, UN * (g + 1)):
                                sp.dma_start(bd[u][p, j, :, h, :],
                                             rec[j, p, bass.ds(at[g], 1), 1:REC].rearrange("p c (q t) -> p (c q) t", t=C)).then_inc(rec_in[u], 16)

                def swap():
                    sp.wait_ge(sx_out, 1)
                    for g in range(G):
                        for h in range(2):
                            sp.dma_start(new_state[0, 0, g].rearrange("(j h) v k -> h v j k", h=2)[h], Xs[g][64 * h:64 * h + 64, :, :]).then_inc(sx_stored, 16)
                            sp.dma_start(SX[64 * h:64 * h + 64, UN * g:UN * (g + 1), h, :],
                                         state_in[0, 0, g].rearrange("(j h) v k -> h v j k", h=2)[h]).then_inc(sx_in, 16)
                    sp.wait_ge(sx_stored, 16 * 4)
                both(sp, load, swap)

            @block.gpsimd
            def _(pool):
                for z in (*(b[:, :, :, :, :] for b in bd), SX[:, :, :, :]):
                    pool.memset(z, 0.0).then_inc(cleared, 1)
                for g in range(G):
                    for z in (LR[g], KR[g]):
                        pool.memset(z[:, :, :, :, :], 0.0).then_inc(cleared, 1)
                    pool.memset(Yd[g][:, :, :, :], 0.0).then_inc(cleared, 1)
                pool.wait_ge(con_in, 16)
                pool.wait_ge(cleared, 3 + 3 * G)

                def chunk(u, m, c, at):
                    for g in range(G):
                        lt = LR[g][:, :, 0, :, :].rearrange("p j h t -> p j (h t)")
                        pool.wait_ge(lr_done[g], c + 1)
                        pool.tensor_tensor(ET[g][:, 0, :, :], lt, mT[g][:, 1:2, :].to_broadcast([P, UN, P]), ALU.mult).then_inc(et_done[g], 1)
                        pool.tensor_tensor(Ui[g][:, :, :], lt, mT[g][:, 0:1, :].to_broadcast([P, UN, P]), ALU.mult).then_inc(u_mask[g], 1)
                        pool.wait_ge(u_mask[g], c + 1)
                        pool.tensor_tensor(Ui[g][:, :, :], Ui[g][:, :, :], eye128.unsqueeze(1).to_broadcast([P, UN, P]), ALU.add).then_inc(u0_done[g], 1)
                        for l in range(1, NL):
                            pool.tensor_tensor(ET[g][:, l, :, :], lt, mT[g][:, l + 1:l + 2, :].to_broadcast([P, UN, P]), ALU.mult).then_inc(et_done[g], 1)
                both(pool, chunk, nothing)

            @block.scalar
            def _(act):
                act.wait_ge(cleared, 3 + 3 * G)

                def chunk(u, m, c, at):
                    for g in range(G):
                        act.wait_ge(mm_v[g], c + 1)
                        act.copy(Vs[g][:, :, :], v3(pV[g][:, 0:UN * C])).then_inc(vs_done[g], 1)
                        act.wait_ge(mm_d[g], c + 1)
                        act.copy(BT[g][:, :, :], v3(pD[:, 0:UN * P])).then_inc(bt_done[g], 1)
                        act.wait_ge(mm_e[g], c + 1)
                        act.copy(KT[g][:, :, :], v3(pE[:, 0:UN * P])).then_inc(kt_done[g], 1)
                    for l in range(1, NL + 1):
                        for g in range(G):
                            y = v3(pY[g][:, 0:UN * C])
                            act.wait_ge(y_mm[g], NL * c + l)
                            act.copy(Ys[g][0:64, :, :], y[0:64])
                            act.copy(Yd[g][0:64, :, 0, :], y[0:64]).then_inc(ys_act[g], 1)
                    for g in range(G):
                        act.wait_ge(x_mm[g], c + 1)
                        act.copy(Xs[g][:, :, :], v3(pX[g][:, 0:UN * C])).then_inc(x_done[g], 1)
                    for g in range(G):
                        act.wait_ge(o_mm[g], c + 1)
                        act.wait_ge(o_out[g][u], 32 * (m - 1))
                        act.copy(Os[g][u][:, :, :], v3(pO[g][:, 0:UN * C])).then_inc(o_done[g], 1)
                    for g in range(G):
                        act.wait_ge(o_done[g], c + 1)
                        rows = o[g, bass.ds(at[g] * C, C), :]
                        for h in range(2):
                            act.dma_start(rows.rearrange("t (j h v) -> h t j v", h=2, j=UN)[h], Os[g][u][64 * h:64 * h + 64, :, :]).then_inc(o_out[g][u], 16)
                both(act, chunk, nothing)
                for g in range(G):
                    for u in range(2):
                        act.wait_ge(o_out[g][u], 32 * NCH // 2)

            @block.tensor
            def _(pe):
                pe.wait_ge(con_in, 16)
                pe.wait_ge(state0, G)

                def chunk(u, m, c, at):
                    n = c + 1
                    pe.wait_ge(rec_in[u], 16 * 14 * m)
                    for g in range(G):
                        js = range(UN * g, UN * (g + 1))
                        if g == 0:
                            for e in (*sa_done, *o_done, *s_sum, kt_done[1]):
                                pe.wait_ge(e, c)
                        else:
                            for e in (lr_done, kr_done, t_mask, vs_done, bt_done, kt_done):
                                pe.wait_ge(e[0], n)
                        for x, j in enumerate(js):
                            mm = pe.matmul(cols(pA, x, P), q_bd(u, j, 2), plain[u][:, j, 1:1 + P], start=True, stop=True)
                        mm.then_inc(mm_a[g], 1)
                        for x, j in enumerate(js):
                            mm = pe.matmul(cols(pC, x, C), q_bd(u, j, 0), plain[u][:, j, 1 + P:1 + 3 * C], start=True, stop=True)
                        mm.then_inc(mm_c[g], 1)
                        for x, j in enumerate(js):
                            mm = pe.matmul(cols(pV[g], x, C), q_bd(u, j, 4), eye, start=True, stop=True)
                        mm.then_inc(mm_v[g], 1)
                        for x, j in enumerate(js):
                            mm = pe.matmul(cols(pB, x, P), q_bd(u, j, 3), plain[u][:, j, 1:1 + P], start=True, stop=True)
                        mm.then_inc(mm_b[g], 1)
                        for ps, q, done in ((pD, 2, mm_d), (pE, 3, mm_e)):
                            for x, j in enumerate(js):
                                mm = pe.transpose(cols(ps, x, P), q_bd(u, j, q), eye128)
                            mm.then_inc(done[g], 1)
                    for l in range(1, NL + 1):
                        for g in range(G):
                            pe.wait_ge(et_done[g], NL * c + l)
                            if l == 1:
                                pe.wait_ge(t0_done[g], n)
                            else:
                                pe.wait_ge(t_step[g], (NL - 1) * c + l - 1)
                            for x in range(UN):
                                mm = pe.matmul(cols(pY[g], x, C), ET[g][:, l - 1, x, :], Ti[g][:, x, :], start=True, stop=True)
                            mm.then_inc(y_mm[g], 1)
                        for g in range(G):
                            pe.wait_ge(ys_act[g], NL * c + l)
                            pe.wait_ge(ys_dve[g], NL * c + l)
                            if l == 1:
                                pe.wait_ge(u0_done[g], n)
                            pe.wait_ge(u_step[g], NL * c + l - 1)
                            if l < NL:
                                for x in range(UN):
                                    mm = pe.matmul(cols(pY[g], x, C), Ui[g][:, x, :], Ys[g][:, x, :], start=True, stop=True)
                                mm.then_inc(ty_mm[g], 1)
                            if l == 1:
                                pe.wait_ge(vs_done[g], n)
                            for x in range(UN):
                                mm = pe.matmul(cols(pYU[g], x, P), Yd[g][:, x, :, :].rearrange("p h t -> p (h t)"), Ui[g][:, x, :], start=True, stop=True)
                            mm.then_inc(yu_mm[g], 1)
                    for g in range(G):
                        for e in (vs_done[g], kr_done[g], lr_done[1], kr_done[1]):
                            pe.wait_ge(e, n)
                        pe.wait_ge(s_done[g], c)
                        for x in range(UN):
                            pe.matmul(cols(pX[g], x, C), q_bd(u, UN * g + x, 0), S[g][:, x, :], start=True, stop=False)
                            mm = pe.matmul(cols(pX[g], x, C), KR[g][:, x, 0, :, :].rearrange("p h t -> p (h t)"), Vs[g][:, x, :], start=False, stop=True)
                        mm.then_inc(x_mm[g], 1)
                    for g in range(G):
                        pe.wait_ge(x_done[g], n)
                        pe.wait_ge(u_step[g], NL * n)
                        for x in range(UN):
                            mm = pe.matmul(cols(pX[g], UN + x, C), Ui[g][:, x, :], Xs[g][:, x, :], start=True, stop=True)
                        mm.then_inc(sa_mm[g], 1)
                    for g in range(G):
                        for e in (bt_done[1], kt_done[1], bt_done[g], kt_done[g], sa_done[g]):
                            pe.wait_ge(e, n)
                        for x in range(UN):
                            pe.matmul(cols(pO[g], x, C), q_bd(u, UN * g + x, 1), S[g][:, x, :], start=True, stop=False)
                            pe.matmul(cols(pO[g], x, C), LR[g][:, x, 1, :, :].rearrange("p h t -> p (h t)"), SAs[g][:, x, :], start=False, stop=False)
                            mm = pe.matmul(cols(pO[g], x, C), KR[g][:, x, 1, :, :].rearrange("p h t -> p (h t)"), Vs[g][:, x, :], start=False, stop=True)
                        mm.then_inc(o_mm[g], 1)
                        for x in range(UN):
                            pe.matmul(cols(pS[g], x, C), BT[g][:, x, :], SAs[g][:, x, :], start=True, stop=False)
                            mm = pe.matmul(cols(pS[g], x, C), KT[g][:, x, :], Vs[g][:, x, :], start=False, stop=True)
                        mm.then_inc(s_mm[g], 1)

                def swap():
                    pe.wait_ge(sx_ready, 1)
                    for j in range(G * UN):
                        mm = pe.matmul(cols(pA, j, C), SX[:, j, :, :].rearrange("p h t -> p (h t)"), eye, start=True, stop=True)
                    mm.then_inc(sx_mm, 1)
                    pe.wait_ge(sx_in, 16 * 4)
                    for j in range(G * UN):
                        mm = pe.matmul(cols(pA, j, C), SX[:, j, :, :].rearrange("p h t -> p (h t)"), eye, start=True, stop=True)
                    mm.then_inc(sx_mm, 1)
                    pe.wait_ge(imported, 1)
                both(pe, chunk, swap)

            @block.vector
            def _(dve):
                for g in range(G):
                    dve.memset(S[g][:, :, :], 0.0).then_inc(state0, 1)
                dve.wait_ge(con_in, 16)
                dve.wait_ge(cleared, 3 + 3 * G)

                def chunk(u, m, c, at):
                    n = c + 1
                    for g in range(G):
                        dve.wait_ge(mm_a[g], n)
                        for h in range(2):
                            p = slice(64 * h, 64 * h + 64)
                            m_b = mask2[g][p].unsqueeze(1).to_broadcast([64, UN, 2, C])
                            last = dve.tensor_tensor(LR[g][p, :, :, h, :], pA[p, 0:UN * P].rearrange("p (j q t) -> p j q t", j=UN, q=2), m_b, ALU.mult)
                        last.then_inc(lr_done[g], 1)
                        dve.wait_ge(mm_c[g], n)
                        dve.tensor_tensor(Ti[g][:, :, :], v3(pC[:, 0:UN * C]), m0[g].unsqueeze(1).to_broadcast([P, UN, C]), ALU.mult).then_inc(t_mask[g], 1)
                        dve.wait_ge(t_mask[g], n)
                        dve.tensor_tensor(Ti[g][:, :, :], Ti[g][:, :, :], eye.unsqueeze(1).to_broadcast([P, UN, C]), ALU.add).then_inc(t0_done[g], 1)
                        dve.wait_ge(mm_b[g], n)
                        for h in range(2):
                            p = slice(64 * h, 64 * h + 64)
                            m_b = mask2[g][p].unsqueeze(1).to_broadcast([64, UN, 2, C])
                            last = dve.tensor_tensor(KR[g][p, :, :, h, :], pB[p, 0:UN * P].rearrange("p (j q t) -> p j q t", j=UN, q=2), m_b, ALU.mult)
                        last.then_inc(kr_done[g], 1)
                    for l in range(1, NL + 1):
                        for g in range(G):
                            dve.wait_ge(y_mm[g], NL * c + l)
                            dve.tensor_copy(Ys[g][64:128, :, :], v3(pY[g][64:128, 0:UN * C]))
                            dve.tensor_copy(Yd[g][64:128, :, 1, :], v3(pY[g][64:128, 0:UN * C])).then_inc(ys_dve[g], 1)
                        for g in range(G):
                            if l < NL:
                                dve.wait_ge(ty_mm[g], (NL - 1) * c + l)
                                dve.tensor_tensor(Ti[g][:, :, :], v3(pY[g][:, 0:UN * C]), Ti[g][:, :, :], ALU.add).then_inc(t_step[g], 1)
                            dve.wait_ge(yu_mm[g], NL * c + l)
                            dve.tensor_tensor(Ui[g][:, :, :], v3(pYU[g][:, 0:UN * P]), Ui[g][:, :, :], ALU.add).then_inc(u_step[g], 1)
                    for g in range(G):
                        dve.wait_ge(sa_mm[g], n)
                        dve.tensor_copy(SAs[g][:, :, :], v3(pX[g][:, UN * C:2 * UN * C])).then_inc(sa_done[g], 1)
                    for g in range(G):
                        dve.wait_ge(s_mm[g], n)
                        dve.tensor_tensor(Sn[g][:, :, :], v3(pS[g][:, 0:UN * C]), S[g][:, :, :], ALU.add).then_inc(s_sum[g], 1)
                        dve.wait_ge(s_sum[g], n)
                        dve.tensor_tensor(S[g][:, :, :], Sn[g][:, :, :], plain[u][:, UN * g:UN * (g + 1), 0:1].to_broadcast([P, UN, C]), ALU.mult).then_inc(s_done[g], 1)

                def swap():
                    dve.wait_ge(cleared, 3 + 3 * G)
                    for g in range(G):
                        dve.wait_ge(s_done[g], NCH_CTX)
                        for h in range(2):
                            last = dve.tensor_copy(SX[64 * h:64 * h + 64, UN * g:UN * (g + 1), h, :], S[g][64 * h:64 * h + 64, :, :])
                    last.then_inc(sx_ready, 1)
                    dve.wait_ge(sx_mm, 1)
                    for g in range(G):
                        last = dve.tensor_copy(Xs[g][:, :, :], v3(pA[:, UN * C * g:UN * C * (g + 1)]))
                    last.then_inc(sx_out, 1)
                    dve.wait_ge(sx_mm, 2)
                    for g in range(G):
                        last = dve.tensor_copy(S[g][:, :, :], v3(pA[:, UN * C * g:UN * C * (g + 1)]))
                    last.then_inc(imported, 1)
                both(dve, chunk, swap)


def stage_rwkv_post(nc, o, bonus, gate, ln_w, ln_b, ident_d, mixT):
    UN = D_RW // P
    GN_EPS = 64e-5
    with Stage(nc, "rwo") as st:
        ident, par = st.sb("ident", [P, P]), st.sb("par", [P, 2, UN])
        of, ob, cen, sq = ([st.sb(f"{x}{u}", [P, D_RW]) for u in range(2)] for x in ("of", "ob", "cen", "sq"))
        bo, ga, mix = ([st.sb(f"{x}{u}", [P, UN, P]) for u in range(2)] for x in ("bo", "ga", "mix"))
        stat = [st.sb(f"stat{u}", [P, 4, RW_HEADS]) for u in range(2)]
        ps = [st.ps(f"t{u}") for u in range(2)]
        par_in = st.sem("par_in")
        tile_in, added, mean, centred, squared, var, root, rstd, normed, turned, step, mixed, stored = (st.sem2(n) for n in (
            "tile_in", "added", "mean", "centred", "squared", "var", "root", "rstd", "normed", "turned", "step", "mixed", "stored"))
        bonused = st.sem2("bonused")

        def heads(ap):
            return ap.rearrange("p (h v) -> p h v", v=RW_HD)

        def rows(tile):
            return bass.ds(tile * P, P)

        def chans(t, tile):
            return t[:, rows(tile)].rearrange("(j p) t -> p j t", p=P)

        with st.block() as block:
            @block.sync
            def _(sp):
                sp.dma_start(ident[:, :], ident_d).then_inc(par_in, 16)
                for j in range(UN):
                    sp.dma_start(par[:, 0, j:j + 1], ln_w[0, j * P:(j + 1) * P].unsqueeze(1)).then_inc(par_in, 16)
                    sp.dma_start(par[:, 1, j:j + 1], ln_b[0, j * P:(j + 1) * P].unsqueeze(1)).then_inc(par_in, 16)

                def load(u, n, tile, seg):
                    sp.wait_ge(mixed[u], n - 1)
                    sp.dma_start(of[u][:, :], o[0, rows(tile), :]).then_inc(tile_in[u], 16)
                    sp.dma_start(ob[u][:, :], o[1, rows(tile), :]).then_inc(tile_in[u], 16)
                    sp.dma_start(bo[u][:, :, :], chans(bonus, tile)).then_inc(tile_in[u], 16)
                    sp.dma_start(ga[u][:, :, :], chans(gate, tile)).then_inc(tile_in[u], 16)
                paired(sp, load, 8)

            @block.gpsimd
            def _(pool):
                def store(u, n, tile, seg):
                    pool.wait_ge(par_in, 16 * (1 + 2 * UN))
                    pool.wait_ge(mixed[u], n)
                    pool.dma_start(chans(mixT[D_LRU:D_LRU + D_RW], tile), mix[u][:, :, :]).then_inc(stored[u], 16)
                paired(pool, store, 8)
                for u in range(2):
                    pool.wait_ge(stored[u], 16 * (9 - u))

            @block.scalar
            def _(act):
                def body(u, n, tile, seg):
                    act.wait_ge(centred[u], n)
                    act.activation(sq[u][:, :], cen[u][:, :], ACT.Square).then_inc(squared[u], 1)
                    act.wait_ge(var[u], 2 * n)
                    act.activation(stat[u][:, 2, :], stat[u][:, 1, :], ACT.Sqrt).then_inc(root[u], 1)
                paired(act, body, 8)

            @block.tensor
            def _(pe):
                pe.wait_ge(par_in, 16 * (1 + 2 * UN))

                def body(u, n, tile, seg):
                    pe.wait_ge(normed[u], n)
                    pe.wait_ge(step[u], n - 1)
                    for j in range(UN):
                        mm = pe.transpose(ps[u][:, j * P:(j + 1) * P], cen[u][:, j * P:(j + 1) * P], ident[:, :])
                    mm.then_inc(turned[u], 1)
                paired(pe, body, 8)

            @block.vector
            def _(dve):
                dve.wait_ge(par_in, 16 * (1 + 2 * UN))

                def body(u, n, tile, seg):
                    s = stat[u]

                    def spread(k):
                        return s[:, k, :].unsqueeze(2).to_broadcast([P, RW_HEADS, RW_HD])
                    dve.wait_ge(tile_in[u], 64 * n)
                    dve.wait_ge(stored[u], 16 * (n - 1))
                    dve.tensor_tensor(of[u][:, :], of[u][:, :], ob[u][:, :], ALU.add).then_inc(added[u], 1)
                    dve.wait_ge(added[u], n)
                    dve.reduce_sum(s[:, 0, :], heads(of[u][:, :]), AX.X).then_inc(mean[u], 1)
                    dve.wait_ge(mean[u], 2 * n - 1)
                    dve.tensor_scalar(s[:, 0, :], s[:, 0, :], 1.0 / RW_HD, None, ALU.mult).then_inc(mean[u], 1)
                    dve.wait_ge(mean[u], 2 * n)
                    dve.tensor_tensor(heads(cen[u][:, :]), heads(of[u][:, :]), spread(0), ALU.subtract).then_inc(centred[u], 1)
                    dve.wait_ge(squared[u], n)
                    dve.reduce_sum(s[:, 1, :], heads(sq[u][:, :]), AX.X).then_inc(var[u], 1)
                    dve.wait_ge(var[u], 2 * n - 1)
                    dve.tensor_scalar(s[:, 1, :], s[:, 1, :], 1.0 / RW_HD, GN_EPS, ALU.mult, ALU.add).then_inc(var[u], 1)
                    dve.wait_ge(root[u], n)
                    dve.reciprocal(s[:, 3, :], s[:, 2, :]).then_inc(rstd[u], 1)
                    dve.wait_ge(rstd[u], n)
                    dve.tensor_tensor(heads(cen[u][:, :]), heads(cen[u][:, :]), spread(3), ALU.mult).then_inc(normed[u], 1)
                    dve.wait_ge(turned[u], n)
                    for j in range(UN):
                        last = dve.tensor_scalar(mix[u][:, j, :], ps[u][:, j * P:(j + 1) * P], par[:, 0, j:j + 1], par[:, 1, j:j + 1], ALU.mult, ALU.add)
                    last.then_inc(step[u], 1)
                    dve.wait_ge(step[u], n)
                    dve.tensor_tensor(bo[u][:, :, :], mix[u][:, :, :], bo[u][:, :, :], ALU.add).then_inc(bonused[u], 1)
                    dve.wait_ge(bonused[u], n)
                    dve.tensor_tensor(mix[u][:, :, :], bo[u][:, :, :], ga[u][:, :, :], ALU.mult).then_inc(mixed[u], 1)
                paired(dve, body, 8)


def stage_gla_turn(nc, proj, ident_d, vt):
    UN = D_GLA // P
    V0 = GLA0 + 2 * D_GLA_K
    with Stage(nc, "gvt") as st:
        ident = st.sb("ident", [P, P])
        x, y = ([st.sb(f"{n}{u}", [P, UN, P]) for u in range(2)] for n in ("x", "y"))
        ps = [st.ps(f"t{u}") for u in range(2)]
        ident_in = st.sem("ident_in")
        x_in, turned, copied, stored = (st.sem2(n) for n in ("x_in", "turned", "copied", "stored"))
        with st.block() as block:
            @block.sync
            def _(sp):
                sp.dma_start(ident[:, :], ident_d).then_inc(ident_in, 16)

                def load(u, n, tile, seg):
                    sp.wait_ge(turned[u], n - 1)
                    sp.dma_start(x[u][:, :, :], proj[V0:V0 + D_GLA, bass.ds(tile * P, P)].rearrange("(j p) t -> p j t", p=P)).then_inc(x_in[u], 16)
                paired(sp, load, 8)

            @block.gpsimd
            def _(pool):
                def store(u, n, tile, seg):
                    pool.wait_ge(ident_in, 16)
                    pool.wait_ge(copied[u], n)
                    pool.dma_start(vt[bass.ds(tile * P, P), :], y[u][:, :, :].rearrange("p j t -> p (j t)")).then_inc(stored[u], 16)
                paired(pool, store, 8)
                for u in range(2):
                    pool.wait_ge(stored[u], 16 * (9 - u))

            @block.tensor
            def _(pe):
                pe.wait_ge(ident_in, 16)

                def body(u, n, tile, seg):
                    pe.wait_ge(x_in[u], 16 * n)
                    pe.wait_ge(copied[u], n - 1)
                    for j in range(UN):
                        mm = pe.transpose(ps[u][:, j * P:(j + 1) * P], x[u][:, j, :], ident[:, :])
                    mm.then_inc(turned[u], 1)
                paired(pe, body, 8)

            @block.vector
            def _(dve):
                def body(u, n, tile, seg):
                    dve.wait_ge(turned[u], n)
                    dve.wait_ge(stored[u], 16 * (n - 1))
                    dve.tensor_copy(y[u][:, :, :].rearrange("p j t -> p (j t)"), ps[u][:, 0:UN * P]).then_inc(copied[u], 1)
                paired(dve, body, 8)


GREC = 4 * C


def column_major(ap):
    return ap[:, T_CTX:T].rearrange("p (c r) -> p r c", r=GRID_H)


def row_major(ap):
    return ap[:, T_CTX:T].rearrange("p (r c) -> p r c", c=GRID_W)


def stage_gla_prep(nc, proj, wg2, bg, grec):
    HP = GLA_HEADS // 2
    NBLK = len(TOK_BLOCKS)
    G0 = GLA0 + 2 * D_GLA_K + 2 * D_GLA
    with Stage(nc, "glp") as st:
        gd = st.sb("gd", [GLA_R, 2, T])
        w = st.sb("w", [GLA_R, 2, HP, P])
        b_g = st.sb("b_g", [P, 2, HP])
        keep = st.sb("keep", [P, T])
        qk = [st.sb(f"qk{i}", [P, T]) for i in range(2)]
        x, ab, la = ([st.sb(f"{n}{d}", [P, T]) for d in range(2)] for n in ("x", "ab", "la"))
        cum = st.sb("cum", [P, T])
        recs = st.sb("recs", [P, NCH, GREC])
        bank = [st.ps(f"b{b}") for b in range(NBLK)]
        zeroed, par_in, qk_in, consts = st.sem("zeroed"), st.sem("par_in"), st.sem("qk_in"), st.sem("consts")
        product, biased, absd, expd, lnd, la_done, summed, rec_act, stored = (st.sem(n) for n in (
            "product", "biased", "absd", "expd", "lnd", "la_done", "summed", "rec_act", "stored"))
        cum_out = st.sem("cum_out")
        with st.block() as block:
            @block.gpsimd
            def _(pool):
                pool.memset(keep[:, :], 1.0).then_inc(consts, 1)
                for z in (w[:, :, :, :], b_g[:, :, :], qk[0][:, :], qk[1][:, :]):
                    pool.memset(z, 0.0).then_inc(zeroed, 1)
                pool.wait_ge(consts, 1)
                pool.memset(in_chunks(keep[:, :])[:, :, 0:1], 0.0).then_inc(consts, 1)

            @block.sync
            def _(sp):
                sp.wait_ge(zeroed, 4)
                for d in range(2):
                    sp.dma_start(gd[:, d, :], proj[G0 + GLA_R * d:G0 + GLA_R * (d + 1), :]).then_inc(par_in, 16)
                    for head in range(GLA_HEADS):
                        j, h, ch = head // 2, head % 2, slice(head * GLA_DK, (head + 1) * GLA_DK)
                        sp.dma_start(w[:, d, j, 64 * h:64 * h + GLA_DK], wg2[0, d, :, ch]).then_inc(par_in, 16)
                        sp.dma_start(b_g[64 * h:64 * h + GLA_DK, d, j:j + 1], bg[0, d, ch].unsqueeze(1)).then_inc(par_in, 16)
                for j in range(HP):
                    if j:
                        sp.wait_ge(rec_act, 2 * j)
                    for i in range(2):
                        for h in range(2):
                            r0 = GLA0 + i * D_GLA_K + (2 * j + h) * GLA_DK
                            sp.dma_start(qk[i][64 * h:64 * h + GLA_DK, :], proj[r0:r0 + GLA_DK, :]).then_inc(qk_in, 16)
                    sp.wait_ge(rec_act, 2 * (j + 1))
                    sp.wait_ge(cum_out, 2 * (j + 1))
                    sp.dma_start(grec[j], recs[:, :, :]).then_inc(stored, 16)
                sp.wait_ge(stored, 16 * HP)

            @block.tensor
            def _(pe):
                pe.wait_ge(par_in, 16 * 18)
                for j in range(HP):
                    for d in range(2):
                        for b, (t0, tn) in enumerate(TOK_BLOCKS):
                            if 2 * j + d:
                                pe.wait_ge(biased, (2 * j + d - 1) * NBLK + b + 1)
                            pe.matmul(bank[b][:, 0:tn], w[:, d, j, :], gd[:, d, t0:t0 + tn], start=True, stop=True).then_inc(product, 1)

            @block.scalar
            def _(act):
                for j in range(HP):
                    act.wait_ge(qk_in, 64 * (j + 1))
                    if j:
                        act.wait_ge(stored, 16 * j)
                    for i in range(2):
                        o = recs[:, :, i * C:(i + 1) * C]
                        s = GLA_DK ** -0.5 if i == 0 else 1.0
                        act.activation(o[:, 0:NCH_CTX, :], in_chunks(qk[i][:, 0:T_CTX]), ACT.Copy, scale=s)
                        for half in range(2):
                            out = o[:, NCH_CTX:, half * GRID_H:(half + 1) * GRID_H]
                            src = qk[i][:, T_CTX:T].rearrange("p (r k e) -> p e k r", k=GRID_W // 2, e=2)[:, half]
                            last = act.activation(out, src, ACT.Copy, scale=s)
                        last.then_inc(rec_act, 1)
                    for d in range(2):
                        act.wait_ge(biased, (2 * j + d + 1) * NBLK)
                        act.activation(ab[d][:, :], x[d][:, :], ACT.Abs).then_inc(absd, 1)
                        act.wait_ge(absd, 2 * j + d + 1)
                        act.activation(ab[d][:, :], ab[d][:, :], ACT.Exp, scale=-1.0).then_inc(expd, 1)
                        act.wait_ge(expd, 2 * j + d + 1)
                        act.activation(ab[d][:, :], ab[d][:, :], ACT.Ln, bias=1.0).then_inc(lnd, 1)

            @block.vector
            def _(dve):
                dve.wait_ge(par_in, 16 * 18)
                dve.wait_ge(consts, 2)
                for j in range(HP):
                    for d in range(2):
                        n = 2 * j + d
                        for b, (t0, tn) in enumerate(TOK_BLOCKS):
                            dve.wait_ge(product, n * NBLK + b + 1)
                            dve.tensor_scalar(x[d][:, t0:t0 + tn], bank[b][:, 0:tn], b_g[:, d, j:j + 1], None, ALU.add).then_inc(biased, 1)
                    for d in range(2):
                        n = 2 * j + d
                        dve.wait_ge(lnd, n + 1)
                        dve.scalar_tensor_tensor(la[d][:, 0:T_CTX], x[d][:, 0:T_CTX], 0.0, ab[d][:, 0:T_CTX], ALU.min, ALU.subtract)
                        dve.scalar_tensor_tensor(column_major(la[d]), row_major(x[d]), 0.0, row_major(ab[d]), ALU.min, ALU.subtract).then_inc(la_done, 1)
                        dve.wait_ge(la_done, n + 1)
                        dve.tensor_tensor_scan(scan_order(cum, d, 0, T), keep[:, :], scan_order(la[d], d, 0, T), 0.0, ALU.mult, ALU.add).then_inc(summed, 1)
                        dve.wait_ge(summed, n + 1)
                        if j:
                            dve.wait_ge(stored, 16 * j)
                        dve.tensor_copy(recs[:, :, (2 + d) * C:(3 + d) * C], in_chunks(cum[:, :])).then_inc(cum_out, 1)


def gla_constants():
    parts = [np.concatenate([m, m], 0) for d in range(2) for m in [j.T for j in joins(d)] + [np.eye(C)]]
    return np.concatenate(parts + [np.kron(np.eye(2), np.ones((C, 1))), np.eye(P)], 1).astype(np.float32)


def stage_gla_scan(nc, grec, vt, consts_d, state_in, new_state, o):
    G, UN = 2, 2
    NS = LEVELS + 2
    NA = LEVELS + 1
    W = gla_constants().shape[1]
    CA = 4
    with Stage(nc, "gls") as st:
        con = st.sb("con", [P, W])
        mask = [con[:, g * NA * C:(g + 1) * NA * C].rearrange("p (l t) -> p l t", l=NA) for g in range(G)]
        own, eye128 = con[:, W - P - 2:W - P], con[:, W - P:W]
        rec = [st.sb(f"rec{u}", [P, G, UN, GREC]) for u in range(2)]
        v = [st.sb(f"v{u}", [P, G, UN, GLA_DV]) for u in range(2)]
        Dd = [st.sb(f"D{g}", [P, NS, UN, C]) for g in range(G)]
        F = [st.sb(f"F{g}", [P, NS, UN, C]) for g in range(G)]
        QF = [st.sb(f"QF{g}", [P, LEVELS, UN, C]) for g in range(G)]
        KF = [st.sb(f"KF{g}", [P, UN, LEVELS, 2, C]) for g in range(G)]
        qo, ko, qe, kh = ([st.sb(f"{x}{g}", [P, UN, 2, C]) for g in range(G)] for x in ("qo", "ko", "qe", "kh"))
        AM = [st.sb(f"AM{g}", [P, NA, UN, C]) for g in range(G)]
        at_, = ([st.sb(f"{x}{g}", [P, UN, C]) for g in range(G)] for x in ("att",))
        ad = [st.sb(f"ad{g}", [P, UN, 2, C]) for g in range(G)]
        kT = [st.sb(f"kT{g}", [P, UN, P]) for g in range(G)]
        S = [st.sb(f"S{g}", [P, UN, GLA_DV]) for g in range(G)]
        Os = [[st.sb(f"O{g}{u}", [P, UN, GLA_DV]) for u in range(2)] for g in range(G)]
        pA, pB, pK, pS = ([st.ps(f"{x}{g}") for g in range(G)] for x in ("pA", "pB", "pK", "pS"))

        def each(name):
            return [st.sem(f"{name}_{g}") for g in range(G)]
        con_in, rec_in, state0 = st.sem("con_in"), st.sem2("rec_in"), st.sem("state0")
        diffs, slot6, absd, expd, owned, qf_done, qk_bd, kf_done, kT_mm, kT_done = (each(n) for n in (
            "diffs", "slot6", "absd", "expd", "owned", "qf_done", "qk_bd", "kf_done", "kT_mm", "kT_done"))
        att_a, att_b, masked, att_sum, att_bd, o_mm, o_done, s_done = (each(n) for n in (
            "att_a", "att_b", "masked", "att_sum", "att_bd", "o_mm", "o_done", "s_done"))
        o_out = [st.sem2(f"o_out{g}") for g in range(G)]
        state_out, state_in_s = st.sem("state_out"), st.sem("state_in_s")

        def both(eng, chunk, between):
            for c in range(NCH_CTX):
                chunk(c % 2, 1, c, (c, NCH_CTX - 1 - c), True)
            between()
            with eng.Fori(0, (NCH - NCH_CTX) // 2) as i:
                for u in range(2):
                    chunk(u, i + 2, 2 * i + 2 + u, (2 * i + 2 + u, NCH - 1 - u - 2 * i), False)

        def nothing():
            pass

        def token_rows(t, at, ctx, half):
            if ctx:
                return t[at * C + 32 * half:at * C + 32 * half + 32, :]
            lat = t[T_CTX:T, :].rearrange("(r c) x -> c r x", c=GRID_W)
            return lat[bass.ds(2 * at - 2 * NCH_CTX + half, 1)].squeeze(0)

        def states(t, g):
            return t[0, 0, g].rearrange("(j h) k v -> h k j v", h=2)

        with st.block() as block:
            @block.sync
            def _(sp):
                sp.dma_start(con[:, :], consts_d).then_inc(con_in, 16)

                def load(u, m, c, at, ctx):
                    for g in range(G):
                        sp.wait_ge(s_done[g], 0 if isinstance(c, int) else c - 1)
                    for g in range(G):
                        sp.dma_start(rec[u][:, g, :, :], grec[:, :, bass.ds(at[g], 1), :].rearrange("j p c w -> p j (c w)")).then_inc(rec_in[u], 16)
                        for h in range(2):
                            for half in range(2):
                                src = token_rows(vt, at[g], ctx, half).rearrange("t (j h x) -> h t j x", h=2, j=UN)[h]
                                sp.dma_start(v[u][64 * h + 32 * half:64 * h + 32 * half + 32, g, :, :], src).then_inc(rec_in[u], 16)

                def swap():
                    for g in range(G):
                        sp.wait_ge(s_done[g], NCH_CTX)
                    for g in range(G):
                        for h in range(2):
                            sp.dma_start(states(new_state, g)[h], S[g][64 * h:64 * h + GLA_DK, :, :]).then_inc(state_out, 16)
                    sp.wait_ge(state_out, 64)
                    for g in range(G):
                        for h in range(2):
                            sp.dma_start(S[g][64 * h:64 * h + GLA_DK, :, :], states(state_in, g)[h]).then_inc(state_in_s, 16)
                both(sp, load, swap)

            @block.gpsimd
            def _(pool):
                pool.wait_ge(con_in, 16)

                def chunk(u, m, c, at, ctx):
                    n = c + 1
                    pool.wait_ge(rec_in[u], 160 * m)
                    for g in range(G):
                        pool.wait_ge(absd[g], c)
                        b = rec[u][:, g, :, (2 + g) * C:(3 + g) * C]
                        for l in range(LEVELS):
                            h = 1 << l
                            m_at = h - 1 if g == 0 else h
                            bl = b.rearrange("p j (s w) -> p j s w", w=2 * h)
                            out = Dd[g][:, l, :, :].rearrange("p j (s w) -> p j s w", w=2 * h)
                            pool.tensor_tensor(out, bl, bl[:, :, :, m_at:m_at + 1].to_broadcast([P, UN, C // (2 * h), 2 * h]), ALU.subtract)
                        end = C - 1 if g == 0 else 0
                        pool.tensor_tensor(Dd[g][:, LEVELS + 1, :, :], b, b[:, :, end:end + 1].to_broadcast([P, UN, C]), ALU.subtract).then_inc(diffs[g], 1)
                        pool.wait_ge(o_mm[g], c)
                        for q, out in ((0, qo), (1, ko)):
                            src = rec[u][:, g, :, q * C:(q + 1) * C].unsqueeze(2).to_broadcast([P, UN, 2, C])
                            last = pool.tensor_tensor(out[g][:, :, :, :], src, own.unsqueeze(1).unsqueeze(3).to_broadcast([P, UN, 2, C]), ALU.mult)
                        last.then_inc(owned[g], 1)
                    for g in range(G):
                        pool.wait_ge(owned[g], n)
                        pool.wait_ge(expd[g], n)
                        q = rec[u][:, g, :, 0:C].unsqueeze(1).to_broadcast([P, LEVELS, UN, C])
                        pool.tensor_tensor(QF[g][:, :, :, :], q, F[g][:, 0:LEVELS, :, :], ALU.mult).then_inc(qf_done[g], 1)
                        for src, slot, out in ((qo, LEVELS, qe), (ko, LEVELS + 1, kh)):
                            last = pool.tensor_tensor(out[g][:, :, :, :], src[g][:, :, :, :], F[g][:, slot, :, :].unsqueeze(2).to_broadcast([P, UN, 2, C]), ALU.mult)
                        last.then_inc(qk_bd[g], 1)
                    for g in range(G):
                        pool.wait_ge(att_sum[g], n)
                        pool.tensor_tensor(ad[g][:, :, :, :], at_[g][:, :, :].unsqueeze(2).to_broadcast([P, UN, 2, C]),
                                           own.unsqueeze(1).unsqueeze(3).to_broadcast([P, UN, 2, C]), ALU.mult).then_inc(att_bd[g], 1)
                both(pool, chunk, nothing)

            @block.scalar
            def _(act):
                def chunk(u, m, c, at, ctx):
                    n = c + 1
                    for g in range(G):
                        act.wait_ge(rec_in[u], 160 * m)
                        act.wait_ge(absd[g], c)
                        act.activation(Dd[g][:, LEVELS, :, :], rec[u][:, g, :, (2 + g) * C:(3 + g) * C], ACT.Copy).then_inc(slot6[g], 1)
                        act.wait_ge(slot6[g], n)
                        act.wait_ge(diffs[g], n)
                        act.wait_ge(qk_bd[g], c)
                        act.wait_ge(kf_done[g], c)
                        act.wait_ge(s_done[g], c)
                        act.activation(F[g][:, :, :, :], Dd[g][:, :, :, :], ACT.Abs).then_inc(absd[g], 1)
                        act.wait_ge(absd[g], n)
                        act.activation(F[g][:, :, :, :], F[g][:, :, :, :], ACT.Exp, scale=-1.0 / 16.0).then_inc(expd[g], 1)
                    for g in range(G):
                        act.wait_ge(kT_mm[g], n)
                        act.copy(kT[g][:, :, :], pK[g][:, 0:UN * P].rearrange("p (j k) -> p j k", j=UN)).then_inc(kT_done[g], 1)
                    for g in range(G):
                        act.wait_ge(o_mm[g], n)
                        act.wait_ge(o_out[g][u], 64 * (m - 1))
                        act.copy(Os[g][u][:, :, :], pK[g][:, 0:UN * GLA_DV].rearrange("p (j x) -> p j x", j=UN)).then_inc(o_done[g], 1)
                        act.wait_ge(o_done[g], n)
                        for h in range(2):
                            for half in range(2):
                                dst = token_rows(o[g], at[g], ctx, half).rearrange("t (j h x) -> h t j x", h=2, j=UN)[h]
                                act.dma_start(dst, Os[g][u][64 * h + 32 * half:64 * h + 32 * half + 32, :, :]).then_inc(o_out[g][u], 16)
                both(act, chunk, nothing)
                for g in range(G):
                    for u in range(2):
                        act.wait_ge(o_out[g][u], 64 * NCH // 2)

            @block.tensor
            def _(pe):
                pe.wait_ge(con_in, 16)
                pe.wait_ge(state0, G)

                def flat(ap):
                    return ap.rearrange("p h t -> p (h t)")

                def chunk(u, m, c, at, ctx):
                    n = c + 1
                    for g in range(G):
                        pe.wait_ge(qk_bd[g], n)
                        pe.wait_ge(o_done[g], c)
                        for j in range(UN):
                            mm = pe.transpose(pK[g][:, j * P:(j + 1) * P], flat(kh[g][:, j, :, :]), eye128)
                        mm.then_inc(kT_mm[g], 1)
                        pe.wait_ge(kf_done[g], n)
                        pe.wait_ge(masked[g], c)
                        for l in range(NA):
                            for j in range(UN):
                                ps = pA[g] if l < CA else pB[g]
                                x = (l % CA * UN + j) * C
                                if l < LEVELS:
                                    mm = pe.matmul(ps[:, x:x + C], flat(KF[g][:, j, l, :, :]), QF[g][:, l, j, :], start=True, stop=True)
                                else:
                                    mm = pe.matmul(ps[:, x:x + C], flat(ko[g][:, j, :, :]), rec[u][:, g, j, 0:C], start=True, stop=True)
                            if l in (CA - 1, NA - 1):
                                mm.then_inc((att_a if l < CA else att_b)[g], 1)
                    for g in range(G):
                        pe.wait_ge(kT_done[g], n)
                        pe.wait_ge(s_done[g], c)
                        for j in range(UN):
                            mm = pe.matmul(pS[g][:, j * GLA_DV:(j + 1) * GLA_DV], kT[g][:, j, :], v[u][:, g, j, :], start=True, stop=True)
                        pe.wait_ge(att_bd[g], n)
                        for j in range(UN):
                            out = pK[g][:, j * GLA_DV:(j + 1) * GLA_DV]
                            pe.matmul(out, flat(qe[g][:, j, :, :]), S[g][:, j, :], start=True, stop=False)
                            mm = pe.matmul(out, flat(ad[g][:, j, :, :]), v[u][:, g, j, :], start=False, stop=True)
                        mm.then_inc(o_mm[g], 1)

                def swap():
                    pe.wait_ge(state_in_s, 64)
                both(pe, chunk, swap)

            @block.vector
            def _(dve):
                for g in range(G):
                    dve.memset(S[g][:, :, :], 0.0).then_inc(state0, 1)
                dve.wait_ge(con_in, 16)

                def chunk(u, m, c, at, ctx):
                    n = c + 1
                    for g in range(G):
                        dve.wait_ge(owned[g], n)
                        dve.wait_ge(expd[g], n)
                        dve.wait_ge(att_b[g], c)
                        for j in range(UN):
                            last = dve.tensor_tensor(KF[g][:, j, :, :, :], ko[g][:, j, :, :].unsqueeze(1).to_broadcast([P, LEVELS, 2, C]),
                                                     F[g][:, 0:LEVELS, j, :].unsqueeze(2).to_broadcast([P, LEVELS, 2, C]), ALU.mult)
                        last.then_inc(kf_done[g], 1)
                    for g in range(G):
                        dve.wait_ge(att_a[g], n)
                        dve.tensor_tensor(AM[g][:, 0:CA, :, :], pA[g][:, 0:CA * UN * C].rearrange("p (l j t) -> p l j t", l=CA, j=UN),
                                          mask[g][:, 0:CA, :].unsqueeze(2).to_broadcast([P, CA, UN, C]), ALU.mult)
                        dve.wait_ge(att_b[g], n)
                        dve.tensor_tensor(AM[g][:, CA:NA, :, :], pB[g][:, 0:(NA - CA) * UN * C].rearrange("p (l j t) -> p l j t", l=NA - CA, j=UN),
                                          mask[g][:, CA:NA, :].unsqueeze(2).to_broadcast([P, NA - CA, UN, C]), ALU.mult).then_inc(masked[g], 1)
                        dve.wait_ge(masked[g], n)
                        dve.reduce_sum(at_[g][:, :, :].rearrange("p j t -> p (j t)"), AM[g][:, :, :, :].rearrange("p l j t -> p (j t) l"), AX.X).then_inc(att_sum[g], 1)
                    for g in range(G):
                        dve.wait_ge(o_mm[g], n)
                        end = C - 1 if g == 0 else 0
                        for j in range(UN):
                            last = dve.scalar_tensor_tensor(S[g][:, j, :], S[g][:, j, :], F[g][:, LEVELS, j, end:end + 1],
                                                            pS[g][:, j * GLA_DV:(j + 1) * GLA_DV], ALU.mult, ALU.add)
                        last.then_inc(s_done[g], 1)

                def swap():
                    dve.wait_ge(state_in_s, 64)
                both(dve, chunk, swap)


def stage_gla_post(nc, o, proj, norm_w, ident_d, mixT):
    UN = D_GLA // P
    GATE0 = GLA0 + 2 * D_GLA_K + D_GLA
    with Stage(nc, "glo") as st:
        ident, par = st.sb("ident", [P, P]), st.sb("par", [P, UN])
        of, ob, sq = ([st.sb(f"{x}{u}", [P, D_GLA]) for u in range(2)] for x in ("of", "ob", "sq"))
        ga, mix = ([st.sb(f"{x}{u}", [P, UN, P]) for u in range(2)] for x in ("ga", "mix"))
        stat = [st.sb(f"stat{u}", [P, 4, GLA_HEADS]) for u in range(2)]
        ps = [st.ps(f"t{u}") for u in range(2)]
        par_in = st.sem("par_in")
        tile_in, added, squared, silud, var, root, rstd, normed, turned, mixed, stored = (st.sem2(n) for n in (
            "tile_in", "added", "squared", "silud", "var", "root", "rstd", "normed", "turned", "mixed", "stored"))

        def heads(ap):
            return ap.rearrange("p (h v) -> p h v", v=GLA_DV)

        def rows(tile):
            return bass.ds(tile * P, P)

        with st.block() as block:
            @block.sync
            def _(sp):
                sp.dma_start(ident[:, :], ident_d).then_inc(par_in, 16)
                for j in range(UN):
                    sp.dma_start(par[:, j:j + 1], norm_w[0].rearrange("h v -> (h v)")[j * P:(j + 1) * P].unsqueeze(1)).then_inc(par_in, 16)

                def load(u, n, tile, seg):
                    sp.wait_ge(mixed[u], n - 1)
                    sp.dma_start(of[u][:, :], o[0, rows(tile), :]).then_inc(tile_in[u], 16)
                    sp.dma_start(ob[u][:, :], o[1, rows(tile), :]).then_inc(tile_in[u], 16)
                    sp.dma_start(ga[u][:, :, :], proj[GATE0:GATE0 + D_GLA, rows(tile)].rearrange("(j p) t -> p j t", p=P)).then_inc(tile_in[u], 16)
                paired(sp, load, 8)

            @block.gpsimd
            def _(pool):
                def store(u, n, tile, seg):
                    pool.wait_ge(par_in, 16 * (1 + UN))
                    pool.wait_ge(mixed[u], n)
                    pool.dma_start(mixT[D_LRU + D_RW:D, rows(tile)].rearrange("(j p) t -> p j t", p=P), mix[u][:, :, :]).then_inc(stored[u], 16)
                paired(pool, store, 8)
                for u in range(2):
                    pool.wait_ge(stored[u], 16 * (9 - u))

            @block.scalar
            def _(act):
                def body(u, n, tile, seg):
                    act.wait_ge(tile_in[u], 48 * n)
                    act.activation(ga[u][:, :, :], ga[u][:, :, :], ACT.Silu).then_inc(silud[u], 1)
                    act.wait_ge(added[u], n)
                    act.activation(sq[u][:, :], of[u][:, :], ACT.Square).then_inc(squared[u], 1)
                    act.wait_ge(var[u], 2 * n)
                    act.activation(stat[u][:, 2, :], stat[u][:, 1, :], ACT.Sqrt).then_inc(root[u], 1)
                paired(act, body, 8)

            @block.tensor
            def _(pe):
                pe.wait_ge(par_in, 16 * (1 + UN))

                def body(u, n, tile, seg):
                    pe.wait_ge(normed[u], n)
                    pe.wait_ge(mixed[u], n - 1)
                    for j in range(UN):
                        mm = pe.transpose(ps[u][:, j * P:(j + 1) * P], of[u][:, j * P:(j + 1) * P], ident[:, :])
                    mm.then_inc(turned[u], 1)
                paired(pe, body, 8)

            @block.vector
            def _(dve):
                dve.wait_ge(par_in, 16 * (1 + UN))

                def body(u, n, tile, seg):
                    s = stat[u]
                    dve.wait_ge(tile_in[u], 48 * n)
                    dve.tensor_tensor(of[u][:, :], of[u][:, :], ob[u][:, :], ALU.add).then_inc(added[u], 1)
                    dve.wait_ge(squared[u], n)
                    dve.reduce_sum(s[:, 1, :], heads(sq[u][:, :]), AX.X).then_inc(var[u], 1)
                    dve.wait_ge(var[u], 2 * n - 1)
                    dve.tensor_scalar(s[:, 1, :], s[:, 1, :], 1.0 / GLA_DV, EPS, ALU.mult, ALU.add).then_inc(var[u], 1)
                    dve.wait_ge(root[u], n)
                    dve.reciprocal(s[:, 3, :], s[:, 2, :]).then_inc(rstd[u], 1)
                    dve.wait_ge(rstd[u], n)
                    dve.tensor_tensor(heads(of[u][:, :]), heads(of[u][:, :]), s[:, 3, :].unsqueeze(2).to_broadcast([P, GLA_HEADS, GLA_DV]), ALU.mult).then_inc(normed[u], 1)
                    dve.wait_ge(turned[u], n)
                    dve.wait_ge(silud[u], n)
                    dve.wait_ge(stored[u], 16 * (n - 1))
                    for j in range(UN):
                        last = dve.scalar_tensor_tensor(mix[u][:, j, :], ps[u][:, j * P:(j + 1) * P], par[:, j:j + 1], ga[u][:, j, :], ALU.mult, ALU.mult)
                    last.then_inc(mixed[u], 1)
                paired(dve, body, 8)


def stage_mix_out(nc, x_prompt, x_sample, mixT, w_out, mods, norm2_g, w_router, ident_d, y, h2, probsT):
    with Stage(nc, "out") as st:
        ident = st.sb("ident", [P, P])
        g_row, scale_row, shift_row = st.sb("g", [P, D]), st.sb("scale", [P, 2, D]), st.sb("shift", [P, 2, D])
        res_row = st.sb("res", [P, 2, D])
        wo, wr = st.sb("wo", [P, KD, D]), st.sb("wr", [P, KD, N_EXP])
        x, y1, h, sq = ([st.sb(f"{n}{u}", [P, D]) for u in range(2)] for n in ("x", "y1", "h", "sq"))
        m = [st.sb(f"m{u}", [P, KD, P]) for u in range(2)]
        hT = [st.sb(f"hT{u}", [P, KD, P]) for u in range(2)]
        ss = [st.sb(f"ss{u}", [P, 8]) for u in range(2)]
        pe_exp = [st.sb(f"e{u}", [P, N_EXP]) for u in range(2)]
        pT = st.sb("pT", [N_EXP, T])
        ps_o = [st.ps(f"o{b}") for b in range(2)]
        ps_t = [st.ps(f"t{b}") for b in range(2)]
        ps_l, ps_p = [st.ps(f"l{u}") for u in range(2)], [st.ps(f"p{u}") for u in range(2)]
        rows_in, w_ld, rows_ready = st.sem("rows_in"), st.sem("w_ld"), st.sem("rows_ready")
        names = ("tile_in", "mixed", "gated", "res_done", "sumsq", "meansq", "root", "rstd", "normed", "h_ready", "turned",
                 "copied", "logits", "top", "ntop", "expd", "inv", "probs", "prob_mm", "prob_out", "y_out", "h_out")
        (tile_in, mixed, gated, res_done, sumsq, meansq, root, rstd, normed, h_ready, turned,
         copied, logits, top, ntop, expd, inv, probs, prob_mm, prob_out, y_out, h_out) = (st.sem2(n) for n in names)
        left, stored = st.sem2("left"), st.sem("stored")

        def x_tile(tile, seg):
            return x_prompt[0] if seg == 0 else x_sample[0, bass.ds((tile - 1) * P, P), :]

        with st.block() as block:
            @block.sync
            def _(sp):
                sp.dma_start(ident[:, :], ident_d).then_inc(w_ld, 16)
                sp.dma_start(wo[:, :, :], w_out[0].rearrange("(k p) n -> p k n", p=P)).then_inc(w_ld, 16)
                sp.dma_start(wr[:, :, :], w_router[0].rearrange("(k p) n -> p k n", p=P)).then_inc(w_ld, 16)
                load_modulated_norm(sp, rows_in, (g_row, scale_row, shift_row), mods, norm2_g, 4, 3)
                for v in range(2):
                    sp.dma_start(res_row[:, v, :], mods[v:v + 1, 2 * D:3 * D].to_broadcast([P, D])).then_inc(rows_in, 16)

                def load(u, n, tile, seg):
                    sp.wait_ge(res_done[u], n - 1)
                    sp.dma_start(x[u][:, :], x_tile(tile, seg)).then_inc(tile_in[u], 16)
                    sp.dma_start(m[u][:, :, :], mixT[:, bass.ds(tile * P, P)].rearrange("(k p) t -> p k t", p=P)).then_inc(tile_in[u], 16)
                paired(sp, load, 8)
                for u in range(2):
                    sp.wait_ge(prob_out[u], 9 - u)
                sp.dma_start(probsT, pT[:, :]).then_inc(stored, 16)
                sp.wait_ge(stored, 16)

            @block.gpsimd
            def _(pool):
                def store(u, n, tile, seg):
                    rows = bass.ds(tile * P, P)
                    pool.wait_ge(w_ld, 48)
                    pool.wait_ge(res_done[u], n)
                    pool.dma_start(y[rows, :], y1[u][:, :]).then_inc(y_out[u], 16)
                    pool.wait_ge(w_ld, 48)
                    pool.wait_ge(h_ready[u], n)
                    pool.dma_start(h2[rows, :], h[u][:, :]).then_inc(h_out[u], 16)
                paired(pool, store, 8)
                for u in range(2):
                    pool.wait_ge(y_out[u], 16 * (9 - u))
                    pool.wait_ge(h_out[u], 16 * (9 - u))

            @block.tensor
            def _(pe):
                pe.wait_ge(w_ld, 48)

                def body(u, n, tile, seg):
                    pe.wait_ge(tile_in[u], 32 * n)
                    for half in range(2):
                        pe.wait_ge(left[half], tile)
                        for k in range(KD):
                            mm = pe.matmul(ps_o[half][:, :], m[u][:, k, :], wo[:, k, half * BANK:(half + 1) * BANK], start=k == 0, stop=k == KD - 1)
                        mm.then_inc(mixed[u], 1)
                    pe.wait_ge(h_ready[u], n)
                    for half in range(2):
                        pe.wait_ge(copied[half], tile)
                        for k in range(4):
                            mm = pe.transpose(ps_t[half][:, k * P:(k + 1) * P], h[u][:, (4 * half + k) * P:(4 * half + k + 1) * P], ident[:, :])
                        mm.then_inc(turned[half], 1)
                    for half in range(2):
                        pe.wait_ge(copied[half], tile + 1)
                    for k in range(KD):
                        mm = pe.matmul(ps_l[u][:, 0:N_EXP], hT[u][:, k, :], wr[:, k, :], start=k == 0, stop=k == KD - 1)
                    mm.then_inc(logits[u], 1)
                    pe.wait_ge(probs[u], n)
                    pe.transpose(ps_p[u][0:N_EXP, 0:P], pe_exp[u][:, :], ident[:, :]).then_inc(prob_mm[u], 1)
                paired(pe, body, 8)

            @block.scalar
            def _(act):
                def body(u, n, tile, seg):
                    act.wait_ge(res_done[u], n)
                    act.activation(sq[u][:, :], y1[u][:, :], ACT.Square, accum_out=ss[u][:, 0:1]).then_inc(sumsq[u], 1)
                    act.wait_ge(meansq[u], n)
                    act.activation(ss[u][:, 2:3], ss[u][:, 1:2], ACT.Sqrt).then_inc(root[u], 1)
                    act.wait_ge(turned[1], tile + 1)
                    act.copy(hT[u][:, 4:8, :], ps_t[1][:, :].rearrange("p (k t) -> p k t", k=4)).then_inc(copied[1], 1)
                    act.wait_ge(ntop[u], n)
                    act.activation(pe_exp[u][:, :], ps_l[u][:, 0:N_EXP], ACT.Exp, bias=ss[u][:, 5:6], accum_out=ss[u][:, 6:7]).then_inc(expd[u], 1)
                paired(act, body, 8)

            @block.vector
            def _(dve):
                dve.wait_ge(rows_in, 7 * 16)
                for v in range(2):
                    dve.scalar_tensor_tensor(scale_row[:, v, :], scale_row[:, v, :], 1.0, g_row[:, :], ALU.add, ALU.mult).then_inc(rows_ready, 1)
                dve.wait_ge(rows_ready, 2)

                def body(u, n, tile, seg):
                    dve.wait_ge(tile_in[u], 32 * n)
                    dve.wait_ge(y_out[u], 16 * (n - 1))
                    dve.wait_ge(sumsq[u], n - 1)
                    for half in range(2):
                        cols = slice(half * BANK, (half + 1) * BANK)
                        dve.wait_ge(mixed[u], 2 * (n - 1) + half + 1)
                        dve.tensor_tensor(y1[u][:, cols], ps_o[half][:, :], res_row[:, seg, cols], ALU.mult).then_inc(left[half], 1)
                    for half in range(2):
                        dve.wait_ge(left[half], tile + 1)
                    dve.tensor_tensor(y1[u][:, :], y1[u][:, :], x[u][:, :], ALU.add).then_inc(res_done[u], 1)
                    dve.wait_ge(sumsq[u], n)
                    dve.tensor_scalar(ss[u][:, 1:2], ss[u][:, 0:1], 1.0 / D, EPS, ALU.mult, ALU.add).then_inc(meansq[u], 1)
                    dve.wait_ge(root[u], n)
                    dve.reciprocal(ss[u][:, 3:4], ss[u][:, 2:3]).then_inc(rstd[u], 1)
                    dve.wait_ge(rstd[u], n)
                    dve.wait_ge(h_out[u], 16 * (n - 1))
                    dve.scalar_tensor_tensor(h[u][:, :], y1[u][:, :], ss[u][:, 3:4], scale_row[:, seg, :], ALU.mult, ALU.mult).then_inc(normed[u], 1)
                    dve.wait_ge(normed[u], n)
                    dve.tensor_tensor(h[u][:, :], h[u][:, :], shift_row[:, seg, :], ALU.add).then_inc(h_ready[u], 1)
                    dve.wait_ge(turned[0], tile + 1)
                    dve.tensor_copy(hT[u][:, 0:4, :], ps_t[0][:, :].rearrange("p (k t) -> p k t", k=4)).then_inc(copied[0], 1)
                    dve.wait_ge(logits[u], n)
                    dve.reduce_max(ss[u][:, 4:5], ps_l[u][:, 0:N_EXP], AX.X).then_inc(top[u], 1)
                    dve.wait_ge(top[u], n)
                    dve.tensor_scalar(ss[u][:, 5:6], ss[u][:, 4:5], -1.0, None, ALU.mult).then_inc(ntop[u], 1)
                    dve.wait_ge(expd[u], n)
                    dve.reciprocal(ss[u][:, 7:8], ss[u][:, 6:7]).then_inc(inv[u], 1)
                    dve.wait_ge(inv[u], n)
                    dve.tensor_scalar(pe_exp[u][:, :], pe_exp[u][:, :], ss[u][:, 7:8], None, ALU.mult).then_inc(probs[u], 1)
                    dve.wait_ge(prob_mm[u], n)
                    dve.tensor_copy(pT[:, bass.ds(tile * P, P)], ps_p[u][0:N_EXP, 0:P]).then_inc(prob_out[u], 1)
                paired(dve, body, 8)


def stage_route(nc, probsT, ident_d, slot_rows, slot_gates):
    N_SLOT = CAP_LAT + CAP_CTX
    with Stage(nc, "rte") as st:
        ident = st.sb("ident", [P, P])
        work = st.sb("work", [N_EXP, T])
        top8, idx8 = st.sb("top8", [N_EXP, 8]), st.sb("idx8", [N_EXP, 8], U32)
        gates, idx = st.sb("gates", [N_EXP, N_SLOT]), st.sb("idx", [N_EXP, N_SLOT], U32)
        rows_f = st.sb("rows_f", [N_EXP, N_SLOT])
        gT, rT = st.sb("gT", [P, 3, N_EXP]), st.sb("rT", [P, 3, N_EXP], U32)
        ps_g, ps_r = st.ps("g"), st.ps("r")
        ld, found, kept, rows_done, turned_g, turned_r, out_done, stored = (st.sem(n) for n in (
            "ld", "found", "kept", "rows_done", "turned_g", "turned_r", "out_done", "stored"))
        blocks = [(0, P), (P, P), (CAP_LAT, CAP_CTX)]
        with st.block() as block:
            @block.sync
            def _(sp):
                sp.dma_start(work[:, :], probsT).then_inc(ld, 16)
                sp.dma_start(ident[:, :], ident_d).then_inc(ld, 16)
                sp.wait_ge(out_done, 8)
                sp.dma_start(slot_rows, rT[:, :, :]).then_inc(stored, 16)
                sp.dma_start(slot_gates, gT[:, :, :]).then_inc(stored, 16)
                sp.wait_ge(stored, 32)

            @block.vector
            def _(dve):
                dve.memset(gT[:, 2, :], 0.0).then_inc(out_done, 1)
                dve.memset(rT[:, 2, :], 0).then_inc(out_done, 1)
                dve.wait_ge(out_done, 2)
                dve.wait_ge(ld, 32)

                def eight(tokens, slot, n):
                    dve.max(top8[:, :], tokens).then_inc(found, 1)
                    dve.wait_ge(found, 3 * n + 1)
                    dve.tensor_copy(gates[:, bass.ds(slot, 8)], top8[:, :]).then_inc(kept, 1)
                    dve.max_index(idx8[:, :], top8[:, :], tokens).then_inc(found, 1)
                    dve.match_replace(tokens, top8[:, :], tokens, -1.0).then_inc(found, 1)
                    dve.wait_ge(found, 3 * n + 3)
                    dve.tensor_copy(idx[:, bass.ds(slot, 8)], idx8[:, :]).then_inc(kept, 1)

                for n in range(CAP_CTX // 8):
                    eight(work[:, 0:T_CTX], CAP_LAT + 8 * n, n)
                with dve.Fori(0, CAP_LAT // 8) as i:
                    eight(work[:, T_CTX:T], 8 * i, i + CAP_CTX // 8)
                dve.wait_ge(kept, 2 * N_SLOT // 8)
                dve.tensor_scalar(rows_f[:, 0:CAP_LAT], idx[:, 0:CAP_LAT], float(T_CTX), None, ALU.add).then_inc(rows_done, 1)
                dve.tensor_copy(rows_f[:, CAP_LAT:], idx[:, CAP_LAT:]).then_inc(rows_done, 1)
                dve.wait_ge(turned_g, 1)
                for b, (s0, n) in enumerate(blocks):
                    dve.tensor_copy(gT[0:n, b, :], ps_g[0:n, b * N_EXP:(b + 1) * N_EXP]).then_inc(out_done, 1)
                dve.wait_ge(turned_r, 1)
                for b, (s0, n) in enumerate(blocks):
                    dve.tensor_copy(rT[0:n, b, :], ps_r[0:n, b * N_EXP:(b + 1) * N_EXP]).then_inc(out_done, 1)

            @block.tensor
            def _(pe):
                pe.wait_ge(ld, 32)
                pe.wait_ge(rows_done, 2)
                pe.wait_ge(kept, 2 * N_SLOT // 8)
                for src, ps, done in ((gates, ps_g, turned_g), (rows_f, ps_r, turned_r)):
                    for b, (s0, n) in enumerate(blocks):
                        mm = pe.transpose(ps[0:n, b * N_EXP:(b + 1) * N_EXP], src[:, s0:s0 + n], ident[0:N_EXP, 0:N_EXP])
                    mm.then_inc(done, 1)


def stage_experts(nc, h2, y, mods, slot_rows, slot_gates, w_gate, w_up, w_down, ident_d):
    blocks = [(0, P), (P, P), (CAP_LAT, CAP_CTX)]
    N_SLOT = CAP_LAT + CAP_CTX
    KE = D_EXP // P
    PARTS, PW = 4, D_EXP // 4
    with Stage(nc, "exp") as st:
        ident = st.sb("ident", [P, P])
        rows_all, gates_all = st.sb("rows_all", [P, 3, N_EXP], U32), st.sb("gates_all", [P, 3, N_EXP])
        res_row = st.sb("res", [P, 2, D])
        wg, wu, wd = (st.sb(n, [P, KD, D]) for n in ("wg", "wu", "wd"))
        xs, yo = st.sb("xs", [P, 3, D]), st.sb("yo", [P, 3, D])
        xT, hid, sil = st.sb("xT", [P, KD, N_SLOT]), st.sb("hid", [P, KE, N_SLOT]), st.sb("sil", [P, 2, N_SLOT])
        ps_t, ps_g, ps_u, ps_o = ([st.ps(f"{n}{b}") for b in range(2)] for n in ("t", "g", "u", "o"))
        par_in, part_in = st.sem("par_in"), [[st.sem(f"{n}{q}") for q in range(PARTS)] for n in ("wg_in", "wu_in", "wd_in")]
        gathered, turned = st.sem("gathered"), st.sem("turned")
        taken, down_free = st.sem2("taken"), st.sem2("down_free")
        part_free = [st.sem(f"part_free{q}") for q in range(PARTS)]
        gate_mm, up_mm, silu_done, hid_done, down_mm, scaled, scattered = (st.sem(n) for n in (
            "gate_mm", "up_mm", "silu_done", "hid_done", "down_mm", "scaled", "scattered"))

        def experts(eng, body):
            with eng.Fori(0, N_EXP) as e:
                body(e)

        with st.block() as block:
            @block.sync
            def _(sp):
                sp.dma_start(ident[:, :], ident_d).then_inc(par_in, 16)
                sp.dma_start(rows_all[:, :, :], slot_rows).then_inc(par_in, 16)
                sp.dma_start(gates_all[:, :, :], slot_gates).then_inc(par_in, 16)
                for v in range(2):
                    sp.dma_start(res_row[:, v, :], mods[v:v + 1, 5 * D:6 * D].to_broadcast([P, D])).then_inc(par_in, 16)

                def body(e):
                    for q in range(PARTS):
                        sp.wait_ge(part_free[q], e)
                        for w, src, done in ((wg, w_gate, part_in[0]), (wu, w_up, part_in[1])):
                            sp.dma_start(w[:, :, q * PW:(q + 1) * PW], src[0, bass.ds(e, 1)].squeeze(0).rearrange("(k p) n -> p k n", p=P)[:, :, q * PW:(q + 1) * PW]).then_inc(done[q], 16)
                    for q in range(2):
                        sp.wait_ge(down_free[q], e)
                        cols = slice(q * BANK, (q + 1) * BANK)
                        sp.dma_start(wd[:, :, cols], w_down[0, bass.ds(e, 1)].squeeze(0).rearrange("(k p) n -> p k n", p=P)[:, :, cols]).then_inc(part_in[2][q], 16)
                experts(sp, body)

            @block.gpsimd
            def _(pool):
                pool.wait_ge(par_in, 80)
                for e in range(N_EXP):
                    if e:
                        pool.wait_ge(turned, KD * e)
                    for b, (s0, n) in enumerate(blocks):
                        pool.indirect_dma_start(out=xs[0:n, b, :], out_offset=None, in_=h2,
                                                in_offset=bass.IndirectOffsetOnAxis(ap=rows_all[0:n, b, e:e + 1], axis=0)).then_inc(gathered, 16)
                    if e:
                        pool.wait_ge(scattered, 48 * e)
                    for b, (s0, n) in enumerate(blocks):
                        pool.wait_ge(scaled, 6 * e + 3 + b + 1)
                        pool.indirect_dma_start(out=y, out_offset=bass.IndirectOffsetOnAxis(ap=rows_all[0:n, b, e:e + 1], axis=0),
                                                in_=yo[0:n, b, :], in_offset=None, compute_op=ALU.add).then_inc(scattered, 16)
                pool.wait_ge(scattered, 48 * N_EXP)

            @block.tensor
            def _(pe):
                pe.wait_ge(par_in, 80)

                def body(e):
                    pe.wait_ge(gathered, 48 * (e + 1))
                    for k in range(KD):
                        pe.wait_ge(taken[k % 2], KD // 2 * e + k // 2)
                        for b, (s0, n) in enumerate(blocks):
                            mm = pe.transpose(ps_t[k % 2][:, s0:s0 + n], xs[0:n, b, k * P:(k + 1) * P], ident[0:n, 0:n])
                        mm.then_inc(turned, 1)
                    for k in range(2):
                        pe.wait_ge(taken[k], KD // 2 * (e + 1))
                    for f in range(KE):
                        q, u = f * P // PW, f % 2
                        pe.wait_ge(part_in[0][q], 16 * (e + 1))
                        pe.wait_ge(part_in[1][q], 16 * (e + 1))
                        if f >= 2:
                            pe.wait_ge(hid_done, KE * e + f - 1)
                        for w, ps, done in ((wg, ps_g, gate_mm), (wu, ps_u, up_mm)):
                            for k in range(KD):
                                mm = pe.matmul(ps[u][:, 0:N_SLOT], w[:, k, f * P:(f + 1) * P], xT[:, k, :], start=k == 0, stop=k == KD - 1)
                            mm.then_inc(part_free[q] if done is up_mm and f % 2 else done, 1)
                    pe.wait_ge(hid_done, KE * (e + 1))
                    i = 0
                    for half in range(2):
                        pe.wait_ge(part_in[2][half], 16 * (e + 1))
                        for b, (s0, n) in enumerate(blocks):
                            if i >= 2:
                                pe.wait_ge(scaled, 6 * e + i - 1)
                            else:
                                pe.wait_ge(scaled, 6 * e)
                            for k in range(KE):
                                mm = pe.matmul(ps_o[i % 2][0:n, :], hid[:, k, s0:s0 + n], wd[:, k, half * BANK:(half + 1) * BANK], start=k == 0, stop=k == KE - 1)
                            mm.then_inc(down_free[half] if b == 2 else down_mm, 1)
                            i += 1
                experts(pe, body)

            @block.scalar
            def _(act):
                def body(e):
                    for k in range(1, KD, 2):
                        act.wait_ge(turned, KD * e + k + 1)
                        act.copy(xT[:, k, :], ps_t[1][:, 0:N_SLOT]).then_inc(taken[1], 1)
                    for f in range(KE):
                        act.wait_ge(gate_mm, KE * e + f + 1)
                        if f >= 2:
                            act.wait_ge(hid_done, KE * e + f - 1)
                        act.activation(sil[:, f % 2, :], ps_g[f % 2][:, 0:N_SLOT], ACT.Silu).then_inc(silu_done, 1)
                experts(act, body)

            @block.vector
            def _(dve):
                dve.wait_ge(par_in, 80)

                def body(e):
                    for k in range(0, KD, 2):
                        dve.wait_ge(turned, KD * e + k + 1)
                        dve.tensor_copy(xT[:, k, :], ps_t[0][:, 0:N_SLOT]).then_inc(taken[0], 1)
                    for f in range(KE):
                        dve.wait_ge(silu_done, KE * e + f + 1)
                        if f % 2:
                            dve.wait_ge(part_free[f // 2], e + 1)
                        else:
                            dve.wait_ge(up_mm, KE // 2 * e + f // 2 + 1)
                        dve.tensor_tensor(hid[:, f, :], ps_u[f % 2][:, 0:N_SLOT], sil[:, f % 2, :], ALU.mult).then_inc(hid_done, 1)
                    dve.wait_ge(par_in, 80)
                    dve.wait_ge(scattered, 48 * e)
                    i = 0
                    for half in range(2):
                        cols = slice(half * BANK, (half + 1) * BANK)
                        for b, (s0, n) in enumerate(blocks):
                            if b == 2:
                                dve.wait_ge(down_free[half], e + 1)
                            else:
                                dve.wait_ge(down_mm, 4 * e + 2 * half + b + 1)
                            dve.scalar_tensor_tensor(yo[0:n, b, cols], ps_o[i % 2][0:n, :], gates_all[0:n, b, bass.ds(e, 1)],
                                                     res_row[0:n, 0 if b == 2 else 1, cols], ALU.mult, ALU.mult).then_inc(scaled, 1)
                            i += 1
                experts(dve, body)


def stage_final(nc, y, final_g, y_prompt, y_sample):
    with Stage(nc, "fin") as st:
        g_row = st.sb("g", [P, D])
        x, sq, out = ([st.sb(f"{n}{u}", [P, D]) for u in range(2)] for n in ("x", "sq", "o"))
        ss = [st.sb(f"ss{u}", [P, 4]) for u in range(2)]
        row_in = st.sem("row_in")
        x_in, sumsq, meansq, root, rstd, normed, stored = (st.sem2(n) for n in ("x_in", "sumsq", "meansq", "root", "rstd", "normed", "stored"))
        with st.block() as block:
            @block.sync
            def _(sp):
                sp.dma_start(g_row[:, :], final_g.unsqueeze(0).to_broadcast([P, D])).then_inc(row_in, 16)

                def load(u, n, tile, seg):
                    sp.wait_ge(normed[u], n - 1)
                    sp.dma_start(x[u][:, :], y[bass.ds(tile * P, P), :]).then_inc(x_in[u], 16)
                paired(sp, load, 8)

            @block.gpsimd
            def _(pool):
                def store(u, n, tile, seg):
                    pool.wait_ge(row_in, 16)
                    pool.wait_ge(normed[u], n)
                    dst = y_prompt[0] if seg == 0 else y_sample[0, bass.ds((tile - 1) * P, P), :]
                    pool.dma_start(dst, out[u][:, :]).then_inc(stored[u], 16)
                paired(pool, store, 8)
                for u in range(2):
                    pool.wait_ge(stored[u], 16 * (9 - u))

            @block.scalar
            def _(act):
                def body(u, n, tile, seg):
                    act.wait_ge(x_in[u], 16 * n)
                    act.activation(sq[u][:, :], x[u][:, :], ACT.Square, accum_out=ss[u][:, 0:1]).then_inc(sumsq[u], 1)
                    act.wait_ge(meansq[u], n)
                    act.activation(ss[u][:, 2:3], ss[u][:, 1:2], ACT.Sqrt).then_inc(root[u], 1)
                paired(act, body, 8)

            @block.vector
            def _(dve):
                dve.wait_ge(row_in, 16)

                def body(u, n, tile, seg):
                    dve.wait_ge(sumsq[u], n)
                    dve.tensor_scalar(ss[u][:, 1:2], ss[u][:, 0:1], 1.0 / D, EPS, ALU.mult, ALU.add).then_inc(meansq[u], 1)
                    dve.wait_ge(root[u], n)
                    dve.reciprocal(ss[u][:, 3:4], ss[u][:, 2:3]).then_inc(rstd[u], 1)
                    dve.wait_ge(rstd[u], n)
                    dve.wait_ge(stored[u], 16 * (n - 1))
                    dve.scalar_tensor_tensor(out[u][:, :], x[u][:, :], ss[u][:, 3:4], g_row[:, :], ALU.mult, ALU.mult).then_inc(normed[u], 1)
                paired(dve, body, 8)


def build_program(nc, a):
    def scratch(name, shape, dt=F32):
        return nc.dram_tensor(name, list(shape), dt, kind="Internal").ap()

    mods, proj, mixT = scratch("mods", (2, 6 * D)), scratch("proj", (N_IN, T)), scratch("mixT", (D, T))
    rec, gate, bonus = scratch("rec", (D_RW // P * 2, P, NCH, REC)), scratch("gate", (D_RW, T)), scratch("bonus", (D_RW, T))
    o_rw, o_gla = scratch("o_rw", (2, T, D_RW)), scratch("o_gla", (2, T, D_GLA))
    vt, grec = scratch("vt", (T, D_GLA)), scratch("grec", (GLA_HEADS // 2, P, NCH, GREC))
    y, h2, probsT = scratch("y", (T, D)), scratch("h2", (T, D)), scratch("probsT", (N_EXP, T))
    slot_rows, slot_gates = scratch("slot_rows", (P, 3, N_EXP), U32), scratch("slot_gates", (P, 3, N_EXP))

    stage_modulation(nc, a["c"], a["c_ctx"], a["w_ada"], a["b_ada"], mods)
    stage_project(nc, a["x_prompt"], a["x_sample"], a["norm1_g"], mods, a["w_in"], a["ident"], proj)
    stage_lru(nc, proj, *(a["lru_" + n] for n in ("conv_w", "conv_b", "wa", "ba", "wx", "bx", "lambda")), a["state_lru"], mixT, a["new_lru"])
    stage_rwkv_prep(nc, proj, *(a["rw_" + n] for n in ("mu", "w0", "w2", "a0", "a2", "g2", "kk", "ka", "rk")), a["head_ones"], rec, gate, bonus)
    stage_rwkv_scan(nc, rec, a["rwkv_con"], a["state_rwkv"], a["new_rwkv"], o_rw)
    stage_rwkv_post(nc, o_rw, bonus, gate, a["rw_ln_w"], a["rw_ln_b"], a["ident"], mixT)
    stage_gla_turn(nc, proj, a["ident"], vt)
    stage_gla_prep(nc, proj, a["gla_wg2"], a["gla_bg"], grec)
    stage_gla_scan(nc, grec, vt, a["gla_con"], a["state_gla"], a["new_gla"], o_gla)
    stage_gla_post(nc, o_gla, proj, a["gla_norm_w"], a["ident"], mixT)
    stage_mix_out(nc, a["x_prompt"], a["x_sample"], mixT, a["w_out"], mods, a["norm2_g"], a["w_router"], a["ident"], y, h2, probsT)
    stage_route(nc, probsT, a["ident"], slot_rows, slot_gates)
    stage_experts(nc, h2, y, mods, slot_rows, slot_gates, a["w_gate"], a["w_up"], a["w_down"], a["ident"])
    stage_final(nc, y, a["final_norm_g"], a["y_prompt"], a["y_sample"])


_OUTS = [("y_prompt", (1, T_CTX, D)), ("y_sample", (1, T_LAT, D)), ("new_lru", (1, 1, 2, D_LRU)),
         ("new_rwkv", (1, 1, 2, RW_HEADS, RW_HD, RW_HD)), ("new_gla", (1, 1, 2, GLA_HEADS, GLA_DK, GLA_DV))]


def kernel(**inputs):
    import concourse.bacc as _bacc
    from concourse.bass_utils import run_bass_kernel_spmd as _run

    nc = _bacc.Bacc("TRN2", target_bir_lowering=False, num_devices=1)
    constants = {"ident": np.eye(P, dtype=np.float32), "rwkv_con": rwkv_constants(), "gla_con": gla_constants(),
                 "head_ones": np.kron(np.eye(2), np.ones((RW_HD, RW_HD))).astype(np.float32)}
    arrays, aps = {}, {}
    for name, value in {**inputs, **constants}.items():
        value = np.ascontiguousarray(value)
        arrays[f"in_{name}"] = value
        aps[name] = nc.dram_tensor(f"in_{name}", value.shape, mybir.dt.from_np(value.dtype), kind="ExternalInput").ap()
    for name, shape in _OUTS:
        aps[name] = nc.dram_tensor(f"out_{name}", list(shape), F32, kind="ExternalOutput").ap()
    build_program(nc, aps)
    r = _run(nc, [arrays], core_ids=[0])
    return tuple(r.results[0][f"out_{name}"] for name, _ in _OUTS)
```

```python
from contextlib import ExitStack

import numpy as np

import concourse.bass as bass
from concourse import mybir

F32 = mybir.dt.float32
F32R = mybir.dt.float32r
U32 = mybir.dt.uint32
ALU = mybir.AluOpType
ACT = mybir.ActivationFunctionType
AX = mybir.AxisListType

P = 128
D = 1024
KD = D // P
T_CTX, T_LAT = 128, 2048
T = T_CTX + T_LAT
GRID_W = 64
GRID_H = T_LAT // GRID_W
SEGS = ((0, T_CTX), (T_CTX, T_LAT))
BANK = 512
D_LRU = 256
RW_HEADS, RW_HD = 6, 64
D_RW = RW_HEADS * RW_HD
GLA_HEADS, GLA_DK, GLA_DV = 4, 48, 96
D_GLA = GLA_HEADS * GLA_DV
D_GLA_K = GLA_HEADS * GLA_DK
GLA_R = 16
RW0 = 2 * D_LRU
RW_LORA = RW0 + 3 * D_RW
GLA0 = RW_LORA + 3 * P
N_IN = GLA0 + 2 * D_GLA_K + 2 * D_GLA + 2 * GLA_R
C = 64
NCH = T // C
NCH_CTX = T_CTX // C
LEVELS = 6
REC = 5 * C
N_EXP, D_EXP = 16, 1024
CAP_LAT, CAP_CTX = 2 * T_LAT // N_EXP, 2 * T_CTX // N_EXP
EPS = 1e-6
TOK_BLOCKS = [(b, min(BANK, T - b)) for b in range(0, T, BANK)]


class Stage:

    def __init__(self, nc, name):
        self.nc, self.name, self.stack, self.sems = nc, name, ExitStack(), {}

    def __enter__(self):
        return self

    def __exit__(self, *_):
        self.stack.close()
        self.nc.clear_and_free_semaphores(list(self.sems.values()))
        self.nc.all_engine_barrier()

    def sb(self, name, shape, dt=F32):
        return self.stack.enter_context(self.nc.sbuf_tensor(f"{self.name}_{name}", shape, dt))

    def ps(self, name, shape=(P, BANK)):
        return self.stack.enter_context(self.nc.psum_tensor(f"{self.name}_{name}", list(shape), F32))

    def sem(self, name):
        self.sems[name] = self.nc.alloc_semaphore(name=f"{self.name}_{name}")
        return self.sems[name]

    def sem2(self, name):
        return [self.sem(f"{name}_{u}") for u in range(2)]

    def block(self):
        return self.nc.Block()


def stage_modulation(nc, c, c_ctx, w_ada, b_ada, mods):
    NB = 6 * D // BANK
    with Stage(nc, "mod") as st:
        cvec, sil = st.sb("cvec", [P, 2, KD]), st.sb("sil", [P, KD, 2])
        w = [st.sb(f"w{u}", [P, KD, BANK]) for u in range(2)]
        bias, out = st.sb("bias", [2, 6 * D]), st.sb("out", [2, 6 * D])
        acc = [st.ps(f"acc{u}") for u in range(2)]
        cvec_in, bias_in, silu_done = st.sem("cvec_in"), st.sem("bias_in"), st.sem("silu_done")
        w_in, product, biased = st.sem2("w_in"), st.sem2("product"), st.sem2("biased")
        stored = st.sem("stored")
        wv = w_ada[0].rearrange("(p k) n -> p k n", k=KD)
        with st.block() as block:
            @block.sync
            def _(sp):
                sp.dma_start(cvec[:, 0, :], c_ctx.rearrange("(p k) -> p k", k=KD)).then_inc(cvec_in, 16)
                sp.dma_start(cvec[:, 1, :], c[0].rearrange("(p k) -> p k", k=KD)).then_inc(cvec_in, 16)
                for v in range(2):
                    sp.dma_start(bias[v:v + 1, :], b_ada).then_inc(bias_in, 16)

                def body(i):
                    for u in range(2):
                        sp.wait_ge(product[u], i)
                        sp.dma_start(w[u][:, :, :], wv[:, :, bass.ds((2 * i + u) * BANK, BANK)]).then_inc(w_in[u], 16)
                looped(sp, NB // 2, body)
                for u in range(2):
                    sp.wait_ge(biased[u], NB // 2)
                sp.dma_start(mods, out[:, :]).then_inc(stored, 16)
                sp.wait_ge(stored, 16)

            @block.scalar
            def _(act):
                act.wait_ge(cvec_in, 32)
                act.activation(sil[:, :, :], cvec[:, :, :].rearrange("p v k -> p k v"), ACT.Silu).then_inc(silu_done, 1)

            @block.tensor
            def _(pe):
                pe.wait_ge(silu_done, 1)

                def body(i):
                    for u in range(2):
                        pe.wait_ge(w_in[u], 16 * i + 16)
                        pe.wait_ge(biased[u], i)
                        for k in range(KD):
                            mm = pe.matmul(acc[u][0:2, :], sil[:, k, :], w[u][:, k, :], start=k == 0, stop=k == KD - 1)
                        mm.then_inc(product[u], 1)
                looped(pe, NB // 2, body)

            @block.vector
            def _(dve):
                dve.wait_ge(bias_in, 32)

                def body(i):
                    for u in range(2):
                        cols = bass.ds((2 * i + u) * BANK, BANK)
                        dve.wait_ge(product[u], i + 1)
                        dve.tensor_tensor(out[:, cols], acc[u][0:2, :], bias[:, cols], ALU.add).then_inc(biased[u], 1)
                looped(dve, NB // 2, body)


def looped(eng, count, body):
    body(0)
    with eng.Fori(1, count) as i:
        body(i)


def paired(eng, body, pairs):
    body(0, 1, 0, 0)
    body(0, 2, 1, 1)
    body(1, 1, 2, 1)
    with eng.Fori(1, pairs) as i:
        body(0, i + 2, 2 * i + 1, 1)
        body(1, i + 1, 2 * i + 2, 1)


def load_modulated_norm(sp, st_sem, rows, mods, norm_g, scale_col, shift_col):
    g_row, scale_row, shift_row = rows
    sp.dma_start(g_row[:, :], norm_g.to_broadcast([P, D])).then_inc(st_sem, 16)
    for v in range(2):
        sp.dma_start(scale_row[:, v, :], mods[v:v + 1, scale_col * D:(scale_col + 1) * D].to_broadcast([P, D])).then_inc(st_sem, 16)
        sp.dma_start(shift_row[:, v, :], mods[v:v + 1, shift_col * D:(shift_col + 1) * D].to_broadcast([P, D])).then_inc(st_sem, 16)


def stage_project(nc, x_prompt, x_sample, norm1_g, mods, w_in, ident_d, proj):
    CT = N_IN // P
    REM = N_IN - CT * P
    with Stage(nc, "proj") as st:
        hT = st.sb("hT", [P, KD, T])
        ident = st.sb("ident", [P, P])
        g_row, scale_row, shift_row = st.sb("g", [P, D]), st.sb("scale", [P, 2, D]), st.sb("shift", [P, 2, D])
        x = [st.sb(f"x{u}", [P, D]) for u in range(2)]
        h = [st.sb(f"h{u}", [P, D]) for u in range(2)]
        ss = [st.sb(f"ss{u}", [P, 4]) for u in range(2)]
        w = [st.sb(f"w{u}", [P, KD, P]) for u in range(2)]
        out = [st.sb(f"out{u}", [P, T]) for u in range(2)]
        ps_t = [st.ps(f"t{u}", [P, D // 2]) for u in range(2)]
        ps = [st.ps(f"acc{b}") for b in range(len(TOK_BLOCKS))]
        rows_in, ident_in, rows_ready, scaled1 = st.sem("rows_in"), st.sem("ident_in"), st.sem("rows_ready"), st.sem("scaled1")
        x_in, sumsq, meansq, root, rstd = (st.sem2(n) for n in ("x_in", "sumsq", "meansq", "root", "rstd"))
        normed, h_ready = st.sem2("normed"), st.sem2("h_ready")
        turned, kept = st.sem2("turned"), st.sem2("kept")
        w_ld, block_done = st.sem2("w_ld"), st.sem2("block_done")
        block_out = [st.sem(f"block_out{b}") for b in range(len(TOK_BLOCKS))]
        stored = st.sem2("stored")
        wv = w_in[0].rearrange("(k p) n -> p k n", p=P)
        NBLK = len(TOK_BLOCKS)

        def x_tile(tile, seg):
            return x_prompt[0] if seg == 0 else x_sample[0, bass.ds((tile - 1) * P, P), :]

        PAIRS = CT // 2
        TAIL = [(0, PAIRS + 1, CT - 1, P), (1, PAIRS + 1, CT, REM)]
        assert CT % 2 == 1 and REM

        def column_tiles(eng, body):
            body(0, 1, 0, P)
            body(1, 1, 1, P)
            with eng.Fori(1, PAIRS) as i:
                body(0, i + 1, 2 * i, P)
                body(1, i + 1, 2 * i + 1, P)
            for t in TAIL:
                body(*t)

        with st.block() as block:
            @block.sync
            def _(sp):
                sp.dma_start(ident[:, :], ident_d).then_inc(ident_in, 16)
                load_modulated_norm(sp, rows_in, (g_row, scale_row, shift_row), mods, norm1_g, 1, 0)

                def load_x(u, n, tile, seg):
                    sp.wait_ge(normed[u], n - 1)
                    sp.dma_start(x[u][:, :], x_tile(tile, seg)).then_inc(x_in[u], 16)
                paired(sp, load_x, 8)

                def store(u, n, ct, width):
                    for b in range(NBLK):
                        sp.wait_ge(block_out[b], ct + 1)
                    sp.dma_start(proj[bass.ds(ct * P, width), :], out[u][0:width, :]).then_inc(stored[u], 16)
                column_tiles(sp, store)
                for u in range(2):
                    sp.wait_ge(stored[u], 16 * (PAIRS + 1))

            @block.gpsimd
            def _(pool):
                def load_w(u, n, ct, width):
                    pool.wait_ge(ident_in, 16)
                    pool.wait_ge(block_done[u], NBLK * (n - 1))
                    pool.dma_start(w[u][:, :, 0:width], wv[:, :, bass.ds(ct * P, width)]).then_inc(w_ld[u], 16)
                column_tiles(pool, load_w)

            @block.scalar
            def _(act):
                def norm(u, n, tile, seg):
                    act.wait_ge(x_in[u], 16 * n)
                    act.wait_ge(normed[u], n - 1)
                    act.wait_ge(turned[u], 2 * n - 2)
                    act.activation(h[u][:, :], x[u][:, :], ACT.Square, accum_out=ss[u][:, 0:1]).then_inc(sumsq[u], 1)
                    act.wait_ge(meansq[u], n)
                    act.activation(ss[u][:, 2:3], ss[u][:, 1:2], ACT.Sqrt).then_inc(root[u], 1)
                    act.wait_ge(turned[u], 2 * n)
                    act.copy(hT[:, 4:8, bass.ds(tile * P, P)], ps_t[1][:, :].rearrange("p (k t) -> p k t", k=4)).then_inc(kept[1], 1)
                paired(act, norm, 8)

                def evacuate(u, n, ct, width):
                    act.wait_ge(stored[u], 16 * n - 16)
                    for b in range(0, NBLK, 2):
                        t0, tn = TOK_BLOCKS[b]
                        act.wait_ge(block_done[u], NBLK * (n - 1) + b + 1)
                        act.copy(out[u][0:width, t0:t0 + tn], ps[b][0:width, 0:tn]).then_inc(block_out[b], 1)
                column_tiles(act, evacuate)

            @block.vector
            def _(dve):
                dve.wait_ge(rows_in, 5 * 16)
                for v in range(2):
                    dve.scalar_tensor_tensor(scale_row[:, v, :], scale_row[:, v, :], 1.0, g_row[:, :], ALU.add, ALU.mult).then_inc(rows_ready, 1)

                def norm(u, n, tile, seg):
                    dve.wait_ge(sumsq[u], n)
                    dve.tensor_scalar(ss[u][:, 1:2], ss[u][:, 0:1], 1.0 / D, EPS, ALU.mult, ALU.add).then_inc(meansq[u], 1)
                    dve.wait_ge(root[u], n)
                    dve.reciprocal(ss[u][:, 3:4], ss[u][:, 2:3]).then_inc(rstd[u], 1)
                    dve.wait_ge(rstd[u], n)
                    dve.wait_ge(rows_ready, 2)
                    dve.scalar_tensor_tensor(h[u][:, :], x[u][:, :], ss[u][:, 3:4], scale_row[:, seg, :], ALU.mult, ALU.mult).then_inc(normed[u], 1)
                    dve.wait_ge(normed[u], n)
                    dve.tensor_tensor(h[u][:, :], h[u][:, :], shift_row[:, seg, :], ALU.add).then_inc(h_ready[u], 1)
                    dve.wait_ge(turned[u], 2 * n - 1)
                    dve.tensor_copy(hT[:, 0:4, bass.ds(tile * P, P)], ps_t[0][:, :].rearrange("p (k t) -> p k t", k=4)).then_inc(kept[0], 1)
                paired(dve, norm, 8)

                def evacuate(u, n, ct, width):
                    dve.wait_ge(stored[u], 16 * n - 16)
                    for b in range(1, NBLK, 2):
                        t0, tn = TOK_BLOCKS[b]
                        dve.wait_ge(block_done[u], NBLK * (n - 1) + b + 1)
                        dve.tensor_copy(out[u][0:width, t0:t0 + tn], ps[b][0:width, 0:tn]).then_inc(block_out[b], 1)
                column_tiles(dve, evacuate)

            @block.tensor
            def _(pe):
                pe.wait_ge(ident_in, 16)

                def turn(u, n, tile, seg):
                    pe.wait_ge(h_ready[u], n)
                    for half in range(2):
                        pe.wait_ge(kept[half], tile)
                        for k in range(4):
                            mm = pe.transpose(ps_t[half][:, k * P:(k + 1) * P], h[u][:, (4 * half + k) * P:(4 * half + k + 1) * P], ident[:, :])
                        mm.then_inc(turned[u], 1)
                paired(pe, turn, 8)
                for half in range(2):
                    pe.wait_ge(kept[half], T // P)

                def product(u, n, ct, width):
                    pe.wait_ge(w_ld[u], 16 * n)
                    for b, (t0, tn) in enumerate(TOK_BLOCKS):
                        pe.wait_ge(block_out[b], ct)
                        for k in range(KD):
                            mm = pe.matmul(ps[b][0:width, 0:tn], w[u][:, k, 0:width], hT[:, k, t0:t0 + tn], start=k == 0, stop=k == KD - 1)
                        mm.then_inc(block_done[u], 1)
                column_tiles(pe, product)


def stage_lru(nc, proj, conv_w, conv_b, wa, ba, wx, bx, lam, h0, mixT, new_state):
    NT = D_LRU // P
    with Stage(nc, "lru") as st:
        xl, yl, xc = st.sb("xl", [P, T]), st.sb("yl", [P, T]), st.sb("xc", [P, T])
        sig = st.sb("sig", [P, 2, 2, T])
        a = st.sb("a", [P, 2, T])
        tanh = st.sb("tanh", [P, 2, T])
        hid = st.sb("hid", [P, 2, T])
        par = st.sb("par", [P, 4 + 1 + 2 + 2 + 2 + 2])
        cw, cb, bias, lm, st0 = par[:, 0:4], par[:, 4:5], par[:, 5:9], par[:, 9:11], par[:, 11:13]
        sp_t = st.sb("sp_t", [P, 6, 2])
        bd = st.sb("bd", [P, 2, 2, P])
        bank = [st.ps(f"b{b}") for b in range(len(TOK_BLOCKS))]
        zeroed, ld, wts_in = st.sem("zeroed"), st.sem("ld"), st.sem("wts_in")
        conv, soft, gate_mm = st.sem("conv"), st.sem("soft"), st.sem("gate_mm")
        gated = [st.sem(f"gated{b}") for b in range(len(TOK_BLOCKS))]
        lam_abs, lam_exp = st.sem("lam_abs"), st.sem("lam_exp")
        decay_done, tanh_done, square_done, under_root, root_done = (st.sem(n) for n in (
            "decay_done", "tanh_done", "square_done", "under_root", "root_done"))
        drive, scanned, summed, gelu_done, out_done = (st.sem(n) for n in ("drive", "scanned", "summed", "gelu_done", "out_done"))
        stored = st.sem("stored")
        SERIES = 9
        N_CONV = 7
        N_LD = 2 + 1 + 1 + 4 + 2 + 2
        N_SOFT = 4 + SERIES + 3
        N_ST = 1 + 2

        def chan(v, i):
            return v[bass.ds(i * P, P)]

        with st.block() as block:
            @block.sync
            def _(sp):

                def body(i):
                    sp.wait_ge(stored, 16 * N_ST * i)
                    sp.dma_start(xl[:, :], proj[bass.ds(i * P, P), :]).then_inc(ld, 16)
                    sp.dma_start(yl[:, :], proj[bass.ds(D_LRU + i * P, P), :]).then_inc(ld, 16)
                    sp.dma_start(cw, conv_w[0, :, bass.ds(i * P, P)].rearrange("w p -> p w"), allow_slow_non_contiguous=True).then_inc(ld, 16)
                    sp.dma_start(cb, chan(conv_b[0], i).unsqueeze(1)).then_inc(ld, 16)
                    for d in range(2):
                        sp.dma_start(bias[:, 2 * d:2 * d + 1], chan(ba[0, d], i).unsqueeze(1)).then_inc(ld, 16)
                        sp.dma_start(bias[:, 2 * d + 1:2 * d + 2], chan(bx[0, d], i).unsqueeze(1)).then_inc(ld, 16)
                        sp.dma_start(lm[:, d:d + 1], chan(lam[0, d], i).unsqueeze(1)).then_inc(ld, 16)
                        sp.dma_start(st0[:, d:d + 1], chan(h0[0, 0, d], i).unsqueeze(1)).then_inc(ld, 16)
                    sp.wait_ge(zeroed, 1)
                    for d in range(2):
                        for g, wt in enumerate((wa, wx)):
                            for n in range(2):
                                sp.dma_start(bd[64 * n:64 * n + 64, d, g, 64 * n:64 * n + 64],
                                             wt[0, d, bass.ds(2 * i + n, 1)].squeeze(0)).then_inc(wts_in, 16)
                    sp.wait_ge(out_done, i + 1)
                    sp.dma_start(mixT[bass.ds(i * P, P), :], xc[:, :]).then_inc(stored, 16)
                    for d, t in ((0, T_CTX - 1), (1, 0)):
                        sp.dma_start(chan(new_state[0, 0, d], i).unsqueeze(1), hid[:, d, t:t + 1]).then_inc(stored, 16)
                looped(sp, NT, body)
                sp.wait_ge(stored, 16 * N_ST * NT)

            @block.gpsimd
            def _(pool):
                pool.memset(bd[:, :, :, :], 0.0).then_inc(zeroed, 1)

            @block.scalar
            def _(act):

                def body(i):
                    act.wait_ge(ld, 16 * N_LD * (i + 1))
                    act.activation(sp_t[:, 0, :], lm, ACT.Abs).then_inc(lam_abs, 1)
                    act.wait_ge(lam_abs, i + 1)
                    act.activation(sp_t[:, 1, :], sp_t[:, 0, :], ACT.Exp, scale=-1.0).then_inc(lam_exp, 1)
                    for d in range(2):
                        for g in range(2):
                            for b, (t0, tn) in enumerate(TOK_BLOCKS):
                                act.wait_ge(gate_mm, (4 * i + 2 * d + g) * len(TOK_BLOCKS) + b + 1)
                                act.activation(sig[:, d, g, t0:t0 + tn], bank[b][:, 0:tn], ACT.Sigmoid,
                                               bias=bias[:, 2 * d + g:2 * d + g + 1]).then_inc(gated[b], 1)
                    act.wait_ge(soft, N_SOFT * (i + 1))
                    for b in range(len(TOK_BLOCKS)):
                        act.wait_ge(gated[b], 4 * i + 4)
                    for d in range(2):
                        act.activation(a[:, d, :], sig[:, d, 0, :], ACT.Exp, scale=sp_t[:, 4, d:d + 1]).then_inc(decay_done, 1)
                    for d in range(2):
                        act.activation(tanh[:, d, :], sig[:, d, 0, :], ACT.Tanh, scale=sp_t[:, 5, d:d + 1]).then_inc(tanh_done, 1)
                    act.wait_ge(decay_done, 2 * i + 2)
                    act.wait_ge(tanh_done, 2 * i + 2)
                    for d in range(2):
                        act.activation(sig[:, d, 0, :], a[:, d, :], ACT.Square).then_inc(square_done, 1)
                    for d in range(2):
                        act.wait_ge(under_root, 2 * i + d + 1)
                        act.activation(tanh[:, d, :], sig[:, d, 0, :], ACT.Sqrt).then_inc(root_done, 1)
                    act.activation(yl[:, :], yl[:, :], ACT.Gelu_apprx_tanh).then_inc(gelu_done, 1)
                looped(act, NT, body)

            @block.tensor
            def _(pe):

                def body(i):
                    pe.wait_ge(wts_in, 16 * 8 * (i + 1))
                    pe.wait_ge(conv, N_CONV * (i + 1))
                    for d in range(2):
                        for g in range(2):
                            for b, (t0, tn) in enumerate(TOK_BLOCKS):
                                pe.wait_ge(gated[b], 4 * i + 2 * d + g)
                                pe.matmul(bank[b][:, 0:tn], bd[:, d, g, :], xc[:, t0:t0 + tn], start=True, stop=True).then_inc(gate_mm, 1)
                looped(pe, NT, body)

            @block.vector
            def _(dve):

                def body(i):
                    dve.wait_ge(ld, 16 * N_LD * (i + 1))
                    dve.tensor_scalar(xc[:, :], xl[:, :], cw[:, 2:3], cb, ALU.mult, ALU.add).then_inc(conv, 1)
                    k = 1
                    for s, n in SEGS:
                        for w in (0, 1, 3):
                            o = w - 2
                            lo, hi = max(s, s - o), min(s + n, s + n - o)
                            dve.wait_ge(conv, N_CONV * i + k)
                            dve.scalar_tensor_tensor(xc[:, lo:hi], xl[:, lo + o:hi + o], cw[:, w:w + 1], xc[:, lo:hi],
                                                     ALU.mult, ALU.add).then_inc(conv, 1)
                            k += 1
                    e, y, y2, acc, neg, pos = sp_t[:, 1, :], sp_t[:, 0, :], sp_t[:, 2, :], sp_t[:, 3, :], sp_t[:, 4, :], sp_t[:, 5, :]
                    k = 0

                    def step(ins):
                        nonlocal k
                        k += 1
                        ins.then_inc(soft, 1)
                        dve.wait_ge(soft, N_SOFT * i + k)
                    dve.wait_ge(lam_exp, i + 1)
                    step(dve.tensor_scalar(y2, e, 2.0, None, ALU.add))
                    step(dve.reciprocal(acc, y2))
                    step(dve.tensor_tensor(y, e, acc, ALU.mult))
                    step(dve.tensor_tensor(y2, y, y, ALU.mult))
                    step(dve.tensor_scalar(acc, y2, 1.0 / (2 * SERIES - 1), None, ALU.mult))
                    for m in range(SERIES - 2, -1, -1):
                        step(dve.scalar_tensor_tensor(acc, acc, 1.0 / (2 * m + 1), y2 if m else y, ALU.add, ALU.mult))
                    step(dve.tensor_scalar(pos, lm, -8.0, 0.0, ALU.mult, ALU.max))
                    step(dve.scalar_tensor_tensor(pos, acc, 16.0, pos, ALU.mult, ALU.add))
                    step(dve.tensor_scalar(neg, pos, -1.0, None, ALU.mult))
                    assert k == N_SOFT, k
                    for d in range(2):
                        dve.wait_ge(square_done, 2 * i + d + 1)
                        dve.scalar_tensor_tensor(sig[:, d, 0, :], sig[:, d, 0, :], 1.0, tanh[:, d, :], ALU.add, ALU.mult).then_inc(under_root, 1)
                        dve.tensor_tensor(hid[:, d, :], sig[:, d, 1, :], xc[:, :], ALU.mult).then_inc(drive, 1)
                    for d in range(2):
                        dve.wait_ge(root_done, 2 * i + d + 1)
                        dve.wait_ge(drive, 4 * i + 2 + d)
                        dve.tensor_tensor(sig[:, d, 1, :], hid[:, d, :], tanh[:, d, :], ALU.mult).then_inc(drive, 1)
                    dve.wait_ge(drive, 4 * i + 4)
                    for d in range(2):
                        for g, (s, n) in enumerate(SEGS):
                            way = slice(s, s + n) if d == 0 else slice(s + n - 1, s - 1 if s else None, -1)
                            dve.tensor_tensor_scan(hid[:, d, way], a[:, d, way], sig[:, d, 1, way],
                                                   st0[:, d:d + 1] if g else 0.0, ALU.mult, ALU.add).then_inc(scanned, 1)
                    dve.wait_ge(scanned, 4 * i + 4)
                    dve.tensor_tensor(sig[:, 0, 0, :], hid[:, 0, :], hid[:, 1, :], ALU.add).then_inc(summed, 1)
                    dve.wait_ge(summed, i + 1)
                    dve.wait_ge(gelu_done, i + 1)
                    dve.tensor_tensor(xc[:, :], sig[:, 0, 0, :], yl[:, :], ALU.mult).then_inc(out_done, 1)
                looped(dve, NT, body)


def scan_order(ap, d, s, n):
    return ap[:, s:s + n] if d == 0 else ap[:, slice(s + n - 1, s - 1 if s else None, -1)]


def in_chunks(ap):
    return ap.rearrange("p (c t) -> p c t", t=C)


def stage_rwkv_prep(nc, proj, mu, w0, w2, a0, a2, g2, kkw, kaw, rk, blockones_d, rec, decay, gate, bonus):
    RATE = float(2.718281828459045 ** -0.5)
    HP = D_RW // P
    NBLK = len(TOK_BLOCKS)
    with Stage(nc, "rwp") as st:
        raw = [st.sb(f"raw{j}", [P, T]) for j in range(3)]
        lora = [st.sb(f"lora{j}", [P, T]) for j in range(3)]
        r, k, v = (st.sb(n, [P, T]) for n in ("r", "k", "v"))
        sg, cum, eb, ebm, ebi, bs = (st.sb(n, [P, T]) for n in ("sg", "cum", "eb", "ebm", "ebi", "bs"))
        kk, kd, av = raw
        recs = st.sb("recs", [P, NCH, REC])
        total = st.sb("total", [P, NCH])
        keep = st.sb("keep", [P, T])
        mus = st.sb("mus", [P, 3, 3])
        par = st.sb("par", [P, 10])
        p_kk, p_ka, p_rk, p_w0, p_a0, p_1ka = par[:, 0:1], par[:, 1:2], par[:, 2:4], par[:, 4:6], par[:, 6:8], par[:, 8:9]
        tiny = st.sb("tiny", [P, 1])
        w2s, a2s, g2s, ones = (st.sb(n, [P, P]) for n in ("w2s", "a2s", "g2s", "ones"))
        bank = [st.ps(f"b{b}") for b in range(NBLK)]
        const_in, consts, lora_in, lora_mu, lora_mixed, lora_act = (st.sem(n) for n in (
            "const_in", "consts", "lora_in", "lora_mu", "lora_mixed", "lora_act"))
        ld, coef, mixed, product = st.sem("ld"), st.sem("coef"), st.sem("mixed"), st.sem("product")
        freed = [st.sem(f"freed{b}") for b in range(NBLK)]
        gate_ready, kk_raw, squares, norm_root, kk_ready = (st.sem(n) for n in ("gate_ready", "kk_raw", "squares", "norm_root", "kk_ready"))
        sig_ready, a_ready, cum_ready, arg_ready, exps, kd_step = (st.sem(n) for n in (
            "sig_ready", "a_ready", "cum_ready", "arg_ready", "exps", "kd_step"))
        rec_dve, rec_pool, rec_act, rec_stored, bonus_step, bonus_out = (st.sem(n) for n in (
            "rec_dve", "rec_pool", "rec_act", "rec_stored", "bonus_step", "bonus_out"))
        gate_stored, bonus_stored = st.sem("gate_stored"), st.sem("bonus_stored")
        N_LD = 3 + 6 + 2 + 6 + 5
        N_COEF = 2
        JOBS = 7

        def column(vec, c0):
            return vec[bass.ds(c0, P)].unsqueeze(1)

        def shift_mix(eng, out, x, m, done, base):
            eng.tensor_scalar(out[:, :], x[:, :], m[:, 2:3], None, ALU.mult).then_inc(done, 1)
            q = 1
            for s, n in SEGS:
                eng.wait_ge(done, base + q)
                eng.scalar_tensor_tensor(out[:, s + 1:s + n], x[:, s:s + n - 1], m[:, 0:1], out[:, s + 1:s + n], ALU.mult, ALU.add).then_inc(done, 1)
                eng.wait_ge(done, base + q + 1)
                eng.scalar_tensor_tensor(out[:, s:s + n - 1], x[:, s + 1:s + n], m[:, 1:2], out[:, s:s + n - 1], ALU.mult, ALU.add).then_inc(done, 1)
                q += 2
        MIX = 5

        with st.block() as block:
            @block.sync
            def _(sp):
                sp.dma_start(ones[:, :], blockones_d).then_inc(const_in, 16)
                for j in range(3):
                    c0 = 3 * D_RW + j * P
                    sp.dma_start(raw[j][:, :], proj[RW0 + c0:RW0 + c0 + P, :]).then_inc(lora_in, 16)
                    for m in range(2):
                        sp.dma_start(mus[:, j, m:m + 1], column(mu[0, m], c0)).then_inc(lora_in, 16)

                def body(i):
                    c0 = i * P
                    sp.wait_ge(bonus_out, NBLK * i)
                    sp.wait_ge(lora_mixed, 3 * MIX)
                    for j in range(3):
                        sp.dma_start(raw[j][:, :], proj[bass.ds(RW0 + j * D_RW + c0, P), :]).then_inc(ld, 16)
                        for m in range(2):
                            sp.dma_start(mus[:, j, m:m + 1], column(mu[0, m], j * D_RW + c0)).then_inc(ld, 16)
                    sp.dma_start(p_kk, column(kkw[0], c0)).then_inc(ld, 16)
                    sp.dma_start(p_ka, column(kaw[0], c0)).then_inc(ld, 16)
                    for d in range(2):
                        sp.dma_start(p_rk[:, d:d + 1], column(rk[0, d].rearrange("h n -> (h n)"), c0)).then_inc(ld, 16)
                        sp.dma_start(p_w0[:, d:d + 1], column(w0[0, d], c0)).then_inc(ld, 16)
                        sp.dma_start(p_a0[:, d:d + 1], column(a0[0, d], c0)).then_inc(ld, 16)
                    for d in range(2):
                        sp.dma_start(w2s[64 * d:64 * d + 64, :], w2[0, d, :, bass.ds(c0, P)]).then_inc(ld, 16)
                        sp.dma_start(a2s[64 * d:64 * d + 64, :], a2[0, d, :, bass.ds(c0, P)]).then_inc(ld, 16)
                    sp.dma_start(g2s[:, :], g2[0, :, bass.ds(c0, P)]).then_inc(ld, 16)
                    sp.wait_ge(gate_ready, NBLK * (i + 1))
                    sp.dma_start(gate[bass.ds(c0, P), :], ebi[:, :]).then_inc(gate_stored, 16)
                    for d in range(2):
                        for part in (rec_dve, rec_pool, rec_act):
                            sp.wait_ge(part, 2 * i + d + 1)
                        sp.dma_start(rec[d, :, :, bass.ds(i, 1), :].squeeze(2), recs[:, :, :]).then_inc(rec_stored, 16)
                        sp.dma_start(decay[:, d, bass.ds(i, 1), :].squeeze(1), total[:, :]).then_inc(rec_stored, 16)
                    sp.wait_ge(bonus_out, NBLK * (i + 1))
                    sp.dma_start(bonus[bass.ds(c0, P), :], bs[:, :]).then_inc(bonus_stored, 16)
                looped(sp, HP, body)
                sp.wait_ge(gate_stored, 16 * HP)
                sp.wait_ge(bonus_stored, 16 * HP)
                sp.wait_ge(rec_stored, 32 * 2 * HP)

            @block.gpsimd
            def _(pool):
                pool.memset(keep[:, :], 1.0).then_inc(consts, 1)
                pool.memset(tiny[:, :], 1e-12).then_inc(consts, 1)
                pool.wait_ge(consts, 2)
                pool.memset(in_chunks(keep[:, :])[:, :, 0:1], 0.0).then_inc(consts, 1)

                def body(i):
                    for d in range(2):
                        pool.wait_ge(kd_step, 3 * (2 * i + d) + 3)
                        pool.wait_ge(exps, 3 * (2 * i + d) + 3)
                        pool.wait_ge(rec_stored, 32 * (2 * i + d))
                        pool.wait_ge(consts, 3)
                        pool.tensor_tensor(recs[:, :, 3 * C:4 * C], in_chunks(kd[:, :]), in_chunks(ebi[:, :]), ALU.mult).then_inc(rec_pool, 1)
                looped(pool, HP, body)

            @block.scalar
            def _(act):
                act.wait_ge(lora_mixed, MIX)
                act.activation(lora[0][:, :], lora[0][:, :], ACT.Tanh).then_inc(lora_act, 1)
                act.wait_ge(lora_mixed, 3 * MIX)
                act.activation(lora[2][:, :], lora[2][:, :], ACT.Sigmoid).then_inc(lora_act, 1)
                act.wait_ge(consts, 3)

                def body(i):
                    def evacuate(job, out, done, func, **kw):
                        for b, (t0, tn) in enumerate(TOK_BLOCKS):
                            act.wait_ge(product, NBLK * (JOBS * i + job) + b + 1)
                            act.activation(out[:, t0:t0 + tn], bank[b][:, 0:tn], func, **kw).then_inc(done, 1)
                    act.wait_ge(rec_dve, 2 * i)
                    act.wait_ge(rec_pool, 2 * i)
                    act.wait_ge(rec_act, 2 * i)
                    evacuate(0, ebi, gate_ready, ACT.Copy)
                    evacuate(1, eb, norm_root, ACT.Sqrt, bias=tiny[:, :])
                    for d in range(2):
                        act.wait_ge(arg_ready, 2 * i + d)
                        act.wait_ge(rec_dve, 2 * i + d)
                        act.wait_ge(mixed, 3 * MIX * (i + 1))
                        evacuate(2 + 2 * d, sg, sig_ready, ACT.Sigmoid, bias=p_w0[:, d:d + 1])
                        evacuate(3 + 2 * d, av, a_ready, ACT.Sigmoid, bias=p_a0[:, d:d + 1])
                        act.wait_ge(kk_ready, 2 * i + 2)
                        act.wait_ge(cum_ready, 2 * i + d + 1)
                        act.wait_ge(arg_ready, 2 * i + d + 1)
                        act.wait_ge(rec_pool, 2 * i + d)
                        act.wait_ge(gate_stored, 16 * (i + 1))
                        act.activation(eb[:, :], cum[:, :], ACT.Exp, scale=-RATE).then_inc(exps, 1)
                        act.activation(ebi[:, :], cum[:, :], ACT.Exp, scale=RATE).then_inc(exps, 1)
                        act.activation(ebm[:, :], ebm[:, :], ACT.Exp, scale=-RATE).then_inc(exps, 1)
                        act.wait_ge(exps, 3 * (2 * i + d) + 3)
                        act.wait_ge(rec_stored, 32 * (2 * i + d))
                        act.copy(recs[:, :, 4 * C:], in_chunks(v[:, :]))
                        end = 0 if d else C - 1
                        act.copy(total[:, :].unsqueeze(2), in_chunks(eb[:, :])[:, :, end:end + 1]).then_inc(rec_act, 1)
                looped(act, HP, body)

            @block.tensor
            def _(pe):
                pe.wait_ge(const_in, 16)

                def body(i):
                    def job(j, lhsT, rhs, also=None, at=0):
                        for b, (t0, tn) in enumerate(TOK_BLOCKS):
                            pe.wait_ge(freed_or(j, b)[0], freed_or(j, b)[1])
                            if also is not None:
                                pe.wait_ge(*also)
                            pe.matmul(bank[b][:, 0:tn], lhsT, rhs[at:at + lhsT.shape[0], t0:t0 + tn], start=True, stop=True).then_inc(product, 1)

                    def freed_or(j, b):
                        return [(bonus_out, NBLK * i), (gate_ready, NBLK * i + b + 1), (norm_root, NBLK * i + b + 1),
                                (sig_ready, NBLK * 2 * i + b + 1), (a_ready, NBLK * 2 * i + b + 1),
                                (sig_ready, NBLK * (2 * i + 1) + b + 1), (a_ready, NBLK * (2 * i + 1) + b + 1)][j]
                    pe.wait_ge(ld, 16 * N_LD * (i + 1))
                    pe.wait_ge(lora_act, 2)
                    job(0, g2s[:, :], lora[2])
                    job(1, ones[:, :], kd, (squares, i + 1))
                    for d in range(2):
                        job(2 + 2 * d, w2s[64 * d:64 * d + 64, :], lora[0], None, 64 * d)
                        job(3 + 2 * d, a2s[64 * d:64 * d + 64, :], lora[1], None, 64 * d)
                    job(6, ones[:, :], bs, (bonus_step, 3 * i + 3))
                looped(pe, HP, body)

            @block.vector
            def _(dve):
                dve.wait_ge(lora_in, 9 * 16)
                dve.tensor_tensor(mus[:, :, 2], mus[:, :, 0], mus[:, :, 1], ALU.add).then_inc(lora_mu, 1)
                dve.wait_ge(lora_mu, 1)
                dve.tensor_scalar(mus[:, :, 2], mus[:, :, 2], -1.0, 1.0, ALU.mult, ALU.add).then_inc(lora_mu, 1)
                dve.wait_ge(lora_mu, 2)
                for j in range(3):
                    shift_mix(dve, lora[j], raw[j], mus[:, j, :], lora_mixed, MIX * j)
                dve.wait_ge(consts, 3)

                def body(i):
                    dve.wait_ge(ld, 16 * N_LD * (i + 1))
                    dve.tensor_tensor(mus[:, :, 2], mus[:, :, 0], mus[:, :, 1], ALU.add).then_inc(coef, 1)
                    dve.tensor_scalar(p_1ka, p_ka, -1.0, 1.0, ALU.mult, ALU.add).then_inc(coef, 1)
                    dve.wait_ge(coef, 3 * i + 2)
                    dve.tensor_scalar(mus[:, :, 2], mus[:, :, 2], -1.0, 1.0, ALU.mult, ALU.add).then_inc(coef, 1)
                    dve.wait_ge(coef, 3 * i + 3)
                    dve.wait_ge(rec_act, 2 * i)
                    for j, out in enumerate((r, k, v)):
                        shift_mix(dve, out, raw[j], mus[:, j, :], mixed, 3 * MIX * i + MIX * j)
                    dve.wait_ge(mixed, 3 * MIX * (i + 1))
                    dve.tensor_scalar(kk[:, :], k[:, :], p_kk, None, ALU.mult).then_inc(kk_raw, 1)
                    dve.wait_ge(kk_raw, i + 1)
                    dve.tensor_tensor(kd[:, :], kk[:, :], kk[:, :], ALU.mult).then_inc(squares, 1)
                    dve.wait_ge(norm_root, NBLK * (i + 1))
                    dve.reciprocal(eb[:, :], eb[:, :]).then_inc(kk_ready, 1)
                    dve.wait_ge(kk_ready, 2 * i + 1)
                    dve.tensor_tensor(kk[:, :], kk[:, :], eb[:, :], ALU.mult).then_inc(kk_ready, 1)
                    for d in range(2):
                        u = 2 * i + d
                        dve.wait_ge(sig_ready, NBLK * (u + 1))
                        dve.wait_ge(exps, 3 * u)
                        dve.tensor_tensor_scan(scan_order(cum, d, 0, T), keep[:, :], scan_order(sg, d, 0, T), 0.0, ALU.mult, ALU.add).then_inc(cum_ready, 1)
                        dve.wait_ge(cum_ready, u + 1)
                        dve.tensor_tensor(ebm[:, :], cum[:, :], sg[:, :], ALU.subtract).then_inc(arg_ready, 1)
                        dve.wait_ge(a_ready, NBLK * (u + 1))
                        dve.wait_ge(rec_pool, u)
                        dve.tensor_scalar(kd[:, :], av[:, :], p_ka, p_1ka, ALU.mult, ALU.add).then_inc(kd_step, 1)
                        dve.wait_ge(kd_step, 3 * u + 1)
                        dve.tensor_tensor(kd[:, :], kd[:, :], k[:, :], ALU.mult).then_inc(kd_step, 1)
                        dve.wait_ge(kk_ready, 2 * i + 2)
                        dve.tensor_tensor(av[:, :], av[:, :], kk[:, :], ALU.mult).then_inc(kd_step, 1)
                        dve.wait_ge(kd_step, 3 * u + 3)
                        if d == 0:
                            dve.wait_ge(bonus_stored, 16 * i)
                            dve.tensor_scalar(bs[:, :], kd[:, :], p_rk[:, 0:1], None, ALU.mult).then_inc(bonus_step, 1)
                        else:
                            dve.wait_ge(bonus_step, 3 * i + 1)
                            dve.scalar_tensor_tensor(bs[:, :], kd[:, :], p_rk[:, 1:2], bs[:, :], ALU.mult, ALU.add).then_inc(bonus_step, 1)
                        dve.wait_ge(rec_stored, 32 * u)
                        dve.wait_ge(exps, 3 * u + 3)
                        for q, (x, y) in enumerate(((kk, ebm), (r, eb), (av, ebi))):
                            out = recs[:, :, q * C:(q + 1) * C]
                            if q == 0:
                                dve.scalar_tensor_tensor(out, in_chunks(x[:, :]), -1.0, in_chunks(y[:, :]), ALU.mult, ALU.mult)
                            else:
                                last = dve.tensor_tensor(out, in_chunks(x[:, :]), in_chunks(y[:, :]), ALU.mult)
                        last.then_inc(rec_dve, 1)
                    dve.wait_ge(bonus_step, 3 * i + 2)
                    dve.tensor_tensor(bs[:, :], bs[:, :], r[:, :], ALU.mult).then_inc(bonus_step, 1)
                    for b, (t0, tn) in enumerate(TOK_BLOCKS):
                        dve.wait_ge(product, NBLK * (JOBS * i + 6) + b + 1)
                        dve.tensor_tensor(bs[:, t0:t0 + tn], bank[b][:, 0:tn], v[:, t0:t0 + tn], ALU.mult).then_inc(bonus_out, 1)
                looped(dve, HP, body)


def joins(d):
    t = np.arange(C)[::-1] if d else np.arange(C)
    return [(t[:, None] >> (l + 1) == t[None, :] >> (l + 1)) & (t[:, None] >> l & 1 == 1) & (t[None, :] >> l & 1 == 0)
            for l in range(LEVELS)]


def rwkv_constants():
    two = lambda m: np.concatenate([m, m], 0)
    diag = lambda m: np.kron(np.eye(2), m)
    parts = []
    for d in range(2):
        later = sum(joins(d)).T
        parts += [two(later), two(later + np.eye(C)), diag(joins(d)[0].T)] + [two(j) for j in joins(d)]
    return np.concatenate(parts + [two(np.eye(C)), np.kron(np.eye(2), np.ones((C, 1))), np.eye(P)], 1).astype(np.float32)


def stage_rwkv_post(nc, o, bonus, gate, ln_w, ln_b, ident_d, mixT):
    UN = D_RW // P
    GN_EPS = 64e-5
    with Stage(nc, "rwo") as st:
        ident, par = st.sb("ident", [P, P]), st.sb("par", [P, 2, UN])
        of, ob, cen, sq = ([st.sb(f"{x}{u}", [P, D_RW]) for u in range(2)] for x in ("of", "ob", "cen", "sq"))
        bo, ga, mix = ([st.sb(f"{x}{u}", [P, UN, P]) for u in range(2)] for x in ("bo", "ga", "mix"))
        stat = [st.sb(f"stat{u}", [P, 4, RW_HEADS]) for u in range(2)]
        ps = [st.ps(f"t{u}") for u in range(2)]
        par_in = st.sem("par_in")
        tile_in, added, mean, centred, squared, var, root, rstd, normed, turned, step, mixed, stored = (st.sem2(n) for n in (
            "tile_in", "added", "mean", "centred", "squared", "var", "root", "rstd", "normed", "turned", "step", "mixed", "stored"))
        bonused = st.sem2("bonused")

        def heads(ap):
            return ap.rearrange("p (h v) -> p h v", v=RW_HD)

        def rows(tile):
            return bass.ds(tile * P, P)

        def chans(t, tile):
            return t[:, rows(tile)].rearrange("(j p) t -> p j t", p=P)

        with st.block() as block:
            @block.sync
            def _(sp):
                sp.dma_start(ident[:, :], ident_d).then_inc(par_in, 16)
                for j in range(UN):
                    sp.dma_start(par[:, 0, j:j + 1], ln_w[0, j * P:(j + 1) * P].unsqueeze(1)).then_inc(par_in, 16)
                    sp.dma_start(par[:, 1, j:j + 1], ln_b[0, j * P:(j + 1) * P].unsqueeze(1)).then_inc(par_in, 16)

                def load(u, n, tile, seg):
                    sp.wait_ge(mixed[u], n - 1)
                    sp.dma_start(of[u][:, :], o[0, rows(tile), :]).then_inc(tile_in[u], 16)
                    sp.dma_start(ob[u][:, :], o[1, rows(tile), :]).then_inc(tile_in[u], 16)
                    sp.dma_start(bo[u][:, :, :], chans(bonus, tile)).then_inc(tile_in[u], 16)
                    sp.dma_start(ga[u][:, :, :], chans(gate, tile)).then_inc(tile_in[u], 16)
                paired(sp, load, 8)

            @block.gpsimd
            def _(pool):
                def store(u, n, tile, seg):
                    pool.wait_ge(par_in, 16 * (1 + 2 * UN))
                    pool.wait_ge(mixed[u], n)
                    pool.dma_start(chans(mixT[D_LRU:D_LRU + D_RW], tile), mix[u][:, :, :]).then_inc(stored[u], 16)
                paired(pool, store, 8)
                for u in range(2):
                    pool.wait_ge(stored[u], 16 * (9 - u))

            @block.scalar
            def _(act):
                def body(u, n, tile, seg):
                    act.wait_ge(centred[u], n)
                    act.activation(sq[u][:, :], cen[u][:, :], ACT.Square).then_inc(squared[u], 1)
                    act.wait_ge(var[u], 2 * n)
                    act.activation(stat[u][:, 2, :], stat[u][:, 1, :], ACT.Sqrt).then_inc(root[u], 1)
                paired(act, body, 8)

            @block.tensor
            def _(pe):
                pe.wait_ge(par_in, 16 * (1 + 2 * UN))

                def body(u, n, tile, seg):
                    pe.wait_ge(normed[u], n)
                    pe.wait_ge(step[u], n - 1)
                    for j in range(UN):
                        mm = pe.transpose(ps[u][:, j * P:(j + 1) * P], cen[u][:, j * P:(j + 1) * P], ident[:, :])
                    mm.then_inc(turned[u], 1)
                paired(pe, body, 8)

            @block.vector
            def _(dve):
                dve.wait_ge(par_in, 16 * (1 + 2 * UN))

                def body(u, n, tile, seg):
                    s = stat[u]

                    def spread(k):
                        return s[:, k, :].unsqueeze(2).to_broadcast([P, RW_HEADS, RW_HD])
                    dve.wait_ge(tile_in[u], 64 * n)
                    dve.wait_ge(stored[u], 16 * (n - 1))
                    dve.tensor_tensor(of[u][:, :], of[u][:, :], ob[u][:, :], ALU.add).then_inc(added[u], 1)
                    dve.wait_ge(added[u], n)
                    dve.reduce_sum(s[:, 0, :], heads(of[u][:, :]), AX.X).then_inc(mean[u], 1)
                    dve.wait_ge(mean[u], 2 * n - 1)
                    dve.tensor_scalar(s[:, 0, :], s[:, 0, :], 1.0 / RW_HD, None, ALU.mult).then_inc(mean[u], 1)
                    dve.wait_ge(mean[u], 2 * n)
                    dve.tensor_tensor(heads(cen[u][:, :]), heads(of[u][:, :]), spread(0), ALU.subtract).then_inc(centred[u], 1)
                    dve.wait_ge(squared[u], n)
                    dve.reduce_sum(s[:, 1, :], heads(sq[u][:, :]), AX.X).then_inc(var[u], 1)
                    dve.wait_ge(var[u], 2 * n - 1)
                    dve.tensor_scalar(s[:, 1, :], s[:, 1, :], 1.0 / RW_HD, GN_EPS, ALU.mult, ALU.add).then_inc(var[u], 1)
                    dve.wait_ge(root[u], n)
                    dve.reciprocal(s[:, 3, :], s[:, 2, :]).then_inc(rstd[u], 1)
                    dve.wait_ge(rstd[u], n)
                    dve.tensor_tensor(heads(cen[u][:, :]), heads(cen[u][:, :]), spread(3), ALU.mult).then_inc(normed[u], 1)
                    dve.wait_ge(turned[u], n)
                    for j in range(UN):
                        last = dve.tensor_scalar(mix[u][:, j, :], ps[u][:, j * P:(j + 1) * P], par[:, 0, j:j + 1], par[:, 1, j:j + 1], ALU.mult, ALU.add)
                    last.then_inc(step[u], 1)
                    dve.wait_ge(step[u], n)
                    dve.tensor_tensor(bo[u][:, :, :], mix[u][:, :, :], bo[u][:, :, :], ALU.add).then_inc(bonused[u], 1)
                    dve.wait_ge(bonused[u], n)
                    dve.tensor_tensor(mix[u][:, :, :], bo[u][:, :, :], ga[u][:, :, :], ALU.mult).then_inc(mixed[u], 1)
                paired(dve, body, 8)


def grid_rows(t, tile, seg, half):
    if seg == 0:
        return t[64 * half:64 * half + 64, :]
    return t[T_CTX:T, :].rearrange("(c r) x -> r c x", r=GRID_H)[bass.ds(2 * tile - 2 + half, 1)].squeeze(0)


def stage_gla_turn(nc, proj, ident_d, vt):
    UN = D_GLA // P
    V0 = GLA0 + 2 * D_GLA_K
    with Stage(nc, "gvt") as st:
        ident = st.sb("ident", [P, P])
        x, y = ([st.sb(f"{n}{u}", [P, UN, P]) for u in range(2)] for n in ("x", "y"))
        ps = [st.ps(f"t{u}") for u in range(2)]
        ident_in = st.sem("ident_in")
        x_in, turned, copied, stored = (st.sem2(n) for n in ("x_in", "turned", "copied", "stored"))
        with st.block() as block:
            @block.sync
            def _(sp):
                sp.dma_start(ident[:, :], ident_d).then_inc(ident_in, 16)

                def load(u, n, tile, seg):
                    sp.wait_ge(turned[u], n - 1)
                    sp.dma_start(x[u][:, :, :], proj[V0:V0 + D_GLA, bass.ds(tile * P, P)].rearrange("(j p) t -> p j t", p=P)).then_inc(x_in[u], 16)
                paired(sp, load, 8)

            @block.gpsimd
            def _(pool):
                def store(u, n, tile, seg):
                    pool.wait_ge(ident_in, 16)
                    pool.wait_ge(copied[u], n)
                    for half in range(2):
                        rows = grid_rows(vt, tile, seg, half)
                        pool.dma_start(rows, y[u][64 * half:64 * half + 64, :, :].rearrange("p j t -> p (j t)")).then_inc(stored[u], 16)
                paired(pool, store, 8)
                for u in range(2):
                    pool.wait_ge(stored[u], 32 * (9 - u))

            @block.tensor
            def _(pe):
                pe.wait_ge(ident_in, 16)

                def body(u, n, tile, seg):
                    pe.wait_ge(x_in[u], 16 * n)
                    pe.wait_ge(copied[u], n - 1)
                    for j in range(UN):
                        mm = pe.transpose(ps[u][:, j * P:(j + 1) * P], x[u][:, j, :], ident[:, :])
                    mm.then_inc(turned[u], 1)
                paired(pe, body, 8)

            @block.vector
            def _(dve):
                def body(u, n, tile, seg):
                    dve.wait_ge(turned[u], n)
                    dve.wait_ge(stored[u], 32 * (n - 1))
                    dve.tensor_copy(y[u][:, :, :].rearrange("p j t -> p (j t)"), ps[u][:, 0:UN * P]).then_inc(copied[u], 1)
                paired(dve, body, 8)


GREC = 4 * C


def column_major(ap):
    return ap[:, T_CTX:T].rearrange("p (c r) -> p r c", r=GRID_H)


def row_major(ap):
    return ap[:, T_CTX:T].rearrange("p (r c) -> p r c", c=GRID_W)


def stage_gla_prep(nc, proj, wg2, bg, grec):
    HP = GLA_HEADS // 2
    NBLK = len(TOK_BLOCKS)
    G0 = GLA0 + 2 * D_GLA_K + 2 * D_GLA
    with Stage(nc, "glp") as st:
        gd = st.sb("gd", [GLA_R, 2, T])
        w = st.sb("w", [GLA_R, 2, HP, P])
        b_g = st.sb("b_g", [P, 2, HP])
        keep = st.sb("keep", [P, T])
        qk = [st.sb(f"qk{i}", [P, T]) for i in range(2)]
        x, ab, la = ([st.sb(f"{n}{d}", [P, T]) for d in range(2)] for n in ("x", "ab", "la"))
        cum = st.sb("cum", [P, T])
        recs = st.sb("recs", [P, NCH, GREC])
        bank = [st.ps(f"b{b}") for b in range(NBLK)]
        zeroed, par_in, qk_in, consts = st.sem("zeroed"), st.sem("par_in"), st.sem("qk_in"), st.sem("consts")
        product, biased, absd, expd, lnd, la_done, summed, rec_act, stored = (st.sem(n) for n in (
            "product", "biased", "absd", "expd", "lnd", "la_done", "summed", "rec_act", "stored"))
        cum_out = st.sem("cum_out")
        with st.block() as block:
            @block.gpsimd
            def _(pool):
                pool.memset(keep[:, :], 1.0).then_inc(consts, 1)
                for z in (w[:, :, :, :], b_g[:, :, :], qk[0][:, :], qk[1][:, :]):
                    pool.memset(z, 0.0).then_inc(zeroed, 1)
                pool.wait_ge(consts, 1)
                pool.memset(in_chunks(keep[:, :])[:, :, 0:1], 0.0).then_inc(consts, 1)

            @block.sync
            def _(sp):
                sp.wait_ge(zeroed, 4)
                for d in range(2):
                    sp.dma_start(gd[:, d, :], proj[G0 + GLA_R * d:G0 + GLA_R * (d + 1), :]).then_inc(par_in, 16)
                    for head in range(GLA_HEADS):
                        j, h, ch = head // 2, head % 2, slice(head * GLA_DK, (head + 1) * GLA_DK)
                        sp.dma_start(w[:, d, j, 64 * h:64 * h + GLA_DK], wg2[0, d, :, ch]).then_inc(par_in, 16)
                        sp.dma_start(b_g[64 * h:64 * h + GLA_DK, d, j:j + 1], bg[0, d, ch].unsqueeze(1)).then_inc(par_in, 16)
                for j in range(HP):
                    if j:
                        sp.wait_ge(rec_act, 2 * j)
                    for i in range(2):
                        for h in range(2):
                            r0 = GLA0 + i * D_GLA_K + (2 * j + h) * GLA_DK
                            sp.dma_start(qk[i][64 * h:64 * h + GLA_DK, :], proj[r0:r0 + GLA_DK, :]).then_inc(qk_in, 16)
                    sp.wait_ge(rec_act, 2 * (j + 1))
                    sp.wait_ge(cum_out, 2 * (j + 1))
                    sp.dma_start(grec[j], recs[:, :, :]).then_inc(stored, 16)
                sp.wait_ge(stored, 16 * HP)

            @block.tensor
            def _(pe):
                pe.wait_ge(par_in, 16 * 18)
                for j in range(HP):
                    for d in range(2):
                        for b, (t0, tn) in enumerate(TOK_BLOCKS):
                            if 2 * j + d:
                                pe.wait_ge(biased, (2 * j + d - 1) * NBLK + b + 1)
                            pe.matmul(bank[b][:, 0:tn], w[:, d, j, :], gd[:, d, t0:t0 + tn], start=True, stop=True).then_inc(product, 1)

            @block.scalar
            def _(act):
                for j in range(HP):
                    act.wait_ge(qk_in, 64 * (j + 1))
                    if j:
                        act.wait_ge(stored, 16 * j)
                    for i in range(2):
                        o = recs[:, :, i * C:(i + 1) * C]
                        s = GLA_DK ** -0.5 if i == 0 else 1.0
                        act.activation(o[:, 0:NCH_CTX, :], in_chunks(qk[i][:, 0:T_CTX]), ACT.Copy, scale=s)
                        for half in range(2):
                            out = o[:, NCH_CTX:, half * GRID_H:(half + 1) * GRID_H]
                            src = qk[i][:, T_CTX:T].rearrange("p (r k e) -> p e k r", k=GRID_W // 2, e=2)[:, half]
                            last = act.activation(out, src, ACT.Copy, scale=s)
                        last.then_inc(rec_act, 1)
                    for d in range(2):
                        act.wait_ge(biased, (2 * j + d + 1) * NBLK)
                        act.activation(ab[d][:, :], x[d][:, :], ACT.Abs).then_inc(absd, 1)
                        act.wait_ge(absd, 2 * j + d + 1)
                        act.activation(ab[d][:, :], ab[d][:, :], ACT.Exp, scale=-1.0).then_inc(expd, 1)
                        act.wait_ge(expd, 2 * j + d + 1)
                        act.activation(ab[d][:, :], ab[d][:, :], ACT.Ln, bias=1.0).then_inc(lnd, 1)

            @block.vector
            def _(dve):
                dve.wait_ge(par_in, 16 * 18)
                dve.wait_ge(consts, 2)
                for j in range(HP):
                    for d in range(2):
                        n = 2 * j + d
                        for b, (t0, tn) in enumerate(TOK_BLOCKS):
                            dve.wait_ge(product, n * NBLK + b + 1)
                            dve.tensor_scalar(x[d][:, t0:t0 + tn], bank[b][:, 0:tn], b_g[:, d, j:j + 1], None, ALU.add).then_inc(biased, 1)
                    for d in range(2):
                        n = 2 * j + d
                        dve.wait_ge(lnd, n + 1)
                        dve.scalar_tensor_tensor(la[d][:, 0:T_CTX], x[d][:, 0:T_CTX], 0.0, ab[d][:, 0:T_CTX], ALU.min, ALU.subtract)
                        dve.scalar_tensor_tensor(column_major(la[d]), row_major(x[d]), 0.0, row_major(ab[d]), ALU.min, ALU.subtract).then_inc(la_done, 1)
                        dve.wait_ge(la_done, n + 1)
                        dve.tensor_tensor_scan(scan_order(cum, d, 0, T), keep[:, :], scan_order(la[d], d, 0, T), 0.0, ALU.mult, ALU.add).then_inc(summed, 1)
                        dve.wait_ge(summed, n + 1)
                        if j:
                            dve.wait_ge(stored, 16 * j)
                        dve.tensor_copy(recs[:, :, (2 + d) * C:(3 + d) * C], in_chunks(cum[:, :])).then_inc(cum_out, 1)


def gla_constants():
    parts = [np.concatenate([m, m], 0) for d in range(2) for m in [j.T for j in joins(d)] + [np.eye(C)]]
    return np.concatenate(parts + [np.kron(np.eye(2), np.ones((C, 1))), np.eye(P)], 1).astype(np.float32)


def stage_scans(nc, rec, decay, consts_d, state_in, new_state, o, grec, vt, gla_consts_d, gla_state_in, gla_new_state, gla_o):
    G, UN, GN = 2, 3, 2
    NL = LEVELS - 1
    W = rwkv_constants().shape[1]
    NS = LEVELS + 2
    NA = LEVELS + 1
    WG = gla_constants().shape[1]
    CA = 4
    KT_AT, KF_AT, ATT_AT, SUM_AT = (2, 3), (1, 2), (3, 4), (4, 5)
    with Stage(nc, "scn") as st:
        con = st.sb("con", [P, W])
        per_d = 4 * C + LEVELS * C
        mask2 = [con[:, g * per_d:g * per_d + 2 * C].rearrange("p (q t) -> p q t", q=2) for g in range(G)]
        mT0 = [con[:, g * per_d + 2 * C:g * per_d + 4 * C] for g in range(G)]
        m_lev = [con[:, g * per_d + 4 * C:(g + 1) * per_d].rearrange("p (l s) -> p l s", l=LEVELS) for g in range(G)]
        eye, eye128 = con[:, G * per_d:G * per_d + C], con[:, W - P:W]
        own = con[:, W - P - 2:W - P]
        plain = [st.sb(f"plain{u}", [P, G * UN, REC]) for u in range(2)]
        bd = [st.sb(f"bd{u}", [P, G * UN, 5, 2, C]) for u in range(2)]
        LR = [st.sb(f"LR{g}", [P, UN, 2, 2, C]) for g in range(G)]
        KR = [st.sb(f"KR{g}", [P, UN, 2, 2, C]) for g in range(G)]
        Ti = [st.sb(f"T{g}", [P, UN, C]) for g in range(G)]
        Ui = [st.sb(f"U{g}", [P, UN, P]) for g in range(G)]
        Ys = [st.sb(f"Ys{g}", [P, UN, C]) for g in range(G)]
        Yd = [st.sb(f"Yd{g}", [P, UN, 2, C]) for g in range(G)]
        Vs, Xs, SAs, S, Sn = ([st.sb(f"{x}{g}", [P, UN, C]) for g in range(G)] for x in ("V", "X", "SA", "S", "Sn"))
        BT, KT = ([st.sb(f"{x}{g}", [P, UN, P]) for g in range(G)] for x in ("BT", "KT"))
        Os = [[st.sb(f"O{g}{u}", [P, UN, C]) for u in range(2)] for g in range(G)]
        SX = st.sb("SX", [P, G * UN, 2, C])
        total = st.sb("total", [P, G, UN, NCH])
        gcon = st.sb("gcon", [P, WG])
        gmask = [gcon[:, g * NA * C:(g + 1) * NA * C].rearrange("p (l t) -> p l t", l=NA) for g in range(G)]
        grc = [st.sb(f"grc{u}", [P, G, GN, GREC]) for u in range(2)]
        gv = [st.sb(f"gv{u}", [P, G, GN, GLA_DV]) for u in range(2)]
        Dd = [st.sb(f"D{g}", [P, NS, GN, C]) for g in range(G)]
        F = [st.sb(f"F{g}", [P, NS, GN, C]) for g in range(G)]
        QF = [st.sb(f"QF{g}", [P, LEVELS, GN, C]) for g in range(G)]
        KF = [st.sb(f"KF{g}", [P, GN, LEVELS, 2, C]) for g in range(G)]
        qo, ko, qe, kh = ([st.sb(f"{x}{g}", [P, GN, 2, C]) for g in range(G)] for x in ("qo", "ko", "qe", "kh"))
        AM = [st.sb(f"AM{g}", [P, NA, GN, C]) for g in range(G)]
        att = [st.sb(f"att{g}", [P, GN, C]) for g in range(G)]
        ad = [st.sb(f"ad{g}", [P, GN, 2, C]) for g in range(G)]
        kT = [st.sb(f"kT{g}", [P, GN, P]) for g in range(G)]
        gS = [st.sb(f"gS{g}", [P, GN, GLA_DV]) for g in range(G)]
        gOs = [[st.sb(f"gO{g}{u}", [P, GN, GLA_DV]) for u in range(2)] for g in range(G)]
        bank = [st.ps(f"b{b}") for b in range(8)]
        pA, pB, pC, pD, pE, pF, pG, pH = bank
        pV, pYU, pS = [pF, pG], [pF, pG], [pF, pG]
        pY, pX = [pH, pC], [pH, pC]
        g1, g2 = [pA, pD], [pB, pE]

        def each(name):
            return [st.sem(f"{name}_{g}") for g in range(G)]
        con_in, cleared, rec_in = st.sem("con_in"), st.sem("cleared"), st.sem2("rec_in")
        mm_v, mm_a, mm_b, mm_c, mm_d, mm_e = (each(n) for n in ("mm_v", "mm_a", "mm_b", "mm_c", "mm_d", "mm_e"))
        lr_done, kr_done, t_mask, t0_done, vs_done, bt_done, kt_done = (each(n) for n in (
            "lr_done", "kr_done", "t_mask", "t0_done", "vs_done", "bt_done", "kt_done"))
        u_mask, u0_done = each("u_mask"), each("u0_done")
        y_mm, ys_done, yd_done, ty_mm, yu_mm, t_step, u_step = (each(n) for n in (
            "y_mm", "ys_done", "yd_done", "ty_mm", "yu_mm", "t_step", "u_step"))
        x_mm, x_done, sa_mm, sa_done, o_mm, o_done, s_mm, s_sum, s_done = (each(n) for n in (
            "x_mm", "x_done", "sa_mm", "sa_done", "o_mm", "o_done", "s_mm", "s_sum", "s_done"))
        o_out = [st.sem2(f"o_out{g}") for g in range(G)]
        state0 = st.sem("state0")
        sx_ready, sx_mm, sx_out, sx_stored, sx_in, imported = (st.sem(n) for n in (
            "sx_ready", "sx_mm", "sx_out", "sx_stored", "sx_in", "imported"))
        grec_in = st.sem2("grec_in")
        diffs, slot6, absd, expd, owned, qf_done, qk_bd, kf_done, kT_mm, kT_done = (each(n) for n in (
            "diffs", "slot6", "absd", "expd", "owned", "qf_done", "qk_bd", "kf_done", "kT_mm", "kT_done"))
        att_a, att_b, masked, att_sum, att_bd, go_mm, go_done, gs_done = (each(n) for n in (
            "att_a", "att_b", "masked", "att_sum", "att_bd", "go_mm", "go_done", "gs_done"))
        go_out = [st.sem2(f"go_out{g}") for g in range(G)]
        gstate_out, gstate_in = st.sem("gstate_out"), st.sem("gstate_in")
        N_CLEARED = 3 + 3 * G

        def q_bd(u, j, q):
            return bd[u][:, j, q, :, :].rearrange("p h t -> p (h t)")

        def cols(ps, j, w):
            return ps[:, j * w:(j + 1) * w]

        def v3(ap):
            return ap.rearrange("p (j t) -> p j t", j=UN)

        def flat(ap):
            return ap.rearrange("p h t -> p (h t)")

        def own_of(g):
            return own.unsqueeze(1).unsqueeze(3).to_broadcast([P, GN, 2, C])

        def both(eng, chunk, between):
            for c in range(NCH_CTX):
                chunk(c % 2, 1, c, (c, NCH_CTX - 1 - c), True)
            between()
            with eng.Fori(0, (NCH - NCH_CTX) // 2) as i:
                for u in range(2):
                    chunk(u, i + 2, 2 * i + 2 + u, (2 * i + 2 + u, NCH - 1 - u - 2 * i), False)

        def nothing():
            pass

        def gla_states(t, g):
            return t[0, 0, g].rearrange("(j h) k v -> h k j v", h=2)

        with st.block() as block:
            @block.sync
            def _(sp):
                sp.dma_start(con[:, :], consts_d).then_inc(con_in, 16)
                sp.dma_start(gcon[:, :], gla_consts_d).then_inc(con_in, 16)
                sp.dma_start(total[:, :, :, :], decay).then_inc(con_in, 16)
                sp.wait_ge(cleared, N_CLEARED)

                def load(u, c, at):
                    for g in range(G):
                        js = slice(UN * g, UN * (g + 1))
                        chunk_rec = rec[g, :, bass.ds(at[g], 1), :, :]
                        sp.dma_start(plain[u][:, js, :].rearrange("p j w -> p (j w)"), chunk_rec.rearrange("p c j w -> p (c j w)")).then_inc(rec_in[u], 16)
                        for h in range(2):
                            p = slice(64 * h, 64 * h + 64)
                            sp.dma_start(bd[u][p, js, :, h, :].rearrange("p j q t -> p (j q) t"),
                                         chunk_rec[p].rearrange("p c j (q t) -> p (c j q) t", t=C)).then_inc(rec_in[u], 16)
                        sp.dma_start(grc[u][:, g, :, :], grec[:, :, bass.ds(at[g], 1), :].rearrange("j p c w -> p j (c w)")).then_inc(grec_in[u], 16)
                        for h in range(2):
                            sp.dma_start(gv[u][64 * h:64 * h + 64, g, :, :],
                                         vt[bass.ds(at[g] * C, C), :].rearrange("t (j h x) -> h t j x", h=2, j=GN)[h]).then_inc(grec_in[u], 16)

                def store(u, c, at):
                    for g in range(G):
                        rows = gla_o[g, bass.ds(at[g] * C, C), :]
                        sp.wait_ge(cleared, N_CLEARED)
                        sp.wait_ge(go_done[g], c + 1)
                        for h in range(2):
                            sp.dma_start(rows.rearrange("t (j h x) -> h t j x", h=2, j=GN)[h], gOs[g][u][64 * h:64 * h + 64, :, :]).then_inc(go_out[g][u], 16)
                    for g in range(G):
                        rows = o[g, bass.ds(at[g] * C, C), :]
                        sp.wait_ge(cleared, N_CLEARED)
                        sp.wait_ge(o_done[g], c + 1)
                        for h in range(2):
                            sp.dma_start(rows.rearrange("t (j h v) -> h t j v", h=2, j=UN)[h], Os[g][u][64 * h:64 * h + 64, :, :]).then_inc(o_out[g][u], 16)

                def freed(c):
                    for g in range(G):
                        sp.wait_ge(s_done[g], c + 1)
                        sp.wait_ge(gs_done[g], c + 1)

                def swap():
                    sp.wait_ge(sx_out, 1)
                    for g in range(G):
                        for h in range(2):
                            sp.dma_start(new_state[0, 0, g].rearrange("(j h) v k -> h v j k", h=2)[h], Xs[g][64 * h:64 * h + 64, :, :]).then_inc(sx_stored, 16)
                            sp.dma_start(SX[64 * h:64 * h + 64, UN * g:UN * (g + 1), h, :],
                                         state_in[0, 0, g].rearrange("(j h) v k -> h v j k", h=2)[h]).then_inc(sx_in, 16)
                    sp.wait_ge(sx_stored, 16 * 4)
                    for g in range(G):
                        sp.wait_ge(gs_done[g], NCH_CTX)
                    for g in range(G):
                        for h in range(2):
                            sp.dma_start(gla_states(gla_new_state, g)[h], gS[g][64 * h:64 * h + GLA_DK, :, :]).then_inc(gstate_out, 16)
                    sp.wait_ge(gstate_out, 64)
                    for g in range(G):
                        for h in range(2):
                            sp.dma_start(gS[g][64 * h:64 * h + GLA_DK, :, :], gla_states(gla_state_in, g)[h]).then_inc(gstate_in, 16)

                def reached(c):
                    return (c, NCH_CTX - 1 - c if isinstance(c, int) and c < NCH_CTX else NCH + NCH_CTX - 1 - c)
                for c in range(NCH_CTX):
                    load(c, c, reached(c))
                for c in range(NCH_CTX):
                    freed(c)
                    load(c, c + 2, reached(c + 2))
                    store(c, c, reached(c))
                swap()
                with sp.Fori(0, (NCH - NCH_CTX) // 2 - 1) as i:
                    for u in range(2):
                        freed(2 * i + 2 + u)
                        load(u, 2 * i + 4 + u, (2 * i + 4 + u, NCH - 3 - u - 2 * i))
                        store(u, 2 * i + 2 + u, (2 * i + 2 + u, NCH - 1 - u - 2 * i))
                for u in range(2):
                    store(u, NCH - 2 + u, reached(NCH - 2 + u))
                for g in range(G):
                    for u in range(2):
                        sp.wait_ge(o_out[g][u], 32 * NCH // 2)
                        sp.wait_ge(go_out[g][u], 32 * NCH // 2)

            @block.gpsimd
            def _(pool):
                for z in (*(b[:, :, :, :, :] for b in bd), SX[:, :, :, :]):
                    pool.memset(z, 0.0).then_inc(cleared, 1)
                for g in range(G):
                    for z in (LR[g], KR[g]):
                        pool.memset(z[:, :, :, :, :], 0.0).then_inc(cleared, 1)
                    pool.memset(Yd[g][:, :, :, :], 0.0).then_inc(cleared, 1)
                pool.wait_ge(con_in, 48)
                pool.wait_ge(cleared, N_CLEARED)

                def chunk(u, m, c, at, ctx):
                    n = c + 1
                    pool.wait_ge(grec_in[u], 96 * m)
                    for g in range(G):
                        pool.wait_ge(absd[g], c)
                        b = grc[u][:, g, :, (2 + g) * C:(3 + g) * C]
                        for l in range(LEVELS):
                            h = 1 << l
                            m_at = h - 1 if g == 0 else h
                            bl = b.rearrange("p j (s w) -> p j s w", w=2 * h)
                            out = Dd[g][:, l, :, :].rearrange("p j (s w) -> p j s w", w=2 * h)
                            pool.tensor_tensor(out, bl, bl[:, :, :, m_at:m_at + 1].to_broadcast([P, GN, C // (2 * h), 2 * h]), ALU.subtract)
                        end = C - 1 if g == 0 else 0
                        pool.tensor_tensor(Dd[g][:, LEVELS + 1, :, :], b, b[:, :, end:end + 1].to_broadcast([P, GN, C]), ALU.subtract).then_inc(diffs[g], 1)
                    for g in range(G):
                        pool.wait_ge(go_mm[g], c)
                        for q, out in ((0, qo), (1, ko)):
                            src = grc[u][:, g, :, q * C:(q + 1) * C].unsqueeze(2).to_broadcast([P, GN, 2, C])
                            last = pool.tensor_tensor(out[g][:, :, :, :], src, own_of(g), ALU.mult)
                        last.then_inc(owned[g], 1)
                    for g in range(G):
                        lt = LR[g][:, :, 0, :, :].rearrange("p j h t -> p j (h t)")
                        pool.wait_ge(lr_done[g], n)
                        pool.tensor_tensor(Ui[g][:, :, :], lt, mT0[g].unsqueeze(1).to_broadcast([P, UN, P]), ALU.mult).then_inc(u_mask[g], 1)
                        pool.wait_ge(u_mask[g], n)
                        pool.tensor_tensor(Ui[g][:, :, :], Ui[g][:, :, :], eye128.unsqueeze(1).to_broadcast([P, UN, P]), ALU.add).then_inc(u0_done[g], 1)
                    for g in range(G):
                        pool.wait_ge(owned[g], n)
                        pool.wait_ge(expd[g], n)
                        for src, slot, out in ((qo, LEVELS, qe), (ko, LEVELS + 1, kh)):
                            last = pool.tensor_tensor(out[g][:, :, :, :], src[g][:, :, :, :], F[g][:, slot, :, :].unsqueeze(2).to_broadcast([P, GN, 2, C]), ALU.mult)
                        last.then_inc(qk_bd[g], 1)
                        q = grc[u][:, g, :, 0:C].unsqueeze(1).to_broadcast([P, LEVELS, GN, C])
                        pool.tensor_tensor(QF[g][:, :, :, :], q, F[g][:, 0:LEVELS, :, :], ALU.mult).then_inc(qf_done[g], 1)
                    for g in range(G):
                        pool.wait_ge(att_sum[g], n)
                        pool.tensor_tensor(ad[g][:, :, :, :], att[g][:, :, :].unsqueeze(2).to_broadcast([P, GN, 2, C]), own_of(g), ALU.mult).then_inc(att_bd[g], 1)
                both(pool, chunk, nothing)

            @block.scalar
            def _(act):
                act.wait_ge(cleared, N_CLEARED)

                def chunk(u, m, c, at, ctx):
                    n = c + 1
                    for g in range(G):
                        act.wait_ge(grec_in[u], 96 * m)
                        act.wait_ge(absd[g], c)
                        act.activation(Dd[g][:, LEVELS, :, :], grc[u][:, g, :, (2 + g) * C:(3 + g) * C], ACT.Copy).then_inc(slot6[g], 1)
                        act.wait_ge(slot6[g], n)
                        act.wait_ge(diffs[g], n)
                        act.wait_ge(qf_done[g], c)
                        act.wait_ge(kf_done[g], c)
                        act.wait_ge(gs_done[g], c)
                        act.activation(F[g][:, :, :, :], Dd[g][:, :, :, :], ACT.Abs).then_inc(absd[g], 1)
                        act.wait_ge(absd[g], n)
                        act.activation(F[g][:, :, :, :], F[g][:, :, :, :], ACT.Exp, scale=-1.0 / 16.0).then_inc(expd[g], 1)
                    for g in range(G):
                        act.wait_ge(mm_v[g], n)
                        act.copy(Vs[g][:, :, :], v3(pV[g][:, 0:UN * C])).then_inc(vs_done[g], 1)
                        act.wait_ge(mm_d[g], n)
                        act.copy(BT[g][:, :, :], v3(pD[:, 0:UN * P])).then_inc(bt_done[g], 1)
                        act.wait_ge(mm_e[g], n)
                        act.copy(KT[g][:, :, :], v3(pE[:, 0:UN * P])).then_inc(kt_done[g], 1)
                    for l in range(1, NL + 1):
                        for g in range(G):
                            act.wait_ge(ys_done[g], NL * c + l)
                            for h in range(2):
                                p = slice(64 * h, 64 * h + 64)
                                last = act.copy(Yd[g][p, :, h, :], Ys[g][p, :, :])
                            last.then_inc(yd_done[g], 1)
                        for g in range(G):
                            if l == KT_AT[g]:
                                act.wait_ge(kT_mm[g], n)
                                act.copy(kT[g][:, :, :], g2[g][:, 0:GN * P].rearrange("p (j k) -> p j k", j=GN)).then_inc(kT_done[g], 1)
                    for g in range(G):
                        act.wait_ge(x_mm[g], n)
                        act.copy(Xs[g][:, :, :], v3(pX[g][:, 0:UN * C])).then_inc(x_done[g], 1)
                    for g in range(G):
                        act.wait_ge(go_mm[g], n)
                        act.wait_ge(go_out[g][u], 32 * (m - 1))
                        act.copy(gOs[g][u][:, :, :], g2[g][:, 0:GN * GLA_DV].rearrange("p (j x) -> p j x", j=GN)).then_inc(go_done[g], 1)
                    for g in range(G):
                        act.wait_ge(o_mm[g], n)
                        act.wait_ge(o_out[g][u], 32 * (m - 1))
                        act.copy(Os[g][u][:, :, :], v3(pX[g][:, 0:UN * C])).then_inc(o_done[g], 1)
                both(act, chunk, nothing)

            @block.tensor
            def _(pe):
                pe.wait_ge(con_in, 48)
                pe.wait_ge(state0, 2 * G)

                def keys_turned(g, u, n):
                    pe.wait_ge(qk_bd[g], n)
                    pe.wait_ge(kr_done[1] if g == 0 else kt_done[1], n)
                    for j in range(GN):
                        mm = pe.transpose(cols(g2[g], j, P), flat(kh[g][:, j, :, :]), eye128)
                    mm.then_inc(kT_mm[g], 1)

                def attention(g, u, n):
                    pe.wait_ge(kf_done[g], n)
                    pe.wait_ge(qf_done[g], n)
                    pe.wait_ge(lr_done[1] if g == 0 else bt_done[1], n)
                    for l in range(NA):
                        if l == CA:
                            pe.wait_ge(kT_done[g], n)
                        for j in range(GN):
                            ps = g1[g] if l < CA else g2[g]
                            x = (l % CA * GN + j) * C
                            if l < LEVELS:
                                mm = pe.matmul(ps[:, x:x + C], flat(KF[g][:, j, l, :, :]), QF[g][:, l, j, :], start=True, stop=True)
                            else:
                                mm = pe.matmul(ps[:, x:x + C], flat(ko[g][:, j, :, :]), grc[u][:, g, j, 0:C], start=True, stop=True)
                        if l in (CA - 1, NA - 1):
                            mm.then_inc((att_a if l < CA else att_b)[g], 1)

                def gla_output(g, u, c):
                    pe.wait_ge(kT_done[g], c + 1)
                    pe.wait_ge(masked[g], c + 1)
                    pe.wait_ge(gs_done[g], c)
                    for j in range(GN):
                        pe.matmul(cols(g1[g], j, GLA_DV), kT[g][:, j, :], gv[u][:, g, j, :], start=True, stop=True)
                    pe.wait_ge(att_bd[g], c + 1)
                    for j in range(GN):
                        out = cols(g2[g], j, GLA_DV)
                        pe.matmul(out, flat(qe[g][:, j, :, :]), gS[g][:, j, :], start=True, stop=False)
                        mm = pe.matmul(out, flat(ad[g][:, j, :, :]), gv[u][:, g, j, :], start=False, stop=True)
                    mm.then_inc(go_mm[g], 1)

                def chunk(u, m, c, at, ctx):
                    n = c + 1
                    pe.wait_ge(rec_in[u], 16 * 6 * m)
                    for g in range(G):
                        js = range(UN * g, UN * (g + 1))

                        def leaves(by_last_chunk, by_group_0):
                            if g == 0:
                                pe.wait_ge(by_last_chunk, c)
                            else:
                                pe.wait_ge(by_group_0, n)
                        leaves(gs_done[0], lr_done[0])
                        for x, j in enumerate(js):
                            mm = pe.matmul(cols(pA, x, P), q_bd(u, j, 2), plain[u][:, j, 0:P], start=True, stop=True)
                        mm.then_inc(mm_a[g], 1)
                        leaves(o_done[1], t_mask[0])
                        for x, j in enumerate(js):
                            mm = pe.matmul(cols(pC, x, C), q_bd(u, j, 0), plain[u][:, j, P:3 * C], start=True, stop=True)
                        mm.then_inc(mm_c[g], 1)
                        leaves(go_done[0], kr_done[0])
                        for x, j in enumerate(js):
                            mm = pe.matmul(cols(pB, x, P), q_bd(u, j, 3), plain[u][:, j, 0:P], start=True, stop=True)
                        mm.then_inc(mm_b[g], 1)
                        pe.wait_ge(s_sum[g], c)
                        for x, j in enumerate(js):
                            mm = pe.matmul(cols(pV[g], x, C), q_bd(u, j, 4), eye, start=True, stop=True)
                        mm.then_inc(mm_v[g], 1)
                        leaves(gs_done[1], bt_done[0])
                        for x, j in enumerate(js):
                            mm = pe.transpose(cols(pD, x, P), q_bd(u, j, 2), eye128)
                        mm.then_inc(mm_d[g], 1)
                        leaves(go_done[1], kt_done[0])
                        for x, j in enumerate(js):
                            mm = pe.transpose(cols(pE, x, P), q_bd(u, j, 3), eye128)
                        mm.then_inc(mm_e[g], 1)
                    for l in range(1, NL + 1):
                        for g in range(G):
                            if l == 1:
                                pe.wait_ge(o_done[g], c)
                                pe.wait_ge(lr_done[g], n)
                                pe.wait_ge(t0_done[g], n)
                            else:
                                pe.wait_ge(t_step[g], (NL - 1) * c + l - 1)
                            for x in range(UN):
                                mm = pe.matmul(cols(pY[g], x, C), flat(LR[g][:, x, 0, :, :]), Ti[g][:, x, :], start=True, stop=True)
                            mm.then_inc(y_mm[g], 1)
                        for g in range(G):
                            if l == KT_AT[g]:
                                keys_turned(g, u, n)
                        for g in range(G):
                            if l == ATT_AT[g]:
                                attention(g, u, n)
                        for g in range(G):
                            pe.wait_ge(ys_done[g], NL * c + l)
                            if l == 1:
                                pe.wait_ge(u0_done[g], n)
                            pe.wait_ge(u_step[g], NL * c + l - 1)
                            if l < NL:
                                for x in range(UN):
                                    mm = pe.matmul(cols(pY[g], x, C), Ui[g][:, x, :], Ys[g][:, x, :], start=True, stop=True)
                                mm.then_inc(ty_mm[g], 1)
                            if l == 1:
                                pe.wait_ge(vs_done[g], n)
                            pe.wait_ge(yd_done[g], NL * c + l)
                            for x in range(UN):
                                mm = pe.matmul(cols(pYU[g], x, P), flat(Yd[g][:, x, :, :]), Ui[g][:, x, :], start=True, stop=True)
                            mm.then_inc(yu_mm[g], 1)
                    for g in range(G):
                        for e in (vs_done[g], kr_done[g], lr_done[1], kr_done[1]):
                            pe.wait_ge(e, n)
                        pe.wait_ge(s_done[g], c)
                        for x in range(UN):
                            pe.matmul(cols(pX[g], x, C), q_bd(u, UN * g + x, 0), S[g][:, x, :], start=True, stop=False)
                            mm = pe.matmul(cols(pX[g], x, C), flat(KR[g][:, x, 0, :, :]), Vs[g][:, x, :], start=False, stop=True)
                        mm.then_inc(x_mm[g], 1)
                    gla_output(0, u, c)
                    for g in range(G):
                        pe.wait_ge(x_done[g], n)
                        pe.wait_ge(u_step[g], NL * n)
                        for x in range(UN):
                            mm = pe.matmul(cols(pX[g], UN + x, C), Ui[g][:, x, :], Xs[g][:, x, :], start=True, stop=True)
                        mm.then_inc(sa_mm[g], 1)
                    gla_output(1, u, c)
                    for g in range(G):
                        for e in (bt_done[1], kt_done[1], bt_done[g], kt_done[g], sa_done[g]):
                            pe.wait_ge(e, n)
                        for x in range(UN):
                            pe.matmul(cols(pX[g], x, C), q_bd(u, UN * g + x, 1), S[g][:, x, :], start=True, stop=False)
                            pe.matmul(cols(pX[g], x, C), flat(LR[g][:, x, 1, :, :]), SAs[g][:, x, :], start=False, stop=False)
                            mm = pe.matmul(cols(pX[g], x, C), flat(KR[g][:, x, 1, :, :]), Vs[g][:, x, :], start=False, stop=True)
                        mm.then_inc(o_mm[g], 1)
                        for x in range(UN):
                            pe.matmul(cols(pS[g], x, C), BT[g][:, x, :], SAs[g][:, x, :], start=True, stop=False)
                            mm = pe.matmul(cols(pS[g], x, C), KT[g][:, x, :], Vs[g][:, x, :], start=False, stop=True)
                        mm.then_inc(s_mm[g], 1)

                def swap():
                    pe.wait_ge(sx_ready, 1)
                    for g in range(G):
                        pe.wait_ge(gs_done[g], NCH_CTX)
                    for j in range(G * UN):
                        mm = pe.matmul(cols(pA, j, C), flat(SX[:, j, :, :]), eye, start=True, stop=True)
                    mm.then_inc(sx_mm, 1)
                    pe.wait_ge(sx_in, 16 * 4)
                    for j in range(G * UN):
                        mm = pe.matmul(cols(pA, j, C), flat(SX[:, j, :, :]), eye, start=True, stop=True)
                    mm.then_inc(sx_mm, 1)
                    pe.wait_ge(imported, 1)
                    pe.wait_ge(gstate_in, 64)
                both(pe, chunk, swap)

            @block.vector
            def _(dve):
                for g in range(G):
                    dve.memset(S[g][:, :, :], 0.0).then_inc(state0, 1)
                    dve.memset(gS[g][:, :, :], 0.0).then_inc(state0, 1)
                dve.wait_ge(con_in, 48)
                dve.wait_ge(cleared, N_CLEARED)

                def keys_decayed(g, c):
                    dve.wait_ge(owned[g], c + 1)
                    dve.wait_ge(expd[g], c + 1)
                    dve.wait_ge(att_b[g], c)
                    for j in range(GN):
                        last = dve.tensor_tensor(KF[g][:, j, :, :, :], ko[g][:, j, :, :].unsqueeze(1).to_broadcast([P, LEVELS, 2, C]),
                                                 F[g][:, 0:LEVELS, j, :].unsqueeze(2).to_broadcast([P, LEVELS, 2, C]), ALU.mult)
                    last.then_inc(kf_done[g], 1)

                def attention_summed(g, n):
                    dve.wait_ge(att_a[g], n)
                    dve.tensor_tensor(AM[g][:, 0:CA, :, :], g1[g][:, 0:CA * GN * C].rearrange("p (l j t) -> p l j t", l=CA, j=GN),
                                      gmask[g][:, 0:CA, :].unsqueeze(2).to_broadcast([P, CA, GN, C]), ALU.mult)
                    dve.wait_ge(att_b[g], n)
                    dve.tensor_tensor(AM[g][:, CA:NA, :, :], g2[g][:, 0:(NA - CA) * GN * C].rearrange("p (l j t) -> p l j t", l=NA - CA, j=GN),
                                      gmask[g][:, CA:NA, :].unsqueeze(2).to_broadcast([P, NA - CA, GN, C]), ALU.mult).then_inc(masked[g], 1)
                    dve.wait_ge(masked[g], n)
                    dve.reduce_sum(att[g][:, :, :].rearrange("p j t -> p (j t)"), AM[g][:, :, :, :].rearrange("p l j t -> p (j t) l"), AX.X).then_inc(att_sum[g], 1)

                def gla_state(g, n):
                    dve.wait_ge(go_mm[g], n)
                    end = C - 1 if g == 0 else 0
                    for j in range(GN):
                        last = dve.scalar_tensor_tensor(gS[g][:, j, :], gS[g][:, j, :], F[g][:, LEVELS, j, end:end + 1],
                                                        cols(g1[g], j, GLA_DV), ALU.mult, ALU.add)
                    last.then_inc(gs_done[g], 1)

                def chunk(u, m, c, at, ctx):
                    n = c + 1
                    for g in range(G):
                        dve.wait_ge(mm_a[g], n)
                        for h in range(2):
                            p = slice(64 * h, 64 * h + 64)
                            m_b = mask2[g][p].unsqueeze(1).to_broadcast([64, UN, 2, C])
                            last = dve.tensor_tensor(LR[g][p, :, :, h, :], pA[p, 0:UN * P].rearrange("p (j q t) -> p j q t", j=UN, q=2), m_b, ALU.mult)
                        last.then_inc(lr_done[g], 1)
                        dve.wait_ge(mm_c[g], n)
                        dve.tensor_tensor(Ti[g][:, :, :], v3(pC[:, 0:UN * C]), m_lev[g][:, 0:1, :].to_broadcast([P, UN, C]), ALU.mult).then_inc(t_mask[g], 1)
                        dve.wait_ge(t_mask[g], n)
                        dve.tensor_tensor(Ti[g][:, :, :], Ti[g][:, :, :], eye.unsqueeze(1).to_broadcast([P, UN, C]), ALU.add).then_inc(t0_done[g], 1)
                        dve.wait_ge(mm_b[g], n)
                        for h in range(2):
                            p = slice(64 * h, 64 * h + 64)
                            m_b = mask2[g][p].unsqueeze(1).to_broadcast([64, UN, 2, C])
                            last = dve.tensor_tensor(KR[g][p, :, :, h, :], pB[p, 0:UN * P].rearrange("p (j q t) -> p j q t", j=UN, q=2), m_b, ALU.mult)
                        last.then_inc(kr_done[g], 1)
                    for l in range(1, NL + 1):
                        for g in range(G):
                            dve.wait_ge(y_mm[g], NL * c + l)
                            dve.wait_ge(yd_done[g], NL * c + l - 1)
                            dve.tensor_tensor(Ys[g][:, :, :], v3(pY[g][:, 0:UN * C]), m_lev[g][:, l:l + 1, :].to_broadcast([P, UN, C]), ALU.mult).then_inc(ys_done[g], 1)
                        for g in range(G):
                            if l == KF_AT[g]:
                                keys_decayed(g, c)
                            if l == SUM_AT[g]:
                                attention_summed(g, n)
                        for g in range(G):
                            if l < NL:
                                dve.wait_ge(ty_mm[g], (NL - 1) * c + l)
                                dve.tensor_tensor(Ti[g][:, :, :], v3(pY[g][:, 0:UN * C]), Ti[g][:, :, :], ALU.add).then_inc(t_step[g], 1)
                            dve.wait_ge(yu_mm[g], NL * c + l)
                            dve.tensor_tensor(Ui[g][:, :, :], v3(pYU[g][:, 0:UN * P]), Ui[g][:, :, :], ALU.add).then_inc(u_step[g], 1)
                    for g in range(G):
                        dve.wait_ge(sa_mm[g], n)
                        dve.tensor_copy(SAs[g][:, :, :], v3(pX[g][:, UN * C:2 * UN * C])).then_inc(sa_done[g], 1)
                    for g in range(G):
                        gla_state(g, n)
                    for g in range(G):
                        dve.wait_ge(s_mm[g], n)
                        dve.tensor_tensor(Sn[g][:, :, :], v3(pS[g][:, 0:UN * C]), S[g][:, :, :], ALU.add).then_inc(s_sum[g], 1)
                        dve.wait_ge(con_in, 48)
                        dve.wait_ge(s_sum[g], n)
                        dve.tensor_tensor(S[g][:, :, :], Sn[g][:, :, :], total[:, g, :, bass.ds(at[g], 1)].to_broadcast([P, UN, C]), ALU.mult).then_inc(s_done[g], 1)

                def swap():
                    dve.wait_ge(cleared, N_CLEARED)
                    for g in range(G):
                        dve.wait_ge(s_done[g], NCH_CTX)
                        for h in range(2):
                            last = dve.tensor_copy(SX[64 * h:64 * h + 64, UN * g:UN * (g + 1), h, :], S[g][64 * h:64 * h + 64, :, :])
                    last.then_inc(sx_ready, 1)
                    dve.wait_ge(sx_mm, 1)
                    for g in range(G):
                        last = dve.tensor_copy(Xs[g][:, :, :], v3(pA[:, UN * C * g:UN * C * (g + 1)]))
                    last.then_inc(sx_out, 1)
                    dve.wait_ge(sx_mm, 2)
                    for g in range(G):
                        last = dve.tensor_copy(S[g][:, :, :], v3(pA[:, UN * C * g:UN * C * (g + 1)]))
                    last.then_inc(imported, 1)
                    dve.wait_ge(gstate_in, 64)
                both(dve, chunk, swap)


def stage_gla_post(nc, o, proj, norm_w, ident_d, mixT):
    UN = D_GLA // P
    GATE0 = GLA0 + 2 * D_GLA_K + D_GLA
    with Stage(nc, "glo") as st:
        ident, par = st.sb("ident", [P, P]), st.sb("par", [P, UN])
        of, ob, sq = ([st.sb(f"{x}{u}", [P, D_GLA]) for u in range(2)] for x in ("of", "ob", "sq"))
        ga, mix = ([st.sb(f"{x}{u}", [P, UN, P]) for u in range(2)] for x in ("ga", "mix"))
        stat = [st.sb(f"stat{u}", [P, 4, GLA_HEADS]) for u in range(2)]
        ps = [st.ps(f"t{u}") for u in range(2)]
        par_in = st.sem("par_in")
        tile_in, added, squared, silud, var, root, rstd, normed, turned, mixed, stored = (st.sem2(n) for n in (
            "tile_in", "added", "squared", "silud", "var", "root", "rstd", "normed", "turned", "mixed", "stored"))

        def heads(ap):
            return ap.rearrange("p (h v) -> p h v", v=GLA_DV)

        def rows(tile):
            return bass.ds(tile * P, P)

        with st.block() as block:
            @block.sync
            def _(sp):
                sp.dma_start(ident[:, :], ident_d).then_inc(par_in, 16)
                for j in range(UN):
                    sp.dma_start(par[:, j:j + 1], norm_w[0].rearrange("h v -> (h v)")[j * P:(j + 1) * P].unsqueeze(1)).then_inc(par_in, 16)

                def load(u, n, tile, seg):
                    sp.wait_ge(mixed[u], n - 1)
                    for half in range(2):
                        p = slice(64 * half, 64 * half + 64)
                        sp.dma_start(of[u][p, :], grid_rows(o[0], tile, seg, half)).then_inc(tile_in[u], 16)
                        sp.dma_start(ob[u][p, :], grid_rows(o[1], tile, seg, half)).then_inc(tile_in[u], 16)
                    sp.dma_start(ga[u][:, :, :], proj[GATE0:GATE0 + D_GLA, rows(tile)].rearrange("(j p) t -> p j t", p=P)).then_inc(tile_in[u], 16)
                paired(sp, load, 8)

            @block.gpsimd
            def _(pool):
                def store(u, n, tile, seg):
                    pool.wait_ge(par_in, 16 * (1 + UN))
                    pool.wait_ge(mixed[u], n)
                    pool.dma_start(mixT[D_LRU + D_RW:D, rows(tile)].rearrange("(j p) t -> p j t", p=P), mix[u][:, :, :]).then_inc(stored[u], 16)
                paired(pool, store, 8)
                for u in range(2):
                    pool.wait_ge(stored[u], 16 * (9 - u))

            @block.scalar
            def _(act):
                def body(u, n, tile, seg):
                    act.wait_ge(tile_in[u], 80 * n)
                    act.activation(ga[u][:, :, :], ga[u][:, :, :], ACT.Silu).then_inc(silud[u], 1)
                    act.wait_ge(added[u], n)
                    act.activation(sq[u][:, :], of[u][:, :], ACT.Square).then_inc(squared[u], 1)
                    act.wait_ge(var[u], 2 * n)
                    act.activation(stat[u][:, 2, :], stat[u][:, 1, :], ACT.Sqrt).then_inc(root[u], 1)
                paired(act, body, 8)

            @block.tensor
            def _(pe):
                pe.wait_ge(par_in, 16 * (1 + UN))

                def body(u, n, tile, seg):
                    pe.wait_ge(normed[u], n)
                    pe.wait_ge(mixed[u], n - 1)
                    for j in range(UN):
                        mm = pe.transpose(ps[u][:, j * P:(j + 1) * P], of[u][:, j * P:(j + 1) * P], ident[:, :])
                    mm.then_inc(turned[u], 1)
                paired(pe, body, 8)

            @block.vector
            def _(dve):
                dve.wait_ge(par_in, 16 * (1 + UN))

                def body(u, n, tile, seg):
                    s = stat[u]
                    dve.wait_ge(tile_in[u], 80 * n)
                    dve.tensor_tensor(of[u][:, :], of[u][:, :], ob[u][:, :], ALU.add).then_inc(added[u], 1)
                    dve.wait_ge(squared[u], n)
                    dve.reduce_sum(s[:, 1, :], heads(sq[u][:, :]), AX.X).then_inc(var[u], 1)
                    dve.wait_ge(var[u], 2 * n - 1)
                    dve.tensor_scalar(s[:, 1, :], s[:, 1, :], 1.0 / GLA_DV, EPS, ALU.mult, ALU.add).then_inc(var[u], 1)
                    dve.wait_ge(root[u], n)
                    dve.reciprocal(s[:, 3, :], s[:, 2, :]).then_inc(rstd[u], 1)
                    dve.wait_ge(rstd[u], n)
                    dve.tensor_tensor(heads(of[u][:, :]), heads(of[u][:, :]), s[:, 3, :].unsqueeze(2).to_broadcast([P, GLA_HEADS, GLA_DV]), ALU.mult).then_inc(normed[u], 1)
                    dve.wait_ge(turned[u], n)
                    dve.wait_ge(silud[u], n)
                    dve.wait_ge(stored[u], 16 * (n - 1))
                    for j in range(UN):
                        last = dve.scalar_tensor_tensor(mix[u][:, j, :], ps[u][:, j * P:(j + 1) * P], par[:, j:j + 1], ga[u][:, j, :], ALU.mult, ALU.mult)
                    last.then_inc(mixed[u], 1)
                paired(dve, body, 8)


def stage_mix_out(nc, x_prompt, x_sample, mixT, w_out, mods, norm2_g, w_router, ident_d, y, h2, probsT):
    with Stage(nc, "out") as st:
        ident = st.sb("ident", [P, P])
        g_row, scale_row, shift_row = st.sb("g", [P, D]), st.sb("scale", [P, 2, D]), st.sb("shift", [P, 2, D])
        res_row = st.sb("res", [P, 2, D])
        wo, wr = st.sb("wo", [P, KD, D]), st.sb("wr", [P, KD, N_EXP])
        x, y1, h, sq = ([st.sb(f"{n}{u}", [P, D]) for u in range(2)] for n in ("x", "y1", "h", "sq"))
        m = [st.sb(f"m{u}", [P, KD, P]) for u in range(2)]
        hT = [st.sb(f"hT{u}", [P, KD, P]) for u in range(2)]
        ss = [st.sb(f"ss{u}", [P, 8]) for u in range(2)]
        pe_exp = [st.sb(f"e{u}", [P, N_EXP]) for u in range(2)]
        pT = st.sb("pT", [N_EXP, T])
        ps_o = [st.ps(f"o{b}") for b in range(2)]
        ps_t = [st.ps(f"t{b}") for b in range(2)]
        ps_l, ps_p = [st.ps(f"l{u}") for u in range(2)], [st.ps(f"p{u}") for u in range(2)]
        rows_in, w_ld, rows_ready = st.sem("rows_in"), st.sem("w_ld"), st.sem("rows_ready")
        names = ("tile_in", "mixed", "gated", "res_done", "sumsq", "meansq", "root", "rstd", "normed", "h_ready", "turned",
                 "copied", "logits", "top", "ntop", "expd", "inv", "probs", "prob_mm", "prob_out", "y_out", "h_out")
        (tile_in, mixed, gated, res_done, sumsq, meansq, root, rstd, normed, h_ready, turned,
         copied, logits, top, ntop, expd, inv, probs, prob_mm, prob_out, y_out, h_out) = (st.sem2(n) for n in names)
        left, stored = st.sem2("left"), st.sem("stored")

        def x_tile(tile, seg):
            return x_prompt[0] if seg == 0 else x_sample[0, bass.ds((tile - 1) * P, P), :]

        with st.block() as block:
            @block.sync
            def _(sp):
                sp.dma_start(ident[:, :], ident_d).then_inc(w_ld, 16)
                sp.dma_start(wo[:, :, :], w_out[0].rearrange("(k p) n -> p k n", p=P)).then_inc(w_ld, 16)
                sp.dma_start(wr[:, :, :], w_router[0].rearrange("(k p) n -> p k n", p=P)).then_inc(w_ld, 16)
                load_modulated_norm(sp, rows_in, (g_row, scale_row, shift_row), mods, norm2_g, 4, 3)
                for v in range(2):
                    sp.dma_start(res_row[:, v, :], mods[v:v + 1, 2 * D:3 * D].to_broadcast([P, D])).then_inc(rows_in, 16)

                def load(u, n, tile, seg):
                    sp.wait_ge(res_done[u], n - 1)
                    sp.dma_start(x[u][:, :], x_tile(tile, seg)).then_inc(tile_in[u], 16)
                    sp.dma_start(m[u][:, :, :], mixT[:, bass.ds(tile * P, P)].rearrange("(k p) t -> p k t", p=P)).then_inc(tile_in[u], 16)
                paired(sp, load, 8)
                for u in range(2):
                    sp.wait_ge(prob_out[u], 9 - u)
                sp.dma_start(probsT, pT[:, :]).then_inc(stored, 16)
                sp.wait_ge(stored, 16)

            @block.gpsimd
            def _(pool):
                def store(u, n, tile, seg):
                    rows = bass.ds(tile * P, P)
                    pool.wait_ge(w_ld, 48)
                    pool.wait_ge(res_done[u], n)
                    pool.dma_start(y[rows, :], y1[u][:, :]).then_inc(y_out[u], 16)
                    pool.wait_ge(w_ld, 48)
                    pool.wait_ge(h_ready[u], n)
                    pool.dma_start(h2[rows, :], h[u][:, :]).then_inc(h_out[u], 16)
                paired(pool, store, 8)
                for u in range(2):
                    pool.wait_ge(y_out[u], 16 * (9 - u))
                    pool.wait_ge(h_out[u], 16 * (9 - u))

            @block.tensor
            def _(pe):
                pe.wait_ge(w_ld, 48)

                def body(u, n, tile, seg):
                    pe.wait_ge(tile_in[u], 32 * n)
                    for half in range(2):
                        pe.wait_ge(left[half], tile)
                        for k in range(KD):
                            mm = pe.matmul(ps_o[half][:, :], m[u][:, k, :], wo[:, k, half * BANK:(half + 1) * BANK], start=k == 0, stop=k == KD - 1)
                        mm.then_inc(mixed[u], 1)
                    pe.wait_ge(h_ready[u], n)
                    for half in range(2):
                        pe.wait_ge(copied[half], tile)
                        for k in range(4):
                            mm = pe.transpose(ps_t[half][:, k * P:(k + 1) * P], h[u][:, (4 * half + k) * P:(4 * half + k + 1) * P], ident[:, :])
                        mm.then_inc(turned[half], 1)
                    for half in range(2):
                        pe.wait_ge(copied[half], tile + 1)
                    for k in range(KD):
                        mm = pe.matmul(ps_l[u][:, 0:N_EXP], hT[u][:, k, :], wr[:, k, :], start=k == 0, stop=k == KD - 1)
                    mm.then_inc(logits[u], 1)
                    pe.wait_ge(probs[u], n)
                    pe.transpose(ps_p[u][0:N_EXP, 0:P], pe_exp[u][:, :], ident[:, :]).then_inc(prob_mm[u], 1)
                paired(pe, body, 8)

            @block.scalar
            def _(act):
                def body(u, n, tile, seg):
                    act.wait_ge(res_done[u], n)
                    act.activation(sq[u][:, :], y1[u][:, :], ACT.Square, accum_out=ss[u][:, 0:1]).then_inc(sumsq[u], 1)
                    act.wait_ge(meansq[u], n)
                    act.activation(ss[u][:, 2:3], ss[u][:, 1:2], ACT.Sqrt).then_inc(root[u], 1)
                    act.wait_ge(turned[1], tile + 1)
                    act.copy(hT[u][:, 4:8, :], ps_t[1][:, :].rearrange("p (k t) -> p k t", k=4)).then_inc(copied[1], 1)
                    act.wait_ge(ntop[u], n)
                    act.activation(pe_exp[u][:, :], ps_l[u][:, 0:N_EXP], ACT.Exp, bias=ss[u][:, 5:6], accum_out=ss[u][:, 6:7]).then_inc(expd[u], 1)
                paired(act, body, 8)

            @block.vector
            def _(dve):
                dve.wait_ge(rows_in, 7 * 16)
                for v in range(2):
                    dve.scalar_tensor_tensor(scale_row[:, v, :], scale_row[:, v, :], 1.0, g_row[:, :], ALU.add, ALU.mult).then_inc(rows_ready, 1)
                dve.wait_ge(rows_ready, 2)

                def body(u, n, tile, seg):
                    dve.wait_ge(tile_in[u], 32 * n)
                    dve.wait_ge(y_out[u], 16 * (n - 1))
                    dve.wait_ge(sumsq[u], n - 1)
                    for half in range(2):
                        cols = slice(half * BANK, (half + 1) * BANK)
                        dve.wait_ge(mixed[u], 2 * (n - 1) + half + 1)
                        dve.tensor_tensor(y1[u][:, cols], ps_o[half][:, :], res_row[:, seg, cols], ALU.mult).then_inc(left[half], 1)
                    for half in range(2):
                        dve.wait_ge(left[half], tile + 1)
                    dve.tensor_tensor(y1[u][:, :], y1[u][:, :], x[u][:, :], ALU.add).then_inc(res_done[u], 1)
                    dve.wait_ge(sumsq[u], n)
                    dve.tensor_scalar(ss[u][:, 1:2], ss[u][:, 0:1], 1.0 / D, EPS, ALU.mult, ALU.add).then_inc(meansq[u], 1)
                    dve.wait_ge(root[u], n)
                    dve.reciprocal(ss[u][:, 3:4], ss[u][:, 2:3]).then_inc(rstd[u], 1)
                    dve.wait_ge(rstd[u], n)
                    dve.wait_ge(h_out[u], 16 * (n - 1))
                    dve.scalar_tensor_tensor(h[u][:, :], y1[u][:, :], ss[u][:, 3:4], scale_row[:, seg, :], ALU.mult, ALU.mult).then_inc(normed[u], 1)
                    dve.wait_ge(normed[u], n)
                    dve.tensor_tensor(h[u][:, :], h[u][:, :], shift_row[:, seg, :], ALU.add).then_inc(h_ready[u], 1)
                    dve.wait_ge(turned[0], tile + 1)
                    dve.tensor_copy(hT[u][:, 0:4, :], ps_t[0][:, :].rearrange("p (k t) -> p k t", k=4)).then_inc(copied[0], 1)
                    dve.wait_ge(logits[u], n)
                    dve.reduce_max(ss[u][:, 4:5], ps_l[u][:, 0:N_EXP], AX.X).then_inc(top[u], 1)
                    dve.wait_ge(top[u], n)
                    dve.tensor_scalar(ss[u][:, 5:6], ss[u][:, 4:5], -1.0, None, ALU.mult).then_inc(ntop[u], 1)
                    dve.wait_ge(expd[u], n)
                    dve.reciprocal(ss[u][:, 7:8], ss[u][:, 6:7]).then_inc(inv[u], 1)
                    dve.wait_ge(inv[u], n)
                    dve.tensor_scalar(pe_exp[u][:, :], pe_exp[u][:, :], ss[u][:, 7:8], None, ALU.mult).then_inc(probs[u], 1)
                    dve.wait_ge(prob_mm[u], n)
                    dve.tensor_copy(pT[:, bass.ds(tile * P, P)], ps_p[u][0:N_EXP, 0:P]).then_inc(prob_out[u], 1)
                paired(dve, body, 8)


def stage_route(nc, probsT, ident_d, slot_rows, slot_gates):
    N_SLOT = CAP_LAT + CAP_CTX
    with Stage(nc, "rte") as st:
        ident = st.sb("ident", [P, P])
        work = st.sb("work", [N_EXP, T])
        top8, idx8 = st.sb("top8", [N_EXP, 8]), st.sb("idx8", [N_EXP, 8], U32)
        gates, idx = st.sb("gates", [N_EXP, N_SLOT]), st.sb("idx", [N_EXP, N_SLOT], U32)
        rows_f = st.sb("rows_f", [N_EXP, N_SLOT])
        gT, rT = st.sb("gT", [P, 3, N_EXP]), st.sb("rT", [P, 3, N_EXP], U32)
        ps_g, ps_r = st.ps("g"), st.ps("r")
        ld, found, kept, rows_done, turned_g, turned_r, out_done, stored = (st.sem(n) for n in (
            "ld", "found", "kept", "rows_done", "turned_g", "turned_r", "out_done", "stored"))
        blocks = [(0, P), (P, P), (CAP_LAT, CAP_CTX)]
        with st.block() as block:
            @block.sync
            def _(sp):
                sp.dma_start(work[:, :], probsT).then_inc(ld, 16)
                sp.dma_start(ident[:, :], ident_d).then_inc(ld, 16)
                sp.wait_ge(out_done, 8)
                sp.dma_start(slot_rows, rT[:, :, :]).then_inc(stored, 16)
                sp.dma_start(slot_gates, gT[:, :, :]).then_inc(stored, 16)
                sp.wait_ge(stored, 32)

            @block.vector
            def _(dve):
                dve.memset(gT[:, 2, :], 0.0).then_inc(out_done, 1)
                dve.memset(rT[:, 2, :], 0).then_inc(out_done, 1)
                dve.wait_ge(out_done, 2)
                dve.wait_ge(ld, 32)

                def eight(tokens, slot, n):
                    dve.max(top8[:, :], tokens).then_inc(found, 1)
                    dve.wait_ge(found, 3 * n + 1)
                    dve.tensor_copy(gates[:, bass.ds(slot, 8)], top8[:, :]).then_inc(kept, 1)
                    dve.max_index(idx8[:, :], top8[:, :], tokens).then_inc(found, 1)
                    dve.match_replace(tokens, top8[:, :], tokens, -1.0).then_inc(found, 1)
                    dve.wait_ge(found, 3 * n + 3)
                    dve.tensor_copy(idx[:, bass.ds(slot, 8)], idx8[:, :]).then_inc(kept, 1)

                for n in range(CAP_CTX // 8):
                    eight(work[:, 0:T_CTX], CAP_LAT + 8 * n, n)
                with dve.Fori(0, CAP_LAT // 8) as i:
                    eight(work[:, T_CTX:T], 8 * i, i + CAP_CTX // 8)
                dve.wait_ge(kept, 2 * N_SLOT // 8)
                dve.tensor_scalar(rows_f[:, 0:CAP_LAT], idx[:, 0:CAP_LAT], float(T_CTX), None, ALU.add).then_inc(rows_done, 1)
                dve.tensor_copy(rows_f[:, CAP_LAT:], idx[:, CAP_LAT:]).then_inc(rows_done, 1)
                dve.wait_ge(turned_g, 1)
                for b, (s0, n) in enumerate(blocks):
                    dve.tensor_copy(gT[0:n, b, :], ps_g[0:n, b * N_EXP:(b + 1) * N_EXP]).then_inc(out_done, 1)
                dve.wait_ge(turned_r, 1)
                for b, (s0, n) in enumerate(blocks):
                    dve.tensor_copy(rT[0:n, b, :], ps_r[0:n, b * N_EXP:(b + 1) * N_EXP]).then_inc(out_done, 1)

            @block.tensor
            def _(pe):
                pe.wait_ge(ld, 32)
                pe.wait_ge(rows_done, 2)
                pe.wait_ge(kept, 2 * N_SLOT // 8)
                for src, ps, done in ((gates, ps_g, turned_g), (rows_f, ps_r, turned_r)):
                    for b, (s0, n) in enumerate(blocks):
                        mm = pe.transpose(ps[0:n, b * N_EXP:(b + 1) * N_EXP], src[:, s0:s0 + n], ident[0:N_EXP, 0:N_EXP])
                    mm.then_inc(done, 1)


def stage_experts(nc, h2, y, mods, slot_rows, slot_gates, w_gate, w_up, w_down, ident_d):
    blocks = [(0, P), (P, P), (CAP_LAT, CAP_CTX)]
    N_SLOT = CAP_LAT + CAP_CTX
    KE = D_EXP // P
    PW = 2 * P
    GU = 2 * (D_EXP // PW)
    PARTS = GU + D // PW
    RAW, RING = 3, 4
    assert PARTS % RAW == 0 and PARTS % RING == 0 and KD == KE
    with Stage(nc, "exp") as st:
        ident = st.sb("ident", [P, P])
        rows_all, gates_all = st.sb("rows_all", [P, 3, N_EXP], U32), st.sb("gates_all", [P, 3, N_EXP])
        res_row = st.sb("res", [P, 2, D])
        raw = [st.sb(f"raw{b}", [P, KD, PW]) for b in range(RAW)]
        w = [[st.sb(f"w{n}{b}", [P, KD, PW], F32R) for n in ("hi", "lo")] for b in range(RING)]
        xs, yo = st.sb("xs", [P, 3, D]), st.sb("yo", [P, 3, D])
        xT = [st.sb(f"xT{n}", [P, KD, N_SLOT], F32R) for n in ("hi", "lo")]
        hid = [st.sb(f"hid{n}", [P, KE, N_SLOT], F32R) for n in ("hi", "lo")]
        sil, act_in, yoT = (st.sb(n, [P, 2, N_SLOT]) for n in ("sil", "act_in", "yoT"))
        ps_g, ps_u, ps_o, ps_t = ([st.ps(f"{n}{b}") for b in range(2)] for n in ("g", "u", "o", "t"))
        par_in, raw_in = st.sem("par_in"), [st.sem(f"raw_in{b}") for b in range(RAW)]
        hi_done, lo_done, used = ([st.sem(f"{n}{b}") for b in range(RING)] for n in ("hi_done", "lo_done", "used"))
        gathered, turned, scattered = st.sem("gathered"), st.sem("turned"), st.sem("scattered")
        gate_mm, up_mm, silu_done, prod_done, hid_hi, hid_lo = (st.sem(n) for n in (
            "gate_mm", "up_mm", "silu_done", "prod_done", "hid_hi", "hid_lo"))
        x_hi, x_lo, down_mm, yt_done, back_mm, scaled = (st.sem2(n) for n in (
            "x_hi", "x_lo", "down_mm", "yt_done", "back_mm", "scaled"))

        def part_source(e, k):
            src, q = (w_down, k - GU) if k >= GU else ((w_gate, w_up)[k % 2], k // 2)
            return src[0, bass.ds(e, 1)].squeeze(0).rearrange("(k p) n -> p k n", p=P)[:, :, q * PW:(q + 1) * PW]

        def part_count(e, k, ring):
            return e * (PARTS // ring) + k // ring + 1

        def experts(eng, body):
            body(0, True)
            with eng.Fori(1, N_EXP - 1) as e:
                body(e, True)
            body(N_EXP - 1, False)

        with st.block() as block:
            @block.sync
            def _(sp):
                sp.dma_start(ident[:, :], ident_d).then_inc(par_in, 16)
                sp.dma_start(rows_all[:, :, :], slot_rows).then_inc(par_in, 16)
                sp.dma_start(gates_all[:, :, :], slot_gates).then_inc(par_in, 16)
                for v in range(2):
                    sp.dma_start(res_row[:, v, :], mods[v:v + 1, 5 * D:6 * D].to_broadcast([P, D])).then_inc(par_in, 16)

                def body(e, more):
                    for k in range(PARTS):
                        sp.wait_ge(lo_done[(k - RAW) % RING], part_count(e, k - RAW, RING))
                        sp.dma_start(raw[k % RAW][:, :, :], part_source(e, k)).then_inc(raw_in[k % RAW], 16)
                experts(sp, body)

            @block.gpsimd
            def _(pool):
                pool.wait_ge(par_in, 80)

                def gather(e):
                    for b, (s0, n) in enumerate(blocks):
                        pool.indirect_dma_start(out=xs[0:n, b, :], out_offset=None, in_=h2,
                                                in_offset=bass.IndirectOffsetOnAxis(ap=rows_all[0:n, b, e:e + 1], axis=0)).then_inc(gathered, 16)
                gather(0)
                for e in range(N_EXP):
                    if e + 1 < N_EXP:
                        pool.wait_ge(turned, KD * (e + 1))
                        gather(e + 1)
                    if e:
                        pool.wait_ge(scattered, 48 * e)
                    for u in range(2):
                        pool.wait_ge(scaled[u], KD // 2 * (e + 1))
                    for b, (s0, n) in enumerate(blocks):
                        pool.indirect_dma_start(out=y, out_offset=bass.IndirectOffsetOnAxis(ap=rows_all[0:n, b, e:e + 1], axis=0),
                                                in_=yo[0:n, b, :], in_offset=None, compute_op=ALU.add).then_inc(scattered, 16)
                pool.wait_ge(scattered, 48 * N_EXP)

            @block.tensor
            def _(pe):
                pe.wait_ge(par_in, 80)

                def product(ps, b, tile, x):
                    for k in range(KD):
                        for i, (wp, xp) in enumerate(((1, 0), (0, 1), (0, 0))):
                            mm = pe.matmul(ps[:, 0:N_SLOT], w[b][wp][:, k, tile * P:(tile + 1) * P], x[xp][:, k, :],
                                           start=k == 0 and i == 0, stop=k == KD - 1 and i == 2)
                    return mm

                def part_ready(e, k):
                    pe.wait_ge(hi_done[k % RING], part_count(e, k, RING))
                    pe.wait_ge(lo_done[k % RING], part_count(e, k, RING))

                def turn(e, k):
                    if k == 0:
                        pe.wait_ge(gathered, 48 * (e + 1))
                    pe.wait_ge(x_lo[k % 2], KD // 2 * e + k // 2)
                    for b, (s0, n) in enumerate(blocks):
                        mm = pe.transpose(ps_g[k % 2][:, s0:s0 + n], xs[0:n, b, k * P:(k + 1) * P], ident[0:n, 0:n])
                    mm.then_inc(turned, 1)

                def back(e, i):
                    pe.wait_ge(yt_done[i % 2], KD // 2 * e + i // 2 + 1)
                    pe.wait_ge(scaled[i % 2], KD // 2 * e + i // 2)
                    for b, (s0, n) in enumerate(blocks):
                        mm = pe.transpose(ps_t[i % 2][0:n, b * P:(b + 1) * P], yoT[:, i % 2, s0:s0 + n], ident[:, :])
                    mm.then_inc(back_mm[i % 2], 1)

                def body(e, more):
                    for u in range(2):
                        pe.wait_ge(x_lo[u], KD // 2 * (e + 1))
                    for q in range(GU // 2):
                        for s, (ps, done) in enumerate(((ps_g, gate_mm), (ps_u, up_mm))):
                            k = 2 * q + s
                            part_ready(e, k)
                            for tile in range(2):
                                f = 2 * q + tile
                                if s == 0:
                                    pe.wait_ge(silu_done, KE * e + f - (1 if f >= 2 else f))
                                else:
                                    pe.wait_ge(prod_done, KE * e + f - (1 if f >= 2 else f))
                                mm = product(ps[tile], k % RING, tile, xT)
                                if tile == 0:
                                    mm.then_inc(done, 1)
                                else:
                                    mm.then_inc(used[k % RING], 1)
                    pe.wait_ge(hid_lo, KE * (e + 1))
                    for i in range(KD):
                        k, tile = GU + i // 2, i % 2
                        if tile == 0:
                            part_ready(e, k)
                        pe.wait_ge(yt_done[tile], KD // 2 * e + i // 2)
                        mm = product(ps_o[tile], k % RING, tile, hid)
                        mm.then_inc(used[k % RING] if tile else down_mm[0], 1)
                        if more:
                            turn(e + 1, i)
                        if i:
                            back(e, i - 1)
                    back(e, KD - 1)
                for k in range(KD):
                    turn(0, k)
                experts(pe, body)

            @block.scalar
            def _(act):
                def split(e, k):
                    act.wait_ge(raw_in[k % RAW], 16 * part_count(e, k, RAW))
                    act.wait_ge(used[k % RING], part_count(e, k, RING) - 1)
                    act.copy(w[k % RING][0][:, :, :], raw[k % RAW][:, :, :]).then_inc(hi_done[k % RING], 1)

                def x_high(e, k):
                    act.wait_ge(turned, KD * e + k + 1)
                    act.copy(xT[0][:, k, :], ps_g[k % 2][:, 0:N_SLOT]).then_inc(x_hi[k % 2], 1)

                def body(e, more):
                    for q in range(GU // 2):
                        for f in (2 * q, 2 * q + 1):
                            if f % 2:
                                act.wait_ge(used[2 * q % RING], part_count(e, 2 * q, RING))
                            else:
                                act.wait_ge(gate_mm, KE // 2 * e + q + 1)
                            act.wait_ge(prod_done, KE * e + f - (1 if f >= 2 else f))
                            act.activation(sil[:, f % 2, :], ps_g[f % 2][:, 0:N_SLOT], ACT.Silu).then_inc(silu_done, 1)
                        split(e, 2 * q + RING)
                        split(e, 2 * q + 1 + RING)
                        for f in (2 * q, 2 * q + 1):
                            act.wait_ge(prod_done, KE * e + f + 1)
                            if q == 0:
                                for u in range(2):
                                    act.wait_ge(yt_done[u], KD // 2 * e)
                            act.copy(hid[0][:, f, :], act_in[:, f % 2, :]).then_inc(hid_hi, 1)
                    for i in range(KD):
                        if i % 2:
                            act.wait_ge(used[(GU + i // 2) % RING], part_count(e, GU + i // 2, RING))
                        else:
                            act.wait_ge(down_mm[0], KD // 2 * e + i // 2 + 1)
                        act.wait_ge(back_mm[i % 2], KD // 2 * e + i // 2)
                        act.copy(yoT[:, i % 2, :], ps_o[i % 2][:, 0:N_SLOT]).then_inc(yt_done[i % 2], 1)
                        if more:
                            x_high(e + 1, i)
                            if i % 2:
                                split(e + 1, i // 2)
                for k in range(KD):
                    if k < RING:
                        split(0, k)
                    x_high(0, k)
                experts(act, body)

            @block.vector
            def _(dve):
                dve.wait_ge(par_in, 80)

                def split(e, k):
                    dve.wait_ge(hi_done[k % RING], part_count(e, k, RING))
                    dve.tensor_tensor(w[k % RING][1][:, :, :], raw[k % RAW][:, :, :], w[k % RING][0][:, :, :], ALU.subtract).then_inc(lo_done[k % RING], 1)

                def x_low(e, k):
                    dve.wait_ge(x_hi[k % 2], KD // 2 * e + k // 2 + 1)
                    dve.tensor_tensor(xT[1][:, k, :], ps_g[k % 2][:, 0:N_SLOT], xT[0][:, k, :], ALU.subtract).then_inc(x_lo[k % 2], 1)

                def scale(e, i):
                    cols = slice(i * P, (i + 1) * P)
                    dve.wait_ge(par_in, 80)
                    dve.wait_ge(back_mm[i % 2], KD // 2 * e + i // 2 + 1)
                    if i == 0:
                        dve.wait_ge(scattered, 48 * e)
                    for b, (s0, n) in enumerate(blocks):
                        last = dve.scalar_tensor_tensor(yo[0:n, b, cols], ps_t[i % 2][0:n, b * P:(b + 1) * P], gates_all[0:n, b, bass.ds(e, 1)],
                                                        res_row[0:n, 0 if b == 2 else 1, cols], ALU.mult, ALU.mult)
                    last.then_inc(scaled[i % 2], 1)

                def body(e, more):
                    for q in range(GU // 2):
                        split(e, 2 * q + RING)
                        for f in (2 * q, 2 * q + 1):
                            dve.wait_ge(silu_done, KE * e + f + 1)
                            if f % 2:
                                dve.wait_ge(used[(2 * q + 1) % RING], part_count(e, 2 * q + 1, RING))
                            else:
                                dve.wait_ge(up_mm, KE // 2 * e + q + 1)
                            dve.wait_ge(hid_lo, KE * e + f - (1 if f >= 2 else f))
                            dve.tensor_tensor(act_in[:, f % 2, :], ps_u[f % 2][:, 0:N_SLOT], sil[:, f % 2, :], ALU.mult).then_inc(prod_done, 1)
                        split(e, 2 * q + 1 + RING)
                        for f in (2 * q, 2 * q + 1):
                            dve.wait_ge(hid_hi, KE * e + f + 1)
                            dve.tensor_tensor(hid[1][:, f, :], act_in[:, f % 2, :], hid[0][:, f, :], ALU.subtract).then_inc(hid_lo, 1)
                    for i in range(KD):
                        if more:
                            x_low(e + 1, i)
                        if i:
                            scale(e, i - 1)
                        if more and i % 2:
                            split(e + 1, i // 2)
                    scale(e, KD - 1)
                for k in range(KD):
                    if k < RING:
                        split(0, k)
                    x_low(0, k)
                experts(dve, body)


def stage_final(nc, y, final_g, y_prompt, y_sample):
    with Stage(nc, "fin") as st:
        g_row = st.sb("g", [P, D])
        x, sq, out = ([st.sb(f"{n}{u}", [P, D]) for u in range(2)] for n in ("x", "sq", "o"))
        ss = [st.sb(f"ss{u}", [P, 4]) for u in range(2)]
        row_in = st.sem("row_in")
        x_in, sumsq, meansq, root, rstd, normed, stored = (st.sem2(n) for n in ("x_in", "sumsq", "meansq", "root", "rstd", "normed", "stored"))
        with st.block() as block:
            @block.sync
            def _(sp):
                sp.dma_start(g_row[:, :], final_g.unsqueeze(0).to_broadcast([P, D])).then_inc(row_in, 16)

                def load(u, n, tile, seg):
                    sp.wait_ge(normed[u], n - 1)
                    sp.dma_start(x[u][:, :], y[bass.ds(tile * P, P), :]).then_inc(x_in[u], 16)
                paired(sp, load, 8)

            @block.gpsimd
            def _(pool):
                def store(u, n, tile, seg):
                    pool.wait_ge(row_in, 16)
                    pool.wait_ge(normed[u], n)
                    dst = y_prompt[0] if seg == 0 else y_sample[0, bass.ds((tile - 1) * P, P), :]
                    pool.dma_start(dst, out[u][:, :]).then_inc(stored[u], 16)
                paired(pool, store, 8)
                for u in range(2):
                    pool.wait_ge(stored[u], 16 * (9 - u))

            @block.scalar
            def _(act):
                def body(u, n, tile, seg):
                    act.wait_ge(x_in[u], 16 * n)
                    act.activation(sq[u][:, :], x[u][:, :], ACT.Square, accum_out=ss[u][:, 0:1]).then_inc(sumsq[u], 1)
                    act.wait_ge(meansq[u], n)
                    act.activation(ss[u][:, 2:3], ss[u][:, 1:2], ACT.Sqrt).then_inc(root[u], 1)
                paired(act, body, 8)

            @block.vector
            def _(dve):
                dve.wait_ge(row_in, 16)

                def body(u, n, tile, seg):
                    dve.wait_ge(sumsq[u], n)
                    dve.tensor_scalar(ss[u][:, 1:2], ss[u][:, 0:1], 1.0 / D, EPS, ALU.mult, ALU.add).then_inc(meansq[u], 1)
                    dve.wait_ge(root[u], n)
                    dve.reciprocal(ss[u][:, 3:4], ss[u][:, 2:3]).then_inc(rstd[u], 1)
                    dve.wait_ge(rstd[u], n)
                    dve.wait_ge(stored[u], 16 * (n - 1))
                    dve.scalar_tensor_tensor(out[u][:, :], x[u][:, :], ss[u][:, 3:4], g_row[:, :], ALU.mult, ALU.mult).then_inc(normed[u], 1)
                paired(dve, body, 8)


def build_program(nc, a):
    def scratch(name, shape, dt=F32):
        return nc.dram_tensor(name, list(shape), dt, kind="Internal").ap()

    mods, proj, mixT = scratch("mods", (2, 6 * D)), scratch("proj", (N_IN, T)), scratch("mixT", (D, T))
    rec, gate, bonus = scratch("rec", (2, P, NCH, D_RW // P, REC)), scratch("gate", (D_RW, T)), scratch("bonus", (D_RW, T))
    decay = scratch("decay", (P, 2, D_RW // P, NCH))
    o_rw, o_gla = scratch("o_rw", (2, T, D_RW)), scratch("o_gla", (2, T, D_GLA))
    vt, grec = scratch("vt", (T, D_GLA)), scratch("grec", (GLA_HEADS // 2, P, NCH, GREC))
    y, h2, probsT = scratch("y", (T, D)), scratch("h2", (T, D)), scratch("probsT", (N_EXP, T))
    slot_rows, slot_gates = scratch("slot_rows", (P, 3, N_EXP), U32), scratch("slot_gates", (P, 3, N_EXP))

    stage_modulation(nc, a["c"], a["c_ctx"], a["w_ada"], a["b_ada"], mods)
    stage_project(nc, a["x_prompt"], a["x_sample"], a["norm1_g"], mods, a["w_in"], a["ident"], proj)
    stage_lru(nc, proj, *(a["lru_" + n] for n in ("conv_w", "conv_b", "wa", "ba", "wx", "bx", "lambda")), a["state_lru"], mixT, a["new_lru"])
    stage_rwkv_prep(nc, proj, *(a["rw_" + n] for n in ("mu", "w0", "w2", "a0", "a2", "g2", "kk", "ka", "rk")), a["head_ones"], rec, decay, gate, bonus)
    stage_gla_turn(nc, proj, a["ident"], vt)
    stage_gla_prep(nc, proj, a["gla_wg2"], a["gla_bg"], grec)
    stage_scans(nc, rec, decay, a["rwkv_con"], a["state_rwkv"], a["new_rwkv"], o_rw,
                grec, vt, a["gla_con"], a["state_gla"], a["new_gla"], o_gla)
    stage_rwkv_post(nc, o_rw, bonus, gate, a["rw_ln_w"], a["rw_ln_b"], a["ident"], mixT)
    stage_gla_post(nc, o_gla, proj, a["gla_norm_w"], a["ident"], mixT)
    stage_mix_out(nc, a["x_prompt"], a["x_sample"], mixT, a["w_out"], mods, a["norm2_g"], a["w_router"], a["ident"], y, h2, probsT)
    stage_route(nc, probsT, a["ident"], slot_rows, slot_gates)
    stage_experts(nc, h2, y, mods, slot_rows, slot_gates, a["w_gate"], a["w_up"], a["w_down"], a["ident"])
    stage_final(nc, y, a["final_norm_g"], a["y_prompt"], a["y_sample"])


_OUTS = [("y_prompt", (1, T_CTX, D)), ("y_sample", (1, T_LAT, D)), ("new_lru", (1, 1, 2, D_LRU)),
         ("new_rwkv", (1, 1, 2, RW_HEADS, RW_HD, RW_HD)), ("new_gla", (1, 1, 2, GLA_HEADS, GLA_DK, GLA_DV))]


def kernel(**inputs):
    import concourse.bacc as _bacc
    from concourse.bass_utils import run_bass_kernel_spmd as _run

    nc = _bacc.Bacc("TRN2", target_bir_lowering=False, num_devices=1)
    constants = {"ident": np.eye(P, dtype=np.float32), "rwkv_con": rwkv_constants(), "gla_con": gla_constants(),
                 "head_ones": np.kron(np.eye(2), np.ones((RW_HD, RW_HD))).astype(np.float32)}
    arrays, aps = {}, {}
    for name, value in {**inputs, **constants}.items():
        value = np.ascontiguousarray(value)
        arrays[f"in_{name}"] = value
        aps[name] = nc.dram_tensor(f"in_{name}", value.shape, mybir.dt.from_np(value.dtype), kind="ExternalInput").ap()
    for name, shape in _OUTS:
        aps[name] = nc.dram_tensor(f"out_{name}", list(shape), F32, kind="ExternalOutput").ap()
    build_program(nc, aps)
    r = _run(nc, [arrays], core_ids=[0])
    return tuple(r.results[0][f"out_{name}"] for name, _ in _OUTS)
```

```python
from contextlib import ExitStack

import numpy as np

import concourse.bass as bass
from concourse import mybir

F32 = mybir.dt.float32
F32R = mybir.dt.float32r
U32 = mybir.dt.uint32
ALU = mybir.AluOpType
ACT = mybir.ActivationFunctionType
AX = mybir.AxisListType

P = 128
D = 1024
KD = D // P
T_CTX, T_LAT = 128, 2048
T = T_CTX + T_LAT
GRID_W = 64
GRID_H = T_LAT // GRID_W
SEGS = ((0, T_CTX), (T_CTX, T_LAT))
BANK = 512
MOD_FIRST = 2 * D
D_LRU = 256
RW_HEADS, RW_HD = 6, 64
D_RW = RW_HEADS * RW_HD
GLA_HEADS, GLA_DK, GLA_DV = 4, 48, 96
D_GLA = GLA_HEADS * GLA_DV
D_GLA_K = GLA_HEADS * GLA_DK
GLA_R = 16
RW0 = 2 * D_LRU
RW_LORA = RW0 + 3 * D_RW
GLA0 = RW_LORA + 3 * P
N_IN = GLA0 + 2 * D_GLA_K + 2 * D_GLA + 2 * GLA_R
C = 64
NCH = T // C
NCH_CTX = T_CTX // C
LEVELS = 6
REC = 5 * C
N_EXP, D_EXP = 16, 1024
CAP_LAT, CAP_CTX = 2 * T_LAT // N_EXP, 2 * T_CTX // N_EXP
EPS = 1e-6
TOK_BLOCKS = [(b, min(BANK, T - b)) for b in range(0, T, BANK)]


class Stage:

    def __init__(self, nc, name):
        self.nc, self.name, self.stack, self.sems = nc, name, ExitStack(), {}

    def __enter__(self):
        return self

    def __exit__(self, *_):
        self.stack.close()
        if self.sems:
            self.nc.clear_and_free_semaphores(list(self.sems.values()))
            self.nc.all_engine_barrier()

    def sb(self, name, shape, dt=F32):
        return self.stack.enter_context(self.nc.sbuf_tensor(f"{self.name}_{name}", shape, dt))

    def ps(self, name, shape=(P, BANK)):
        return self.stack.enter_context(self.nc.psum_tensor(f"{self.name}_{name}", list(shape), F32))

    def sem(self, name):
        self.sems[name] = self.nc.alloc_semaphore(name=f"{self.name}_{name}")
        return self.sems[name]

    def sem2(self, name):
        return [self.sem(f"{name}_{u}") for u in range(2)]

    def block(self):
        return self.nc.Block()


def stage_modulation(nc, c, c_ctx, w_ada, b_ada, mods):
    NB = MOD_FIRST // BANK
    with Stage(nc, "mod") as st:
        cvec, sil = st.sb("cvec", [P, 2, KD]), st.sb("sil", [P, KD, 2])
        w = [st.sb(f"w{u}", [P, KD, BANK]) for u in range(2)]
        bias, out = st.sb("bias", [2, MOD_FIRST]), st.sb("out", [2, MOD_FIRST])
        acc = [st.ps(f"acc{u}") for u in range(2)]
        cvec_in, bias_in, silu_done = st.sem("cvec_in"), st.sem("bias_in"), st.sem("silu_done")
        w_in, product, biased = st.sem2("w_in"), st.sem2("product"), st.sem2("biased")
        stored = st.sem("stored")
        wv = w_ada[0].rearrange("(p k) n -> p k n", k=KD)
        with st.block() as block:
            @block.sync
            def _(sp):
                sp.dma_start(cvec[:, 0, :], c_ctx.rearrange("(p k) -> p k", k=KD)).then_inc(cvec_in, 16)
                sp.dma_start(cvec[:, 1, :], c[0].rearrange("(p k) -> p k", k=KD)).then_inc(cvec_in, 16)
                for v in range(2):
                    sp.dma_start(bias[v:v + 1, :], b_ada[:, 0:MOD_FIRST]).then_inc(bias_in, 16)

                def body(i):
                    for u in range(2):
                        sp.wait_ge(product[u], i)
                        sp.dma_start(w[u][:, :, :], wv[:, :, bass.ds((2 * i + u) * BANK, BANK)]).then_inc(w_in[u], 16)
                looped(sp, NB // 2, body)
                for u in range(2):
                    sp.wait_ge(biased[u], NB // 2)
                sp.dma_start(mods[:, 0:MOD_FIRST], out[:, :]).then_inc(stored, 16)
                sp.wait_ge(stored, 16)

            @block.scalar
            def _(act):
                act.wait_ge(cvec_in, 32)
                act.activation(sil[:, :, :], cvec[:, :, :].rearrange("p v k -> p k v"), ACT.Silu).then_inc(silu_done, 1)

            @block.tensor
            def _(pe):
                pe.wait_ge(silu_done, 1)

                def body(i):
                    for u in range(2):
                        pe.wait_ge(w_in[u], 16 * i + 16)
                        pe.wait_ge(biased[u], i)
                        for k in range(KD):
                            mm = pe.matmul(acc[u][0:2, :], sil[:, k, :], w[u][:, k, :], start=k == 0, stop=k == KD - 1)
                        mm.then_inc(product[u], 1)
                looped(pe, NB // 2, body)

            @block.vector
            def _(dve):
                dve.wait_ge(bias_in, 32)

                def body(i):
                    for u in range(2):
                        cols = bass.ds((2 * i + u) * BANK, BANK)
                        dve.wait_ge(product[u], i + 1)
                        dve.tensor_tensor(out[:, cols], acc[u][0:2, :], bias[:, cols], ALU.add).then_inc(biased[u], 1)
                looped(dve, NB // 2, body)


def looped(eng, count, body):
    body(0)
    with eng.Fori(1, count) as i:
        body(i)


def staged(eng, *steps):
    behind, tiles = len(steps) - 1, T // P

    def static(at):
        for j, step in enumerate(steps):
            tile = at - j
            if 0 <= tile < tiles:
                step(tile % 2, tile // 2 + 1, tile, min(tile, 1))
    first, last = behind // 2 + 1, tiles // 2
    for at in range(2 * first):
        static(at)
    with eng.Fori(first, last) as i:
        for r in range(2):
            for j, step in enumerate(steps):
                step((r - j) % 2, i + (r - j) // 2 + 1, 2 * i + r - j, 1)
    for at in range(2 * last, tiles + behind):
        static(at)


def other_engines(u, n, tile, seg):
    pass


def load_modulated_norm(sp, st_sem, rows, mods, norm_g, scale_col, shift_col):
    g_row, scale_row, shift_row = rows
    sp.dma_start(g_row[:, :], norm_g.to_broadcast([P, D])).then_inc(st_sem, 16)
    for v in range(2):
        sp.dma_start(scale_row[:, v, :], mods[v:v + 1, scale_col * D:(scale_col + 1) * D].to_broadcast([P, D])).then_inc(st_sem, 16)
        sp.dma_start(shift_row[:, v, :], mods[v:v + 1, shift_col * D:(shift_col + 1) * D].to_broadcast([P, D])).then_inc(st_sem, 16)


def stage_project(nc, x_prompt, x_sample, norm1_g, mods, w_in, ident_d, proj):
    with Stage(nc, "proj") as st:
        hT = [st.sb(f"hT{n}", [P, KD, T], F32R) for n in ("hi", "lo")]
        project_norm(nc, x_prompt, x_sample, norm1_g, mods, ident_d, hT)
        project_products(nc, w_in, hT, proj)


def project_norm(nc, x_prompt, x_sample, norm1_g, mods, ident_d, hT):
    with Stage(nc, "norm") as st:
        ident = st.sb("ident", [P, P])
        g_row, scale_row, shift_row = st.sb("g", [P, D]), st.sb("scale", [P, 2, D]), st.sb("shift", [P, 2, D])
        x = [st.sb(f"x{u}", [P, D]) for u in range(2)]
        h = [st.sb(f"h{u}", [P, D]) for u in range(2)]
        ss = [st.sb(f"ss{u}", [P, 4]) for u in range(2)]
        ps_t = [[st.ps(f"t{u}{half}") for half in range(2)] for u in range(2)]
        rows_in, ident_in, rows_ready = st.sem("rows_in"), st.sem("ident_in"), st.sem("rows_ready")
        x_in, sumsq, meansq, root, rstd, normed, h_ready, turned, high, low = (st.sem2(n) for n in (
            "x_in", "sumsq", "meansq", "root", "rstd", "normed", "h_ready", "turned", "high", "low"))

        def part(t, half, tile):
            return t[:, 4 * half:4 * half + 4, bass.ds(tile * P, P)]

        def in_psum(u, half):
            return ps_t[u][half][:, :].rearrange("p (k t) -> p k t", k=4)

        with st.block() as block:
            @block.sync
            def _(sp):
                sp.dma_start(ident[:, :], ident_d).then_inc(ident_in, 16)
                load_modulated_norm(sp, rows_in, (g_row, scale_row, shift_row), mods, norm1_g, 1, 0)

                def load_x(u, n, tile, seg):
                    sp.wait_ge(normed[u], n - 1)
                    src = x_prompt[0] if seg == 0 else x_sample[0, bass.ds((tile - 1) * P, P), :]
                    sp.dma_start(x[u][:, :], src).then_inc(x_in[u], 16)
                staged(sp, load_x)

            @block.scalar
            def _(act):
                def norm(u, n, tile, seg):
                    act.wait_ge(x_in[u], 16 * n)
                    act.wait_ge(turned[u], n - 1)
                    act.activation(h[u][:, :], x[u][:, :], ACT.Square, accum_out=ss[u][:, 0:1]).then_inc(sumsq[u], 1)
                    act.wait_ge(meansq[u], n)
                    act.activation(ss[u][:, 2:3], ss[u][:, 1:2], ACT.Sqrt).then_inc(root[u], 1)

                def keep_high(u, n, tile, seg):
                    act.wait_ge(turned[u], n)
                    for half in range(2):
                        last = act.copy(part(hT[0], half, tile), in_psum(u, half))
                    last.then_inc(high[u], 1)
                staged(act, norm, keep_high)

            @block.vector
            def _(dve):
                dve.wait_ge(rows_in, 5 * 16)
                for v in range(2):
                    dve.scalar_tensor_tensor(scale_row[:, v, :], scale_row[:, v, :], 1.0, g_row[:, :], ALU.add, ALU.mult).then_inc(rows_ready, 1)

                def norm(u, n, tile, seg):
                    dve.wait_ge(sumsq[u], n)
                    dve.tensor_scalar(ss[u][:, 1:2], ss[u][:, 0:1], 1.0 / D, EPS, ALU.mult, ALU.add).then_inc(meansq[u], 1)
                    dve.wait_ge(root[u], n)
                    dve.reciprocal(ss[u][:, 3:4], ss[u][:, 2:3]).then_inc(rstd[u], 1)
                    dve.wait_ge(rstd[u], n)
                    dve.wait_ge(rows_ready, 2)
                    dve.scalar_tensor_tensor(h[u][:, :], x[u][:, :], ss[u][:, 3:4], scale_row[:, seg, :], ALU.mult, ALU.mult).then_inc(normed[u], 1)
                    dve.wait_ge(normed[u], n)
                    dve.tensor_tensor(h[u][:, :], h[u][:, :], shift_row[:, seg, :], ALU.add).then_inc(h_ready[u], 1)

                def keep_low(u, n, tile, seg):
                    dve.wait_ge(high[u], n)
                    for half in range(2):
                        last = dve.tensor_tensor(part(hT[1], half, tile), in_psum(u, half), part(hT[0], half, tile), ALU.subtract)
                    last.then_inc(low[u], 1)
                staged(dve, norm, keep_low)

            @block.tensor
            def _(pe):
                pe.wait_ge(ident_in, 16)

                def turn(u, n, tile, seg):
                    pe.wait_ge(h_ready[u], n)
                    pe.wait_ge(low[u], n - 1)
                    for k in range(KD):
                        mm = pe.transpose(ps_t[u][k // 4][:, k % 4 * P:(k % 4 + 1) * P], h[u][:, k * P:(k + 1) * P], ident[:, :])
                    mm.then_inc(turned[u], 1)
                staged(pe, turn)


def project_products(nc, w_in, hT, proj):
    CT = N_IN // P
    REM = N_IN - CT * P
    PAIRS = CT // 2
    TAIL = [(0, PAIRS + 1, CT - 1, P), (1, PAIRS + 1, CT, REM)]
    NBLK = len(TOK_BLOCKS)
    assert CT % 2 == 1 and REM
    with Stage(nc, "prod") as st:
        raw = [st.sb(f"raw{u}", [P, KD, P]) for u in range(2)]
        w = [[st.sb(f"w{n}{u}", [P, KD, P], F32R) for n in ("hi", "lo")] for u in range(2)]
        out = [st.sb(f"out{u}", [P, T]) for u in range(2)]
        ps = [st.ps(f"acc{b}") for b in range(NBLK)]
        raw_in, high, low, block_done, stored = (st.sem2(n) for n in ("raw_in", "high", "low", "block_done", "stored"))
        block_out = [st.sem(f"block_out{b}") for b in range(NBLK)]
        wv = w_in[0].rearrange("(k p) n -> p k n", p=P)

        def column_tiles(eng, *steps):
            behind, tiles = len(steps) - 1, CT + 1

            def static(at):
                for j, step in enumerate(steps):
                    ct = at - j
                    if 0 <= ct < tiles:
                        step(ct % 2, ct // 2 + 1, ct, P if ct < CT else REM)
            first = behind // 2 + 1
            for at in range(2 * first):
                static(at)
            with eng.Fori(first, PAIRS) as i:
                for r in range(2):
                    for j, step in enumerate(steps):
                        step((r - j) % 2, i + (r - j) // 2 + 1, 2 * i + r - j, P)
            for at in range(2 * PAIRS, tiles + behind):
                static(at)

        with st.block() as block:
            @block.sync
            def _(sp):
                def load(u, n, ct, width):
                    sp.wait_ge(low[u], n - 1)
                    sp.dma_start(raw[u][:, :, 0:width], wv[:, :, bass.ds(ct * P, width)]).then_inc(raw_in[u], 16)
                column_tiles(sp, load)

            @block.gpsimd
            def _(pool):
                pool.wait_ge(raw_in[0], 16)

                def store(u, n, ct, width):
                    pool.wait_ge(raw_in[0], 16)
                    for b in range(NBLK):
                        pool.wait_ge(block_out[b], ct + 1)
                    pool.dma_start(proj[bass.ds(ct * P, width), :], out[u][0:width, :]).then_inc(stored[u], 16)
                column_tiles(pool, store)
                for u in range(2):
                    pool.wait_ge(stored[u], 16 * (PAIRS + 1))

            @block.scalar
            def _(act):
                def split(u, n, ct, width):
                    act.wait_ge(raw_in[u], 16 * n)
                    act.wait_ge(block_done[u], NBLK * (n - 1))
                    act.copy(w[u][0][:, :, 0:width], raw[u][:, :, 0:width]).then_inc(high[u], 1)

                def evacuate(u, n, ct, width):
                    act.wait_ge(stored[u], 16 * n - 16)
                    for b in range(0, NBLK, 2):
                        t0, tn = TOK_BLOCKS[b]
                        act.wait_ge(block_done[u], NBLK * (n - 1) + b + 1)
                        act.copy(out[u][0:width, t0:t0 + tn], ps[b][0:width, 0:tn]).then_inc(block_out[b], 1)
                column_tiles(act, split, evacuate)

            @block.vector
            def _(dve):
                def split(u, n, ct, width):
                    dve.wait_ge(high[u], n)
                    dve.tensor_tensor(w[u][1][:, :, 0:width], raw[u][:, :, 0:width], w[u][0][:, :, 0:width], ALU.subtract).then_inc(low[u], 1)

                def evacuate(u, n, ct, width):
                    dve.wait_ge(stored[u], 16 * n - 16)
                    for b in range(1, NBLK, 2):
                        t0, tn = TOK_BLOCKS[b]
                        dve.wait_ge(block_done[u], NBLK * (n - 1) + b + 1)
                        dve.tensor_copy(out[u][0:width, t0:t0 + tn], ps[b][0:width, 0:tn]).then_inc(block_out[b], 1)
                column_tiles(dve, split, evacuate)

            @block.tensor
            def _(pe):
                def product(u, n, ct, width):
                    pe.wait_ge(high[u], n)
                    pe.wait_ge(low[u], n)
                    for b, (t0, tn) in enumerate(TOK_BLOCKS):
                        pe.wait_ge(block_out[b], ct)
                        for k in range(KD):
                            for i, (wp, hp) in enumerate(((1, 0), (0, 1), (0, 0))):
                                mm = pe.matmul(ps[b][0:width, 0:tn], w[u][wp][:, k, 0:width], hT[hp][:, k, t0:t0 + tn],
                                               start=k == 0 and i == 0, stop=k == KD - 1 and i == 2)
                        mm.then_inc(block_done[u], 1)
                column_tiles(pe, product)


def stage_lru(nc, proj, conv_w, conv_b, wa, ba, wx, bx, lam, h0, mixT, new_state, c, c_ctx, w_ada, b_ada, mods):
    NT = D_LRU // P
    MOD_LATER = 6 * D - MOD_FIRST
    MB = MOD_LATER // BANK // NT
    with Stage(nc, "lru") as st:
        xl, yl, xc = st.sb("xl", [P, T]), st.sb("yl", [P, T]), st.sb("xc", [P, T])
        sig = st.sb("sig", [P, 2, 2, T])
        a = st.sb("a", [P, 2, T])
        tanh = st.sb("tanh", [P, 2, T])
        hid = st.sb("hid", [P, 2, T])
        par = st.sb("par", [P, 4 + 1 + 2 + 2 + 2 + 2])
        cw, cb, bias, lm, st0 = par[:, 0:4], par[:, 4:5], par[:, 5:9], par[:, 9:11], par[:, 11:13]
        sp_t = st.sb("sp_t", [P, 6, 2])
        bd = st.sb("bd", [P, 2, 2, P])
        bank = [st.ps(f"b{b}") for b in range(len(TOK_BLOCKS))]
        cvec, sil = st.sb("cvec", [P, 2, KD]), st.sb("sil", [P, KD, 2])
        mod_w = [st.sb(f"mod_w{u}", [P, KD, BANK]) for u in range(2)]
        mod_bias, mod_out = st.sb("mod_bias", [2, MOD_LATER]), st.sb("mod_out", [2, MOD_LATER])
        wv = w_ada[0].rearrange("(p k) n -> p k n", k=KD)
        cvec_in, silu_done, mod_bias_in, mod_biased, mod_stored = (st.sem(n) for n in (
            "cvec_in", "silu_done", "mod_bias_in", "mod_biased", "mod_stored"))
        mod_w_in, mod_mm = st.sem2("mod_w_in"), st.sem2("mod_mm")
        zeroed, ld, wts_in = st.sem("zeroed"), st.sem("ld"), st.sem("wts_in")
        conv, soft, gate_mm = st.sem("conv"), st.sem("soft"), st.sem("gate_mm")
        gated = [st.sem(f"gated{b}") for b in range(len(TOK_BLOCKS))]
        lam_abs, lam_exp = st.sem("lam_abs"), st.sem("lam_exp")
        decay_done, tanh_done, square_done, under_root, root_done = (st.sem(n) for n in (
            "decay_done", "tanh_done", "square_done", "under_root", "root_done"))
        drive, scanned, summed, gelu_done, out_done = (st.sem(n) for n in ("drive", "scanned", "summed", "gelu_done", "out_done"))
        stored = st.sem("stored")
        SERIES = 9
        N_CONV = 7
        N_LD = 2 + 1 + 1 + 4 + 2 + 2
        N_SOFT = 4 + SERIES + 3
        N_ST = 1 + 2

        def chan(v, i):
            return v[bass.ds(i * P, P)]

        with st.block() as block:
            @block.sync
            def _(sp):
                sp.dma_start(cvec[:, 0, :], c_ctx.rearrange("(p k) -> p k", k=KD)).then_inc(cvec_in, 16)
                sp.dma_start(cvec[:, 1, :], c[0].rearrange("(p k) -> p k", k=KD)).then_inc(cvec_in, 16)
                for v in range(2):
                    sp.dma_start(mod_bias[v:v + 1, :], b_ada[:, MOD_FIRST:]).then_inc(mod_bias_in, 16)

                def body(i):
                    sp.wait_ge(stored, 16 * N_ST * i)
                    sp.dma_start(xl[:, :], proj[bass.ds(i * P, P), :]).then_inc(ld, 16)
                    sp.dma_start(yl[:, :], proj[bass.ds(D_LRU + i * P, P), :]).then_inc(ld, 16)
                    sp.dma_start(cw, conv_w[0, :, bass.ds(i * P, P)].rearrange("w p -> p w"), allow_slow_non_contiguous=True).then_inc(ld, 16)
                    sp.dma_start(cb, chan(conv_b[0], i).unsqueeze(1)).then_inc(ld, 16)
                    for d in range(2):
                        sp.dma_start(bias[:, 2 * d:2 * d + 1], chan(ba[0, d], i).unsqueeze(1)).then_inc(ld, 16)
                        sp.dma_start(bias[:, 2 * d + 1:2 * d + 2], chan(bx[0, d], i).unsqueeze(1)).then_inc(ld, 16)
                        sp.dma_start(lm[:, d:d + 1], chan(lam[0, d], i).unsqueeze(1)).then_inc(ld, 16)
                        sp.dma_start(st0[:, d:d + 1], chan(h0[0, 0, d], i).unsqueeze(1)).then_inc(ld, 16)
                    sp.wait_ge(zeroed, 1)
                    for d in range(2):
                        for g, wt in enumerate((wa, wx)):
                            for n in range(2):
                                sp.dma_start(bd[64 * n:64 * n + 64, d, g, 64 * n:64 * n + 64],
                                             wt[0, d, bass.ds(2 * i + n, 1)].squeeze(0)).then_inc(wts_in, 16)
                    sp.wait_ge(out_done, i + 1)
                    sp.dma_start(mixT[bass.ds(i * P, P), :], xc[:, :]).then_inc(stored, 16)
                    for d, t in ((0, T_CTX - 1), (1, 0)):
                        sp.dma_start(chan(new_state[0, 0, d], i).unsqueeze(1), hid[:, d, t:t + 1]).then_inc(stored, 16)
                looped(sp, NT, body)
                sp.wait_ge(mod_biased, MB * NT)
                sp.dma_start(mods[:, MOD_FIRST:], mod_out[:, :]).then_inc(mod_stored, 16)
                sp.wait_ge(stored, 16 * N_ST * NT)
                sp.wait_ge(mod_stored, 16)

            @block.gpsimd
            def _(pool):
                pool.memset(bd[:, :, :, :], 0.0).then_inc(zeroed, 1)

                def body(i):
                    for q in range(MB):
                        pool.wait_ge(zeroed, 1)
                        pool.wait_ge(mod_mm[q % 2], MB // 2 * i + q // 2)
                        pool.dma_start(mod_w[q % 2][:, :, :], wv[:, :, bass.ds(MOD_FIRST + (MB * i + q) * BANK, BANK)]).then_inc(mod_w_in[q % 2], 16)
                looped(pool, NT, body)

            @block.scalar
            def _(act):
                act.wait_ge(cvec_in, 32)
                act.activation(sil[:, :, :], cvec[:, :, :].rearrange("p v k -> p k v"), ACT.Silu).then_inc(silu_done, 1)

                def body(i):
                    act.wait_ge(ld, 16 * N_LD * (i + 1))
                    act.activation(sp_t[:, 0, :], lm, ACT.Abs).then_inc(lam_abs, 1)
                    act.wait_ge(lam_abs, i + 1)
                    act.activation(sp_t[:, 1, :], sp_t[:, 0, :], ACT.Exp, scale=-1.0).then_inc(lam_exp, 1)
                    for d in range(2):
                        for g in range(2):
                            for b, (t0, tn) in enumerate(TOK_BLOCKS):
                                act.wait_ge(gate_mm, (4 * i + 2 * d + g) * len(TOK_BLOCKS) + b + 1)
                                act.activation(sig[:, d, g, t0:t0 + tn], bank[b][:, 0:tn], ACT.Sigmoid,
                                               bias=bias[:, 2 * d + g:2 * d + g + 1]).then_inc(gated[b], 1)
                    act.wait_ge(soft, N_SOFT * (i + 1))
                    for b in range(len(TOK_BLOCKS)):
                        act.wait_ge(gated[b], 4 * i + 4)
                    for d in range(2):
                        act.activation(a[:, d, :], sig[:, d, 0, :], ACT.Exp, scale=sp_t[:, 4, d:d + 1]).then_inc(decay_done, 1)
                    for d in range(2):
                        act.activation(tanh[:, d, :], sig[:, d, 0, :], ACT.Tanh, scale=sp_t[:, 5, d:d + 1]).then_inc(tanh_done, 1)
                    act.wait_ge(decay_done, 2 * i + 2)
                    act.wait_ge(tanh_done, 2 * i + 2)
                    for d in range(2):
                        act.activation(sig[:, d, 0, :], a[:, d, :], ACT.Square).then_inc(square_done, 1)
                    for d in range(2):
                        act.wait_ge(under_root, 2 * i + d + 1)
                        act.activation(tanh[:, d, :], sig[:, d, 0, :], ACT.Sqrt).then_inc(root_done, 1)
                    act.activation(yl[:, :], yl[:, :], ACT.Gelu_apprx_tanh).then_inc(gelu_done, 1)
                looped(act, NT, body)

            @block.tensor
            def _(pe):

                def body(i):
                    pe.wait_ge(wts_in, 16 * 8 * (i + 1))
                    pe.wait_ge(conv, N_CONV * (i + 1))
                    pe.wait_ge(mod_biased, MB * i)
                    for d in range(2):
                        for g in range(2):
                            for b, (t0, tn) in enumerate(TOK_BLOCKS):
                                pe.wait_ge(gated[b], 4 * i + 2 * d + g)
                                pe.matmul(bank[b][:, 0:tn], bd[:, d, g, :], xc[:, t0:t0 + tn], start=True, stop=True).then_inc(gate_mm, 1)
                    pe.wait_ge(silu_done, 1)
                    for q in range(MB):
                        pe.wait_ge(gated[q], 4 * i + 4)
                        pe.wait_ge(mod_w_in[q % 2], 16 * (MB // 2 * i + q // 2 + 1))
                        for k in range(KD):
                            mm = pe.matmul(bank[q][0:2, :], sil[:, k, :], mod_w[q % 2][:, k, :], start=k == 0, stop=k == KD - 1)
                        mm.then_inc(mod_mm[q % 2], 1)
                looped(pe, NT, body)

            @block.vector
            def _(dve):

                def body(i):
                    dve.wait_ge(ld, 16 * N_LD * (i + 1))
                    dve.tensor_scalar(xc[:, :], xl[:, :], cw[:, 2:3], cb, ALU.mult, ALU.add).then_inc(conv, 1)
                    k = 1
                    for s, n in SEGS:
                        for w in (0, 1, 3):
                            o = w - 2
                            lo, hi = max(s, s - o), min(s + n, s + n - o)
                            dve.wait_ge(conv, N_CONV * i + k)
                            dve.scalar_tensor_tensor(xc[:, lo:hi], xl[:, lo + o:hi + o], cw[:, w:w + 1], xc[:, lo:hi],
                                                     ALU.mult, ALU.add).then_inc(conv, 1)
                            k += 1
                    e, y, y2, acc, neg, pos = sp_t[:, 1, :], sp_t[:, 0, :], sp_t[:, 2, :], sp_t[:, 3, :], sp_t[:, 4, :], sp_t[:, 5, :]
                    k = 0

                    def step(ins):
                        nonlocal k
                        k += 1
                        ins.then_inc(soft, 1)
                        dve.wait_ge(soft, N_SOFT * i + k)
                    dve.wait_ge(lam_exp, i + 1)
                    step(dve.tensor_scalar(y2, e, 2.0, None, ALU.add))
                    step(dve.reciprocal(acc, y2))
                    step(dve.tensor_tensor(y, e, acc, ALU.mult))
                    step(dve.tensor_tensor(y2, y, y, ALU.mult))
                    step(dve.tensor_scalar(acc, y2, 1.0 / (2 * SERIES - 1), None, ALU.mult))
                    for m in range(SERIES - 2, -1, -1):
                        step(dve.scalar_tensor_tensor(acc, acc, 1.0 / (2 * m + 1), y2 if m else y, ALU.add, ALU.mult))
                    step(dve.tensor_scalar(pos, lm, -8.0, 0.0, ALU.mult, ALU.max))
                    step(dve.scalar_tensor_tensor(pos, acc, 16.0, pos, ALU.mult, ALU.add))
                    step(dve.tensor_scalar(neg, pos, -1.0, None, ALU.mult))
                    assert k == N_SOFT, k
                    for d in range(2):
                        dve.wait_ge(square_done, 2 * i + d + 1)
                        dve.scalar_tensor_tensor(sig[:, d, 0, :], sig[:, d, 0, :], 1.0, tanh[:, d, :], ALU.add, ALU.mult).then_inc(under_root, 1)
                        dve.tensor_tensor(hid[:, d, :], sig[:, d, 1, :], xc[:, :], ALU.mult).then_inc(drive, 1)
                    for d in range(2):
                        dve.wait_ge(root_done, 2 * i + d + 1)
                        dve.wait_ge(drive, 4 * i + 2 + d)
                        dve.tensor_tensor(sig[:, d, 1, :], hid[:, d, :], tanh[:, d, :], ALU.mult).then_inc(drive, 1)
                    dve.wait_ge(drive, 4 * i + 4)
                    for d in range(2):
                        for g, (s, n) in enumerate(SEGS):
                            way = slice(s, s + n) if d == 0 else slice(s + n - 1, s - 1 if s else None, -1)
                            dve.tensor_tensor_scan(hid[:, d, way], a[:, d, way], sig[:, d, 1, way],
                                                   st0[:, d:d + 1] if g else 0.0, ALU.mult, ALU.add).then_inc(scanned, 1)
                    dve.wait_ge(scanned, 4 * i + 4)
                    dve.tensor_tensor(sig[:, 0, 0, :], hid[:, 0, :], hid[:, 1, :], ALU.add).then_inc(summed, 1)
                    dve.wait_ge(summed, i + 1)
                    dve.wait_ge(gelu_done, i + 1)
                    dve.tensor_tensor(xc[:, :], sig[:, 0, 0, :], yl[:, :], ALU.mult).then_inc(out_done, 1)
                    for q in range(MB):
                        cols = bass.ds((MB * i + q) * BANK, BANK)
                        dve.wait_ge(mod_bias_in, 32)
                        dve.wait_ge(mod_mm[q % 2], MB // 2 * i + q // 2 + 1)
                        dve.tensor_tensor(mod_out[:, cols], bank[q][0:2, :], mod_bias[:, cols], ALU.add).then_inc(mod_biased, 1)
                looped(dve, NT, body)


def scan_order(ap, d, s, n):
    return ap[:, s:s + n] if d == 0 else ap[:, slice(s + n - 1, s - 1 if s else None, -1)]


def in_chunks(ap):
    return ap.rearrange("p (c t) -> p c t", t=C)


def stage_rwkv_prep(nc, proj, mu, w0, w2, a0, a2, g2, kkw, kaw, rk, blockones_d, rec, decay, gate, bonus):
    RATE = float(2.718281828459045 ** -0.5)
    HP = D_RW // P
    NBLK = len(TOK_BLOCKS)
    with Stage(nc, "rwp") as st:
        raw = [st.sb(f"raw{j}", [P, T]) for j in range(3)]
        lora = [st.sb(f"lora{j}", [P, T]) for j in range(3)]
        r, k, v = (st.sb(n, [P, T]) for n in ("r", "k", "v"))
        sg, cum, eb, ebm, ebi, bs = (st.sb(n, [P, T]) for n in ("sg", "cum", "eb", "ebm", "ebi", "bs"))
        kk, kd, av = raw
        recs = st.sb("recs", [P, NCH, REC])
        total = st.sb("total", [P, NCH])
        keep = st.sb("keep", [P, T])
        mus = st.sb("mus", [P, 3, 3])
        par = st.sb("par", [P, 10])
        p_kk, p_ka, p_rk, p_w0, p_a0, p_1ka = par[:, 0:1], par[:, 1:2], par[:, 2:4], par[:, 4:6], par[:, 6:8], par[:, 8:9]
        tiny = st.sb("tiny", [P, 1])
        w2s, a2s, g2s, ones = (st.sb(n, [P, P]) for n in ("w2s", "a2s", "g2s", "ones"))
        bank = [st.ps(f"b{b}") for b in range(NBLK)]
        const_in, consts, lora_in, lora_mu, lora_mixed, lora_act = (st.sem(n) for n in (
            "const_in", "consts", "lora_in", "lora_mu", "lora_mixed", "lora_act"))
        ld, coef, mixed, product = st.sem("ld"), st.sem("coef"), st.sem("mixed"), st.sem("product")
        freed = [st.sem(f"freed{b}") for b in range(NBLK)]
        gate_ready, kk_raw, squares, norm_root, kk_ready = (st.sem(n) for n in ("gate_ready", "kk_raw", "squares", "norm_root", "kk_ready"))
        sig_ready, a_ready, cum_ready, arg_ready, exps, kd_step = (st.sem(n) for n in (
            "sig_ready", "a_ready", "cum_ready", "arg_ready", "exps", "kd_step"))
        rec_dve, rec_pool, rec_act, rec_stored, bonus_step, bonus_out = (st.sem(n) for n in (
            "rec_dve", "rec_pool", "rec_act", "rec_stored", "bonus_step", "bonus_out"))
        gate_stored, bonus_stored = st.sem("gate_stored"), st.sem("bonus_stored")
        N_LD = 3 + 6 + 2 + 6 + 5
        N_COEF = 2
        JOBS = 7

        def column(vec, c0):
            return vec[bass.ds(c0, P)].unsqueeze(1)

        def shift_mix(eng, out, x, m, done, base):
            eng.tensor_scalar(out[:, :], x[:, :], m[:, 2:3], None, ALU.mult).then_inc(done, 1)
            q = 1
            for s, n in SEGS:
                eng.wait_ge(done, base + q)
                eng.scalar_tensor_tensor(out[:, s + 1:s + n], x[:, s:s + n - 1], m[:, 0:1], out[:, s + 1:s + n], ALU.mult, ALU.add).then_inc(done, 1)
                eng.wait_ge(done, base + q + 1)
                eng.scalar_tensor_tensor(out[:, s:s + n - 1], x[:, s + 1:s + n], m[:, 1:2], out[:, s:s + n - 1], ALU.mult, ALU.add).then_inc(done, 1)
                q += 2
        MIX = 5

        with st.block() as block:
            @block.sync
            def _(sp):
                sp.dma_start(ones[:, :], blockones_d).then_inc(const_in, 16)
                for j in range(3):
                    c0 = 3 * D_RW + j * P
                    sp.dma_start(raw[j][:, :], proj[RW0 + c0:RW0 + c0 + P, :]).then_inc(lora_in, 16)
                    for m in range(2):
                        sp.dma_start(mus[:, j, m:m + 1], column(mu[0, m], c0)).then_inc(lora_in, 16)

                def body(i):
                    c0 = i * P
                    sp.wait_ge(bonus_out, NBLK * i)
                    for j in range(3):
                        sp.wait_ge(lora_mixed, MIX * (j + 1))
                        sp.dma_start(raw[j][:, :], proj[bass.ds(RW0 + j * D_RW + c0, P), :]).then_inc(ld, 16)
                        for m in range(2):
                            sp.dma_start(mus[:, j, m:m + 1], column(mu[0, m], j * D_RW + c0)).then_inc(ld, 16)
                    sp.dma_start(p_kk, column(kkw[0], c0)).then_inc(ld, 16)
                    sp.dma_start(p_ka, column(kaw[0], c0)).then_inc(ld, 16)
                    for d in range(2):
                        sp.dma_start(p_rk[:, d:d + 1], column(rk[0, d].rearrange("h n -> (h n)"), c0)).then_inc(ld, 16)
                        sp.dma_start(p_w0[:, d:d + 1], column(w0[0, d], c0)).then_inc(ld, 16)
                        sp.dma_start(p_a0[:, d:d + 1], column(a0[0, d], c0)).then_inc(ld, 16)
                    for d in range(2):
                        sp.dma_start(w2s[64 * d:64 * d + 64, :], w2[0, d, :, bass.ds(c0, P)]).then_inc(ld, 16)
                        sp.dma_start(a2s[64 * d:64 * d + 64, :], a2[0, d, :, bass.ds(c0, P)]).then_inc(ld, 16)
                    sp.dma_start(g2s[:, :], g2[0, :, bass.ds(c0, P)]).then_inc(ld, 16)
                    sp.wait_ge(gate_ready, NBLK * (i + 1))
                    sp.dma_start(gate[bass.ds(c0, P), :], ebi[:, :]).then_inc(gate_stored, 16)
                    for d in range(2):
                        for part in (rec_dve, rec_pool, rec_act):
                            sp.wait_ge(part, 2 * i + d + 1)
                        sp.dma_start(rec[d, :, :, bass.ds(i, 1), :].squeeze(2), recs[:, :, :]).then_inc(rec_stored, 16)
                        sp.dma_start(decay[:, d, bass.ds(i, 1), :].squeeze(1), total[:, :]).then_inc(rec_stored, 16)
                    sp.wait_ge(bonus_out, NBLK * (i + 1))
                    sp.dma_start(bonus[bass.ds(c0, P), :], bs[:, :]).then_inc(bonus_stored, 16)
                looped(sp, HP, body)
                sp.wait_ge(gate_stored, 16 * HP)
                sp.wait_ge(bonus_stored, 16 * HP)
                sp.wait_ge(rec_stored, 32 * 2 * HP)

            @block.gpsimd
            def _(pool):
                pool.memset(keep[:, :], 1.0).then_inc(consts, 1)
                pool.memset(tiny[:, :], 1e-12).then_inc(consts, 1)
                pool.wait_ge(consts, 2)
                pool.memset(in_chunks(keep[:, :])[:, :, 0:1], 0.0).then_inc(consts, 1)

                def body(i):
                    for d in range(2):
                        pool.wait_ge(kd_step, 3 * (2 * i + d) + 3)
                        pool.wait_ge(exps, 3 * (2 * i + d) + 3)
                        pool.wait_ge(rec_stored, 32 * (2 * i + d))
                        pool.wait_ge(consts, 3)
                        pool.tensor_tensor(recs[:, :, 3 * C:4 * C], in_chunks(kd[:, :]), in_chunks(ebi[:, :]), ALU.mult).then_inc(rec_pool, 1)
                looped(pool, HP, body)

            @block.scalar
            def _(act):
                act.wait_ge(lora_mixed, MIX)
                act.activation(lora[0][:, :], lora[0][:, :], ACT.Tanh).then_inc(lora_act, 1)
                act.wait_ge(lora_mixed, 3 * MIX)
                act.activation(lora[2][:, :], lora[2][:, :], ACT.Sigmoid).then_inc(lora_act, 1)
                act.wait_ge(consts, 3)

                def body(i):
                    def evacuate(job, out, done, func, **kw):
                        for b, (t0, tn) in enumerate(TOK_BLOCKS):
                            act.wait_ge(product, NBLK * (JOBS * i + job) + b + 1)
                            act.activation(out[:, t0:t0 + tn], bank[b][:, 0:tn], func, **kw).then_inc(done, 1)
                    act.wait_ge(rec_dve, 2 * i)
                    act.wait_ge(rec_pool, 2 * i)
                    act.wait_ge(rec_act, 2 * i)
                    evacuate(0, ebi, gate_ready, ACT.Copy)
                    evacuate(1, eb, norm_root, ACT.Sqrt, bias=tiny[:, :])
                    for d in range(2):
                        act.wait_ge(arg_ready, 2 * i + d)
                        act.wait_ge(rec_dve, 2 * i + d)
                        act.wait_ge(mixed, 3 * MIX * (i + 1))
                        evacuate(2 + 2 * d, sg, sig_ready, ACT.Sigmoid, bias=p_w0[:, d:d + 1])
                        evacuate(3 + 2 * d, av, a_ready, ACT.Sigmoid, bias=p_a0[:, d:d + 1])
                        act.wait_ge(kk_ready, 2 * i + 2)
                        act.wait_ge(cum_ready, 2 * i + d + 1)
                        act.wait_ge(arg_ready, 2 * i + d + 1)
                        act.wait_ge(rec_pool, 2 * i + d)
                        act.wait_ge(gate_stored, 16 * (i + 1))
                        act.activation(eb[:, :], cum[:, :], ACT.Exp, scale=-RATE).then_inc(exps, 1)
                        act.activation(ebi[:, :], cum[:, :], ACT.Exp, scale=RATE).then_inc(exps, 1)
                        act.activation(ebm[:, :], ebm[:, :], ACT.Exp, scale=-RATE).then_inc(exps, 1)
                        act.wait_ge(exps, 3 * (2 * i + d) + 3)
                        act.wait_ge(rec_stored, 32 * (2 * i + d))
                        act.copy(recs[:, :, 4 * C:], in_chunks(v[:, :]))
                        end = 0 if d else C - 1
                        act.copy(total[:, :].unsqueeze(2), in_chunks(eb[:, :])[:, :, end:end + 1]).then_inc(rec_act, 1)
                looped(act, HP, body)

            @block.tensor
            def _(pe):
                pe.wait_ge(const_in, 16)

                def body(i):
                    def job(j, lhsT, rhs, also=None, at=0):
                        for b, (t0, tn) in enumerate(TOK_BLOCKS):
                            pe.wait_ge(freed_or(j, b)[0], freed_or(j, b)[1])
                            if also is not None:
                                pe.wait_ge(*also)
                            pe.matmul(bank[b][:, 0:tn], lhsT, rhs[at:at + lhsT.shape[0], t0:t0 + tn], start=True, stop=True).then_inc(product, 1)

                    def freed_or(j, b):
                        return [(bonus_out, NBLK * i), (gate_ready, NBLK * i + b + 1), (norm_root, NBLK * i + b + 1),
                                (sig_ready, NBLK * 2 * i + b + 1), (a_ready, NBLK * 2 * i + b + 1),
                                (sig_ready, NBLK * (2 * i + 1) + b + 1), (a_ready, NBLK * (2 * i + 1) + b + 1)][j]
                    pe.wait_ge(ld, 16 * N_LD * (i + 1))
                    pe.wait_ge(lora_act, 2)
                    job(0, g2s[:, :], lora[2])
                    job(1, ones[:, :], kd, (squares, i + 1))
                    for d in range(2):
                        job(2 + 2 * d, w2s[64 * d:64 * d + 64, :], lora[0], None, 64 * d)
                        job(3 + 2 * d, a2s[64 * d:64 * d + 64, :], lora[1], None, 64 * d)
                    job(6, ones[:, :], bs, (bonus_step, 3 * i + 3))
                looped(pe, HP, body)

            @block.vector
            def _(dve):
                dve.wait_ge(lora_in, 9 * 16)
                dve.tensor_tensor(mus[:, :, 2], mus[:, :, 0], mus[:, :, 1], ALU.add).then_inc(lora_mu, 1)
                dve.wait_ge(lora_mu, 1)
                dve.tensor_scalar(mus[:, :, 2], mus[:, :, 2], -1.0, 1.0, ALU.mult, ALU.add).then_inc(lora_mu, 1)
                dve.wait_ge(lora_mu, 2)
                for j in range(3):
                    shift_mix(dve, lora[j], raw[j], mus[:, j, :], lora_mixed, MIX * j)
                dve.wait_ge(consts, 3)

                def body(i):
                    dve.wait_ge(ld, 16 * N_LD * (i + 1))
                    dve.tensor_tensor(mus[:, :, 2], mus[:, :, 0], mus[:, :, 1], ALU.add).then_inc(coef, 1)
                    dve.tensor_scalar(p_1ka, p_ka, -1.0, 1.0, ALU.mult, ALU.add).then_inc(coef, 1)
                    dve.wait_ge(coef, 3 * i + 2)
                    dve.tensor_scalar(mus[:, :, 2], mus[:, :, 2], -1.0, 1.0, ALU.mult, ALU.add).then_inc(coef, 1)
                    dve.wait_ge(coef, 3 * i + 3)
                    dve.wait_ge(rec_act, 2 * i)
                    for j, out in enumerate((r, k, v)):
                        shift_mix(dve, out, raw[j], mus[:, j, :], mixed, 3 * MIX * i + MIX * j)
                    dve.wait_ge(mixed, 3 * MIX * (i + 1))
                    dve.tensor_scalar(kk[:, :], k[:, :], p_kk, None, ALU.mult).then_inc(kk_raw, 1)
                    dve.wait_ge(kk_raw, i + 1)
                    dve.tensor_tensor(kd[:, :], kk[:, :], kk[:, :], ALU.mult).then_inc(squares, 1)
                    dve.wait_ge(norm_root, NBLK * (i + 1))
                    dve.reciprocal(eb[:, :], eb[:, :]).then_inc(kk_ready, 1)
                    dve.wait_ge(kk_ready, 2 * i + 1)
                    dve.tensor_tensor(kk[:, :], kk[:, :], eb[:, :], ALU.mult).then_inc(kk_ready, 1)
                    for d in range(2):
                        u = 2 * i + d
                        dve.wait_ge(sig_ready, NBLK * (u + 1))
                        dve.wait_ge(exps, 3 * u)
                        dve.tensor_tensor_scan(scan_order(cum, d, 0, T), keep[:, :], scan_order(sg, d, 0, T), 0.0, ALU.mult, ALU.add).then_inc(cum_ready, 1)
                        dve.wait_ge(cum_ready, u + 1)
                        dve.tensor_tensor(ebm[:, :], cum[:, :], sg[:, :], ALU.subtract).then_inc(arg_ready, 1)
                        dve.wait_ge(a_ready, NBLK * (u + 1))
                        dve.wait_ge(rec_pool, u)
                        dve.tensor_scalar(kd[:, :], av[:, :], p_ka, p_1ka, ALU.mult, ALU.add).then_inc(kd_step, 1)
                        dve.wait_ge(kd_step, 3 * u + 1)
                        dve.tensor_tensor(kd[:, :], kd[:, :], k[:, :], ALU.mult).then_inc(kd_step, 1)
                        dve.wait_ge(kk_ready, 2 * i + 2)
                        dve.tensor_tensor(av[:, :], av[:, :], kk[:, :], ALU.mult).then_inc(kd_step, 1)
                        dve.wait_ge(kd_step, 3 * u + 3)
                        if d == 0:
                            dve.wait_ge(bonus_stored, 16 * i)
                            dve.tensor_scalar(bs[:, :], kd[:, :], p_rk[:, 0:1], None, ALU.mult).then_inc(bonus_step, 1)
                        else:
                            dve.wait_ge(bonus_step, 3 * i + 1)
                            dve.scalar_tensor_tensor(bs[:, :], kd[:, :], p_rk[:, 1:2], bs[:, :], ALU.mult, ALU.add).then_inc(bonus_step, 1)
                        dve.wait_ge(rec_stored, 32 * u)
                        dve.wait_ge(exps, 3 * u + 3)
                        for q, (x, y) in enumerate(((kk, ebm), (r, eb), (av, ebi))):
                            out = recs[:, :, q * C:(q + 1) * C]
                            if q == 0:
                                dve.scalar_tensor_tensor(out, in_chunks(x[:, :]), -1.0, in_chunks(y[:, :]), ALU.mult, ALU.mult)
                            else:
                                last = dve.tensor_tensor(out, in_chunks(x[:, :]), in_chunks(y[:, :]), ALU.mult)
                        last.then_inc(rec_dve, 1)
                    dve.wait_ge(bonus_step, 3 * i + 2)
                    dve.tensor_tensor(bs[:, :], bs[:, :], r[:, :], ALU.mult).then_inc(bonus_step, 1)
                    for b, (t0, tn) in enumerate(TOK_BLOCKS):
                        dve.wait_ge(product, NBLK * (JOBS * i + 6) + b + 1)
                        dve.tensor_tensor(bs[:, t0:t0 + tn], bank[b][:, 0:tn], v[:, t0:t0 + tn], ALU.mult).then_inc(bonus_out, 1)
                looped(dve, HP, body)


def joins(d):
    t = np.arange(C)[::-1] if d else np.arange(C)
    return [(t[:, None] >> (l + 1) == t[None, :] >> (l + 1)) & (t[:, None] >> l & 1 == 1) & (t[None, :] >> l & 1 == 0)
            for l in range(LEVELS)]


def rwkv_constants():
    two = lambda m: np.concatenate([m, m], 0)
    diag = lambda m: np.kron(np.eye(2), m)
    parts = []
    for d in range(2):
        later = sum(joins(d)).T
        parts += [two(later), two(later + np.eye(C)), diag(joins(d)[0].T)] + [two(j) for j in joins(d)]
    return np.concatenate(parts + [two(np.eye(C)), np.kron(np.eye(2), np.ones((C, 1))), np.eye(P)], 1).astype(np.float32)


def grid_rows(t, tile, seg, half):
    if seg == 0:
        return t[64 * half:64 * half + 64, :]
    return t[T_CTX:T, :].rearrange("(c r) x -> r c x", r=GRID_H)[bass.ds(2 * tile - 2 + half, 1)].squeeze(0)


def stage_gla_turn(nc, proj, ident_d, vt):
    UN = D_GLA // P
    V0 = GLA0 + 2 * D_GLA_K
    with Stage(nc, "gvt") as st:
        ident = st.sb("ident", [P, P])
        x, y = ([st.sb(f"{n}{u}", [P, UN, P]) for u in range(2)] for n in ("x", "y"))
        ps = [st.ps(f"t{u}") for u in range(2)]
        ident_in = st.sem("ident_in")
        x_in, turned, copied, stored = (st.sem2(n) for n in ("x_in", "turned", "copied", "stored"))
        with st.block() as block:
            @block.sync
            def _(sp):
                sp.dma_start(ident[:, :], ident_d).then_inc(ident_in, 16)

                def load(u, n, tile, seg):
                    sp.wait_ge(turned[u], n - 1)
                    sp.dma_start(x[u][:, :, :], proj[V0:V0 + D_GLA, bass.ds(tile * P, P)].rearrange("(j p) t -> p j t", p=P)).then_inc(x_in[u], 16)
                staged(sp, load)

            @block.gpsimd
            def _(pool):
                def store(u, n, tile, seg):
                    pool.wait_ge(ident_in, 16)
                    pool.wait_ge(copied[u], n)
                    for half in range(2):
                        rows = grid_rows(vt, tile, seg, half)
                        pool.dma_start(rows, y[u][64 * half:64 * half + 64, :, :].rearrange("p j t -> p (j t)")).then_inc(stored[u], 16)
                staged(pool, store)
                for u in range(2):
                    pool.wait_ge(stored[u], 32 * (9 - u))

            @block.tensor
            def _(pe):
                pe.wait_ge(ident_in, 16)

                def body(u, n, tile, seg):
                    pe.wait_ge(x_in[u], 16 * n)
                    pe.wait_ge(copied[u], n - 1)
                    for j in range(UN):
                        mm = pe.transpose(ps[u][:, j * P:(j + 1) * P], x[u][:, j, :], ident[:, :])
                    mm.then_inc(turned[u], 1)
                staged(pe, body)

            @block.vector
            def _(dve):
                def body(u, n, tile, seg):
                    dve.wait_ge(turned[u], n)
                    dve.wait_ge(stored[u], 32 * (n - 1))
                    dve.tensor_copy(y[u][:, :, :].rearrange("p j t -> p (j t)"), ps[u][:, 0:UN * P]).then_inc(copied[u], 1)
                staged(dve, body)


GREC = 4 * C


def column_major(ap):
    return ap[:, T_CTX:T].rearrange("p (c r) -> p r c", r=GRID_H)


def row_major(ap):
    return ap[:, T_CTX:T].rearrange("p (r c) -> p r c", c=GRID_W)


def stage_gla_prep(nc, proj, wg2, bg, grec):
    HP = GLA_HEADS // 2
    NBLK = len(TOK_BLOCKS)
    G0 = GLA0 + 2 * D_GLA_K + 2 * D_GLA
    with Stage(nc, "glp") as st:
        gd = st.sb("gd", [GLA_R, 2, T])
        w = st.sb("w", [GLA_R, 2, HP, P])
        b_g = st.sb("b_g", [P, 2, HP])
        keep = st.sb("keep", [P, T])
        qk = [st.sb(f"qk{i}", [P, T]) for i in range(2)]
        x, ab, la = ([st.sb(f"{n}{d}", [P, T]) for d in range(2)] for n in ("x", "ab", "la"))
        cum = st.sb("cum", [P, T])
        recs = st.sb("recs", [P, NCH, GREC])
        bank = [st.ps(f"b{b}") for b in range(NBLK)]
        zeroed, par_in, qk_in, consts = st.sem("zeroed"), st.sem("par_in"), st.sem("qk_in"), st.sem("consts")
        product, biased, absd, expd, lnd, la_done, summed, rec_act, stored = (st.sem(n) for n in (
            "product", "biased", "absd", "expd", "lnd", "la_done", "summed", "rec_act", "stored"))
        cum_out = st.sem("cum_out")
        with st.block() as block:
            @block.gpsimd
            def _(pool):
                pool.memset(keep[:, :], 1.0).then_inc(consts, 1)
                for z in (w[:, :, :, :], b_g[:, :, :], qk[0][:, :], qk[1][:, :]):
                    pool.memset(z, 0.0).then_inc(zeroed, 1)
                pool.wait_ge(consts, 1)
                pool.memset(in_chunks(keep[:, :])[:, :, 0:1], 0.0).then_inc(consts, 1)

            @block.sync
            def _(sp):
                sp.wait_ge(zeroed, 4)
                for d in range(2):
                    sp.dma_start(gd[:, d, :], proj[G0 + GLA_R * d:G0 + GLA_R * (d + 1), :]).then_inc(par_in, 16)
                    for head in range(GLA_HEADS):
                        j, h, ch = head // 2, head % 2, slice(head * GLA_DK, (head + 1) * GLA_DK)
                        sp.dma_start(w[:, d, j, 64 * h:64 * h + GLA_DK], wg2[0, d, :, ch]).then_inc(par_in, 16)
                        sp.dma_start(b_g[64 * h:64 * h + GLA_DK, d, j:j + 1], bg[0, d, ch].unsqueeze(1)).then_inc(par_in, 16)
                for j in range(HP):
                    if j:
                        sp.wait_ge(rec_act, 2 * j)
                    for i in range(2):
                        for h in range(2):
                            r0 = GLA0 + i * D_GLA_K + (2 * j + h) * GLA_DK
                            sp.dma_start(qk[i][64 * h:64 * h + GLA_DK, :], proj[r0:r0 + GLA_DK, :]).then_inc(qk_in, 16)
                    sp.wait_ge(rec_act, 2 * (j + 1))
                    sp.wait_ge(cum_out, 2 * (j + 1))
                    sp.dma_start(grec[j], recs[:, :, :]).then_inc(stored, 16)
                sp.wait_ge(stored, 16 * HP)

            @block.tensor
            def _(pe):
                pe.wait_ge(par_in, 16 * 18)
                for j in range(HP):
                    for d in range(2):
                        for b, (t0, tn) in enumerate(TOK_BLOCKS):
                            if 2 * j + d:
                                pe.wait_ge(biased, (2 * j + d - 1) * NBLK + b + 1)
                            pe.matmul(bank[b][:, 0:tn], w[:, d, j, :], gd[:, d, t0:t0 + tn], start=True, stop=True).then_inc(product, 1)

            @block.scalar
            def _(act):
                for j in range(HP):
                    act.wait_ge(qk_in, 64 * (j + 1))
                    if j:
                        act.wait_ge(stored, 16 * j)
                    for i in range(2):
                        o = recs[:, :, i * C:(i + 1) * C]
                        s = GLA_DK ** -0.5 if i == 0 else 1.0
                        act.activation(o[:, 0:NCH_CTX, :], in_chunks(qk[i][:, 0:T_CTX]), ACT.Copy, scale=s)
                        for half in range(2):
                            out = o[:, NCH_CTX:, half * GRID_H:(half + 1) * GRID_H]
                            src = qk[i][:, T_CTX:T].rearrange("p (r k e) -> p e k r", k=GRID_W // 2, e=2)[:, half]
                            last = act.activation(out, src, ACT.Copy, scale=s)
                        last.then_inc(rec_act, 1)
                    for d in range(2):
                        act.wait_ge(biased, (2 * j + d + 1) * NBLK)
                        act.activation(ab[d][:, :], x[d][:, :], ACT.Abs).then_inc(absd, 1)
                        act.wait_ge(absd, 2 * j + d + 1)
                        act.activation(ab[d][:, :], ab[d][:, :], ACT.Exp, scale=-1.0).then_inc(expd, 1)
                        act.wait_ge(expd, 2 * j + d + 1)
                        act.activation(ab[d][:, :], ab[d][:, :], ACT.Ln, bias=1.0).then_inc(lnd, 1)

            @block.vector
            def _(dve):
                dve.wait_ge(par_in, 16 * 18)
                dve.wait_ge(consts, 2)
                for j in range(HP):
                    for d in range(2):
                        n = 2 * j + d
                        for b, (t0, tn) in enumerate(TOK_BLOCKS):
                            dve.wait_ge(product, n * NBLK + b + 1)
                            dve.tensor_scalar(x[d][:, t0:t0 + tn], bank[b][:, 0:tn], b_g[:, d, j:j + 1], None, ALU.add).then_inc(biased, 1)
                    for d in range(2):
                        n = 2 * j + d
                        dve.wait_ge(lnd, n + 1)
                        dve.scalar_tensor_tensor(la[d][:, 0:T_CTX], x[d][:, 0:T_CTX], 0.0, ab[d][:, 0:T_CTX], ALU.min, ALU.subtract)
                        dve.scalar_tensor_tensor(column_major(la[d]), row_major(x[d]), 0.0, row_major(ab[d]), ALU.min, ALU.subtract).then_inc(la_done, 1)
                        dve.wait_ge(la_done, n + 1)
                        dve.tensor_tensor_scan(scan_order(cum, d, 0, T), keep[:, :], scan_order(la[d], d, 0, T), 0.0, ALU.mult, ALU.add).then_inc(summed, 1)
                        dve.wait_ge(summed, n + 1)
                        if j:
                            dve.wait_ge(stored, 16 * j)
                        dve.tensor_copy(recs[:, :, (2 + d) * C:(3 + d) * C], in_chunks(cum[:, :])).then_inc(cum_out, 1)


def gla_constants():
    parts = [np.concatenate([m, m], 0) for d in range(2) for m in [j.T for j in joins(d)] + [np.eye(C)]]
    return np.concatenate(parts + [np.kron(np.eye(2), np.ones((C, 1))), np.eye(P)], 1).astype(np.float32)


def stage_scans(nc, rec, decay, consts_d, state_in, new_state, o, grec, vt, gla_consts_d, gla_state_in, gla_new_state, gla_o):
    G, UN, GN = 2, 3, 2
    NL = LEVELS - 1
    W = rwkv_constants().shape[1]
    NS = LEVELS + 2
    NA = LEVELS + 1
    WG = gla_constants().shape[1]
    CA = 4
    KT_AT, KF_AT, ATT_AT, SUM_AT = (2, 3), (1, 2), (3, 4), (4, 5)
    with Stage(nc, "scn") as st:
        con = st.sb("con", [P, W])
        per_d = 4 * C + LEVELS * C
        mask2 = [con[:, g * per_d:g * per_d + 2 * C].rearrange("p (q t) -> p q t", q=2) for g in range(G)]
        mT0 = [con[:, g * per_d + 2 * C:g * per_d + 4 * C] for g in range(G)]
        m_lev = [con[:, g * per_d + 4 * C:(g + 1) * per_d].rearrange("p (l s) -> p l s", l=LEVELS) for g in range(G)]
        eye, eye128 = con[:, G * per_d:G * per_d + C], con[:, W - P:W]
        own = con[:, W - P - 2:W - P]
        plain = [st.sb(f"plain{u}", [P, G * UN, REC]) for u in range(2)]
        bd = [st.sb(f"bd{u}", [P, G * UN, 5, 2, C]) for u in range(2)]
        LR = [st.sb(f"LR{g}", [P, UN, 2, 2, C]) for g in range(G)]
        KR = [st.sb(f"KR{g}", [P, UN, 2, 2, C]) for g in range(G)]
        Ti = [st.sb(f"T{g}", [P, UN, C]) for g in range(G)]
        Ui = [st.sb(f"U{g}", [P, UN, P]) for g in range(G)]
        Ys = [st.sb(f"Ys{g}", [P, UN, C]) for g in range(G)]
        Yd = [st.sb(f"Yd{g}", [P, UN, 2, C]) for g in range(G)]
        Vs, Xs, SAs, S, Sn = ([st.sb(f"{x}{g}", [P, UN, C]) for g in range(G)] for x in ("V", "X", "SA", "S", "Sn"))
        BT, KT = ([st.sb(f"{x}{g}", [P, UN, P]) for g in range(G)] for x in ("BT", "KT"))
        Os = [[st.sb(f"O{g}{u}", [P, UN, C]) for u in range(2)] for g in range(G)]
        SX = st.sb("SX", [P, G * UN, 2, C])
        total = st.sb("total", [P, G, UN, NCH])
        gcon = st.sb("gcon", [P, WG])
        gmask = [gcon[:, g * NA * C:(g + 1) * NA * C].rearrange("p (l t) -> p l t", l=NA) for g in range(G)]
        grc = [st.sb(f"grc{u}", [P, G, GN, GREC]) for u in range(2)]
        gv = [st.sb(f"gv{u}", [P, G, GN, GLA_DV]) for u in range(2)]
        Dd = [st.sb(f"D{g}", [P, NS, GN, C]) for g in range(G)]
        F = [st.sb(f"F{g}", [P, NS, GN, C]) for g in range(G)]
        QF = [st.sb(f"QF{g}", [P, LEVELS, GN, C]) for g in range(G)]
        KF = [st.sb(f"KF{g}", [P, GN, LEVELS, 2, C]) for g in range(G)]
        qo, ko, qe, kh = ([st.sb(f"{x}{g}", [P, GN, 2, C]) for g in range(G)] for x in ("qo", "ko", "qe", "kh"))
        AM = [st.sb(f"AM{g}", [P, NA, GN, C]) for g in range(G)]
        att = [st.sb(f"att{g}", [P, GN, C]) for g in range(G)]
        ad = [st.sb(f"ad{g}", [P, GN, 2, C]) for g in range(G)]
        kT = [st.sb(f"kT{g}", [P, GN, P]) for g in range(G)]
        gS = [st.sb(f"gS{g}", [P, GN, GLA_DV]) for g in range(G)]
        gOs = [[st.sb(f"gO{g}{u}", [P, GN, GLA_DV]) for u in range(2)] for g in range(G)]
        bank = [st.ps(f"b{b}") for b in range(8)]
        pA, pB, pC, pD, pE, pF, pG, pH = bank
        pV, pYU, pS = [pF, pG], [pF, pG], [pF, pG]
        pY, pX = [pH, pC], [pH, pC]
        g1, g2 = [pA, pD], [pB, pE]

        def each(name):
            return [st.sem(f"{name}_{g}") for g in range(G)]
        con_in, cleared, rec_in = st.sem("con_in"), st.sem("cleared"), st.sem2("rec_in")
        mm_v, mm_a, mm_b, mm_c, mm_d, mm_e = (each(n) for n in ("mm_v", "mm_a", "mm_b", "mm_c", "mm_d", "mm_e"))
        lr_done, kr_done, t_mask, t0_done, vs_done, bt_done, kt_done = (each(n) for n in (
            "lr_done", "kr_done", "t_mask", "t0_done", "vs_done", "bt_done", "kt_done"))
        u_mask, u0_done = each("u_mask"), each("u0_done")
        y_mm, ys_done, yd_done, ty_mm, yu_mm, t_step, u_step = (each(n) for n in (
            "y_mm", "ys_done", "yd_done", "ty_mm", "yu_mm", "t_step", "u_step"))
        x_mm, x_done, sa_mm, sa_done, o_mm, o_done, s_mm, s_sum, s_done = (each(n) for n in (
            "x_mm", "x_done", "sa_mm", "sa_done", "o_mm", "o_done", "s_mm", "s_sum", "s_done"))
        o_out = [st.sem2(f"o_out{g}") for g in range(G)]
        state0 = st.sem("state0")
        sx_ready, sx_mm, sx_out, sx_stored, sx_in, imported = (st.sem(n) for n in (
            "sx_ready", "sx_mm", "sx_out", "sx_stored", "sx_in", "imported"))
        grec_in = st.sem2("grec_in")
        diffs, slot6, absd, expd, owned, qf_done, qk_bd, kf_done, kT_mm, kT_done = (each(n) for n in (
            "diffs", "slot6", "absd", "expd", "owned", "qf_done", "qk_bd", "kf_done", "kT_mm", "kT_done"))
        att_a, att_b, masked, att_sum, att_bd, go_mm, go_done, gs_done = (each(n) for n in (
            "att_a", "att_b", "masked", "att_sum", "att_bd", "go_mm", "go_done", "gs_done"))
        go_out = [st.sem2(f"go_out{g}") for g in range(G)]
        gstate_out, gstate_in = st.sem("gstate_out"), st.sem("gstate_in")
        N_CLEARED = 3 + 3 * G

        def q_bd(u, j, q):
            return bd[u][:, j, q, :, :].rearrange("p h t -> p (h t)")

        def cols(ps, j, w):
            return ps[:, j * w:(j + 1) * w]

        def v3(ap):
            return ap.rearrange("p (j t) -> p j t", j=UN)

        def flat(ap):
            return ap.rearrange("p h t -> p (h t)")

        def own_of(g):
            return own.unsqueeze(1).unsqueeze(3).to_broadcast([P, GN, 2, C])

        def both(eng, chunk, between):
            for c in range(NCH_CTX):
                chunk(c % 2, 1, c, (c, NCH_CTX - 1 - c), True)
            between()
            with eng.Fori(0, (NCH - NCH_CTX) // 2) as i:
                for u in range(2):
                    chunk(u, i + 2, 2 * i + 2 + u, (2 * i + 2 + u, NCH - 1 - u - 2 * i), False)

        def nothing():
            pass

        def gla_states(t, g):
            return t[0, 0, g].rearrange("(j h) k v -> h k j v", h=2)

        with st.block() as block:
            @block.sync
            def _(sp):
                sp.dma_start(con[:, :], consts_d).then_inc(con_in, 16)
                sp.dma_start(gcon[:, :], gla_consts_d).then_inc(con_in, 16)
                sp.dma_start(total[:, :, :, :], decay).then_inc(con_in, 16)
                sp.wait_ge(cleared, N_CLEARED)

                def load(u, c, at):
                    for g in range(G):
                        js = slice(UN * g, UN * (g + 1))
                        chunk_rec = rec[g, :, bass.ds(at[g], 1), :, :]
                        sp.dma_start(plain[u][:, js, :].rearrange("p j w -> p (j w)"), chunk_rec.rearrange("p c j w -> p (c j w)")).then_inc(rec_in[u], 16)
                        for h in range(2):
                            p = slice(64 * h, 64 * h + 64)
                            sp.dma_start(bd[u][p, js, :, h, :].rearrange("p j q t -> p (j q) t"),
                                         chunk_rec[p].rearrange("p c j (q t) -> p (c j q) t", t=C)).then_inc(rec_in[u], 16)
                        sp.dma_start(grc[u][:, g, :, :], grec[:, :, bass.ds(at[g], 1), :].rearrange("j p c w -> p j (c w)")).then_inc(grec_in[u], 16)
                        for h in range(2):
                            sp.dma_start(gv[u][64 * h:64 * h + 64, g, :, :],
                                         vt[bass.ds(at[g] * C, C), :].rearrange("t (j h x) -> h t j x", h=2, j=GN)[h]).then_inc(grec_in[u], 16)

                def store(u, c, at):
                    for g in range(G):
                        rows = gla_o[g, bass.ds(at[g] * C, C), :]
                        sp.wait_ge(cleared, N_CLEARED)
                        sp.wait_ge(go_done[g], c + 1)
                        for h in range(2):
                            sp.dma_start(rows.rearrange("t (j h x) -> h t j x", h=2, j=GN)[h], gOs[g][u][64 * h:64 * h + 64, :, :]).then_inc(go_out[g][u], 16)
                    for g in range(G):
                        rows = o[g, bass.ds(at[g] * C, C), :]
                        sp.wait_ge(cleared, N_CLEARED)
                        sp.wait_ge(o_done[g], c + 1)
                        for h in range(2):
                            sp.dma_start(rows.rearrange("t (j h v) -> h t j v", h=2, j=UN)[h], Os[g][u][64 * h:64 * h + 64, :, :]).then_inc(o_out[g][u], 16)

                def freed(c):
                    for g in range(G):
                        sp.wait_ge(s_done[g], c + 1)
                        sp.wait_ge(gs_done[g], c + 1)

                def swap():
                    sp.wait_ge(sx_out, 1)
                    for g in range(G):
                        for h in range(2):
                            sp.dma_start(new_state[0, 0, g].rearrange("(j h) v k -> h v j k", h=2)[h], Xs[g][64 * h:64 * h + 64, :, :]).then_inc(sx_stored, 16)
                            sp.dma_start(SX[64 * h:64 * h + 64, UN * g:UN * (g + 1), h, :],
                                         state_in[0, 0, g].rearrange("(j h) v k -> h v j k", h=2)[h]).then_inc(sx_in, 16)
                    sp.wait_ge(sx_stored, 16 * 4)
                    for g in range(G):
                        sp.wait_ge(gs_done[g], NCH_CTX)
                    for g in range(G):
                        for h in range(2):
                            sp.dma_start(gla_states(gla_new_state, g)[h], gS[g][64 * h:64 * h + GLA_DK, :, :]).then_inc(gstate_out, 16)
                    sp.wait_ge(gstate_out, 64)
                    for g in range(G):
                        for h in range(2):
                            sp.dma_start(gS[g][64 * h:64 * h + GLA_DK, :, :], gla_states(gla_state_in, g)[h]).then_inc(gstate_in, 16)

                def reached(c):
                    return (c, NCH_CTX - 1 - c if isinstance(c, int) and c < NCH_CTX else NCH + NCH_CTX - 1 - c)
                for c in range(NCH_CTX):
                    load(c, c, reached(c))
                for c in range(NCH_CTX):
                    freed(c)
                    load(c, c + 2, reached(c + 2))
                    store(c, c, reached(c))
                swap()
                with sp.Fori(0, (NCH - NCH_CTX) // 2 - 1) as i:
                    for u in range(2):
                        freed(2 * i + 2 + u)
                        load(u, 2 * i + 4 + u, (2 * i + 4 + u, NCH - 3 - u - 2 * i))
                        store(u, 2 * i + 2 + u, (2 * i + 2 + u, NCH - 1 - u - 2 * i))
                for u in range(2):
                    store(u, NCH - 2 + u, reached(NCH - 2 + u))
                for g in range(G):
                    for u in range(2):
                        sp.wait_ge(o_out[g][u], 32 * NCH // 2)
                        sp.wait_ge(go_out[g][u], 32 * NCH // 2)

            @block.gpsimd
            def _(pool):
                for z in (*(b[:, :, :, :, :] for b in bd), SX[:, :, :, :]):
                    pool.memset(z, 0.0).then_inc(cleared, 1)
                for g in range(G):
                    for z in (LR[g], KR[g]):
                        pool.memset(z[:, :, :, :, :], 0.0).then_inc(cleared, 1)
                    pool.memset(Yd[g][:, :, :, :], 0.0).then_inc(cleared, 1)
                pool.wait_ge(con_in, 48)
                pool.wait_ge(cleared, N_CLEARED)

                def chunk(u, m, c, at, ctx):
                    n = c + 1
                    pool.wait_ge(grec_in[u], 96 * m)
                    for g in range(G):
                        pool.wait_ge(absd[g], c)
                        b = grc[u][:, g, :, (2 + g) * C:(3 + g) * C]
                        for l in range(LEVELS):
                            h = 1 << l
                            m_at = h - 1 if g == 0 else h
                            bl = b.rearrange("p j (s w) -> p j s w", w=2 * h)
                            out = Dd[g][:, l, :, :].rearrange("p j (s w) -> p j s w", w=2 * h)
                            pool.tensor_tensor(out, bl, bl[:, :, :, m_at:m_at + 1].to_broadcast([P, GN, C // (2 * h), 2 * h]), ALU.subtract)
                        end = C - 1 if g == 0 else 0
                        pool.tensor_tensor(Dd[g][:, LEVELS + 1, :, :], b, b[:, :, end:end + 1].to_broadcast([P, GN, C]), ALU.subtract).then_inc(diffs[g], 1)
                    for g in range(G):
                        pool.wait_ge(go_mm[g], c)
                        for q, out in ((0, qo), (1, ko)):
                            src = grc[u][:, g, :, q * C:(q + 1) * C].unsqueeze(2).to_broadcast([P, GN, 2, C])
                            last = pool.tensor_tensor(out[g][:, :, :, :], src, own_of(g), ALU.mult)
                        last.then_inc(owned[g], 1)
                    for g in range(G):
                        lt = LR[g][:, :, 0, :, :].rearrange("p j h t -> p j (h t)")
                        pool.wait_ge(lr_done[g], n)
                        pool.tensor_tensor(Ui[g][:, :, :], lt, mT0[g].unsqueeze(1).to_broadcast([P, UN, P]), ALU.mult).then_inc(u_mask[g], 1)
                        pool.wait_ge(u_mask[g], n)
                        pool.tensor_tensor(Ui[g][:, :, :], Ui[g][:, :, :], eye128.unsqueeze(1).to_broadcast([P, UN, P]), ALU.add).then_inc(u0_done[g], 1)
                    for g in range(G):
                        pool.wait_ge(owned[g], n)
                        pool.wait_ge(expd[g], n)
                        for src, slot, out in ((qo, LEVELS, qe), (ko, LEVELS + 1, kh)):
                            last = pool.tensor_tensor(out[g][:, :, :, :], src[g][:, :, :, :], F[g][:, slot, :, :].unsqueeze(2).to_broadcast([P, GN, 2, C]), ALU.mult)
                        last.then_inc(qk_bd[g], 1)
                        q = grc[u][:, g, :, 0:C].unsqueeze(1).to_broadcast([P, LEVELS, GN, C])
                        pool.tensor_tensor(QF[g][:, :, :, :], q, F[g][:, 0:LEVELS, :, :], ALU.mult).then_inc(qf_done[g], 1)
                    for g in range(G):
                        pool.wait_ge(att_sum[g], n)
                        pool.tensor_tensor(ad[g][:, :, :, :], att[g][:, :, :].unsqueeze(2).to_broadcast([P, GN, 2, C]), own_of(g), ALU.mult).then_inc(att_bd[g], 1)
                both(pool, chunk, nothing)

            @block.scalar
            def _(act):
                act.wait_ge(cleared, N_CLEARED)

                def chunk(u, m, c, at, ctx):
                    n = c + 1
                    for g in range(G):
                        act.wait_ge(grec_in[u], 96 * m)
                        act.wait_ge(absd[g], c)
                        act.activation(Dd[g][:, LEVELS, :, :], grc[u][:, g, :, (2 + g) * C:(3 + g) * C], ACT.Copy).then_inc(slot6[g], 1)
                        act.wait_ge(slot6[g], n)
                        act.wait_ge(diffs[g], n)
                        act.wait_ge(qf_done[g], c)
                        act.wait_ge(kf_done[g], c)
                        act.wait_ge(gs_done[g], c)
                        act.activation(F[g][:, :, :, :], Dd[g][:, :, :, :], ACT.Abs).then_inc(absd[g], 1)
                        act.wait_ge(absd[g], n)
                        act.activation(F[g][:, :, :, :], F[g][:, :, :, :], ACT.Exp, scale=-1.0 / 16.0).then_inc(expd[g], 1)
                    for g in range(G):
                        act.wait_ge(mm_v[g], n)
                        act.copy(Vs[g][:, :, :], v3(pV[g][:, 0:UN * C])).then_inc(vs_done[g], 1)
                        act.wait_ge(mm_d[g], n)
                        act.copy(BT[g][:, :, :], v3(pD[:, 0:UN * P])).then_inc(bt_done[g], 1)
                        act.wait_ge(mm_e[g], n)
                        act.copy(KT[g][:, :, :], v3(pE[:, 0:UN * P])).then_inc(kt_done[g], 1)
                    for l in range(1, NL + 1):
                        for g in range(G):
                            act.wait_ge(ys_done[g], NL * c + l)
                            for h in range(2):
                                p = slice(64 * h, 64 * h + 64)
                                last = act.copy(Yd[g][p, :, h, :], Ys[g][p, :, :])
                            last.then_inc(yd_done[g], 1)
                        for g in range(G):
                            if l == KT_AT[g]:
                                act.wait_ge(kT_mm[g], n)
                                act.copy(kT[g][:, :, :], g2[g][:, 0:GN * P].rearrange("p (j k) -> p j k", j=GN)).then_inc(kT_done[g], 1)
                    for g in range(G):
                        act.wait_ge(x_mm[g], n)
                        act.copy(Xs[g][:, :, :], v3(pX[g][:, 0:UN * C])).then_inc(x_done[g], 1)
                    for g in range(G):
                        act.wait_ge(go_mm[g], n)
                        act.wait_ge(go_out[g][u], 32 * (m - 1))
                        act.copy(gOs[g][u][:, :, :], g2[g][:, 0:GN * GLA_DV].rearrange("p (j x) -> p j x", j=GN)).then_inc(go_done[g], 1)
                    for g in range(G):
                        act.wait_ge(o_mm[g], n)
                        act.wait_ge(o_out[g][u], 32 * (m - 1))
                        act.copy(Os[g][u][:, :, :], v3(pX[g][:, 0:UN * C])).then_inc(o_done[g], 1)
                both(act, chunk, nothing)

            @block.tensor
            def _(pe):
                pe.wait_ge(con_in, 48)
                pe.wait_ge(state0, 2 * G)

                def keys_turned(g, u, n):
                    pe.wait_ge(qk_bd[g], n)
                    pe.wait_ge(kr_done[1] if g == 0 else kt_done[1], n)
                    for j in range(GN):
                        mm = pe.transpose(cols(g2[g], j, P), flat(kh[g][:, j, :, :]), eye128)
                    mm.then_inc(kT_mm[g], 1)

                def attention(g, u, n):
                    pe.wait_ge(kf_done[g], n)
                    pe.wait_ge(qf_done[g], n)
                    pe.wait_ge(lr_done[1] if g == 0 else bt_done[1], n)
                    for l in range(NA):
                        if l == CA:
                            pe.wait_ge(kT_done[g], n)
                        for j in range(GN):
                            ps = g1[g] if l < CA else g2[g]
                            x = (l % CA * GN + j) * C
                            if l < LEVELS:
                                mm = pe.matmul(ps[:, x:x + C], flat(KF[g][:, j, l, :, :]), QF[g][:, l, j, :], start=True, stop=True)
                            else:
                                mm = pe.matmul(ps[:, x:x + C], flat(ko[g][:, j, :, :]), grc[u][:, g, j, 0:C], start=True, stop=True)
                        if l in (CA - 1, NA - 1):
                            mm.then_inc((att_a if l < CA else att_b)[g], 1)

                def gla_output(g, u, c):
                    pe.wait_ge(kT_done[g], c + 1)
                    pe.wait_ge(masked[g], c + 1)
                    pe.wait_ge(gs_done[g], c)
                    for j in range(GN):
                        pe.matmul(cols(g1[g], j, GLA_DV), kT[g][:, j, :], gv[u][:, g, j, :], start=True, stop=True)
                    pe.wait_ge(att_bd[g], c + 1)
                    for j in range(GN):
                        out = cols(g2[g], j, GLA_DV)
                        pe.matmul(out, flat(qe[g][:, j, :, :]), gS[g][:, j, :], start=True, stop=False)
                        mm = pe.matmul(out, flat(ad[g][:, j, :, :]), gv[u][:, g, j, :], start=False, stop=True)
                    mm.then_inc(go_mm[g], 1)

                def chunk(u, m, c, at, ctx):
                    n = c + 1
                    pe.wait_ge(rec_in[u], 16 * 6 * m)
                    for g in range(G):
                        js = range(UN * g, UN * (g + 1))

                        def leaves(by_last_chunk, by_group_0):
                            if g == 0:
                                pe.wait_ge(by_last_chunk, c)
                            else:
                                pe.wait_ge(by_group_0, n)
                        leaves(gs_done[0], lr_done[0])
                        for x, j in enumerate(js):
                            mm = pe.matmul(cols(pA, x, P), q_bd(u, j, 2), plain[u][:, j, 0:P], start=True, stop=True)
                        mm.then_inc(mm_a[g], 1)
                        leaves(o_done[1], t_mask[0])
                        for x, j in enumerate(js):
                            mm = pe.matmul(cols(pC, x, C), q_bd(u, j, 0), plain[u][:, j, P:3 * C], start=True, stop=True)
                        mm.then_inc(mm_c[g], 1)
                        leaves(go_done[0], kr_done[0])
                        for x, j in enumerate(js):
                            mm = pe.matmul(cols(pB, x, P), q_bd(u, j, 3), plain[u][:, j, 0:P], start=True, stop=True)
                        mm.then_inc(mm_b[g], 1)
                        pe.wait_ge(s_sum[g], c)
                        for x, j in enumerate(js):
                            mm = pe.matmul(cols(pV[g], x, C), q_bd(u, j, 4), eye, start=True, stop=True)
                        mm.then_inc(mm_v[g], 1)
                        leaves(gs_done[1], bt_done[0])
                        for x, j in enumerate(js):
                            mm = pe.transpose(cols(pD, x, P), q_bd(u, j, 2), eye128)
                        mm.then_inc(mm_d[g], 1)
                        leaves(go_done[1], kt_done[0])
                        for x, j in enumerate(js):
                            mm = pe.transpose(cols(pE, x, P), q_bd(u, j, 3), eye128)
                        mm.then_inc(mm_e[g], 1)
                    for l in range(1, NL + 1):
                        for g in range(G):
                            if l == 1:
                                pe.wait_ge(o_done[g], c)
                                pe.wait_ge(lr_done[g], n)
                                pe.wait_ge(t0_done[g], n)
                            else:
                                pe.wait_ge(t_step[g], (NL - 1) * c + l - 1)
                            for x in range(UN):
                                mm = pe.matmul(cols(pY[g], x, C), flat(LR[g][:, x, 0, :, :]), Ti[g][:, x, :], start=True, stop=True)
                            mm.then_inc(y_mm[g], 1)
                        for g in range(G):
                            if l == KT_AT[g]:
                                keys_turned(g, u, n)
                        for g in range(G):
                            if l == ATT_AT[g]:
                                attention(g, u, n)
                        if l == NL:
                            gla_output(0, u, c)
                        for g in range(G):
                            pe.wait_ge(ys_done[g], NL * c + l)
                            if l == 1:
                                pe.wait_ge(u0_done[g], n)
                            pe.wait_ge(u_step[g], NL * c + l - 1)
                            if l < NL:
                                for x in range(UN):
                                    mm = pe.matmul(cols(pY[g], x, C), Ui[g][:, x, :], Ys[g][:, x, :], start=True, stop=True)
                                mm.then_inc(ty_mm[g], 1)
                            if l == 1:
                                pe.wait_ge(vs_done[g], n)
                            pe.wait_ge(yd_done[g], NL * c + l)
                            for x in range(UN):
                                mm = pe.matmul(cols(pYU[g], x, P), flat(Yd[g][:, x, :, :]), Ui[g][:, x, :], start=True, stop=True)
                            mm.then_inc(yu_mm[g], 1)
                    for g in range(G):
                        for e in (vs_done[g], kr_done[g], lr_done[1], kr_done[1]):
                            pe.wait_ge(e, n)
                        pe.wait_ge(s_done[g], c)
                        for x in range(UN):
                            pe.matmul(cols(pX[g], x, C), q_bd(u, UN * g + x, 0), S[g][:, x, :], start=True, stop=False)
                            mm = pe.matmul(cols(pX[g], x, C), flat(KR[g][:, x, 0, :, :]), Vs[g][:, x, :], start=False, stop=True)
                        mm.then_inc(x_mm[g], 1)
                    gla_output(1, u, c)
                    for g in range(G):
                        pe.wait_ge(x_done[g], n)
                        pe.wait_ge(u_step[g], NL * n)
                        for x in range(UN):
                            mm = pe.matmul(cols(pX[g], UN + x, C), Ui[g][:, x, :], Xs[g][:, x, :], start=True, stop=True)
                        mm.then_inc(sa_mm[g], 1)
                    for g in range(G):
                        for e in (bt_done[1], kt_done[1], bt_done[g], kt_done[g], sa_done[g]):
                            pe.wait_ge(e, n)
                        for x in range(UN):
                            pe.matmul(cols(pX[g], x, C), q_bd(u, UN * g + x, 1), S[g][:, x, :], start=True, stop=False)
                            pe.matmul(cols(pX[g], x, C), flat(LR[g][:, x, 1, :, :]), SAs[g][:, x, :], start=False, stop=False)
                            mm = pe.matmul(cols(pX[g], x, C), flat(KR[g][:, x, 1, :, :]), Vs[g][:, x, :], start=False, stop=True)
                        mm.then_inc(o_mm[g], 1)
                        for x in range(UN):
                            pe.matmul(cols(pS[g], x, C), BT[g][:, x, :], SAs[g][:, x, :], start=True, stop=False)
                            mm = pe.matmul(cols(pS[g], x, C), KT[g][:, x, :], Vs[g][:, x, :], start=False, stop=True)
                        mm.then_inc(s_mm[g], 1)

                def swap():
                    pe.wait_ge(sx_ready, 1)
                    for g in range(G):
                        pe.wait_ge(gs_done[g], NCH_CTX)
                    for j in range(G * UN):
                        mm = pe.matmul(cols(pA, j, C), flat(SX[:, j, :, :]), eye, start=True, stop=True)
                    mm.then_inc(sx_mm, 1)
                    pe.wait_ge(sx_in, 16 * 4)
                    for j in range(G * UN):
                        mm = pe.matmul(cols(pA, j, C), flat(SX[:, j, :, :]), eye, start=True, stop=True)
                    mm.then_inc(sx_mm, 1)
                    pe.wait_ge(imported, 1)
                    pe.wait_ge(gstate_in, 64)
                both(pe, chunk, swap)

            @block.vector
            def _(dve):
                for g in range(G):
                    dve.memset(S[g][:, :, :], 0.0).then_inc(state0, 1)
                    dve.memset(gS[g][:, :, :], 0.0).then_inc(state0, 1)
                dve.wait_ge(con_in, 48)
                dve.wait_ge(cleared, N_CLEARED)

                def keys_decayed(g, c):
                    dve.wait_ge(owned[g], c + 1)
                    dve.wait_ge(expd[g], c + 1)
                    dve.wait_ge(att_b[g], c)
                    for j in range(GN):
                        last = dve.tensor_tensor(KF[g][:, j, :, :, :], ko[g][:, j, :, :].unsqueeze(1).to_broadcast([P, LEVELS, 2, C]),
                                                 F[g][:, 0:LEVELS, j, :].unsqueeze(2).to_broadcast([P, LEVELS, 2, C]), ALU.mult)
                    last.then_inc(kf_done[g], 1)

                def attention_summed(g, n):
                    dve.wait_ge(att_a[g], n)
                    dve.tensor_tensor(AM[g][:, 0:CA, :, :], g1[g][:, 0:CA * GN * C].rearrange("p (l j t) -> p l j t", l=CA, j=GN),
                                      gmask[g][:, 0:CA, :].unsqueeze(2).to_broadcast([P, CA, GN, C]), ALU.mult)
                    dve.wait_ge(att_b[g], n)
                    dve.tensor_tensor(AM[g][:, CA:NA, :, :], g2[g][:, 0:(NA - CA) * GN * C].rearrange("p (l j t) -> p l j t", l=NA - CA, j=GN),
                                      gmask[g][:, CA:NA, :].unsqueeze(2).to_broadcast([P, NA - CA, GN, C]), ALU.mult).then_inc(masked[g], 1)
                    dve.wait_ge(masked[g], n)
                    dve.reduce_sum(att[g][:, :, :].rearrange("p j t -> p (j t)"), AM[g][:, :, :, :].rearrange("p l j t -> p (j t) l"), AX.X).then_inc(att_sum[g], 1)

                def gla_state(g, n):
                    dve.wait_ge(go_mm[g], n)
                    end = C - 1 if g == 0 else 0
                    for j in range(GN):
                        last = dve.scalar_tensor_tensor(gS[g][:, j, :], gS[g][:, j, :], F[g][:, LEVELS, j, end:end + 1],
                                                        cols(g1[g], j, GLA_DV), ALU.mult, ALU.add)
                    last.then_inc(gs_done[g], 1)

                def chunk(u, m, c, at, ctx):
                    n = c + 1
                    for g in range(G):
                        dve.wait_ge(mm_a[g], n)
                        for h in range(2):
                            p = slice(64 * h, 64 * h + 64)
                            m_b = mask2[g][p].unsqueeze(1).to_broadcast([64, UN, 2, C])
                            last = dve.tensor_tensor(LR[g][p, :, :, h, :], pA[p, 0:UN * P].rearrange("p (j q t) -> p j q t", j=UN, q=2), m_b, ALU.mult)
                        last.then_inc(lr_done[g], 1)
                        dve.wait_ge(mm_c[g], n)
                        dve.tensor_tensor(Ti[g][:, :, :], v3(pC[:, 0:UN * C]), m_lev[g][:, 0:1, :].to_broadcast([P, UN, C]), ALU.mult).then_inc(t_mask[g], 1)
                        dve.wait_ge(t_mask[g], n)
                        dve.tensor_tensor(Ti[g][:, :, :], Ti[g][:, :, :], eye.unsqueeze(1).to_broadcast([P, UN, C]), ALU.add).then_inc(t0_done[g], 1)
                        dve.wait_ge(mm_b[g], n)
                        for h in range(2):
                            p = slice(64 * h, 64 * h + 64)
                            m_b = mask2[g][p].unsqueeze(1).to_broadcast([64, UN, 2, C])
                            last = dve.tensor_tensor(KR[g][p, :, :, h, :], pB[p, 0:UN * P].rearrange("p (j q t) -> p j q t", j=UN, q=2), m_b, ALU.mult)
                        last.then_inc(kr_done[g], 1)
                    for l in range(1, NL + 1):
                        for g in range(G):
                            dve.wait_ge(y_mm[g], NL * c + l)
                            dve.wait_ge(yd_done[g], NL * c + l - 1)
                            dve.tensor_tensor(Ys[g][:, :, :], v3(pY[g][:, 0:UN * C]), m_lev[g][:, l:l + 1, :].to_broadcast([P, UN, C]), ALU.mult).then_inc(ys_done[g], 1)
                        for g in range(G):
                            if l == KF_AT[g]:
                                keys_decayed(g, c)
                            if l == SUM_AT[g]:
                                attention_summed(g, n)
                        for g in range(G):
                            if l < NL:
                                dve.wait_ge(ty_mm[g], (NL - 1) * c + l)
                                dve.tensor_tensor(Ti[g][:, :, :], v3(pY[g][:, 0:UN * C]), Ti[g][:, :, :], ALU.add).then_inc(t_step[g], 1)
                            dve.wait_ge(yu_mm[g], NL * c + l)
                            dve.tensor_tensor(Ui[g][:, :, :], v3(pYU[g][:, 0:UN * P]), Ui[g][:, :, :], ALU.add).then_inc(u_step[g], 1)
                    for g in range(G):
                        dve.wait_ge(sa_mm[g], n)
                        dve.tensor_copy(SAs[g][:, :, :], v3(pX[g][:, UN * C:2 * UN * C])).then_inc(sa_done[g], 1)
                    for g in range(G):
                        gla_state(g, n)
                    for g in range(G):
                        dve.wait_ge(s_mm[g], n)
                        dve.tensor_tensor(Sn[g][:, :, :], v3(pS[g][:, 0:UN * C]), S[g][:, :, :], ALU.add).then_inc(s_sum[g], 1)
                        dve.wait_ge(con_in, 48)
                        dve.wait_ge(s_sum[g], n)
                        dve.tensor_tensor(S[g][:, :, :], Sn[g][:, :, :], total[:, g, :, bass.ds(at[g], 1)].to_broadcast([P, UN, C]), ALU.mult).then_inc(s_done[g], 1)

                def swap():
                    dve.wait_ge(cleared, N_CLEARED)
                    for g in range(G):
                        dve.wait_ge(s_done[g], NCH_CTX)
                        for h in range(2):
                            last = dve.tensor_copy(SX[64 * h:64 * h + 64, UN * g:UN * (g + 1), h, :], S[g][64 * h:64 * h + 64, :, :])
                    last.then_inc(sx_ready, 1)
                    dve.wait_ge(sx_mm, 1)
                    for g in range(G):
                        last = dve.tensor_copy(Xs[g][:, :, :], v3(pA[:, UN * C * g:UN * C * (g + 1)]))
                    last.then_inc(sx_out, 1)
                    dve.wait_ge(sx_mm, 2)
                    for g in range(G):
                        last = dve.tensor_copy(S[g][:, :, :], v3(pA[:, UN * C * g:UN * C * (g + 1)]))
                    last.then_inc(imported, 1)
                    dve.wait_ge(gstate_in, 64)
                both(dve, chunk, swap)


def stage_post(nc, rw_o, bonus, gate, ln_w, ln_b, gla_o, proj, norm_w, ident_d, mixT):
    UN = D_RW // P
    GN_EPS = 64e-5
    GATE0 = GLA0 + 2 * D_GLA_K + D_GLA
    assert D_GLA == D_RW
    with Stage(nc, "post") as st:
        ident, rw_par, gl_par = st.sb("ident", [P, P]), st.sb("rw_par", [P, 2, UN]), st.sb("gl_par", [P, UN])
        rw_of, rw_ob, rw_cen, rw_sq, gl_of, gl_ob, gl_sq = ([st.sb(f"{x}{u}", [P, D_RW]) for u in range(2)] for x in (
            "rw_of", "rw_ob", "rw_cen", "rw_sq", "gl_of", "gl_ob", "gl_sq"))
        rw_bo, rw_ga, rw_mix, gl_ga, gl_mix = ([st.sb(f"{x}{u}", [P, UN, P]) for u in range(2)] for x in (
            "rw_bo", "rw_ga", "rw_mix", "gl_ga", "gl_mix"))
        rw_stat = [st.sb(f"rw_stat{u}", [P, 4, RW_HEADS]) for u in range(2)]
        gl_stat = [st.sb(f"gl_stat{u}", [P, 4, GLA_HEADS]) for u in range(2)]
        rw_ps, gl_ps = [st.ps(f"rw_t{u}") for u in range(2)], [st.ps(f"gl_t{u}") for u in range(2)]
        par_in, rw_gates_in, gl_gates_in = st.sem("par_in"), st.sem2("rw_gates_in"), st.sem2("gl_gates_in")
        N_PAR = 16 * (1 + 3 * UN)
        (rw_in, rw_added, rw_mean, rw_centred, rw_squared, rw_var, rw_root, rw_rstd, rw_normed, rw_turned, rw_affine, rw_bonused,
         rw_mixed, rw_stored) = (st.sem2("rw_" + n) for n in (
            "in", "added", "mean", "centred", "squared", "var", "root", "rstd", "normed", "turned", "affine", "bonused",
            "mixed", "stored"))
        gl_in, gl_added, gl_squared, gl_silud, gl_var, gl_root, gl_rstd, gl_normed, gl_turned, gl_mixed, gl_stored = (
            st.sem2("gl_" + n) for n in ("in", "added", "squared", "silud", "var", "root", "rstd", "normed", "turned", "mixed", "stored"))

        def rw_heads(ap):
            return ap.rearrange("p (h v) -> p h v", v=RW_HD)

        def gl_heads(ap):
            return ap.rearrange("p (h v) -> p h v", v=GLA_DV)

        def rows(tile):
            return bass.ds(tile * P, P)

        def chans(t, tile):
            return t[:, rows(tile)].rearrange("(j p) t -> p j t", p=P)

        with st.block() as block:
            @block.sync
            def _(sp):
                sp.dma_start(ident[:, :], ident_d).then_inc(par_in, 16)
                for j in range(UN):
                    ch = slice(j * P, (j + 1) * P)
                    sp.dma_start(rw_par[:, 0, j:j + 1], ln_w[0, ch].unsqueeze(1)).then_inc(par_in, 16)
                    sp.dma_start(rw_par[:, 1, j:j + 1], ln_b[0, ch].unsqueeze(1)).then_inc(par_in, 16)
                    sp.dma_start(gl_par[:, j:j + 1], norm_w[0].rearrange("h v -> (h v)")[ch].unsqueeze(1)).then_inc(par_in, 16)

                def load(u, n, tile, seg):
                    sp.wait_ge(rw_centred[u], n - 1)
                    sp.dma_start(rw_of[u][:, :], rw_o[0, rows(tile), :]).then_inc(rw_in[u], 16)
                    sp.dma_start(rw_ob[u][:, :], rw_o[1, rows(tile), :]).then_inc(rw_in[u], 16)
                    sp.wait_ge(gl_turned[u], n - 1)
                    for half in range(2):
                        p = slice(64 * half, 64 * half + 64)
                        sp.dma_start(gl_of[u][p, :], grid_rows(gla_o[0], tile, seg, half)).then_inc(gl_in[u], 16)
                        sp.dma_start(gl_ob[u][p, :], grid_rows(gla_o[1], tile, seg, half)).then_inc(gl_in[u], 16)
                    sp.wait_ge(par_in, N_PAR)
                    sp.wait_ge(rw_mixed[u], n - 1)
                    sp.dma_start(rw_bo[u][:, :, :], chans(bonus, tile)).then_inc(rw_gates_in[u], 16)
                    sp.dma_start(rw_ga[u][:, :, :], chans(gate, tile)).then_inc(rw_gates_in[u], 16)
                    sp.wait_ge(gl_mixed[u], n - 1)
                    sp.dma_start(gl_ga[u][:, :, :], chans(proj[GATE0:GATE0 + D_GLA], tile)).then_inc(gl_gates_in[u], 16)
                staged(sp, load)

            @block.gpsimd
            def _(pool):
                def store(u, n, tile, seg):
                    pool.wait_ge(par_in, N_PAR)
                    pool.wait_ge(rw_mixed[u], n)
                    pool.dma_start(chans(mixT[D_LRU:D_LRU + D_RW], tile), rw_mix[u][:, :, :]).then_inc(rw_stored[u], 16)
                    pool.wait_ge(par_in, N_PAR)
                    pool.wait_ge(gl_mixed[u], n)
                    pool.dma_start(chans(mixT[D_LRU + D_RW:D], tile), gl_mix[u][:, :, :]).then_inc(gl_stored[u], 16)
                staged(pool, store)
                for u in range(2):
                    pool.wait_ge(rw_stored[u], 16 * (9 - u))
                    pool.wait_ge(gl_stored[u], 16 * (9 - u))

            @block.scalar
            def _(act):
                def body(u, n, tile, seg):
                    act.wait_ge(rw_centred[u], n)
                    act.activation(rw_sq[u][:, :], rw_cen[u][:, :], ACT.Square).then_inc(rw_squared[u], 1)
                    act.wait_ge(gl_added[u], n)
                    act.activation(gl_sq[u][:, :], gl_of[u][:, :], ACT.Square).then_inc(gl_squared[u], 1)
                    act.wait_ge(rw_var[u], 2 * n)
                    act.activation(rw_stat[u][:, 2, :], rw_stat[u][:, 1, :], ACT.Sqrt).then_inc(rw_root[u], 1)
                    act.wait_ge(gl_var[u], 2 * n)
                    act.activation(gl_stat[u][:, 2, :], gl_stat[u][:, 1, :], ACT.Sqrt).then_inc(gl_root[u], 1)
                    act.wait_ge(gl_gates_in[u], 16 * n)
                    act.activation(gl_ga[u][:, :, :], gl_ga[u][:, :, :], ACT.Silu).then_inc(gl_silud[u], 1)
                staged(act, body)

            @block.tensor
            def _(pe):
                pe.wait_ge(par_in, N_PAR)

                def body(u, n, tile, seg):
                    pe.wait_ge(rw_normed[u], n)
                    pe.wait_ge(rw_affine[u], n - 1)
                    for j in range(UN):
                        mm = pe.transpose(rw_ps[u][:, j * P:(j + 1) * P], rw_cen[u][:, j * P:(j + 1) * P], ident[:, :])
                    mm.then_inc(rw_turned[u], 1)
                    pe.wait_ge(gl_normed[u], n)
                    pe.wait_ge(gl_mixed[u], n - 1)
                    for j in range(UN):
                        mm = pe.transpose(gl_ps[u][:, j * P:(j + 1) * P], gl_of[u][:, j * P:(j + 1) * P], ident[:, :])
                    mm.then_inc(gl_turned[u], 1)
                staged(pe, body)

            @block.vector
            def _(dve):
                dve.wait_ge(par_in, N_PAR)

                def rw_spread(u, k):
                    return rw_stat[u][:, k, :].unsqueeze(2).to_broadcast([P, RW_HEADS, RW_HD])

                def body(u, n, tile, seg):
                    rs, gs = rw_stat[u], gl_stat[u]
                    dve.wait_ge(rw_in[u], 32 * n)
                    dve.tensor_tensor(rw_of[u][:, :], rw_of[u][:, :], rw_ob[u][:, :], ALU.add).then_inc(rw_added[u], 1)
                    dve.wait_ge(rw_added[u], n)
                    dve.reduce_sum(rs[:, 0, :], rw_heads(rw_of[u][:, :]), AX.X).then_inc(rw_mean[u], 1)
                    dve.wait_ge(rw_mean[u], 2 * n - 1)
                    dve.tensor_scalar(rs[:, 0, :], rs[:, 0, :], 1.0 / RW_HD, None, ALU.mult).then_inc(rw_mean[u], 1)
                    dve.wait_ge(rw_mean[u], 2 * n)
                    dve.tensor_tensor(rw_heads(rw_cen[u][:, :]), rw_heads(rw_of[u][:, :]), rw_spread(u, 0), ALU.subtract).then_inc(rw_centred[u], 1)
                    dve.wait_ge(gl_in[u], 64 * n)
                    dve.tensor_tensor(gl_of[u][:, :], gl_of[u][:, :], gl_ob[u][:, :], ALU.add).then_inc(gl_added[u], 1)
                    dve.wait_ge(rw_squared[u], n)
                    dve.reduce_sum(rs[:, 1, :], rw_heads(rw_sq[u][:, :]), AX.X).then_inc(rw_var[u], 1)
                    dve.wait_ge(rw_var[u], 2 * n - 1)
                    dve.tensor_scalar(rs[:, 1, :], rs[:, 1, :], 1.0 / RW_HD, GN_EPS, ALU.mult, ALU.add).then_inc(rw_var[u], 1)
                    dve.wait_ge(gl_squared[u], n)
                    dve.reduce_sum(gs[:, 1, :], gl_heads(gl_sq[u][:, :]), AX.X).then_inc(gl_var[u], 1)
                    dve.wait_ge(gl_var[u], 2 * n - 1)
                    dve.tensor_scalar(gs[:, 1, :], gs[:, 1, :], 1.0 / GLA_DV, EPS, ALU.mult, ALU.add).then_inc(gl_var[u], 1)
                    dve.wait_ge(rw_root[u], n)
                    dve.reciprocal(rs[:, 3, :], rs[:, 2, :]).then_inc(rw_rstd[u], 1)
                    dve.wait_ge(rw_rstd[u], n)
                    dve.tensor_tensor(rw_heads(rw_cen[u][:, :]), rw_heads(rw_cen[u][:, :]), rw_spread(u, 3), ALU.mult).then_inc(rw_normed[u], 1)
                    dve.wait_ge(gl_root[u], n)
                    dve.reciprocal(gs[:, 3, :], gs[:, 2, :]).then_inc(gl_rstd[u], 1)
                    dve.wait_ge(gl_rstd[u], n)
                    dve.tensor_tensor(gl_heads(gl_of[u][:, :]), gl_heads(gl_of[u][:, :]), gs[:, 3, :].unsqueeze(2).to_broadcast([P, GLA_HEADS, GLA_DV]), ALU.mult).then_inc(gl_normed[u], 1)

                def finish(u, n, tile, seg):
                    dve.wait_ge(rw_turned[u], n)
                    dve.wait_ge(rw_stored[u], 16 * (n - 1))
                    for j in range(UN):
                        last = dve.tensor_scalar(rw_mix[u][:, j, :], rw_ps[u][:, j * P:(j + 1) * P], rw_par[:, 0, j:j + 1], rw_par[:, 1, j:j + 1], ALU.mult, ALU.add)
                    last.then_inc(rw_affine[u], 1)
                    dve.wait_ge(rw_affine[u], n)
                    dve.wait_ge(rw_gates_in[u], 32 * n)
                    dve.tensor_tensor(rw_bo[u][:, :, :], rw_mix[u][:, :, :], rw_bo[u][:, :, :], ALU.add).then_inc(rw_bonused[u], 1)
                    dve.wait_ge(rw_bonused[u], n)
                    dve.tensor_tensor(rw_mix[u][:, :, :], rw_bo[u][:, :, :], rw_ga[u][:, :, :], ALU.mult).then_inc(rw_mixed[u], 1)
                    dve.wait_ge(gl_turned[u], n)
                    dve.wait_ge(gl_silud[u], n)
                    dve.wait_ge(gl_stored[u], 16 * (n - 1))
                    for j in range(UN):
                        last = dve.scalar_tensor_tensor(gl_mix[u][:, j, :], gl_ps[u][:, j * P:(j + 1) * P], gl_par[:, j:j + 1], gl_ga[u][:, j, :], ALU.mult, ALU.mult)
                    last.then_inc(gl_mixed[u], 1)
                staged(dve, body, finish)


def stage_mix_out(nc, x_prompt, x_sample, mixT, w_out, mods, norm2_g, w_router, ident_d, y, h2, probsT):
    PW = 2 * P
    PARTS = D // PW
    with Stage(nc, "out") as st:
        ident = st.sb("ident", [P, P])
        g_row, scale_row, shift_row = st.sb("g", [P, D]), st.sb("scale", [P, 2, D]), st.sb("shift", [P, 2, D])
        res_row = st.sb("res", [P, 2, D])
        w_raw = [st.sb(f"w_raw{b}", [P, KD, PW]) for b in range(2)]
        wo = [st.sb(f"wo{n}", [P, KD, D], F32R) for n in ("hi", "lo")]
        wr = st.sb("wr", [P, KD, N_EXP])
        x, y1, h = ([st.sb(f"{n}{u}", [P, D]) for u in range(2)] for n in ("x", "y1", "h"))
        m_raw = [st.sb(f"m_raw{u}", [P, KD, P]) for u in range(2)]
        m = [[st.sb(f"m{n}{u}", [P, KD, P], F32R) for n in ("hi", "lo")] for u in range(2)]
        hT = [st.sb(f"hT{u}", [P, KD, P]) for u in range(2)]
        ss = [st.sb(f"ss{u}", [P, 8]) for u in range(2)]
        pe_exp = [st.sb(f"e{u}", [P, N_EXP]) for u in range(2)]
        pT = st.sb("pT", [N_EXP, T])
        ps_o = [[st.ps(f"o{u}{half}") for half in range(2)] for u in range(2)]
        ps_t = [st.ps(f"t{b}") for b in range(2)]
        ps_l, ps_p = st.ps("l"), st.ps("p")
        rows_in, w_ld, rows_ready, w_high, w_low = (st.sem(n) for n in ("rows_in", "w_ld", "rows_ready", "w_high", "w_low"))
        w_raw_in = st.sem2("w_raw_in")
        names = ("mix_in", "x_in", "m_high", "m_low", "mixed", "res_done", "sumsq", "meansq", "root", "rstd", "normed", "h_ready", "turned",
                 "copied", "logits", "top", "ntop", "expd", "inv", "probs", "prob_mm", "prob_out", "y_out", "h_out")
        (mix_in, x_in, m_high, m_low, mixed, res_done, sumsq, meansq, root, rstd, normed, h_ready, turned,
         copied, logits, top, ntop, expd, inv, probs, prob_mm, prob_out, y_out, h_out) = (st.sem2(n) for n in names)
        left, stored = st.sem2("left"), st.sem("stored")

        with st.block() as block:
            @block.sync
            def _(sp):
                sp.dma_start(ident[:, :], ident_d).then_inc(w_ld, 16)
                sp.dma_start(wr[:, :, :], w_router[0].rearrange("(k p) n -> p k n", p=P)).then_inc(w_ld, 16)
                for q in range(PARTS):
                    if q >= 2:
                        sp.wait_ge(w_low, q - 1)
                    sp.dma_start(w_raw[q % 2][:, :, :], w_out[0].rearrange("(k p) n -> p k n", p=P)[:, :, q * PW:(q + 1) * PW]).then_inc(w_raw_in[q % 2], 16)
                load_modulated_norm(sp, rows_in, (g_row, scale_row, shift_row), mods, norm2_g, 4, 3)
                for v in range(2):
                    sp.dma_start(res_row[:, v, :], mods[v:v + 1, 2 * D:3 * D].to_broadcast([P, D])).then_inc(rows_in, 16)

                def load_mix(u, n, tile, seg):
                    sp.wait_ge(m_low[u], n - 1)
                    sp.dma_start(m_raw[u][:, :, :], mixT[:, bass.ds(tile * P, P)].rearrange("(k p) t -> p k t", p=P)).then_inc(mix_in[u], 16)

                def load_x(u, n, tile, seg):
                    sp.wait_ge(res_done[u], n - 1)
                    src = x_prompt[0] if seg == 0 else x_sample[0, bass.ds((tile - 1) * P, P), :]
                    sp.dma_start(x[u][:, :], src).then_inc(x_in[u], 16)
                staged(sp, load_mix, load_x)
                for u in range(2):
                    sp.wait_ge(prob_out[u], 9 - u)
                sp.dma_start(probsT, pT[:, :]).then_inc(stored, 16)
                sp.wait_ge(stored, 16)

            @block.gpsimd
            def _(pool):
                def store(u, n, tile, seg):
                    rows = bass.ds(tile * P, P)
                    pool.wait_ge(w_ld, 32)
                    pool.wait_ge(res_done[u], n)
                    pool.dma_start(y[rows, :], y1[u][:, :]).then_inc(y_out[u], 16)
                    pool.wait_ge(w_ld, 32)
                    pool.wait_ge(h_ready[u], n)
                    pool.dma_start(h2[rows, :], h[u][:, :]).then_inc(h_out[u], 16)
                staged(pool, store)
                for u in range(2):
                    pool.wait_ge(y_out[u], 16 * (9 - u))
                    pool.wait_ge(h_out[u], 16 * (9 - u))

            @block.tensor
            def _(pe):
                pe.wait_ge(w_ld, 32)
                pe.wait_ge(w_high, PARTS)
                pe.wait_ge(w_low, PARTS)

                def product(u, n, tile, seg):
                    pe.wait_ge(m_low[u], n)
                    for half in range(2):
                        cols = slice(half * BANK, (half + 1) * BANK)
                        pe.wait_ge(left[u], 2 * (n - 1))
                        for k in range(KD):
                            for i, (mp, wp) in enumerate(((1, 0), (0, 1), (0, 0))):
                                mm = pe.matmul(ps_o[u][half][:, :], m[u][mp][:, k, :], wo[wp][:, k, cols], start=k == 0 and i == 0, stop=k == KD - 1 and i == 2)
                        mm.then_inc(mixed[u], 1)

                def route(u, n, tile, seg):
                    pe.wait_ge(h_ready[u], n)
                    for half in range(2):
                        pe.wait_ge(copied[half], tile)
                        for k in range(4):
                            mm = pe.transpose(ps_t[half][:, k * P:(k + 1) * P], h[u][:, (4 * half + k) * P:(4 * half + k + 1) * P], ident[:, :])
                        mm.then_inc(turned[half], 1)
                    for half in range(2):
                        pe.wait_ge(copied[half], tile + 1)
                    pe.wait_ge(expd[1 - u], n - 1 + u)
                    for k in range(KD):
                        mm = pe.matmul(ps_l[:, 0:N_EXP], hT[u][:, k, :], wr[:, k, :], start=k == 0, stop=k == KD - 1)
                    mm.then_inc(logits[u], 1)

                def turn_probs(u, n, tile, seg):
                    pe.wait_ge(probs[u], n)
                    pe.wait_ge(prob_out[1 - u], n - 1 + u)
                    pe.transpose(ps_p[0:N_EXP, 0:P], pe_exp[u][:, :], ident[:, :]).then_inc(prob_mm[u], 1)

                staged(pe, other_engines, product, other_engines, route, turn_probs)

            @block.scalar
            def _(act):
                for q in range(PARTS):
                    act.wait_ge(w_raw_in[q % 2], 16 * (q // 2 + 1))
                    act.copy(wo[0][:, :, q * PW:(q + 1) * PW], w_raw[q % 2][:, :, :]).then_inc(w_high, 1)

                def split(u, n, tile, seg):
                    act.wait_ge(mix_in[u], 16 * n)
                    act.wait_ge(mixed[u], 2 * (n - 1))
                    act.copy(m[u][0][:, :, :], m_raw[u][:, :, :]).then_inc(m_high[u], 1)

                def norm(u, n, tile, seg):
                    act.wait_ge(res_done[u], n)
                    act.wait_ge(h_out[u], 16 * (n - 1))
                    act.wait_ge(turned[1], tile - seg)
                    act.activation(h[u][:, :], y1[u][:, :], ACT.Square, accum_out=ss[u][:, 0:1]).then_inc(sumsq[u], 1)
                    act.wait_ge(meansq[u], n)
                    act.activation(ss[u][:, 2:3], ss[u][:, 1:2], ACT.Sqrt).then_inc(root[u], 1)

                def softmax(u, n, tile, seg):
                    act.wait_ge(turned[1], tile + 1)
                    act.copy(hT[u][:, 4:8, :], ps_t[1][:, :].rearrange("p (k t) -> p k t", k=4)).then_inc(copied[1], 1)
                    act.wait_ge(ntop[u], n)
                    act.activation(pe_exp[u][:, :], ps_l[:, 0:N_EXP], ACT.Exp, bias=ss[u][:, 5:6], accum_out=ss[u][:, 6:7]).then_inc(expd[u], 1)
                staged(act, split, other_engines, norm, softmax)

            @block.vector
            def _(dve):
                for q in range(PARTS):
                    dve.wait_ge(w_high, q + 1)
                    cols = slice(q * PW, (q + 1) * PW)
                    dve.tensor_tensor(wo[1][:, :, cols], w_raw[q % 2][:, :, :], wo[0][:, :, cols], ALU.subtract).then_inc(w_low, 1)
                dve.wait_ge(rows_in, 7 * 16)
                for v in range(2):
                    dve.scalar_tensor_tensor(scale_row[:, v, :], scale_row[:, v, :], 1.0, g_row[:, :], ALU.add, ALU.mult).then_inc(rows_ready, 1)
                dve.wait_ge(rows_ready, 2)

                def split(u, n, tile, seg):
                    dve.wait_ge(m_high[u], n)
                    dve.tensor_tensor(m[u][1][:, :, :], m_raw[u][:, :, :], m[u][0][:, :, :], ALU.subtract).then_inc(m_low[u], 1)

                def norm(u, n, tile, seg):
                    dve.wait_ge(y_out[u], 16 * (n - 1))
                    dve.wait_ge(sumsq[u], n - 1)
                    for half in range(2):
                        cols = slice(half * BANK, (half + 1) * BANK)
                        dve.wait_ge(mixed[u], 2 * (n - 1) + half + 1)
                        dve.tensor_tensor(y1[u][:, cols], ps_o[u][half][:, :], res_row[:, seg, cols], ALU.mult).then_inc(left[u], 1)
                    dve.wait_ge(left[u], 2 * n)
                    dve.wait_ge(x_in[u], 16 * n)
                    dve.tensor_tensor(y1[u][:, :], y1[u][:, :], x[u][:, :], ALU.add).then_inc(res_done[u], 1)
                    dve.wait_ge(sumsq[u], n)
                    dve.tensor_scalar(ss[u][:, 1:2], ss[u][:, 0:1], 1.0 / D, EPS, ALU.mult, ALU.add).then_inc(meansq[u], 1)
                    dve.wait_ge(root[u], n)
                    dve.reciprocal(ss[u][:, 3:4], ss[u][:, 2:3]).then_inc(rstd[u], 1)
                    dve.wait_ge(rstd[u], n)
                    dve.scalar_tensor_tensor(h[u][:, :], y1[u][:, :], ss[u][:, 3:4], scale_row[:, seg, :], ALU.mult, ALU.mult).then_inc(normed[u], 1)
                    dve.wait_ge(normed[u], n)
                    dve.tensor_tensor(h[u][:, :], h[u][:, :], shift_row[:, seg, :], ALU.add).then_inc(h_ready[u], 1)

                def softmax(u, n, tile, seg):
                    dve.wait_ge(turned[0], tile + 1)
                    dve.tensor_copy(hT[u][:, 0:4, :], ps_t[0][:, :].rearrange("p (k t) -> p k t", k=4)).then_inc(copied[0], 1)
                    dve.wait_ge(logits[u], n)
                    dve.reduce_max(ss[u][:, 4:5], ps_l[:, 0:N_EXP], AX.X).then_inc(top[u], 1)
                    dve.wait_ge(top[u], n)
                    dve.tensor_scalar(ss[u][:, 5:6], ss[u][:, 4:5], -1.0, None, ALU.mult).then_inc(ntop[u], 1)
                    dve.wait_ge(expd[u], n)
                    dve.reciprocal(ss[u][:, 7:8], ss[u][:, 6:7]).then_inc(inv[u], 1)
                    dve.wait_ge(inv[u], n)
                    dve.tensor_scalar(pe_exp[u][:, :], pe_exp[u][:, :], ss[u][:, 7:8], None, ALU.mult).then_inc(probs[u], 1)

                def keep_probs(u, n, tile, seg):
                    dve.wait_ge(prob_mm[u], n)
                    dve.tensor_copy(pT[:, bass.ds(tile * P, P)], ps_p[0:N_EXP, 0:P]).then_inc(prob_out[u], 1)
                staged(dve, split, other_engines, norm, softmax, keep_probs)


def stage_route(nc, probsT, ident_d, slot_rows, slot_gates):
    N_SLOT = CAP_LAT + CAP_CTX
    with Stage(nc, "rte") as st:
        ident = st.sb("ident", [P, P])
        work = st.sb("work", [N_EXP, T])
        top8, idx8 = st.sb("top8", [N_EXP, 8]), st.sb("idx8", [N_EXP, 8], U32)
        gates, idx = st.sb("gates", [N_EXP, N_SLOT]), st.sb("idx", [N_EXP, N_SLOT], U32)
        rows_f = st.sb("rows_f", [N_EXP, N_SLOT])
        gT, rT = st.sb("gT", [P, 3, N_EXP]), st.sb("rT", [P, 3, N_EXP], U32)
        ps_g, ps_r = st.ps("g"), st.ps("r")
        ld, found, kept, rows_done, turned_g, turned_r, out_done, stored = (st.sem(n) for n in (
            "ld", "found", "kept", "rows_done", "turned_g", "turned_r", "out_done", "stored"))
        blocks = [(0, P), (P, P), (CAP_LAT, CAP_CTX)]
        with st.block() as block:
            @block.sync
            def _(sp):
                sp.dma_start(work[:, :], probsT).then_inc(ld, 16)
                sp.dma_start(ident[:, :], ident_d).then_inc(ld, 16)
                sp.wait_ge(out_done, 8)
                sp.dma_start(slot_rows, rT[:, :, :]).then_inc(stored, 16)
                sp.dma_start(slot_gates, gT[:, :, :]).then_inc(stored, 16)
                sp.wait_ge(stored, 32)

            @block.vector
            def _(dve):
                dve.memset(gT[:, 2, :], 0.0).then_inc(out_done, 1)
                dve.memset(rT[:, 2, :], 0).then_inc(out_done, 1)
                dve.wait_ge(out_done, 2)
                dve.wait_ge(ld, 32)

                def eight(tokens, slot, n):
                    dve.max(top8[:, :], tokens).then_inc(found, 1)
                    dve.wait_ge(found, 3 * n + 1)
                    dve.tensor_copy(gates[:, bass.ds(slot, 8)], top8[:, :]).then_inc(kept, 1)
                    dve.max_index(idx8[:, :], top8[:, :], tokens).then_inc(found, 1)
                    dve.match_replace(tokens, top8[:, :], tokens, -1.0).then_inc(found, 1)
                    dve.wait_ge(found, 3 * n + 3)
                    dve.tensor_copy(idx[:, bass.ds(slot, 8)], idx8[:, :]).then_inc(kept, 1)

                for n in range(CAP_CTX // 8):
                    eight(work[:, 0:T_CTX], CAP_LAT + 8 * n, n)
                with dve.Fori(0, CAP_LAT // 8) as i:
                    eight(work[:, T_CTX:T], 8 * i, i + CAP_CTX // 8)
                dve.wait_ge(kept, 2 * N_SLOT // 8)
                dve.tensor_scalar(rows_f[:, 0:CAP_LAT], idx[:, 0:CAP_LAT], float(T_CTX), None, ALU.add).then_inc(rows_done, 1)
                dve.tensor_copy(rows_f[:, CAP_LAT:], idx[:, CAP_LAT:]).then_inc(rows_done, 1)
                dve.wait_ge(turned_g, 1)
                for b, (s0, n) in enumerate(blocks):
                    dve.tensor_copy(gT[0:n, b, :], ps_g[0:n, b * N_EXP:(b + 1) * N_EXP]).then_inc(out_done, 1)
                dve.wait_ge(turned_r, 1)
                for b, (s0, n) in enumerate(blocks):
                    dve.tensor_copy(rT[0:n, b, :], ps_r[0:n, b * N_EXP:(b + 1) * N_EXP]).then_inc(out_done, 1)

            @block.tensor
            def _(pe):
                pe.wait_ge(ld, 32)
                pe.wait_ge(rows_done, 2)
                pe.wait_ge(kept, 2 * N_SLOT // 8)
                for src, ps, done in ((gates, ps_g, turned_g), (rows_f, ps_r, turned_r)):
                    for b, (s0, n) in enumerate(blocks):
                        mm = pe.transpose(ps[0:n, b * N_EXP:(b + 1) * N_EXP], src[:, s0:s0 + n], ident[0:N_EXP, 0:N_EXP])
                    mm.then_inc(done, 1)


def stage_experts(nc, h2, y, mods, slot_rows, slot_gates, w_gate, w_up, w_down, ident_d):
    blocks = [(0, P), (P, P), (CAP_LAT, CAP_CTX)]
    N_SLOT = CAP_LAT + CAP_CTX
    KE = D_EXP // P
    PW = 2 * P
    GU = 2 * (D_EXP // PW)
    PARTS = GU + D // PW
    RAW, RING = 3, 4
    assert PARTS % RAW == 0 and PARTS % RING == 0 and KD == KE
    with Stage(nc, "exp") as st:
        ident = st.sb("ident", [P, P])
        rows_all, gates_all = st.sb("rows_all", [P, 3, N_EXP], U32), st.sb("gates_all", [P, 3, N_EXP])
        res_row = st.sb("res", [P, 2, D])
        raw = [st.sb(f"raw{b}", [P, KD, PW]) for b in range(RAW)]
        w = [[st.sb(f"w{n}{b}", [P, KD, PW], F32R) for n in ("hi", "lo")] for b in range(RING)]
        xs, yo = st.sb("xs", [P, 3, D]), st.sb("yo", [P, 3, D])
        xT = [st.sb(f"xT{n}", [P, KD, N_SLOT], F32R) for n in ("hi", "lo")]
        hid = [st.sb(f"hid{n}", [P, KE, N_SLOT], F32R) for n in ("hi", "lo")]
        sil, act_in, yoT = (st.sb(n, [P, 2, N_SLOT]) for n in ("sil", "act_in", "yoT"))
        ps_g, ps_u, ps_o, ps_t = ([st.ps(f"{n}{b}") for b in range(2)] for n in ("g", "u", "o", "t"))
        par_in, raw_in = st.sem("par_in"), [st.sem(f"raw_in{b}") for b in range(RAW)]
        hi_done, lo_done, used = ([st.sem(f"{n}{b}") for b in range(RING)] for n in ("hi_done", "lo_done", "used"))
        gathered, turned, scattered = st.sem("gathered"), st.sem("turned"), st.sem("scattered")
        gate_mm, up_mm, silu_done, prod_done, hid_hi, hid_lo = (st.sem(n) for n in (
            "gate_mm", "up_mm", "silu_done", "prod_done", "hid_hi", "hid_lo"))
        x_hi, x_lo, down_mm, yt_done, back_mm, scaled = (st.sem2(n) for n in (
            "x_hi", "x_lo", "down_mm", "yt_done", "back_mm", "scaled"))

        def part_source(e, k):
            src, q = (w_down, k - GU) if k >= GU else ((w_gate, w_up)[k % 2], k // 2)
            return src[0, bass.ds(e, 1)].squeeze(0).rearrange("(k p) n -> p k n", p=P)[:, :, q * PW:(q + 1) * PW]

        def part_count(e, k, ring):
            return e * (PARTS // ring) + k // ring + 1

        def experts(eng, body):
            body(0, True)
            with eng.Fori(1, N_EXP - 1) as e:
                body(e, True)
            body(N_EXP - 1, False)

        with st.block() as block:
            @block.sync
            def _(sp):
                sp.dma_start(ident[:, :], ident_d).then_inc(par_in, 16)
                sp.dma_start(rows_all[:, :, :], slot_rows).then_inc(par_in, 16)
                sp.dma_start(gates_all[:, :, :], slot_gates).then_inc(par_in, 16)
                for v in range(2):
                    sp.dma_start(res_row[:, v, :], mods[v:v + 1, 5 * D:6 * D].to_broadcast([P, D])).then_inc(par_in, 16)

                def body(e, more):
                    for k in range(PARTS):
                        sp.wait_ge(lo_done[(k - RAW) % RING], part_count(e, k - RAW, RING))
                        sp.dma_start(raw[k % RAW][:, :, :], part_source(e, k)).then_inc(raw_in[k % RAW], 16)
                experts(sp, body)

            @block.gpsimd
            def _(pool):
                pool.wait_ge(par_in, 80)

                def gather(e):
                    for b, (s0, n) in enumerate(blocks):
                        pool.indirect_dma_start(out=xs[0:n, b, :], out_offset=None, in_=h2,
                                                in_offset=bass.IndirectOffsetOnAxis(ap=rows_all[0:n, b, e:e + 1], axis=0)).then_inc(gathered, 16)
                gather(0)
                for e in range(N_EXP):
                    if e + 1 < N_EXP:
                        pool.wait_ge(turned, KD * (e + 1))
                        gather(e + 1)
                    if e:
                        pool.wait_ge(scattered, 48 * e)
                    for u in range(2):
                        pool.wait_ge(scaled[u], KD // 2 * (e + 1))
                    for b, (s0, n) in enumerate(blocks):
                        pool.indirect_dma_start(out=y, out_offset=bass.IndirectOffsetOnAxis(ap=rows_all[0:n, b, e:e + 1], axis=0),
                                                in_=yo[0:n, b, :], in_offset=None, compute_op=ALU.add).then_inc(scattered, 16)
                pool.wait_ge(scattered, 48 * N_EXP)

            @block.tensor
            def _(pe):
                pe.wait_ge(par_in, 80)

                def product(ps, b, tile, x, expert=None):
                    for k in range(KD):
                        if expert is not None:
                            pe.wait_ge(hid_lo, KE * expert + k + 1)
                        for i, (wp, xp) in enumerate(((1, 0), (0, 1), (0, 0))):
                            mm = pe.matmul(ps[:, 0:N_SLOT], w[b][wp][:, k, tile * P:(tile + 1) * P], x[xp][:, k, :],
                                           start=k == 0 and i == 0, stop=k == KD - 1 and i == 2)
                    return mm

                def part_ready(e, k):
                    pe.wait_ge(hi_done[k % RING], part_count(e, k, RING))
                    pe.wait_ge(lo_done[k % RING], part_count(e, k, RING))

                def turn(e, k):
                    if k == 0:
                        pe.wait_ge(gathered, 48 * (e + 1))
                    pe.wait_ge(x_lo[k % 2], KD // 2 * e + k // 2)
                    for b, (s0, n) in enumerate(blocks):
                        mm = pe.transpose(ps_g[k % 2][:, s0:s0 + n], xs[0:n, b, k * P:(k + 1) * P], ident[0:n, 0:n])
                    mm.then_inc(turned, 1)

                def back(e, i):
                    pe.wait_ge(yt_done[i % 2], KD // 2 * e + i // 2 + 1)
                    pe.wait_ge(scaled[i % 2], KD // 2 * e + i // 2)
                    for b, (s0, n) in enumerate(blocks):
                        mm = pe.transpose(ps_t[i % 2][0:n, b * P:(b + 1) * P], yoT[:, i % 2, s0:s0 + n], ident[:, :])
                    mm.then_inc(back_mm[i % 2], 1)

                def body(e, more):
                    for u in range(2):
                        pe.wait_ge(x_lo[u], KD // 2 * (e + 1))
                    for q in range(GU // 2):
                        for s, (ps, done) in enumerate(((ps_g, gate_mm), (ps_u, up_mm))):
                            k = 2 * q + s
                            part_ready(e, k)
                            for tile in range(2):
                                f = 2 * q + tile
                                if s == 0:
                                    pe.wait_ge(silu_done, KE * e + f - (1 if f >= 2 else f))
                                else:
                                    pe.wait_ge(prod_done, KE * e + f - (1 if f >= 2 else f))
                                mm = product(ps[tile], k % RING, tile, xT)
                                if tile == 0:
                                    mm.then_inc(done, 1)
                                else:
                                    mm.then_inc(used[k % RING], 1)
                    for i in range(KD):
                        k, tile = GU + i // 2, i % 2
                        if tile == 0:
                            part_ready(e, k)
                        pe.wait_ge(yt_done[tile], KD // 2 * e + i // 2)
                        mm = product(ps_o[tile], k % RING, tile, hid, None if i else e)
                        mm.then_inc(used[k % RING] if tile else down_mm[0], 1)
                        if more:
                            turn(e + 1, i)
                        if i:
                            back(e, i - 1)
                    back(e, KD - 1)
                for k in range(KD):
                    turn(0, k)
                experts(pe, body)

            @block.scalar
            def _(act):
                def split(e, k):
                    act.wait_ge(raw_in[k % RAW], 16 * part_count(e, k, RAW))
                    act.wait_ge(used[k % RING], part_count(e, k, RING) - 1)
                    act.copy(w[k % RING][0][:, :, :], raw[k % RAW][:, :, :]).then_inc(hi_done[k % RING], 1)

                def x_high(e, k):
                    act.wait_ge(turned, KD * e + k + 1)
                    act.copy(xT[0][:, k, :], ps_g[k % 2][:, 0:N_SLOT]).then_inc(x_hi[k % 2], 1)

                def body(e, more):
                    for q in range(GU // 2):
                        for f in (2 * q, 2 * q + 1):
                            if f % 2:
                                act.wait_ge(used[2 * q % RING], part_count(e, 2 * q, RING))
                            else:
                                act.wait_ge(gate_mm, KE // 2 * e + q + 1)
                            act.wait_ge(prod_done, KE * e + f - (1 if f >= 2 else f))
                            act.activation(sil[:, f % 2, :], ps_g[f % 2][:, 0:N_SLOT], ACT.Silu).then_inc(silu_done, 1)
                        split(e, 2 * q + RING)
                        for f in (2 * q, 2 * q + 1):
                            act.wait_ge(prod_done, KE * e + f + 1)
                            if q == 0:
                                for u in range(2):
                                    act.wait_ge(yt_done[u], KD // 2 * e)
                            act.copy(hid[0][:, f, :], act_in[:, f % 2, :]).then_inc(hid_hi, 1)
                        split(e, 2 * q + 1 + RING)
                    for i in range(KD):
                        if i % 2:
                            act.wait_ge(used[(GU + i // 2) % RING], part_count(e, GU + i // 2, RING))
                        else:
                            act.wait_ge(down_mm[0], KD // 2 * e + i // 2 + 1)
                        act.wait_ge(back_mm[i % 2], KD // 2 * e + i // 2)
                        act.copy(yoT[:, i % 2, :], ps_o[i % 2][:, 0:N_SLOT]).then_inc(yt_done[i % 2], 1)
                        if more:
                            x_high(e + 1, i)
                            if i % 2:
                                split(e + 1, i // 2)
                for k in range(KD):
                    if k < RING:
                        split(0, k)
                    x_high(0, k)
                experts(act, body)

            @block.vector
            def _(dve):
                dve.wait_ge(par_in, 80)

                def split(e, k):
                    dve.wait_ge(hi_done[k % RING], part_count(e, k, RING))
                    dve.tensor_tensor(w[k % RING][1][:, :, :], raw[k % RAW][:, :, :], w[k % RING][0][:, :, :], ALU.subtract).then_inc(lo_done[k % RING], 1)

                def x_low(e, k):
                    dve.wait_ge(x_hi[k % 2], KD // 2 * e + k // 2 + 1)
                    dve.tensor_tensor(xT[1][:, k, :], ps_g[k % 2][:, 0:N_SLOT], xT[0][:, k, :], ALU.subtract).then_inc(x_lo[k % 2], 1)

                def scale(e, i):
                    cols = slice(i * P, (i + 1) * P)
                    dve.wait_ge(par_in, 80)
                    dve.wait_ge(back_mm[i % 2], KD // 2 * e + i // 2 + 1)
                    if i == 0:
                        dve.wait_ge(scattered, 48 * e)
                    for b, (s0, n) in enumerate(blocks):
                        last = dve.scalar_tensor_tensor(yo[0:n, b, cols], ps_t[i % 2][0:n, b * P:(b + 1) * P], gates_all[0:n, b, bass.ds(e, 1)],
                                                        res_row[0:n, 0 if b == 2 else 1, cols], ALU.mult, ALU.mult)
                    last.then_inc(scaled[i % 2], 1)

                def body(e, more):
                    for q in range(GU // 2):
                        split(e, 2 * q + RING)
                        for f in (2 * q, 2 * q + 1):
                            dve.wait_ge(silu_done, KE * e + f + 1)
                            if f % 2:
                                dve.wait_ge(used[(2 * q + 1) % RING], part_count(e, 2 * q + 1, RING))
                            else:
                                dve.wait_ge(up_mm, KE // 2 * e + q + 1)
                            dve.wait_ge(hid_lo, KE * e + f - (1 if f >= 2 else f))
                            dve.tensor_tensor(act_in[:, f % 2, :], ps_u[f % 2][:, 0:N_SLOT], sil[:, f % 2, :], ALU.mult).then_inc(prod_done, 1)
                        for f in (2 * q, 2 * q + 1):
                            dve.wait_ge(hid_hi, KE * e + f + 1)
                            dve.tensor_tensor(hid[1][:, f, :], act_in[:, f % 2, :], hid[0][:, f, :], ALU.subtract).then_inc(hid_lo, 1)
                        split(e, 2 * q + 1 + RING)
                    for i in range(KD):
                        if more:
                            x_low(e + 1, i)
                        if i:
                            scale(e, i - 1)
                        if more and i % 2:
                            split(e + 1, i // 2)
                    scale(e, KD - 1)
                for k in range(KD):
                    if k < RING:
                        split(0, k)
                    x_low(0, k)
                experts(dve, body)


def stage_final(nc, y, final_g, y_prompt, y_sample):
    with Stage(nc, "fin") as st:
        g_row = st.sb("g", [P, D])
        x, sq, out = ([st.sb(f"{n}{u}", [P, D]) for u in range(2)] for n in ("x", "sq", "o"))
        ss = [st.sb(f"ss{u}", [P, 4]) for u in range(2)]
        row_in = st.sem("row_in")
        x_in, sumsq, meansq, root, rstd, normed, stored = (st.sem2(n) for n in ("x_in", "sumsq", "meansq", "root", "rstd", "normed", "stored"))
        with st.block() as block:
            @block.sync
            def _(sp):
                sp.dma_start(g_row[:, :], final_g.unsqueeze(0).to_broadcast([P, D])).then_inc(row_in, 16)

                def load(u, n, tile, seg):
                    sp.wait_ge(normed[u], n - 1)
                    sp.dma_start(x[u][:, :], y[bass.ds(tile * P, P), :]).then_inc(x_in[u], 16)
                staged(sp, load)

            @block.gpsimd
            def _(pool):
                def store(u, n, tile, seg):
                    pool.wait_ge(row_in, 16)
                    pool.wait_ge(normed[u], n)
                    dst = y_prompt[0] if seg == 0 else y_sample[0, bass.ds((tile - 1) * P, P), :]
                    pool.dma_start(dst, out[u][:, :]).then_inc(stored[u], 16)
                staged(pool, store)
                for u in range(2):
                    pool.wait_ge(stored[u], 16 * (9 - u))

            @block.scalar
            def _(act):
                def body(u, n, tile, seg):
                    act.wait_ge(x_in[u], 16 * n)
                    act.activation(sq[u][:, :], x[u][:, :], ACT.Square, accum_out=ss[u][:, 0:1]).then_inc(sumsq[u], 1)
                    act.wait_ge(meansq[u], n)
                    act.activation(ss[u][:, 2:3], ss[u][:, 1:2], ACT.Sqrt).then_inc(root[u], 1)
                staged(act, body)

            @block.vector
            def _(dve):
                dve.wait_ge(row_in, 16)

                def body(u, n, tile, seg):
                    dve.wait_ge(sumsq[u], n)
                    dve.tensor_scalar(ss[u][:, 1:2], ss[u][:, 0:1], 1.0 / D, EPS, ALU.mult, ALU.add).then_inc(meansq[u], 1)
                    dve.wait_ge(root[u], n)
                    dve.reciprocal(ss[u][:, 3:4], ss[u][:, 2:3]).then_inc(rstd[u], 1)
                    dve.wait_ge(rstd[u], n)
                    dve.wait_ge(stored[u], 16 * (n - 1))
                    dve.scalar_tensor_tensor(out[u][:, :], x[u][:, :], ss[u][:, 3:4], g_row[:, :], ALU.mult, ALU.mult).then_inc(normed[u], 1)
                staged(dve, body)


def build_program(nc, a):
    def scratch(name, shape, dt=F32):
        return nc.dram_tensor(name, list(shape), dt, kind="Internal").ap()

    mods, proj, mixT = scratch("mods", (2, 6 * D)), scratch("proj", (N_IN, T)), scratch("mixT", (D, T))
    rec, gate, bonus = scratch("rec", (2, P, NCH, D_RW // P, REC)), scratch("gate", (D_RW, T)), scratch("bonus", (D_RW, T))
    decay = scratch("decay", (P, 2, D_RW // P, NCH))
    o_rw, o_gla = scratch("o_rw", (2, T, D_RW)), scratch("o_gla", (2, T, D_GLA))
    vt, grec = scratch("vt", (T, D_GLA)), scratch("grec", (GLA_HEADS // 2, P, NCH, GREC))
    y, h2, probsT = scratch("y", (T, D)), scratch("h2", (T, D)), scratch("probsT", (N_EXP, T))
    slot_rows, slot_gates = scratch("slot_rows", (P, 3, N_EXP), U32), scratch("slot_gates", (P, 3, N_EXP))

    stage_modulation(nc, a["c"], a["c_ctx"], a["w_ada"], a["b_ada"], mods)
    stage_project(nc, a["x_prompt"], a["x_sample"], a["norm1_g"], mods, a["w_in"], a["ident"], proj)
    stage_lru(nc, proj, *(a["lru_" + n] for n in ("conv_w", "conv_b", "wa", "ba", "wx", "bx", "lambda")), a["state_lru"], mixT, a["new_lru"],
              a["c"], a["c_ctx"], a["w_ada"], a["b_ada"], mods)
    stage_rwkv_prep(nc, proj, *(a["rw_" + n] for n in ("mu", "w0", "w2", "a0", "a2", "g2", "kk", "ka", "rk")), a["head_ones"], rec, decay, gate, bonus)
    stage_gla_turn(nc, proj, a["ident"], vt)
    stage_gla_prep(nc, proj, a["gla_wg2"], a["gla_bg"], grec)
    stage_scans(nc, rec, decay, a["rwkv_con"], a["state_rwkv"], a["new_rwkv"], o_rw,
                grec, vt, a["gla_con"], a["state_gla"], a["new_gla"], o_gla)
    stage_post(nc, o_rw, bonus, gate, a["rw_ln_w"], a["rw_ln_b"], o_gla, proj, a["gla_norm_w"], a["ident"], mixT)
    stage_mix_out(nc, a["x_prompt"], a["x_sample"], mixT, a["w_out"], mods, a["norm2_g"], a["w_router"], a["ident"], y, h2, probsT)
    stage_route(nc, probsT, a["ident"], slot_rows, slot_gates)
    stage_experts(nc, h2, y, mods, slot_rows, slot_gates, a["w_gate"], a["w_up"], a["w_down"], a["ident"])
    stage_final(nc, y, a["final_norm_g"], a["y_prompt"], a["y_sample"])


_OUTS = [("y_prompt", (1, T_CTX, D)), ("y_sample", (1, T_LAT, D)), ("new_lru", (1, 1, 2, D_LRU)),
         ("new_rwkv", (1, 1, 2, RW_HEADS, RW_HD, RW_HD)), ("new_gla", (1, 1, 2, GLA_HEADS, GLA_DK, GLA_DV))]


def kernel(**inputs):
    import concourse.bacc as _bacc
    from concourse.bass_utils import run_bass_kernel_spmd as _run

    nc = _bacc.Bacc("TRN2", target_bir_lowering=False, num_devices=1)
    constants = {"ident": np.eye(P, dtype=np.float32), "rwkv_con": rwkv_constants(), "gla_con": gla_constants(),
                 "head_ones": np.kron(np.eye(2), np.ones((RW_HD, RW_HD))).astype(np.float32)}
    arrays, aps = {}, {}
    for name, value in {**inputs, **constants}.items():
        value = np.ascontiguousarray(value)
        arrays[f"in_{name}"] = value
        aps[name] = nc.dram_tensor(f"in_{name}", value.shape, mybir.dt.from_np(value.dtype), kind="ExternalInput").ap()
    for name, shape in _OUTS:
        aps[name] = nc.dram_tensor(f"out_{name}", list(shape), F32, kind="ExternalOutput").ap()
    build_program(nc, aps)
    r = _run(nc, [arrays], core_ids=[0])
    return tuple(r.results[0][f"out_{name}"] for name, _ in _OUTS)
```
